# Optimizing a Trainium2 kernel written in Bass

```python
import math
import jax, jax.numpy as jnp
from jax import lax
import numpy as np

D_MODEL = 1024
BATCH = 1
SEQ = 256
DEPTH = 1

PLE_DIM = 256
EPS = 1e-6
SSD_HEADS = 16
SSD_HEAD_DIM = 64
SSD_INNER = SSD_HEADS * SSD_HEAD_DIM
SSD_GROUPS = 2
SSD_STATE = 64
SSD_CONV = 4
SSD_CHUNK = 128
SSD_CONV_CH = SSD_INNER + 2 * SSD_GROUPS * SSD_STATE
ATT_HEADS = 16
ATT_HEAD_DIM = 64
ATT_INNER = ATT_HEADS * ATT_HEAD_DIM
MOBA_BLOCK = 256
MOBA_TOPK = 3
MOBA_QCHUNK = 16
ROPE_THETA = 10000.0
IN_SPLITS = (SSD_INNER, SSD_CONV_CH, SSD_HEADS, ATT_INNER, ATT_INNER, ATT_INNER, D_MODEL, D_MODEL)
IN_WIDTH = 7440
N_GROUPS = 4
EXPERTS_PER_GROUP = 8
TOPK_IN_GROUP = 2
D_EXPERT = 256


def rms_norm(x, w):
    xf = x.astype(jnp.float32)
    inv = lax.rsqrt(jnp.mean(xf * xf, axis=-1, keepdims=True) + EPS)
    return (xf * inv).astype(x.dtype) * w

def split_columns(proj):
    offs = np.cumsum(IN_SPLITS)[:-1].tolist()
    return jnp.split(proj, offs, axis=-1)

def rope(x, positions):
    half = x.shape[-1] // 2
    inv_freq = ROPE_THETA ** (-jnp.arange(half, dtype=jnp.float32) / half)
    ang = positions.astype(jnp.float32)[..., None] * inv_freq
    cos = jnp.cos(ang)[:, :, None, :].astype(x.dtype)
    sin = jnp.sin(ang)[:, :, None, :].astype(x.dtype)
    x1, x2 = x[..., :half], x[..., half:]
    return jnp.concatenate([x1 * cos - x2 * sin, x2 * cos + x1 * sin], axis=-1)

def causal_dwconv(u, w, b):
    out = lax.conv_general_dilated(
        u, w[:, None, :].astype(u.dtype), window_strides=(1,),
        padding=((SSD_CONV - 1, 0),), dimension_numbers=("NWC", "WIO", "NWC"),
        feature_group_count=u.shape[-1])
    return out + b

def ssd_mixer(z, xbc, dt_raw, conv_w, conv_b, dt_bias, a_log, d_skip, norm_w):
    b, L, _ = z.shape
    nc = L // SSD_CHUNK
    E = SSD_HEADS // SSD_GROUPS
    xbc = jax.nn.silu(causal_dwconv(xbc, conv_w, conv_b))
    xs, Bm, Cm = jnp.split(xbc, [SSD_INNER, SSD_INNER + SSD_GROUPS * SSD_STATE], axis=-1)
    dt = jax.nn.softplus(dt_raw.astype(jnp.float32) + dt_bias.astype(jnp.float32))
    A = -jnp.exp(a_log.astype(jnp.float32)).reshape(SSD_GROUPS, E)
    X = xs.reshape(b, nc, SSD_CHUNK, SSD_GROUPS, E, SSD_HEAD_DIM)
    Bc = Bm.reshape(b, nc, SSD_CHUNK, SSD_GROUPS, SSD_STATE)
    Cc = Cm.reshape(b, nc, SSD_CHUNK, SSD_GROUPS, SSD_STATE)
    dtc = dt.reshape(b, nc, SSD_CHUNK, SSD_GROUPS, E)
    Xdt = X * dtc[..., None].astype(X.dtype)
    dA = jnp.transpose(dtc * A, (0, 1, 3, 4, 2))
    A_cum = jnp.cumsum(dA, axis=-1)
    idx = jnp.arange(SSD_CHUNK)
    causal = idx[:, None] >= idx[None, :]
    Lmat = jnp.exp(jnp.where(causal, A_cum[..., :, None] - A_cum[..., None, :], -jnp.inf))
    CB = jnp.einsum("bclgn,bcsgn->bcgls", Cc, Bc)
    M = (CB[:, :, :, None] * Lmat).astype(X.dtype)
    y_diag = jnp.einsum("bcgels,bcsgep->bclgep", M, Xdt)
    decay_states = jnp.exp(A_cum[..., -1:] - A_cum).astype(X.dtype)
    states = jnp.einsum("bclgn,bcgel,bclgep->bcgepn", Bc, decay_states, Xdt)
    chunk_decay = jnp.exp(A_cum[..., -1])

    def step(h, inp):
        s_c, d_c = inp
        return h * d_c[..., None, None] + s_c, h

    h0 = jnp.zeros((b, SSD_GROUPS, E, SSD_HEAD_DIM, SSD_STATE), jnp.float32)
    _, prev = lax.scan(step, h0, (jnp.moveaxis(states, 1, 0).astype(jnp.float32),
                                  jnp.moveaxis(chunk_decay, 1, 0)))
    prev = jnp.moveaxis(prev, 0, 1).astype(X.dtype)
    y_off = jnp.einsum("bclgn,bcgepn,bcgel->bclgep", Cc, prev, jnp.exp(A_cum).astype(X.dtype))
    y = y_diag + y_off + X * d_skip.reshape(SSD_GROUPS, E)[:, :, None].astype(X.dtype)
    y = y.reshape(b, L, SSD_INNER)
    yg = (y * jax.nn.silu(z)).reshape(b, L, SSD_GROUPS, SSD_INNER // SSD_GROUPS)
    return rms_norm(yg, norm_w.reshape(SSD_GROUPS, -1)).reshape(b, L, SSD_INNER)

def moba_attention(q, k, v):
    b, L, H, Dh = q.shape
    Lp = -(-L // MOBA_BLOCK) * MOBA_BLOCK
    nb = Lp // MOBA_BLOCK
    n_sel = min(MOBA_TOPK, nb - 1)
    pad = ((0, 0), (0, Lp - L), (0, 0), (0, 0))
    qh = jnp.pad(q, pad).transpose(0, 2, 1, 3)
    k_blocks = jnp.pad(k, pad).transpose(0, 2, 1, 3).reshape(b, H, nb, MOBA_BLOCK, Dh)
    v_blocks = jnp.pad(v, pad).transpose(0, 2, 1, 3).reshape(b, H, nb, MOBA_BLOCK, Dh)
    k_mean = jnp.mean(k_blocks.astype(jnp.float32), axis=3).astype(q.dtype)
    scale = Dh ** -0.5
    bi = jnp.arange(b)[:, None, None, None]
    hi = jnp.arange(H)[None, :, None, None]
    kpos_in_blk = jnp.arange(MOBA_BLOCK)

    def chunk(c):
        q0 = c * MOBA_QCHUNK
        qc = lax.dynamic_slice_in_dim(qh, q0, MOBA_QCHUNK, axis=2)
        qpos = q0 + jnp.arange(MOBA_QCHUNK)
        own = q0 // MOBA_BLOCK
        own_idx = jnp.broadcast_to(own, (b, H, MOBA_QCHUNK, 1)).astype(jnp.int32)
        if n_sel > 0:
            gate = jnp.einsum("bhqd,bhnd->bhqn", qc, k_mean).astype(jnp.float32)
            gate = jnp.where(jnp.arange(nb) < own, gate, -jnp.inf)
            _, sel = lax.top_k(gate, n_sel)
            sel = sel.astype(jnp.int32)
            blk_idx = jnp.concatenate([sel, own_idx], axis=-1)
            slot_ok = jnp.concatenate([sel < own, jnp.ones(own_idx.shape, bool)], axis=-1)
        else:
            blk_idx = own_idx
            slot_ok = jnp.ones(own_idx.shape, bool)
        kg = k_blocks[bi, hi, blk_idx]
        vg = v_blocks[bi, hi, blk_idx]
        s = jnp.einsum("bhqd,bhqjkd->bhqjk", qc, kg).astype(jnp.float32) * scale
        kpos = blk_idx[..., None] * MOBA_BLOCK + kpos_in_blk
        mask = slot_ok[..., None] & (kpos <= qpos[:, None, None])
        s = jnp.where(mask, s, -jnp.inf)
        pr = jax.nn.softmax(s.reshape(b, H, MOBA_QCHUNK, -1), axis=-1).reshape(s.shape)
        return jnp.einsum("bhqjk,bhqjkd->bhqd", pr.astype(vg.dtype), vg)

    out = lax.map(chunk, jnp.arange(Lp // MOBA_QCHUNK))
    out = out.transpose(1, 0, 3, 2, 4).reshape(b, Lp, H, Dh)
    return out[:, :L]

def hybrid_mixer(h, positions, w_in, conv_w, conv_b, dt_bias, a_log, d_skip, ssd_norm_w,
                 w_ssd_out, w_attn_out, w_out):
    b, L, _ = h.shape
    z, xbc, dt_raw, q, k, v, g_ssd, g_att = split_columns(h @ w_in)
    y_ssd = ssd_mixer(z, xbc, dt_raw, conv_w, conv_b, dt_bias, a_log, d_skip, ssd_norm_w) @ w_ssd_out
    q = rope(q.reshape(b, L, ATT_HEADS, ATT_HEAD_DIM), positions)
    k = rope(k.reshape(b, L, ATT_HEADS, ATT_HEAD_DIM), positions)
    v = v.reshape(b, L, ATT_HEADS, ATT_HEAD_DIM)
    y_att = moba_attention(q, k, v).reshape(b, L, ATT_INNER) @ w_attn_out
    merged = jax.nn.sigmoid(g_ssd) * y_ssd + jax.nn.sigmoid(g_att) * y_att
    return merged @ w_out

def hier_moe(h, w_rg, b_rg, w_re, b_re, w_gate, w_up, w_down):
    b, L, _ = h.shape
    gl = (h @ w_rg).astype(jnp.float32) + b_rg.astype(jnp.float32)
    gp = jax.nn.softmax(gl, axis=-1)
    _, gi = lax.top_k(gl, 1)
    g_oh = jax.nn.one_hot(gi[..., 0], N_GROUPS, dtype=jnp.float32)
    g_w = jnp.sum(gp * g_oh, axis=-1)
    el = ((h @ w_re).astype(jnp.float32) + b_re.astype(jnp.float32)).reshape(b, L, N_GROUPS, EXPERTS_PER_GROUP)
    el_sel = jnp.einsum("blge,blg->ble", el, g_oh)
    top_v, top_i = lax.top_k(el_sel, TOPK_IN_GROUP)
    top_w = jax.nn.softmax(top_v, axis=-1) * g_w[..., None]
    e_w = jnp.sum(jax.nn.one_hot(top_i, EXPERTS_PER_GROUP, dtype=jnp.float32) * top_w[..., None], axis=-2)
    comb = (g_oh[..., None] * e_w[..., None, :]).astype(h.dtype)
    out = jnp.zeros_like(h)
    for g in range(N_GROUPS):
        hid = jax.nn.silu(jnp.einsum("bld,edf->blef", h, w_gate[g])) * jnp.einsum("bld,edf->blef", h, w_up[g])
        out = out + jnp.einsum("blef,ble,efd->bld", hid, comb[:, :, g], w_down[g])
    return out

def first_inputs(seed: int = 0) -> dict:
    key = jax.random.key(seed)
    ks = jax.random.split(key, 32)
    f32 = jnp.float32

    def nrm(k, shape, fan_in):
        return jax.random.normal(k, shape, f32) * (fan_in ** -0.5)

    def gain(k, shape):
        return 1.0 + 0.05 * jax.random.normal(k, shape, f32)

    dt0 = jnp.exp(jax.random.uniform(ks[5], (DEPTH, SSD_HEADS), f32, math.log(1e-3), math.log(1e-1)))
    dt_bias = dt0 + jnp.log(-jnp.expm1(-dt0))
    return {
        "x": jax.random.normal(ks[0], (BATCH, SEQ, D_MODEL), f32),
        "p": jax.random.normal(ks[1], (DEPTH, BATCH, SEQ, PLE_DIM), f32),
        "positions": (jnp.arange(SEQ, dtype=jnp.int32)[None, :]
                      + jax.random.randint(ks[2], (BATCH, 1), 0, 1024, dtype=jnp.int32)),
        "attn_norm_w": gain(ks[3], (DEPTH, D_MODEL)),
        "w_in": nrm(ks[4], (DEPTH, D_MODEL, IN_WIDTH), D_MODEL),
        "conv_w": nrm(ks[6], (DEPTH, SSD_CONV, SSD_CONV_CH), SSD_CONV),
        "conv_b": 0.02 * jax.random.normal(ks[7], (DEPTH, SSD_CONV_CH), f32),
        "dt_bias": dt_bias,
        "a_log": jnp.log(jax.random.uniform(ks[8], (DEPTH, SSD_HEADS), f32, 1.0, 16.0)),
        "d_skip": 1.0 + 0.1 * jax.random.normal(ks[9], (DEPTH, SSD_HEADS), f32),
        "ssd_norm_w": gain(ks[10], (DEPTH, SSD_INNER)),
        "w_ssd_out": nrm(ks[11], (DEPTH, SSD_INNER, D_MODEL), SSD_INNER),
        "w_attn_out": nrm(ks[12], (DEPTH, ATT_INNER, D_MODEL), ATT_INNER),
        "w_out": nrm(ks[13], (DEPTH, D_MODEL, D_MODEL), D_MODEL),
        "moe_norm_w": gain(ks[14], (DEPTH, D_MODEL)),
        "w_router_group": nrm(ks[15], (DEPTH, D_MODEL, N_GROUPS), D_MODEL),
        "b_router_group": 0.01 * jax.random.normal(ks[16], (DEPTH, N_GROUPS), f32),
        "w_router_expert": nrm(ks[17], (DEPTH, D_MODEL, N_GROUPS * EXPERTS_PER_GROUP), D_MODEL),
        "b_router_expert": 0.01 * jax.random.normal(ks[18], (DEPTH, N_GROUPS * EXPERTS_PER_GROUP), f32),
        "w_exp_gate": nrm(ks[19], (DEPTH, N_GROUPS, EXPERTS_PER_GROUP, D_MODEL, D_EXPERT), D_MODEL),
        "w_exp_up": nrm(ks[20], (DEPTH, N_GROUPS, EXPERTS_PER_GROUP, D_MODEL, D_EXPERT), D_MODEL),
        "w_exp_down": nrm(ks[21], (DEPTH, N_GROUPS, EXPERTS_PER_GROUP, D_EXPERT, D_MODEL), D_EXPERT),
        "ple_norm_w": gain(ks[22], (DEPTH, D_MODEL)),
        "w_ple": nrm(ks[23], (DEPTH, PLE_DIM, D_MODEL), PLE_DIM),
        "w_ple_gate": nrm(ks[24], (DEPTH, D_MODEL, D_MODEL), D_MODEL),
        "final_norm_w": gain(ks[25], (D_MODEL,)),
    }

def first_block(x, p, positions, attn_norm_w, w_in, conv_w, conv_b, dt_bias, a_log, d_skip,
              ssd_norm_w, w_ssd_out, w_attn_out, w_out, moe_norm_w, w_router_group,
              b_router_group, w_router_expert, b_router_expert, w_exp_gate, w_exp_up,
              w_exp_down, ple_norm_w, w_ple, w_ple_gate, final_norm_w):
    for i in range(DEPTH):
        h = rms_norm(x, attn_norm_w[i])
        x = x + hybrid_mixer(h, positions, w_in[i], conv_w[i], conv_b[i], dt_bias[i], a_log[i],
                             d_skip[i], ssd_norm_w[i], w_ssd_out[i], w_attn_out[i], w_out[i])
        h = rms_norm(x, moe_norm_w[i])
        x = x + hier_moe(h, w_router_group[i], b_router_group[i], w_router_expert[i],
                         b_router_expert[i], w_exp_gate[i], w_exp_up[i], w_exp_down[i])
        gate = jax.nn.sigmoid(rms_norm(x, ple_norm_w[i]) @ w_ple_gate[i])
        x = x + gate * (p[i] @ w_ple[i])
    return rms_norm(x, final_norm_w)


CHUNK = 64
HEAD_SIZE = 64
D_RWKV = D_MODEL
N_RWKV_HEADS = D_RWKV // HEAD_SIZE
D_CONV = D_MODEL
CONV_WIDTH = 31
D_DECAY_LORA = 64
D_AAA_LORA = 64
D_GATE_LORA = 128
D_FF = 4 * D_MODEL
N_BRANCHES = 2
RMS_EPS = 1e-6
LN_EPS = 1e-5
GN_EPS = 64e-5
DECAY_OFFSET = 0.5
COL_RKV = 3 * D_RWKV
COL_GLU = 2 * D_CONV
COL_GATE = N_BRANCHES * D_MODEL
IN_COLS = COL_RKV + COL_GLU + COL_GATE


def _rmsnorm(x, g):
    xf = x.astype(jnp.float32)
    y = xf * lax.rsqrt(jnp.mean(xf * xf, axis=-1, keepdims=True) + RMS_EPS)
    return (y * g.astype(jnp.float32)).astype(x.dtype)

def _layernorm(x, g, b):
    xf = x.astype(jnp.float32)
    mu = jnp.mean(xf, axis=-1, keepdims=True)
    var = jnp.mean(jnp.square(xf - mu), axis=-1, keepdims=True)
    y = (xf - mu) * lax.rsqrt(var + LN_EPS)
    return (y * g.astype(jnp.float32) + b.astype(jnp.float32)).astype(x.dtype)

def _token_shift(z):
    return jnp.pad(z, ((0, 0), (1, 0), (0, 0)))[:, :-1]

def _heads(z):
    b, t, _ = z.shape
    return z.reshape(b, t, N_RWKV_HEADS, HEAD_SIZE)

def _wkv7_scan(r, w, k, v, kk, a):
    b, t, h, n = r.shape
    n_chunks = t // CHUNK

    def to_chunks(z):
        return jnp.moveaxis(z.astype(jnp.float32).reshape(b, n_chunks, CHUNK, h, n), (1, 2), (0, 1))

    def frame_step(S, inp):
        r_t, w_t, k_t, v_t, kk_t, a_t = inp
        sa = jnp.einsum('bhvk,bhk->bhv', S, -kk_t)
        S = (S * w_t[:, :, None, :]
             + sa[..., None] * (kk_t * a_t)[:, :, None, :]
             + v_t[..., None] * k_t[:, :, None, :])
        o_t = jnp.einsum('bhvk,bhk->bhv', S, r_t)
        return S, o_t

    def chunk_step(S, chunk_inp):
        return lax.scan(frame_step, S, chunk_inp)

    S0 = jnp.zeros((b, h, n, n), jnp.float32)
    inputs = (to_chunks(r), to_chunks(w), to_chunks(k), to_chunks(v), to_chunks(kk), to_chunks(a))
    _, o = lax.scan(chunk_step, S0, inputs)
    return jnp.moveaxis(o, (0, 1), (1, 2)).reshape(b, t, h, n)

def _rwkv7_mixer(h, r, k, v, mu_lora, w0, w1, w2, a0, a1, a2, g1, g2, k_k, k_a, r_k, ln_g, ln_b):
    dh = _token_shift(h) - h
    xw = h + dh * mu_lora[0]
    xa = h + dh * mu_lora[1]
    xg = h + dh * mu_lora[2]
    w_log = -jax.nn.softplus(-(w0 + jnp.tanh(xw @ w1) @ w2)) - DECAY_OFFSET
    decay = jnp.exp(-jnp.exp(w_log.astype(jnp.float32)))
    a = jax.nn.sigmoid(a0 + (xa @ a1) @ a2)
    g = jax.nn.sigmoid(xg @ g1) @ g2
    kk = _heads(k * k_k).astype(jnp.float32)
    kk = kk / jnp.maximum(jnp.linalg.norm(kk, axis=-1, keepdims=True), 1e-12)
    k = k * (1.0 + (a - 1.0) * k_a)
    rh, kh, vh, ah = _heads(r), _heads(k), _heads(v), _heads(a)
    o = _wkv7_scan(rh, _heads(decay), kh, vh, kk, ah)
    mu = jnp.mean(o, axis=-1, keepdims=True)
    var = jnp.mean(jnp.square(o - mu), axis=-1, keepdims=True)
    o = ((o - mu) * lax.rsqrt(var + GN_EPS)).reshape(h.shape[0], h.shape[1], D_RWKV)
    o = (o * ln_g.astype(jnp.float32) + ln_b.astype(jnp.float32)).astype(h.dtype)
    bonus = jnp.sum(rh * kh * r_k, axis=-1, keepdims=True) * vh
    o = o + bonus.reshape(o.shape)
    return o * g

def _conformer_conv_mixer(glu_in, conv_w, conv_b, ln_g, ln_b):
    u = glu_in[..., :D_CONV] * jax.nn.sigmoid(glu_in[..., D_CONV:])
    u = lax.conv_general_dilated(
        u, conv_w[:, None, :], window_strides=(1,), padding=((CONV_WIDTH - 1, 0),),
        dimension_numbers=('NWC', 'WIO', 'NWC'), feature_group_count=D_CONV) + conv_b
    u = _layernorm(u, ln_g, ln_b)
    return jax.nn.silu(u)

def second_inputs(seed: int = 0) -> dict:
    key = jax.random.key(seed)
    ks = iter(jax.random.split(key, 40))
    L = DEPTH
    f32 = jnp.float32

    def nrm(shape, scale):
        return jax.random.normal(next(ks), shape, f32) * scale

    def unif(shape, lo, hi):
        return jax.random.uniform(next(ks), shape, f32, minval=lo, maxval=hi)

    return {
        "x": nrm((BATCH, SEQ, D_MODEL), 1.0),
        "norm_mix_g": 1.0 + nrm((L, D_MODEL), 0.05),
        "w_in": nrm((L, D_MODEL, IN_COLS), D_MODEL ** -0.5),
        "b_gate": nrm((L, COL_GATE), 0.1),
        "mu_rkv": unif((L, COL_RKV), 0.0, 1.0),
        "mu_lora": unif((L, 3, D_MODEL), 0.0, 1.0),
        "decay_w0": unif((L, D_RWKV), -3.0, 2.0),
        "decay_w1": nrm((L, D_MODEL, D_DECAY_LORA), D_MODEL ** -0.5),
        "decay_w2": nrm((L, D_DECAY_LORA, D_RWKV), 0.1),
        "aaa_a0": nrm((L, D_RWKV), 0.1),
        "aaa_a1": nrm((L, D_MODEL, D_AAA_LORA), D_MODEL ** -0.5),
        "aaa_a2": nrm((L, D_AAA_LORA, D_RWKV), 0.5 * D_AAA_LORA ** -0.5),
        "gate_g1": nrm((L, D_MODEL, D_GATE_LORA), D_MODEL ** -0.5),
        "gate_g2": nrm((L, D_GATE_LORA, D_RWKV), D_GATE_LORA ** -0.5),
        "k_k": 0.85 + nrm((L, D_RWKV), 0.05),
        "k_a": 1.0 + nrm((L, D_RWKV), 0.05),
        "r_k": nrm((L, N_RWKV_HEADS, HEAD_SIZE), 0.1),
        "ln_x_g": 1.0 + nrm((L, D_RWKV), 0.05),
        "ln_x_b": nrm((L, D_RWKV), 0.02),
        "w_rwkv_proj": nrm((L, D_RWKV, D_MODEL), D_RWKV ** -0.5),
        "conv_w": nrm((L, CONV_WIDTH, D_CONV), CONV_WIDTH ** -0.5),
        "conv_b": nrm((L, D_CONV), 0.02),
        "conv_ln_g": 1.0 + nrm((L, D_CONV), 0.05),
        "conv_ln_b": nrm((L, D_CONV), 0.02),
        "w_conv_proj": nrm((L, D_CONV, D_MODEL), D_CONV ** -0.5),
        "w_out": nrm((L, D_MODEL, D_MODEL), D_MODEL ** -0.5),
        "norm_ff_g": 1.0 + nrm((L, D_MODEL), 0.05),
        "w_ff1": nrm((L, D_MODEL, D_FF), D_MODEL ** -0.5),
        "w_ff2": nrm((L, D_FF, D_MODEL), 0.5 * D_FF ** -0.5),
        "norm_final_g": 1.0 + nrm((D_MODEL,), 0.05),
    }

def second_block(x, norm_mix_g, w_in, b_gate, mu_rkv, mu_lora, decay_w0, decay_w1, decay_w2,
              aaa_a0, aaa_a1, aaa_a2, gate_g1, gate_g2, k_k, k_a, r_k, ln_x_g, ln_x_b,
              w_rwkv_proj, conv_w, conv_b, conv_ln_g, conv_ln_b, w_conv_proj, w_out,
              norm_ff_g, w_ff1, w_ff2, norm_final_g):
    b, t, _ = x.shape
    for l in range(DEPTH):
        h = _rmsnorm(x, norm_mix_g[l])
        proj = h @ w_in[l]
        rkv = proj[..., :COL_RKV]
        glu_in = proj[..., COL_RKV:COL_RKV + COL_GLU]
        gate_logits = proj[..., COL_RKV + COL_GLU:] + b_gate[l]
        rkv = rkv + (_token_shift(rkv) - rkv) * mu_rkv[l]
        r = rkv[..., :D_RWKV]
        k = rkv[..., D_RWKV:2 * D_RWKV]
        v = rkv[..., 2 * D_RWKV:]
        a_out = _rwkv7_mixer(h, r, k, v, mu_lora[l], decay_w0[l], decay_w1[l], decay_w2[l],
                             aaa_a0[l], aaa_a1[l], aaa_a2[l], gate_g1[l], gate_g2[l],
                             k_k[l], k_a[l], r_k[l], ln_x_g[l], ln_x_b[l])
        c_out = _conformer_conv_mixer(glu_in, conv_w[l], conv_b[l], conv_ln_g[l], conv_ln_b[l])
        gates = jax.nn.sigmoid(gate_logits).reshape(b, t, N_BRANCHES, D_MODEL)
        merged = gates[:, :, 0] * (a_out @ w_rwkv_proj[l]) + gates[:, :, 1] * (c_out @ w_conv_proj[l])
        x = x + merged @ w_out[l]
        h2 = _rmsnorm(x, norm_ff_g[l])
        x = x + jnp.square(jax.nn.relu(h2 @ w_ff1[l])) @ w_ff2[l]
    return _rmsnorm(x, norm_final_g)


def setup_inputs(seed=0):
    out = dict(first_inputs(seed))
    for name, value in second_inputs(seed + 1).items():
        if name != "x":
            out[name + "_2"] = value
    return out


def reference(
    x, p, positions, attn_norm_w, w_in, conv_w, conv_b, dt_bias, a_log, d_skip, ssd_norm_w,
    w_ssd_out, w_attn_out, w_out, moe_norm_w, w_router_group, b_router_group, w_router_expert,
    b_router_expert, w_exp_gate, w_exp_up, w_exp_down, ple_norm_w, w_ple, w_ple_gate,
    final_norm_w, norm_mix_g_2, w_in_2, b_gate_2, mu_rkv_2, mu_lora_2, decay_w0_2, decay_w1_2,
    decay_w2_2, aaa_a0_2, aaa_a1_2, aaa_a2_2, gate_g1_2, gate_g2_2, k_k_2, k_a_2, r_k_2,
    ln_x_g_2, ln_x_b_2, w_rwkv_proj_2, conv_w_2, conv_b_2, conv_ln_g_2, conv_ln_b_2,
    w_conv_proj_2, w_out_2, norm_ff_g_2, w_ff1_2, w_ff2_2, norm_final_g_2,
):
    x = first_block(
        x, p, positions, attn_norm_w, w_in, conv_w, conv_b, dt_bias, a_log, d_skip, ssd_norm_w,
        w_ssd_out, w_attn_out, w_out, moe_norm_w, w_router_group, b_router_group,
        w_router_expert, b_router_expert, w_exp_gate, w_exp_up, w_exp_down, ple_norm_w, w_ple,
        w_ple_gate, final_norm_w,
    )
    return second_block(
        x, norm_mix_g_2, w_in_2, b_gate_2, mu_rkv_2, mu_lora_2, decay_w0_2, decay_w1_2,
        decay_w2_2, aaa_a0_2, aaa_a1_2, aaa_a2_2, gate_g1_2, gate_g2_2, k_k_2, k_a_2, r_k_2,
        ln_x_g_2, ln_x_b_2, w_rwkv_proj_2, conv_w_2, conv_b_2, conv_ln_g_2, conv_ln_b_2,
        w_conv_proj_2, w_out_2, norm_ff_g_2, w_ff1_2, w_ff2_2, norm_final_g_2,
    )


_drawn_inputs = setup_inputs


def setup_inputs(seed=0):
    import zlib

    import numpy as np

    out = dict(_drawn_inputs(seed))
    spreads = {}
    factors = {'b_router_group': 8.0,
     'b_router_expert': 3.037,
     'ple_norm_w': 5.988,
     'b_gate_2': 3.402,
     'aaa_a0_2': 4.016,
     'k_k_2': 47.617,
     'k_a_2': 3.591,
     'ln_x_g_2': 4.08,
     'ln_x_b_2': 8.0,
     'conv_b_2': 4.31,
     'conv_ln_g_2': 3.192,
     'conv_ln_b_2': 8.0,
     'norm_ff_g_2': 3.181}
    for name, (base, spread) in spreads.items():
        noise = np.random.default_rng([zlib.crc32(name.encode()), seed]).standard_normal(out[name].shape)
        drawn = base * np.exp(spread * noise) if base else spread * noise
        out[name] = __import__('jax').numpy.asarray(drawn.astype(out[name].dtype))
    for name, factor in factors.items():
        out[name] = (out[name] * factor).astype(out[name].dtype)
    return out
```

```python
import math
from contextlib import ExitStack

import numpy as np

import concourse.bass as bass
from concourse import mybir

F32 = mybir.dt.float32
F32R = mybir.dt.float32r
I32 = mybir.dt.int32
ALU = mybir.AluOpType
ACT = mybir.ActivationFunctionType
AX = mybir.AxisListType
ds = bass.ds

P = 128
SEQ = 256
NT = SEQ // P
D = 1024
KC = D // P
EPS = 1e-6
IN_W = 7440
IN_TW = 496
IN_T = IN_W // IN_TW
IN2_W = 7168
TW = 512
QF = 2 * TW
RING = 4

C_Z, C_XBC, C_DT, C_Q, C_K, C_V, C_GS, C_GA = 0, 1024, 2304, 2320, 3344, 4368, 5392, 6416
NH, DH = 16, 64
XCH = 10
PAD = 3
TWO_PI = 2.0 * math.pi

Q_IN = 0
Q_SSD = Q_IN + 4 * IN_T
Q_ATT = Q_SSD + 8
Q_OUT = Q_ATT + 8
Q_MOE = Q_OUT + 8
N_EXP = 32
DE = 256
Q_PLE = Q_MOE + 6 * N_EXP
Q_GATE = Q_PLE + 2
Q_IN2 = Q_GATE + 8
Q_CONV = Q_IN2 + 4 * (IN2_W // TW)
Q_RWKV = Q_CONV + 8
Q_OUT2 = Q_RWKV + 8
Q_FF = Q_OUT2 + 8
FF_J = 8
Q_END = Q_FF + 8 * FF_J

CONST = {}


def constants():
    i = np.arange(P)
    parts = []

    def put(name, a):
        at = sum(x.shape[1] for x in parts)
        CONST[name] = (at, at + a.shape[1])
        parts.append(np.ascontiguousarray(a, dtype=np.float32))

    put("ident", np.eye(P))
    put("strict", (i[:, None] < i[None, :]) * 1.0)
    put("tri", (i[:, None] <= i[None, :]) * 1.0)
    put("centred", (i[:, None] <= i[None, :]) * 1.0 - (i[:, None] < 64) * np.ones((P, P)))
    put("ones", np.ones((P, P)))
    neg = np.where(i[None, :] <= i[:, None], 0.0, -1e30)
    put("amask", np.concatenate([neg, np.zeros((P, P)), neg], axis=1))
    for lev in range(7):
        m = 1 << lev
        pick = ((i[:, None] // m) % 2 == 1) & (i[None, :] // m == i[:, None] // m - 1)
        put(f"level{lev}", np.eye(P) + pick)
        if lev == 0:
            put("level0_t", np.eye(P) + pick.T)
    put("heads", (i[:, None] // 64 == i[None, :] // 64) * 1.0)
    put("low", (i[:, None] < 64) * 1.0)
    put("high", (i[:, None] >= 64) * 1.0)
    half = DH // 2
    freq = (np.float32(10000.0) ** (-np.arange(half, dtype=np.float32) / np.float32(half))).astype(np.float32)
    put("freq", np.broadcast_to(freq, (P, half)))
    put("slot", np.broadcast_to(np.arange(P), (P, P)))
    put("rev8", np.broadcast_to(8.0 - np.arange(8), (P, 8)))
    put("rev4", np.broadcast_to(4.0 - np.arange(4), (P, 4)))
    return np.concatenate(parts, axis=1)


constants()
N_CONST = max(b for _, b in CONST.values())


class Order:

    def __init__(self, eng, sem):
        self.eng, self.sem, self.base, self.n = eng, sem, 0, 0

    def mark(self, ins):
        ins.then_inc(self.sem, 1)
        self.n += 1

    def settle(self):
        self.eng.wait_ge(self.sem, self.base + self.n)

    def step(self, ins):
        self.mark(ins)
        self.settle()

    def body(self, start, i, per):
        self.base, self.n = start + i * per, 0

    def after(self, start, times, per):
        assert self.n == per, (self.n, per)
        self.base, self.n = start + times * per, 0

    def count(self):
        return self.base + self.n


class Again:

    def __init__(self, sem, before):
        self.sem, self.before = sem, before

    def at(self, n):
        return self.sem, self.before + n


def wait_from(eng, sem, value):
    if not (isinstance(value, int) and value <= 0):
        eng.wait_ge(sem, value)



JOB = 6 * 8


def moe_gate_up(n):
    if not Q_MOE <= n < Q_PLE:
        return False
    at = (n - Q_MOE) % JOB
    return at < 4 or (at < JOB - 2 and (at - 4) % 6 < 4)


def split_by_vector(n):
    return Q_MOE - RING <= n < Q_PLE and n % 2 == 1


RAW_DONE, LOW_DONE = [], []
for _n in range(Q_END):
    RAW_DONE.append((RAW_DONE[_n - RING] if _n >= RING else 0) + (32 if moe_gate_up(_n) else 16))
    LOW_DONE.append(sum(split_by_vector(m) == split_by_vector(_n) for m in range(_n + 1)))


def at_turn(counts, n, i, per):
    if not per:
        return counts[n]
    span = JOB if per < JOB and JOB % per == 0 and n + JOB < Q_PLE and n >= Q_MOE - RING else per
    return counts[n] + (counts[n + span] - counts[n]) * per // span * i


NORMS = ["attn_norm_w", "moe_norm_w", "ple_norm_w", "ssd_norm_w", "norm_mix_g_2", "norm_ff_g_2",
         "conv_ln_g_2", "conv_ln_b_2"]


def build(nc, A, out):
    ctx = ExitStack()
    with ctx:
        def sb(name, shape, dt=F32):
            return ctx.enter_context(nc.sbuf_tensor(name, shape, dt))

        def sem(name):
            return ctx.enter_context(nc.semaphore(name))

        raw = sb("raw", [P, RING, QF])
        whi = sb("whi", [P, RING, QF], F32R)
        wlo = sb("wlo", [P, RING, QF], F32R)
        const = sb("const", [P, N_CONST])
        cols = sb("cols", [P, len(NORMS), KC])
        mul = sb("mul", [P, 3, KC])
        xres = sb("xres", [P, NT, D])
        t0h = sb("t0h", [P, KC, SEQ], F32R)
        t0l = sb("t0l", [P, KC, SEQ], F32R)
        t1h = sb("t1h", [P, 4, SEQ], F32R)
        t1l = sb("t1l", [P, 4, SEQ], F32R)
        proj = sb("proj", [P, NT, IN_W])
        WORK = 13700
        work = sb("work", [P, WORK])
        small = sb("small", [P, 360])
        bank = [ctx.enter_context(nc.psum_tensor(f"bank{b}", [P, 512], F32)) for b in range(8)]

        def con(name):
            a, b = CONST[name]
            return const[:, a:b]

        ident = con("ident")

        def carve(at, *shape):
            n = int(np.prod(shape))
            assert at + n <= WORK, (at, n)
            v = work[:, at:at + n]
            if len(shape) == 1:
                return v
            names = "abcd"[:len(shape)]
            return v.rearrange(f"p ({' '.join(names)}) -> p {' '.join(names)}", **dict(zip(names, shape)))

        def tiny(at, *shape):
            n = int(np.prod(shape))
            v = small[:, at:at + n]
            if len(shape) == 1:
                return v
            names = "abcd"[:len(shape)]
            return v.rearrange(f"p ({' '.join(names)}) -> p {' '.join(names)}", **dict(zip(names, shape)))

        raw_full = [sem(f"raw_full{s}") for s in range(RING)]
        hi_ready = sem("hi_ready")
        lo_by_pool = sem("lo_by_pool")
        lo_by_dve = sem("lo_by_dve")
        quarter_done = sem("quarter_done")
        consts_loaded = sem("consts_loaded")
        x_loaded = sem("x_loaded")
        vec_loaded = sem("vec_loaded")
        dve_order = sem("dve_order")
        act_order = sem("act_order")

        def wait_low(eng, n, i=0, per=0):
            eng.wait_ge(lo_by_dve if split_by_vector(n) else lo_by_pool, at_turn(LOW_DONE, n, i, per))

        def load(sp, n, pairs, i=0, per=0):
            if n >= RING:
                wait_low(sp, n - RING, i, per)
            for dst, src in pairs:
                sp.dma_start(dst, src).then_inc(raw_full[n % RING], 16)

        def split_high(act, n, i=0, per=0, width=QF):
            s = n % RING
            act.wait_ge(raw_full[s], at_turn(RAW_DONE, n, i, per))
            wait_from(act, quarter_done, n - RING + 1 + per * i)
            nc.scalar.activation(whi[:, s, 0:width], raw[:, s, 0:width], ACT.Copy).then_inc(hi_ready, 1)

        def split_low(eng, n, i=0, per=0, width=QF):
            s = n % RING
            eng.wait_ge(hi_ready, n + 1 + per * i)
            ins = (nc.vector if split_by_vector(n) else nc.gpsimd).tensor_tensor(
                wlo[:, s, 0:width], raw[:, s, 0:width], whi[:, s, 0:width].bitcast(F32), ALU.subtract)
            ins.then_inc(lo_by_dve if split_by_vector(n) else lo_by_pool, 1)

        def times(dst, hi, lo, wh, wl, first, last):
            nc.tensor.matmul(dst, hi, wh, start=first, stop=False)
            nc.tensor.matmul(dst, hi, wl, start=False, stop=False)
            return nc.tensor.matmul(dst, lo, wh, start=False, stop=last)

        def pair_view(buf, n, width):
            return buf[:, n % RING, 0:2 * width].rearrange("p (k n) -> p k n", k=2)

        def wide_quarter(pe, n, q, dst, hi, lo, width=TW, i=0, per=0):
            wait_low(pe, n, i, per)
            wh, wl = pair_view(whi, n, width), pair_view(wlo, n, width)
            for t in range(NT):
                for kk in range(2):
                    k = 2 * q + kk
                    mm = times(dst[t][:, 0:width], hi[:, k, t * P:(t + 1) * P], lo[:, k, t * P:(t + 1) * P],
                               wh[:, kk, :], wl[:, kk, :], k == 0, k == KC - 1)
            mm.then_inc(quarter_done, 1)

        def load_square(sp, n, w):
            v = w.rearrange("(p k) n -> p k n", k=KC)
            for c in range(2):
                for q in range(4):
                    m = n + 4 * c + q
                    load(sp, m, [(pair_view(raw, m, TW), v[:, 2 * q:2 * q + 2, c * TW:(c + 1) * TW])])

        def square_product(pe, n, hi, lo, waits):
            for s, v in waits:
                pe.wait_ge(s, v)
            for c in range(2):
                for q in range(4):
                    wide_quarter(pe, n + 4 * c + q, q, bank[2 * c:2 * c + 2], hi, lo)

        class Turn:
            turned = sem("turned")
            high = sem("turned_high")
            low = sem("turned_low")
            index = splits = 0

            def __init__(self, src, gain, hi, lo):
                self.src = src.rearrange("p t (f k) -> p t f k", k=KC)
                self.gain, self.hi, self.lo = gain, hi, lo
                self.banks, self.chunks = Turn.index * (KC // 2), Turn.splits * KC
                Turn.index += 1
                Turn.splits += hi is not None

            def written(self, banks=KC // 2):
                return self.turned, self.banks + banks

            def done(self):
                return self.low, self.chunks + KC

            def part(self, k):
                return bank[4 + k // 2][:, (k % 2) * SEQ:(k % 2) * SEQ + SEQ]

            def pe(self, pe, waits):
                for s, v in waits:
                    pe.wait_ge(s, v)
                for b in range(KC // 2):
                    for kk in range(2):
                        for t in range(NT):
                            at = kk * SEQ + t * P
                            tr = nc.tensor.transpose(bank[4 + b][:, at:at + P], self.src[:, t, :, 2 * b + kk],
                                                     ident)
                    tr.then_inc(self.turned, 1)

            def act(self, act, used):
                wait_from(act, quarter_done, used)
                for k in range(KC):
                    if k % 2 == 0:
                        act.wait_ge(*self.written(k // 2 + 1))
                    scale = 1.0 if self.gain is None else self.gain[:, k:k + 1]
                    nc.scalar.activation(self.hi[:, k, :], self.part(k), ACT.Copy if self.gain is None else ACT.Identity,
                                         scale=scale).then_inc(self.high, 1)

            def dve(self, dve):
                for k in range(KC):
                    dve.wait_ge(self.high, self.chunks + 2 * (k // 2) + 2)
                    hi = self.hi[:, k, :].bitcast(F32)
                    if self.gain is None:
                        ins = nc.vector.tensor_tensor(self.lo[:, k, :], self.part(k), hi, ALU.subtract)
                    else:
                        ins = nc.vector.scalar_tensor_tensor(out=self.lo[:, k, :], in0=self.part(k),
                                                             scalar=self.gain[:, k:k + 1], in1=hi,
                                                             op0=ALU.mult, op1=ALU.subtract)
                    ins.then_inc(self.low, 1)

        class RmsNorm:
            squared, mean, root, normed = sem("rms_squared"), sem("rms_mean"), sem("rms_root"), sem("rms_normed")
            index = 0

            def __init__(self, src, xn, stat):
                self.src, self.xn, self.stat = src, xn, stat
                self.before = RmsNorm.index
                RmsNorm.index += 1

            def ready(self, tiles=NT):
                return self.normed, NT * self.before + tiles

            def act(self, act, waits):
                for s, v in waits:
                    act.wait_ge(s, v)
                for t in range(NT):
                    nc.scalar.activation(self.xn[:, t, :], self.src[:, t, :], ACT.Square,
                                         accum_out=self.stat[:, t:t + 1]).then_inc(self.squared, 1)
                act.wait_ge(self.mean, self.before + 1)
                nc.scalar.activation(self.stat[:, 0:NT], self.stat[:, 0:NT], ACT.Sqrt).then_inc(self.root, 1)

            def dve(self, dve, order):
                dve.wait_ge(self.squared, NT * self.before + NT)
                nc.vector.tensor_scalar(self.stat[:, 0:NT], self.stat[:, 0:NT], 1.0 / D, EPS,
                                        ALU.mult, ALU.add).then_inc(self.mean, 1)
                dve.wait_ge(self.root, self.before + 1)
                order.step(nc.vector.reciprocal(self.stat[:, 0:NT], self.stat[:, 0:NT]))
                for t in range(NT):
                    nc.vector.tensor_scalar(self.xn[:, t, :], self.src[:, t, :], self.stat[:, t:t + 1], None,
                                            ALU.mult).then_inc(self.normed, 1)

        def gain(name):
            return cols[:, NORMS.index(name), :]

        xn = carve(0, NT, D)
        stat = tiny(0, 8)
        norm_a = RmsNorm(xres, xn, stat)
        turn_a = Turn(xn, gain("attn_norm_w"), t0h, t0l)
        evac_in = sem("evac_in")

        y = carve(0, NT, D)
        xbcT = carve(2048, XCH, PAD + SEQ)
        convT = carve(2048 + 2590, XCH, SEQ)
        xdt = carve(7198, NT, D)
        xdtd = carve(9246, D)
        dif = carve(10270, NT, 4, P)
        mt = carve(11294, NT, 4, P)
        prevT = carve(12318, 512)
        cbm = carve(12830, 4, P)
        btok = carve(13342, P)
        xs = proj[:, :, C_XBC:C_XBC + D]
        cwT = tiny(8, 50)
        dtb, alog, dsk = tiny(58, 16), tiny(74, 16), tiny(90, 16)
        s_raw, s_neg, s_exp, s_u = (tiny(106 + 32 * j, NT, 16) for j in range(4))
        dt, dA = tiny(234, NT, 16), tiny(266, NT, 16)
        ecum = tiny(298, NT, 16)
        edec = tiny(330, 16)
        acum = dif[:, 0, 0, 0:64].rearrange("p (t a h) -> p t a h", t=NT, a=2)
        rows = carve(13470, P)
        cum = carve(13598, NT, 2, 16)
        xbc_turned, xbc_copied = sem("xbc_turned"), sem("xbc_copied")
        taps_turned, taps_ready = sem("taps_turned"), sem("taps_ready")
        conv_done, conv_active = sem("conv_done"), sem("conv_active")
        x_back, cb_done = sem("x_back"), sem("cb_done")
        dt_arg, dt_exp, dt_ln_arg, dt_ln = sem("dt_arg"), sem("dt_exp"), sem("dt_ln_arg"), sem("dt_ln")
        dA_ready, cum_done, cum_ready, dec_arg, dec_ready = (
            sem(s) for s in ("dA_ready", "cum_done", "cum_ready", "dec_arg", "dec_ready"))
        xdt_ready, state_done, state_ready, off_done = (
            sem(s) for s in ("xdt_ready", "state_done", "state_ready", "off_done"))
        abc_done, dif_ready, lmat_ready, mt_ready, diag_done, y_ready = (
            sem(s) for s in ("abc_done", "dif_ready", "lmat_ready", "mt_ready", "diag_done", "y_ready"))
        z_active, gate_active, y_gated, y_squared, y_normed = (
            sem(s) for s in ("z_active", "gate_active", "y_gated", "y_squared", "y_normed"))
        y_mean, y_root = sem("y_mean"), sem("y_root")
        turn_y = Turn(y, gain("ssd_norm_w"), t0h, t0l)
        ssd_merged = sem("ssd_merged")

        yatt = carve(0, NT, D)
        rot = [carve(2048 + 512 * x, 2, NT, P) for x in range(2)]
        rtmp = [carve(3072 + 128 * x, NT, 2, 32) for x in range(2)]
        qkT = [carve(3328 + 512 * x, 4, P) for x in range(2)]
        sc = [carve(4352 + 384 * x, 384) for x in range(4)]
        pT = [carve(5888 + 384 * x, 384) for x in range(4)]
        cosb, sinb = carve(7424, NT, 32), carve(7488, NT, 32)
        ang, tr1 = carve(7552, NT, 32), carve(7616, NT, 32)
        posf = tiny(0, NT)
        amax, asum = tiny(2, 4, 2), tiny(10, 2, 2, 2)
        posi = sb("posi", [P, NT], I32)
        pos_loaded = sem("pos_loaded")
        sin_arg, sin_done = sem("sin_arg"), sem("sin_done")
        rot_ready, qk_turned, qk_copied, scored, maxed, exped, p_turned, p_copied, pv_done, att_ready = (
            sem(s) for s in ("rot_ready", "qk_turned", "qk_copied", "scored", "maxed", "exped", "p_turned",
                             "p_copied", "pv_done", "att_ready"))
        turn_att = Turn(yatt, None, t0h, t0l)
        merged = proj[:, :, C_GS:C_GS + D]
        att_merged = sem("att_merged")
        turn_m = Turn(merged, None, t0h, t0l)
        mixed = sem("mixed")

        PAIRS = NH // 2

        def in_views(q, j):
            v = A["w_in"][0].rearrange("(p k) n -> p k n", k=KC)
            return v[:, 2 * q:2 * q + 2, ds(IN_TW * j, IN_TW)]

        def sp_block1(sp):
            sp.dma_start(xres[:, :, :], A["x"][0].rearrange("(t p) n -> p t n", p=P)).then_inc(x_loaded, 16)
            for q in range(4):
                load(sp, q, [(pair_view(raw, q, IN_TW), in_views(q, 0))])
            with sp.Fori(1, IN_T) as j:
                for q in range(4):
                    load(sp, 4 + q, [(pair_view(raw, q, IN_TW), in_views(q, j))], i=j - 1, per=4)
            load_square(sp, Q_SSD, A["w_ssd_out"][0])
            load_square(sp, Q_ATT, A["w_attn_out"][0])
            load_square(sp, Q_OUT, A["w_out"][0])

        def row(ap, n):
            return ap.rearrange("(a n) -> a n", a=1).to_broadcast([P, n])

        def act_loads(act):
            act.dma_start(const[:, :], A["const"]).then_inc(consts_loaded, 16)
            for j, name in enumerate(NORMS):
                v = A[name][0]
                act.dma_start(cols[:, j, :], v.rearrange("(p k) -> p k", k=KC)).then_inc(vec_loaded, 16)
            act.dma_start(rows[0:40, :], A["conv_w"][0].rearrange("w (k p) -> (w k) p", p=P)).then_inc(vec_loaded, 16)
            act.dma_start(rows[40:50, :], A["conv_b"][0].rearrange("(k p) -> k p", p=P)).then_inc(vec_loaded, 16)
            for dst, name in ((dtb, "dt_bias"), (alog, "a_log"), (dsk, "d_skip")):
                act.dma_start(dst, row(A[name][0], NH)).then_inc(vec_loaded, 16)
            act.dma_start(mul[:, :, :], A["mu_lora_2"][0].rearrange("a (p k) -> p a k", k=KC)).then_inc(vec_loaded, 16)
            with nc.allow_non_contiguous_dma(reason="256 positions, one per partition"):
                act.dma_start(posi[:, :], A["positions"][0].rearrange("(t p) -> p t", p=P)).then_inc(pos_loaded, 16)

        N_VEC = 16 * (len(NORMS) + 6)

        def pool_stream(pool):
            with pool.Fori(0, IN_T) as j:
                for q in range(4):
                    split_low(pool, q, j, 4, 2 * IN_TW)
            with pool.Fori(0, (Q_MOE - Q_SSD) // 4 - 1) as j:
                for q in range(4):
                    split_low(pool, Q_SSD + q, j, 4)
            with pool.Fori(0, (Q_PLE - Q_MOE) // 4 + 1) as j:
                for q in range(0, 4, 2):
                    split_low(pool, Q_MOE - RING + q, j, 4)
            with pool.Fori(0, (Q_END_RUN - Q_PLE) // 4) as j:
                for q in range(4):
                    split_low(pool, Q_PLE + q, j, 4)
            for n in range(Q_END_RUN - (Q_END_RUN - Q_PLE) % 4, Q_END_RUN):
                split_low(pool, n)

        def pe_in(pe):
            pe.wait_ge(consts_loaded, 16)
            turn_a.pe(pe, [norm_a.ready()])
            pe.wait_ge(*turn_a.done())

            def tile(j, c):
                b = bank[2 * c:2 * c + 2]
                wait_from(pe, evac_in, NT * (j - 1))
                for q in range(4):
                    i = 0 if isinstance(j, int) else j
                    wide_quarter(pe, (4 * j if isinstance(j, int) else 0) + q, q, b, t0h, t0l, IN_TW, i,
                                 0 if isinstance(j, int) else 4)

            tile(0, 0)
            tile(1, 1)
            with pe.Fori(1, IN_T // 2) as i:
                for c in range(2):
                    tile(2 * i + c, c)
            tile(IN_T - 1, 0)

        def act_in(act):
            for q in range(4):
                split_high(act, q, width=2 * IN_TW)

            def evac(j, c):
                act.wait_ge(quarter_done, 4 * j + 4)
                for t in range(NT):
                    nc.scalar.copy(proj[:, t, ds(IN_TW * j, IN_TW)], bank[2 * c + t][:, 0:IN_TW]).then_inc(evac_in, 1)

            with act.Fori(0, IN_T // 2) as i:
                for c in range(2):
                    j = 2 * i + 1 + c
                    for q in range(4):
                        split_high(act, 4 * (1 + c) + q, i, 8, 2 * IN_TW)
                    evac(j - 1, c)
            for q in range(4):
                split_high(act, Q_SSD + q)
            evac(IN_T - 1, 0)

        def pe_ssd(pe):
            pe.wait_ge(evac_in, NT * IN_T)
            pe.wait_ge(vec_loaded, N_VEC)
            nc.tensor.transpose(bank[1][:, 0:50], rows[0:50, :], ident[0:50, 0:50]).then_inc(taps_turned, 1)
            pe.wait_ge(*turn_a.done())
            for b in range(XCH // 2):
                dst = bank[4 + b] if b < 4 else bank[0]
                for kk in range(2):
                    for t in range(NT):
                        c = C_XBC + (2 * b + kk) * P
                        tr = nc.tensor.transpose(dst[:, kk * SEQ + t * P:kk * SEQ + (t + 1) * P],
                                                 proj[:, t, c:c + P], ident)
                tr.then_inc(xbc_turned, 1)
            pe.wait_ge(dA_ready, 1)
            for t in range(NT):
                nc.tensor.matmul(bank[3][:, 32 * t:32 * t + 16], con("tri"), dA[:, t, :], start=True, stop=True)
                mm = nc.tensor.matmul(bank[3][:, 32 * t + 16:32 * t + 32], con("ones"), dA[:, t, :],
                                      start=True, stop=True)
            mm.then_inc(cum_done, 1)
            pe.wait_ge(conv_active, XCH)
            pe.wait_ge(xbc_copied, XCH // 2)
            pe.wait_ge(taps_ready, 1)
            for t in range(NT):
                for h in range(2):
                    for c in range(4):
                        tr = nc.tensor.transpose(bank[4 + 2 * t + h][:, c * P:(c + 1) * P],
                                                 convT[:, 4 * h + c, t * P:(t + 1) * P], ident)
                    tr.then_inc(x_back, 1)
            nc.tensor.transpose(bank[1][:, 0:P], convT[:, 8, 0:P], ident)
            pe.wait_ge(cum_ready, 1)
            for g in range(2):
                for t in range(NT):
                    mm = nc.tensor.matmul(bank[2 + g][:, (1 + t) * P:(2 + t) * P],
                                          convT[64 * g:64 * g + 64, 8, t * P:(t + 1) * P],
                                          convT[64 * g:64 * g + 64, 9, t * P:(t + 1) * P], start=True, stop=True)
            mm.then_inc(cb_done, 1)
            pe.wait_ge(xdt_ready, 1)
            for g in range(2):
                mm = nc.tensor.matmul(bank[0][64 * g:64 * g + 64, :], btok[:, 64 * g:64 * g + 64],
                                      xdtd[:, 512 * g:512 * g + 512], start=True, stop=True)
            mm.then_inc(state_done, 1)
            pe.wait_ge(state_ready, 1)
            for g in range(2):
                mm = nc.tensor.matmul(bank[6 + g][:, :], convT[64 * g:64 * g + 64, 9, P:2 * P],
                                      prevT[64 * g:64 * g + 64, :], start=True, stop=True)
            mm.then_inc(off_done, 1)

            def sums(q):
                for t in range(NT):
                    wait_from(pe, dif_ready, 2 * (q - 1) + t + 1)
                    for h in range(4):
                        e = 4 * q + h
                        mm = nc.tensor.matmul(bank[t][:, h * P:(h + 1) * P],
                                              dA[:, t, e:e + 1].to_broadcast([P, P]), con("tri"),
                                              start=True, stop=True)
                    mm.then_inc(abc_done, 1)

            def diagonal(q):
                for t in range(NT):
                    pe.wait_ge(mt_ready, 2 * q + t + 1)
                    wait_from(pe, y_ready, 2 * (q - 1) + t + 1)
                    for h in range(4):
                        e = 4 * q + h
                        mm = nc.tensor.matmul(bank[4 + t][:, h * DH:(h + 1) * DH], mt[:, t, h, :],
                                              xdt[:, t, e * DH:(e + 1) * DH], start=True, stop=True)
                    mm.then_inc(diag_done, 1)

            sums(0)
            for q in range(4):
                if q < 3:
                    sums(q + 1)
                diagonal(q)
            turn_y.pe(pe, [(y_normed, 4)])
            square_product(pe, Q_SSD, t0h, t0l, [turn_y.done(), (dif_ready, 8)])

        def dve_ssd(dve, order):
            dve.wait_ge(vec_loaded, N_VEC)
            dve.wait_ge(evac_in, NT * IN_T)
            order.mark(nc.vector.memset(xbcT[:, :, 0:PAD], 0.0))
            order.step(nc.vector.tensor_tensor(s_raw, proj[:, :, C_DT:C_DT + NH],
                                               dtb.unsqueeze(1).to_broadcast([P, NT, NH]), ALU.add))
            nc.vector.scalar_tensor_tensor(out=s_neg, in0=s_raw, scalar=-1.0, in1=s_raw, op0=ALU.mult,
                                           op1=ALU.min).then_inc(dt_arg, 1)
            dve.wait_ge(taps_turned, 1)
            nc.vector.tensor_copy(cwT, bank[1][:, 0:50]).then_inc(taps_ready, 1)
            for b in range(XCH // 2):
                dve.wait_ge(xbc_turned, b + 1)
                src = (bank[4 + b] if b < 4 else bank[0])[:, :].rearrange("p (k s) -> p k s", k=2)
                nc.vector.tensor_copy(xbcT[:, 2 * b:2 * b + 2, PAD:PAD + SEQ], src).then_inc(xbc_copied, 1)
            dve.wait_ge(xbc_copied, XCH // 2)
            dve.wait_ge(taps_ready, 1)
            for w in range(4):
                for c in range(XCH):
                    tap = cwT[:, w * XCH + c:w * XCH + c + 1]
                    if w == 0:
                        order.mark(nc.vector.tensor_scalar(convT[:, c, :], xbcT[:, c, 0:SEQ], tap, None, ALU.mult))
                    else:
                        ins = nc.vector.scalar_tensor_tensor(out=convT[:, c, :], in0=xbcT[:, c, w:w + SEQ], scalar=tap,
                                                             in1=convT[:, c, :], op0=ALU.mult, op1=ALU.add)
                        if w < 3:
                            order.mark(ins)
                        else:
                            ins.then_inc(conv_done, 1)
                order.settle()
            dve.wait_ge(dt_exp, 2)
            order.step(nc.vector.tensor_scalar(s_u, s_exp, 1.0, None, ALU.add))
            order.step(nc.vector.tensor_scalar(dt, s_u, 1.0, None, ALU.subtract))
            order.mark(nc.vector.reciprocal(dA, s_u))
            order.step(nc.vector.tensor_tensor(dt, s_exp, dt, ALU.subtract))
            nc.vector.tensor_tensor(dt, dt, dA, ALU.mult).then_inc(dt_ln_arg, 1)
            dve.wait_ge(dt_ln_arg, 1)
            dve.wait_ge(dt_ln, 1)
            order.step(nc.vector.tensor_tensor(dt, dt, s_neg, ALU.add))
            order.step(nc.vector.scalar_tensor_tensor(out=dt, in0=s_raw, scalar=0.0, in1=dt, op0=ALU.max, op1=ALU.add))
            nc.vector.scalar_tensor_tensor(out=dA, in0=dt, scalar=-1.0,
                                           in1=alog.unsqueeze(1).to_broadcast([P, NT, NH]),
                                           op0=ALU.mult, op1=ALU.mult).then_inc(dA_ready, 1)
            dve.wait_ge(cum_done, 1)
            nc.vector.tensor_copy(cum, bank[3][:, 0:64].rearrange("p (t a h) -> p t a h", t=NT, a=2)).then_inc(cum_ready, 1)
            dve.wait_ge(cum_ready, 1)
            nc.vector.tensor_tensor(edec, cum[:, 0, 1, :], cum[:, 0, 0, :], ALU.subtract).then_inc(dec_arg, 1)
            for t in range(NT):
                for h in range(2):
                    dve.wait_ge(x_back, 2 * t + h + 1)
                    src = bank[4 + 2 * t + h]
                    order.mark(nc.vector.tensor_copy(xs[:, t, 512 * h:512 * h + 512], src[:, :]))
                    order.mark(nc.vector.tensor_tensor(
                        xdt[:, t, 512 * h:512 * h + 512].rearrange("p (e d) -> p e d", d=DH),
                        src[:, :].rearrange("p (e d) -> p e d", d=DH),
                        dt[:, t, 8 * h:8 * h + 8].unsqueeze(2).to_broadcast([P, 8, DH]), ALU.mult))
            dve.wait_ge(cb_done, 1)
            order.mark(nc.vector.tensor_copy(btok, bank[1][:, 0:P]))
            for g in range(2):
                order.mark(nc.vector.tensor_tensor(cbm[:, 2 * g:2 * g + 2, :],
                                                   bank[2 + g][:, P:3 * P].rearrange("p (a l) -> p a l", a=2),
                                                   con("tri").unsqueeze(1).to_broadcast([P, 2, P]), ALU.mult))
            order.settle()
            dve.wait_ge(dec_ready, 2)
            nc.vector.tensor_tensor(xdtd.rearrange("p (e d) -> p e d", d=DH),
                                    xdt[:, 0, :].rearrange("p (e d) -> p e d", d=DH),
                                    edec.unsqueeze(2).to_broadcast([P, NH, DH]), ALU.mult).then_inc(xdt_ready, 1)
            dve.wait_ge(state_done, 1)
            nc.vector.tensor_copy(prevT, bank[0][:, :]).then_inc(state_ready, 1)
            for t in range(NT):
                order.mark(nc.vector.tensor_tensor(y[:, t, :].rearrange("p (e d) -> p e d", d=DH),
                                                   xs[:, t, :].rearrange("p (e d) -> p e d", d=DH),
                                                   dsk.unsqueeze(2).to_broadcast([P, NH, DH]), ALU.mult))
            dve.wait_ge(off_done, 1)
            for g in range(2):
                order.mark(nc.vector.tensor_tensor(xdtd[:, 512 * g:512 * g + 512].rearrange("p (e d) -> p e d", d=DH),
                                                   bank[6 + g][:, :].rearrange("p (e d) -> p e d", d=DH),
                                                   ecum[:, 1, 8 * g:8 * g + 8].unsqueeze(2).to_broadcast([P, 8, DH]),
                                                   ALU.mult))
            order.settle()
            order.step(nc.vector.tensor_tensor(y[:, 1, :], y[:, 1, :], xdtd, ALU.add))

            def differences(q):
                for t in range(NT):
                    dve.wait_ge(abc_done, 2 * q + t + 1)
                    wait_from(dve, mt_ready, 2 * (q - 1) + t + 1)
                    for h in range(4):
                        e = 4 * q + h
                        ins = nc.vector.tensor_scalar(dif[:, t, h, :], bank[t][:, h * P:(h + 1) * P],
                                                      cum[:, t, 0, e:e + 1], 0.0, ALU.subtract, ALU.min)
                        if h < 3:
                            order.mark(ins)
                    ins.then_inc(dif_ready, 1)

            def add_diagonal(q):
                for t in range(NT):
                    dve.wait_ge(diag_done, 2 * q + t + 1)
                    o = y[:, t, 256 * q:256 * q + 256]
                    nc.vector.tensor_tensor(o, o, bank[4 + t][:, 0:256], ALU.add).then_inc(y_ready, 1)

            for q in range(4):
                differences(q)
                if q:
                    add_diagonal(q - 1)
                for t in range(NT):
                    dve.wait_ge(lmat_ready, 2 * q + t + 1)
                    nc.vector.tensor_tensor(mt[:, t], dif[:, t],
                                            cbm[:, 2 * (q // 2) + t, :].unsqueeze(1).to_broadcast([P, 4, P]),
                                            ALU.mult).then_inc(mt_ready, 1)
            add_diagonal(3)
            dve.wait_ge(z_active, NT)
            dve.wait_ge(y_ready, 8)
            for t in range(NT):
                nc.vector.tensor_tensor(y[:, t, :], y[:, t, :], proj[:, t, C_Z:C_Z + D], ALU.mult).then_inc(y_gated, 1)
            dve.wait_ge(y_squared, 4)
            nc.vector.tensor_scalar(stat[:, 0:4], stat[:, 0:4], 1.0 / 512, EPS, ALU.mult, ALU.add).then_inc(y_mean, 1)
            dve.wait_ge(y_root, 1)
            order.step(nc.vector.reciprocal(stat[:, 0:4], stat[:, 0:4]))
            for t in range(NT):
                for g in range(2):
                    o = y[:, t, 512 * g:512 * g + 512]
                    nc.vector.tensor_scalar(o, o, stat[:, 2 * t + g:2 * t + g + 1], None, ALU.mult).then_inc(y_normed, 1)
            turn_y.dve(dve)
            dve.wait_ge(gate_active, 4)
            for c in range(2):
                dve.wait_ge(quarter_done, Q_SSD + 4 * c + 4)
                for t in range(NT):
                    o = merged[:, t, c * TW:(c + 1) * TW]
                    nc.vector.tensor_tensor(o, o, bank[2 * c + t][:, :], ALU.mult).then_inc(ssd_merged, 1)

        def act_ssd(act):
            act.wait_ge(vec_loaded, N_VEC)
            act.wait_ge(dt_arg, 1)
            nc.scalar.activation(s_exp, s_neg, ACT.Exp).then_inc(dt_exp, 1)
            nc.scalar.activation(alog, alog, ACT.Exp).then_inc(dt_exp, 1)
            act.wait_ge(dt_ln_arg, 1)
            nc.scalar.activation(s_neg, s_u, ACT.Ln).then_inc(dt_ln, 1)
            for c in range(XCH):
                act.wait_ge(conv_done, c + 1)
                nc.scalar.activation(convT[:, c, :], convT[:, c, :], ACT.Silu,
                                     bias=cwT[:, 40 + c:41 + c]).then_inc(conv_active, 1)
            act.wait_ge(evac_in, NT * IN_T)
            for t in range(NT):
                z = proj[:, t, C_Z:C_Z + D]
                nc.scalar.activation(z, z, ACT.Silu).then_inc(z_active, 1)
            act.wait_ge(cum_ready, 1)
            nc.scalar.activation(ecum, cum[:, :, 0, :], ACT.Exp).then_inc(dec_ready, 1)
            act.wait_ge(dec_arg, 1)
            nc.scalar.activation(edec, edec, ACT.Exp).then_inc(dec_ready, 1)
            for q in range(4):
                for t in range(NT):
                    act.wait_ge(dif_ready, 2 * q + t + 1)
                    nc.scalar.activation(dif[:, t], dif[:, t], ACT.Exp).then_inc(lmat_ready, 1)
            act.wait_ge(y_gated, NT)
            act.wait_ge(diag_done, 8)
            for t in range(NT):
                for g in range(2):
                    nc.scalar.activation(xdt[:, t, 512 * g:512 * g + 512], y[:, t, 512 * g:512 * g + 512], ACT.Square,
                                         accum_out=stat[:, 2 * t + g:2 * t + g + 1]).then_inc(y_squared, 1)
            act.wait_ge(y_mean, 1)
            nc.scalar.activation(stat[:, 0:4], stat[:, 0:4], ACT.Sqrt).then_inc(y_root, 1)
            for c in (C_GS, C_GA):
                for t in range(NT):
                    g = proj[:, t, c:c + D]
                    nc.scalar.activation(g, g, ACT.Sigmoid).then_inc(gate_active, 1)
            turn_y.act(act, Q_SSD)
            for q in range(4, 8):
                split_high(act, Q_SSD + q)
            for q in range(4):
                split_high(act, Q_ATT + q)

        def dve_angles(dve, order):
            dve.wait_ge(pos_loaded, 16)
            dve.wait_ge(ssd_merged, 4)
            order.step(nc.vector.tensor_copy(posf, posi[:, :]))
            for t in range(NT):
                order.mark(nc.vector.tensor_scalar(ang[:, t, :], con("freq"), posf[:, t:t + 1], None, ALU.mult))
            order.settle()
            order.step(nc.vector.tensor_scalar(tr1, ang, 1.0 / TWO_PI, None, ALU.mult))
            order.step(nc.vector.tensor_scalar(tr1, tr1, 12582912.0, None, ALU.add))
            order.step(nc.vector.tensor_scalar(tr1, tr1, 12582912.0, None, ALU.subtract))
            c1 = 6.28125
            c2 = float(np.float32(np.round((TWO_PI - c1) * 2.0 ** 20) / 2.0 ** 20))
            c3 = TWO_PI - c1 - c2
            for c in (c1, c2, c3):
                order.step(nc.vector.scalar_tensor_tensor(out=ang, in0=tr1, scalar=-c, in1=ang, op0=ALU.mult, op1=ALU.add))
            top = float(np.nextafter(np.float32(math.pi), np.float32(0)))
            order.step(nc.vector.tensor_scalar(sinb, ang, top, -top, ALU.min, ALU.max))
            order.step(nc.vector.tensor_scalar(ang, ang, math.pi / 2, None, ALU.add))
            order.step(nc.vector.tensor_scalar(tr1, ang, math.pi, -TWO_PI, ALU.is_gt, ALU.mult))
            order.step(nc.vector.tensor_tensor(ang, ang, tr1, ALU.add))
            nc.vector.tensor_scalar(cosb, ang, top, -top, ALU.min, ALU.max).then_inc(sin_arg, 1)

        def act_angles(act):
            act.wait_ge(sin_arg, 1)
            nc.scalar.activation(sinb, sinb, ACT.Sin).then_inc(sin_done, 1)
            nc.scalar.activation(cosb, cosb, ACT.Sin).then_inc(sin_done, 1)

        ATT_DVE = 36

        def dve_attention(dve, order):
            dve.wait_ge(sin_done, 2)
            cos = cosb.unsqueeze(2).to_broadcast([P, NT, 2, 32])
            sin = sinb.unsqueeze(2).to_broadcast([P, NT, 2, 32])
            start = order.count()

            def body(i):
                order.body(start, i, ATT_DVE)
                for x in range(2):
                    for a, c in ((0, C_Q), (1, C_K)):
                        src = proj[:, :, ds(c + P * (2 * i + x), P)].rearrange("p t (h a d) -> p t h a d", h=2, a=2)
                        x1, x2 = src[:, :, :, 0, :], src[:, :, :, 1, :]
                        dst = rot[x][:, a].rearrange("p t (h a d) -> p t h a d", h=2, a=2)
                        o1, o2 = dst[:, :, :, 0, :], dst[:, :, :, 1, :]
                        order.mark(nc.vector.tensor_tensor(o1, x1, cos, ALU.mult))
                        order.mark(nc.vector.tensor_tensor(rtmp[0], x2, sin, ALU.mult))
                        order.mark(nc.vector.tensor_tensor(o2, x2, cos, ALU.mult))
                        order.step(nc.vector.tensor_tensor(rtmp[1], x1, sin, ALU.mult))
                        order.mark(nc.vector.tensor_tensor(o1, o1, rtmp[0], ALU.subtract))
                        last = nc.vector.tensor_tensor(o2, o2, rtmp[1], ALU.add)
                        if a == 0:
                            order.step(last)
                    last.then_inc(rot_ready, 1)
                    dve.wait_ge(rot_ready, 2 * i + x + 1)
                for z in range(4):
                    dve.wait_ge(scored, 4 * i + z + 1)
                    order.step(nc.vector.tensor_tensor(sc[z], bank[2 + z][:, 0:384], con("amask"), ALU.add))
                    order.mark(nc.vector.tensor_reduce(amax[:, z, 0:1], sc[z][:, 0:P], AX.X, ALU.max))
                    order.step(nc.vector.tensor_reduce(amax[:, z, 1:2], sc[z][:, P:384], AX.X, ALU.max))
                    nc.vector.tensor_scalar(amax[:, z, :], amax[:, z, :], -(DH ** -0.5), None, ALU.mult).then_inc(maxed, 1)
                for x in range(2):
                    dve.wait_ge(pv_done, 2 * i + x + 1)
                    order.step(nc.vector.reciprocal(asum[:, x], asum[:, x]))
                    nc.vector.tensor_tensor(
                        yatt[:, :, ds(P * (2 * i + x), P)].rearrange("p t (h d) -> p t h d", h=2),
                        bank[6 + x][:, 0:256].rearrange("p (h t d) -> p t h d", h=2, t=NT),
                        asum[:, x].unsqueeze(3).to_broadcast([P, NT, 2, DH]), ALU.mult).then_inc(att_ready, 1)

            body(0)
            with dve.Fori(1, PAIRS // 2) as i:
                body(i)
            order.after(start, PAIRS // 2, ATT_DVE)
            turn_att.dve(dve)
            for c in range(2):
                dve.wait_ge(quarter_done, Q_ATT + 4 * c + 4)
                for t in range(NT):
                    g = proj[:, t, C_GA + c * TW:C_GA + (c + 1) * TW]
                    order.step(nc.vector.tensor_tensor(g, g, bank[2 * c + t][:, :], ALU.mult))
                    o = merged[:, t, c * TW:(c + 1) * TW]
                    nc.vector.tensor_tensor(o, o, g, ALU.add).then_inc(att_merged, 1)
            turn_m.dve(dve)
            for c in range(2):
                split_low(dve, Q_OUT + 5 + 2 * c)
                dve.wait_ge(quarter_done, Q_OUT + 4 * c + 4)
                for t in range(NT):
                    o = xres[:, t, c * TW:(c + 1) * TW]
                    nc.vector.tensor_tensor(o, o, bank[2 * c + t][:, :], ALU.add).then_inc(mixed, 1)

        def act_attention(act):
            def body(i):
                for x in range(2):
                    act.wait_ge(qk_turned, 2 * i + x + 1)
                    nc.scalar.copy(qkT[x].rearrange("p a s -> p (a s)"), bank[x][:, :]).then_inc(qk_copied, 1)
                for z in range(4):
                    act.wait_ge(maxed, 4 * i + z + 1)
                    wait_from(act, att_ready, 2 * i)
                    x, h = z // 2, z % 2
                    nc.scalar.activation(sc[z][:, 0:P], sc[z][:, 0:P], ACT.Exp, bias=amax[:, z, 0:1], scale=DH ** -0.5,
                                         accum_out=asum[:, x, 0, h:h + 1]).then_inc(exped, 1)
                    nc.scalar.activation(sc[z][:, P:384], sc[z][:, P:384], ACT.Exp, bias=amax[:, z, 1:2],
                                         scale=DH ** -0.5, accum_out=asum[:, x, 1, h:h + 1]).then_inc(exped, 1)
                for z in range(4):
                    act.wait_ge(p_turned, 4 * i + z + 1)
                    nc.scalar.copy(pT[z], bank[2 + z][:, 0:384]).then_inc(p_copied, 1)

            body(0)
            with act.Fori(1, PAIRS // 2) as i:
                body(i)
            turn_att.act(act, Q_ATT)
            for q in range(4, 8):
                split_high(act, Q_ATT + q)
            for q in range(4):
                split_high(act, Q_OUT + q)
            turn_m.act(act, Q_OUT)
            for q in range(4, 8):
                split_high(act, Q_OUT + q)

        def pe_attention(pe):
            pe.wait_ge(ssd_merged, 4)

            def body(i):
                for x in range(2):
                    pe.wait_ge(rot_ready, 2 * i + x + 1)
                    for a in range(2):
                        for t in range(NT):
                            tr = nc.tensor.transpose(bank[x][:, (2 * a + t) * P:(2 * a + t + 1) * P], rot[x][:, a, t, :],
                                                     ident)
                    tr.then_inc(qk_turned, 1)
                for x in range(2):
                    pe.wait_ge(qk_copied, 2 * i + x + 1)
                    for h in range(2):
                        r = slice(64 * h, 64 * h + 64)
                        keys = qkT[x][r, 2:4, :].rearrange("p t s -> p (t s)")
                        b = bank[2 + 2 * x + h]
                        nc.tensor.matmul(b[:, 0:P], qkT[x][r, 0, :], keys[:, 0:P], start=True, stop=True)
                        nc.tensor.matmul(b[:, P:384], qkT[x][r, 1, :], keys, start=True, stop=True).then_inc(scored, 1)
                for z in range(4):
                    pe.wait_ge(exped, 8 * i + 2 * z + 2)
                    for blk in range(3):
                        tr = nc.tensor.transpose(bank[2 + z][:, blk * P:(blk + 1) * P], sc[z][:, blk * P:(blk + 1) * P],
                                                 ident)
                    tr.then_inc(p_turned, 1)
                for x in range(2):
                    wait_from(pe, att_ready, 2 * i)
                    for h in range(2):
                        z = 2 * x + h
                        pe.wait_ge(p_copied, 4 * i + z + 1)
                        c = C_V + P * (2 * i + x) + DH * h
                        o = bank[6 + x][:, h * P:(h + 1) * P]
                        nc.tensor.matmul(o[:, 0:DH], pT[z][:, 0:P], proj[:, 0, ds(c, DH)], start=True, stop=True)
                        nc.tensor.matmul(o[:, DH:P], pT[z][:, P:2 * P], proj[:, 0, ds(c, DH)], start=True, stop=False)
                        mm = nc.tensor.matmul(o[:, DH:P], pT[z][:, 2 * P:384], proj[:, 1, ds(c, DH)], start=False, stop=True)
                    mm.then_inc(pv_done, 1)

            body(0)
            with pe.Fori(1, PAIRS // 2) as i:
                body(i)
            turn_att.pe(pe, [(att_ready, PAIRS)])
            square_product(pe, Q_ATT, t0h, t0l, [turn_att.done()])
            turn_m.pe(pe, [(att_merged, 4)])
            square_product(pe, Q_OUT, t0h, t0l, [turn_m.done(), (att_merged, 4)])


        pw = proj[:, :, :].rearrange("p t n -> p (t n)")

        def lay(at, *shape):
            n = int(np.prod(shape))
            assert at + n <= NT * IN_W
            v = pw[:, at:at + n]
            if len(shape) == 1:
                return v
            names = "abcd"[:len(shape)]
            return v.rearrange(f"p ({' '.join(names)}) -> p {' '.join(names)}", **dict(zip(names, shape)))

        NG, EG = 4, 8
        JOBS = NG + 1
        xgf = lay(0, KC, P)
        pick = lay(1024, JOBS, NT, P)
        back = lay(2304, JOBS, NT, P)
        back_now = lay(3584, NT, P)
        ysum = lay(3840, D)
        sg = [lay(4864 + DE * x, DE) for x in range(2)]
        hid = [lay(5376 + DE * x, DE) for x in range(2)]
        comb = lay(5888, JOBS, EG)
        rw = lay(5928, KC, 36)
        rbias = lay(6216, 36)
        logit = lay(6252, NT, 36)
        one_g, key_g = lay(6324, NT, NG), lay(6332, NT, NG)
        key = lay(6340, NT, JOBS)
        eg = lay(6350, NT, NG, EG)
        el, one1, one2, tmp8 = (lay(6414 + 16 * j, NT, EG) for j in range(4))
        ew = lay(6478, NT, EG)
        r1 = [lay(6494 + 2 * j, NT) for j in range(8)]
        cnt, over = lay(6510, NG), lay(6514, NG)
        flagf = lay(6518, 2)
        flag = sb("flag", [P, 2], I32)
        rwh = sb("rwh", [P, KC, 36], F32R)
        rwl = sb("rwl", [P, KC, 36], F32R)
        zero = sb("zero", [P, P], F32R)
        emb = lay(6600, NT, DE)
        ple = lay(7112, NT, D)
        fnw = lay(9160, D)
        sgate = lay(10184, NT, D)
        norm_m = RmsNorm(xres, xn, stat)
        turn_e = Turn(xn, gain("moe_norm_w"), t0h, t0l)
        router_loaded, zeroed = sem("router_loaded"), sem("zeroed")
        rw_high, rw_low, logits_done = (sem(s) for s in ("rw_high", "rw_low", "logits_done"))
        exp_arg, exp_done, group_ready, ranked, picked = (
            sem(s) for s in ("exp_arg", "exp_done", "group_ready", "ranked", "picked"))
        e2_arg, e2_done, weights_ready, combed, comb_ready, back_turned, back_ready = (
            sem(s) for s in ("e2_arg", "e2_done", "weights_ready", "combed", "comb_ready", "back_turned", "back_ready"))
        gathered, xg_raw, xg_high, xg_low = (sem(s) for s in ("gathered", "xg_raw", "xg_high", "xg_low"))
        silu_done, hid_ready, hid_turned, hid_high, hid_low = (
            sem(s) for s in ("silu_done", "hid_ready", "hid_turned", "hid_high", "hid_low"))
        acc_zeroed, ysum_ready, back_copied, scattered, x_added = (
            sem(s) for s in ("acc_zeroed", "ysum_ready", "back_copied", "scattered", "x_added"))
        flag_ready = sem("flag_ready")
        ov = {s: sem("over_" + s) for s in ("loaded", "up", "silu", "hid", "turned", "copied", "down", "summed",
                                            "zeroed", "scattered", "added")}

        def gu_loads(sp, n, e, q, u=0, per=0):
            pairs = []
            for j, name in enumerate(("w_exp_gate", "w_exp_up")):
                v = A[name][0].rearrange("g e (p k) n -> p (g e) k n", k=KC)[:, ds(e, 1), 2 * q:2 * q + 2, :]
                dst = raw[:, n % RING, 512 * j:512 * j + 512].rearrange("p (a k n) -> p a k n", a=1, k=2)
                pairs.append((dst, v))
            load(sp, n, pairs, u, per)

        def down_load(sp, n, e, c, u=0, per=0):
            v = A["w_exp_down"][0].rearrange("g e (p k) n -> p (g e) k n", k=2)[:, ds(e, 1), c:c + 1, :]
            load(sp, n, [(raw[:, n % RING, :].rearrange("p (a k n) -> p a k n", a=1, k=1), v)], u, per)

        U = 12

        def jobs(eng, job):
            with eng.Fori(0, NG // 2) as jj:
                for par in range(2):
                    job(2 * jj + par, par, Q_MOE + JOB * par, 8 * jj)

        def sp_experts(sp):
            def job(J, par, n, u):
                for q in range(4):
                    gu_loads(sp, n + q, EG * J, q, u, U)
                with sp.Fori(0, 3) as i:
                    for b in range(2):
                        m = n + 4 + 6 * b
                        for q in range(4):
                            gu_loads(sp, m + q, EG * J + 2 * i + b + 1, q, u + i, U)
                        for c in range(2):
                            down_load(sp, m + 4 + c, EG * J + 2 * i + b, c, u + i, U)
                m = n + 40
                for q in range(4):
                    gu_loads(sp, m + q, EG * J + 7, q, u, U)
                for c in range(2):
                    down_load(sp, m + 4 + c, EG * J + 6, c, u, U)
                for c in range(2):
                    down_load(sp, m + 6 + c, EG * J + 7, c, u, U)

            jobs(sp, job)

        def router_loads(act):
            act.wait_ge(att_merged, 4)
            v = A["w_router_group"][0].rearrange("(p k) n -> p k n", k=KC)
            act.dma_start(rw[:, :, 0:NG], v).then_inc(router_loaded, 16)
            v = A["w_router_expert"][0].rearrange("(p k) n -> p k n", k=KC)
            act.dma_start(rw[:, :, NG:36], v).then_inc(router_loaded, 16)
            act.dma_start(rbias[:, 0:NG], row(A["b_router_group"][0], NG)).then_inc(router_loaded, 16)
            act.dma_start(rbias[:, NG:36], row(A["b_router_expert"][0], 32)).then_inc(router_loaded, 16)
            act.dma_start(emb[:, :, :], A["p"][0, 0].rearrange("(t p) n -> p t n", p=P)).then_inc(router_loaded, 16)
            act.dma_start(fnw, row(A["final_norm_w"], D)).then_inc(router_loaded, 16)

        def act_router(act):
            act.wait_ge(router_loaded, 96)
            nc.scalar.activation(rwh[:, :, :], rw, ACT.Copy).then_inc(rw_high, 1)
            norm_m.act(act, [(mixed, 4)])
            turn_e.act(act, Q_MOE)
            act.wait_ge(exp_arg, 1)
            nc.scalar.activation(key_g, key_g, ACT.Exp).then_inc(exp_done, 1)
            act.wait_ge(e2_arg, 1)
            nc.scalar.activation(r1[4], r1[4], ACT.Exp).then_inc(e2_done, 1)

        def pe_router(pe):
            turn_e.pe(pe, [norm_m.ready(), (mixed, 4)])
            pe.wait_ge(rw_low, 1)
            pe.wait_ge(*turn_e.done())
            for t in range(NT):
                for k in range(KC):
                    mm = times(bank[t][:, 0:36], t0h[:, k, t * P:(t + 1) * P], t0l[:, k, t * P:(t + 1) * P],
                               rwh[:, k, :], rwl[:, k, :], k == 0, k == KC - 1)
            mm.then_inc(logits_done, 1)
            pe.wait_ge(group_ready, 1)
            nc.tensor.matmul(bank[2][:, 0:NG], con("strict"), one_g[:, 0, :], start=True, stop=True)
            nc.tensor.matmul(bank[2][:, NG:2 * NG], con("strict"), one_g[:, 1, :], start=True, stop=False)
            nc.tensor.matmul(bank[2][:, NG:2 * NG], con("ones"), one_g[:, 0, :], start=False, stop=True)
            nc.tensor.matmul(bank[2][:, 2 * NG:3 * NG], con("ones"), one_g[:, 0, :], start=True, stop=False)
            nc.tensor.matmul(bank[2][:, 2 * NG:3 * NG], con("ones"), one_g[:, 1, :], start=False, stop=True
                             ).then_inc(ranked, 1)
            pe.wait_ge(picked, 1)
            for j in range(JOBS):
                for t in range(NT):
                    at = (j % 2) * SEQ + t * P
                    tr = nc.tensor.transpose(bank[(0, 1, 3)[j // 2]][:, at:at + P], pick[:, j, t, :], ident)
            tr.then_inc(back_turned, 1)
            pe.wait_ge(weights_ready, 1)
            for j in range(JOBS):
                for t in range(NT):
                    mm = nc.tensor.matmul(bank[2][:, 16 + EG * j:16 + EG * (j + 1)], pick[:, j, t, :], ew[:, t, :],
                                          start=t == 0, stop=t == NT - 1)
            mm.then_inc(combed, 1)

        def dve_router(dve, order):
            dve.wait_ge(rw_high, 1)
            nc.vector.tensor_tensor(rwl[:, :, :], rw, rwh[:, :, :].bitcast(F32), ALU.subtract).then_inc(rw_low, 1)
            norm_m.dve(dve, order)
            turn_e.dve(dve)
            nc.vector.memset(zero[:, :].bitcast(F32), 0.0).then_inc(zeroed, 1)
            for h in range(2):
                nc.vector.memset(ysum[:, 512 * h:512 * h + 512], 0.0).then_inc(ysum_ready, 1)
            nc.vector.memset(back_now, 0.0).then_inc(back_copied, 1)
            dve.wait_ge(logits_done, 1)
            for t in range(NT):
                order.mark(nc.vector.tensor_tensor(logit[:, t, :], bank[t][:, 0:36], rbias, ALU.add))
            order.settle()
            gl = logit[:, :, 0:NG]
            ex = logit[:, :, NG:36].rearrange("p t (g e) -> p t g e", g=NG)

            def wide(v, n):
                return v.unsqueeze(2).to_broadcast([P, NT, n])

            def first_max(hot, val, top, tmp, rev, n):
                order.step(nc.vector.tensor_reduce(top, val, AX.X, ALU.max))
                order.step(nc.vector.tensor_tensor(tmp, val, wide(top, n), ALU.is_equal))
                order.step(nc.vector.tensor_tensor(tmp, tmp, con(rev).unsqueeze(1).to_broadcast([P, NT, n]), ALU.mult))
                order.step(nc.vector.tensor_reduce(r1[7], tmp, AX.X, ALU.max))
                order.step(nc.vector.tensor_tensor(hot, tmp, wide(r1[7], n), ALU.is_equal))

            first_max(one_g, gl, r1[0], key_g, "rev4", NG)
            nc.vector.tensor_tensor(key_g, gl, wide(r1[0], NG), ALU.subtract).then_inc(exp_arg, 1)
            order.step(nc.vector.tensor_tensor(eg, ex, one_g.unsqueeze(3).to_broadcast([P, NT, NG, EG]), ALU.mult))
            nc.vector.tensor_reduce(el, eg.rearrange("p t g e -> p t e g"), AX.X, ALU.add).then_inc(group_ready, 1)
            dve.wait_ge(group_ready, 1)
            first_max(one1, el, r1[1], tmp8, "rev8", EG)
            order.step(nc.vector.scalar_tensor_tensor(out=el, in0=one1, scalar=-3e38, in1=el, op0=ALU.mult, op1=ALU.add))
            first_max(one2, el, r1[2], tmp8, "rev8", EG)
            nc.vector.tensor_tensor(r1[4], r1[2], r1[1], ALU.subtract).then_inc(e2_arg, 1)
            dve.wait_ge(ranked, 1)
            dve.wait_ge(exp_done, 1)
            order.step(nc.vector.tensor_reduce(r1[3], key_g, AX.X, ALU.add))
            order.mark(nc.vector.reciprocal(r1[3], r1[3]))
            order.mark(nc.vector.tensor_copy(cnt, bank[2][:, 2 * NG:3 * NG]))
            order.step(nc.vector.scalar_tensor_tensor(out=key_g, in0=bank[2][:, 0:2 * NG].rearrange("p (t g) -> p t g", t=NT),
                                                      scalar=1.0, in1=one_g, op0=ALU.add, op1=ALU.mult))
            order.mark(nc.vector.tensor_reduce(key[:, :, NG], key_g, AX.X, ALU.add))
            order.step(nc.vector.tensor_scalar(key[:, :, 0:NG], key_g, 1.0, None, ALU.subtract))
            order.step(nc.vector.tensor_scalar(key[:, :, NG], key[:, :, NG], float(P + 1), None, ALU.subtract))
            for j in range(JOBS):
                for t in range(NT):
                    ins = nc.vector.tensor_scalar(pick[:, j, t, :], con("slot"), key[:, t, j:j + 1], None, ALU.is_equal)
                    if (j, t) != (JOBS - 1, NT - 1):
                        order.mark(ins)
            ins.then_inc(picked, 1)
            dve.wait_ge(e2_done, 1)
            order.step(nc.vector.tensor_scalar(r1[5], r1[4], 1.0, None, ALU.add))
            order.step(nc.vector.reciprocal(r1[5], r1[5]))
            order.step(nc.vector.tensor_tensor(r1[5], r1[5], r1[3], ALU.mult))
            order.mark(nc.vector.tensor_tensor(r1[6], r1[5], r1[4], ALU.mult))
            order.step(nc.vector.tensor_tensor(ew, one1, wide(r1[5], EG), ALU.mult))
            order.step(nc.vector.tensor_tensor(tmp8, one2, wide(r1[6], EG), ALU.mult))
            nc.vector.tensor_tensor(ew, ew, tmp8, ALU.add).then_inc(weights_ready, 1)
            order.step(nc.vector.tensor_scalar(over, cnt, P + 0.5, None, ALU.is_gt))
            order.mark(nc.vector.tensor_reduce(flagf[:, 0:1], over, AX.X, ALU.max))
            order.step(nc.vector.tensor_scalar(cnt, con("rev4"), -1.0, float(NG), ALU.mult, ALU.add))
            order.step(nc.vector.tensor_tensor(cnt, cnt, over, ALU.mult))
            order.step(nc.vector.tensor_reduce(flagf[:, 1:2], cnt, AX.X, ALU.add))
            nc.vector.tensor_copy(flag[:, :], flagf).then_inc(flag_ready, 1)
            dve.wait_ge(back_turned, 1)
            for j in range(0, JOBS, 2):
                n = min(2, JOBS - j)
                order.mark(nc.vector.tensor_copy(back[:, j:j + n].rearrange("p j t s -> p (j t s)"),
                                                 bank[(0, 1, 3)[j // 2]][:, 0:n * SEQ]))
            nc.vector.tensor_copy(logit[:, 0, 0:1], flagf[:, 0:1]).then_inc(back_ready, 1)
            dve.wait_ge(combed, 1)
            nc.vector.tensor_copy(comb.rearrange("p j e -> p (j e)"), bank[2][:, 16:16 + EG * JOBS]).then_inc(comb_ready, 1)
            for b in range(2):
                nc.vector.memset(hid[b], 0.0).then_inc(hid_ready, 1)
            dve.wait_ge(hid_ready, 2)

        def pe_gather(J):
            for b in range(2):
                for kk in range(4):
                    for t in range(NT):
                        mm = nc.tensor.matmul(bank[6 + b][:, kk * P:(kk + 1) * P],
                                              xn.rearrange("p t (f k) -> p t f k", k=KC)[:, t, :, 4 * b + kk],
                                              pick[:, ds(J, 1), t, :].rearrange("p a s -> p (a s)"),
                                              start=t == 0, stop=t == NT - 1)
                mm.then_inc(gathered, 1)

        def dve_gather(dve, J):
            g = gain("moe_norm_w")
            for b in range(2):
                dve.wait_ge(gathered, 2 * J + b + 1)
                nc.vector.tensor_tensor(xgf[:, 4 * b:4 * b + 4, :], bank[6 + b][:, :].rearrange("p (k s) -> p k s", k=4),
                                        g[:, 4 * b:4 * b + 4].unsqueeze(2).to_broadcast([P, 4, P]),
                                        ALU.mult).then_inc(xg_raw, 1)

        def act_gather(act, J, par):
            act.wait_ge(xg_raw, 2 * J + 2)
            nc.scalar.activation(t0h[:, :, par * P:(par + 1) * P], xgf, ACT.Copy).then_inc(xg_high, 1)

        def dve_gather_low(dve, J, par):
            dve.wait_ge(xg_high, J + 1)
            s = slice(par * P, (par + 1) * P)
            nc.vector.tensor_tensor(t0l[:, :, s], xgf, t0h[:, :, s].bitcast(F32), ALU.subtract).then_inc(xg_low, 1)

        def pe_experts(pe):
            pe.wait_ge(zeroed, 1)
            pe.wait_ge(picked, 1)
            pe.wait_ge(*turn_e.done())
            pe_gather(0)

            def gate_up(n, q, E, e_par, par, u, per):
                if q == 0:
                    pe.wait_ge(hid_ready, E + 1)
                wait_low(pe, n, u, per)
                s = n % RING
                wh, wl = (w[:, s, :].rearrange("p (a k n) -> p a k n", a=2, k=2) for w in (whi, wlo))
                dst = bank[e_par][:, :].rearrange("p (a n) -> p a n", a=2)
                r = slice(par * P, (par + 1) * P)
                for kk in range(2):
                    k = 2 * q + kk
                    mm = times(dst, t0h[:, k, r], t0l[:, k, r], wh[:, :, kk, :], wl[:, :, kk, :], k == 0, k == KC - 1)
                mm.then_inc(quarter_done, 1)

            def turn_hidden(E, e_par):
                pe.wait_ge(hid_ready, E + 3)
                for c in range(2):
                    tr = nc.tensor.transpose(bank[2][:, c * P:(c + 1) * P],
                                             hid[e_par].rearrange("p (f c) -> p f c", c=2)[:, :, c], ident)
                tr.then_inc(hid_turned, 1)

            def down(n, c, E, e_par, u, per, last):
                if c == 0:
                    pe.wait_ge(hid_low, E + 1)
                wait_low(pe, n, u, per)
                s = n % RING
                for h in range(2):
                    f = slice(512 * h, 512 * h + 512)
                    hh, hl = t1h[:, 2 * e_par + c, 0:P], t1l[:, 2 * e_par + c, 0:P]
                    nc.tensor.matmul(bank[4 + h][:, :], hh, whi[:, s, f], start=False, stop=False, skip_group_check=True)
                    nc.tensor.matmul(bank[4 + h][:, :], hh, wlo[:, s, f], start=False, stop=False, skip_group_check=True)
                    mm = nc.tensor.matmul(bank[4 + h][:, :], hl, whi[:, s, f], start=False, stop=last,
                                          skip_group_check=True)
                mm.then_inc(quarter_done, 1)

            def job(J, par, n, u):
                pe.wait_ge(xg_low, J + 1)
                for q in range(4):
                    gate_up(n + q, q, EG * J, 0, par, u, U)
                pe_scatter(pe, J)
                for h in range(2):
                    nc.tensor.matmul(bank[4 + h][:, :].rearrange("p (k s) -> p k s", k=4), zero[:, :],
                                     t0h[:, 0:4, par * P:(par + 1) * P], start=True, stop=False, skip_group_check=True)
                with pe.Fori(0, 3) as i:
                    for b in range(2):
                        E, m = EG * J + 2 * i + b, n + 4 + 6 * b
                        for q in range(4):
                            gate_up(m + q, q, E + 1, 1 - b, par, u + i, U)
                            if q == 1:
                                turn_hidden(E, b)
                        for c in range(2):
                            down(m + 4 + c, c, E, b, u + i, U, False)
                E, m = EG * J + 6, n + 40
                for q in range(4):
                    gate_up(m + q, q, E + 1, 1, par, u, U)
                    if q == 1:
                        turn_hidden(E, 0)
                for c in range(2):
                    down(m + 4 + c, c, E, 0, u, U, False)
                pe.wait_ge(x_added, 4 * J + 4)
                pe_gather(J + 1)
                turn_hidden(E + 1, 1)
                for c in range(2):
                    down(m + 6 + c, c, E + 1, 1, u, U, c == 1)

            jobs(pe, job)
            pe_scatter(pe, NG)

        def pe_scatter(pe, J):
            pe.wait_ge(ysum_ready, 2 * J + 2)
            pe.wait_ge(back_copied, J + 1)
            pe.wait_ge(xg_raw, 2 * J + 2)
            for z in range(4):
                t, h = z // 2, z % 2
                if z == 3:
                    pe.wait_ge(x_added, 4 * J + 1)
                nc.tensor.matmul(bank[(3, 6, 7, 3)[z]][:, :], back_now[:, t, :], ysum[:, 512 * h:512 * h + 512],
                                 start=True, stop=True).then_inc(scattered, 1)

        def dve_scatter(dve, J):
            for z in range(4):
                t, h = z // 2, z % 2
                dve.wait_ge(scattered, 4 * J + z + 1)
                o = xres[:, t, 512 * h:512 * h + 512]
                nc.vector.tensor_tensor(o, o, bank[(3, 6, 7, 3)[z]][:, :], ALU.add).then_inc(x_added, 1)

        def act_experts(act):
            def silu(e_par, n, u):
                act.wait_ge(quarter_done, n + 1 + U * u)
                nc.scalar.activation(sg[e_par], bank[e_par][:, 0:DE], ACT.Silu).then_inc(silu_done, 1)

            def high(E, e_par):
                act.wait_ge(hid_turned, E + 1)
                nc.scalar.activation(t1h[:, 2 * e_par:2 * e_par + 2, 0:P],
                                     bank[2][:, 0:2 * P].rearrange("p (c s) -> p c s", c=2),
                                     ACT.Copy).then_inc(hid_high, 1)

            act_gather(act, 0, 0)

            def job(J, par, n, u):
                for q in range(4):
                    split_high(act, n + q, u, U)

                def block(E, b, m, v, gate_quarter):
                    split_high(act, m, v, U)
                    silu(b, gate_quarter, v)
                    for q in range(1, 4):
                        split_high(act, m + q, v, U)
                    high(E, b)
                    for c in range(2):
                        split_high(act, m + 4 + c, v, U)

                block(EG * J, 0, n + 4, u, n + 3)
                block(EG * J + 1, 1, n + 10, u, n + 7)
                with act.Fori(1, 3) as i:
                    block(EG * J + 2 * i, 0, n + 4, u + i, n + 1)
                    block(EG * J + 2 * i + 1, 1, n + 10, u + i, n + 7)
                block(EG * J + 6, 0, n + 40, u, n + 37)
                silu(1, n + 43, u)
                split_high(act, n + 46, u, U)
                act_gather(act, J + 1, 1 - par)
                high(EG * J + 7, 1)
                split_high(act, n + 47, u, U)

            jobs(act, job)

        def dve_experts(dve):
            def hidden(J, e, E, e_par):
                dve.wait_ge(silu_done, E + 1)
                w = comb[:, ds(J, 1), ds(e, 1)].rearrange("p a b -> p (a b)")
                nc.vector.scalar_tensor_tensor(out=hid[e_par], in0=bank[e_par][:, DE:2 * DE], scalar=w, in1=sg[e_par],
                                               op0=ALU.mult, op1=ALU.mult).then_inc(hid_ready, 1)

            def low(E, e_par):
                dve.wait_ge(hid_high, E + 1)
                nc.vector.tensor_tensor(t1l[:, 2 * e_par:2 * e_par + 2, 0:P],
                                        bank[2][:, 0:2 * P].rearrange("p (c s) -> p c s", c=2),
                                        t1h[:, 2 * e_par:2 * e_par + 2, 0:P].bitcast(F32),
                                        ALU.subtract).then_inc(hid_low, 1)

            dve_gather(dve, 0)
            dve_gather_low(dve, 0, 0)

            def job(J, par, n, u):
                for q in (1, 3):
                    split_low(dve, n + q, u, U)
                dve_scatter(dve, J)

                def block(e, b, m, v):
                    E = EG * J + e
                    hidden(J, e, E, b)
                    for q in (1, 3):
                        split_low(dve, m + q, v, U)
                    low(E, b)
                    split_low(dve, m + 5, v, U)

                with dve.Fori(0, 3) as i:
                    for b in range(2):
                        block(2 * i + b, b, n + 4 + 6 * b, u + i)
                block(6, 0, n + 40, u)
                hidden(J, 7, EG * J + 7, 1)
                dve_gather(dve, J + 1)
                low(EG * J + 7, 1)
                split_low(dve, n + 47, u, U)
                dve_gather_low(dve, J + 1, 1 - par)
                dve.wait_ge(quarter_done, n + 48 + U * u)
                dve.wait_ge(x_added, 4 * J + 4)
                for h in range(2):
                    nc.vector.tensor_copy(ysum[:, 512 * h:512 * h + 512], bank[4 + h][:, :]).then_inc(ysum_ready, 1)
                nc.vector.tensor_copy(back_now, back[:, ds(J, 1)].rearrange("p a t s -> p (a t) s")).then_inc(back_copied, 1)

            jobs(dve, job)
            dve_scatter(dve, NG)

        over_gu = lay(10184, KC, 2 * DE)
        over_d = lay(7112, 2, D)
        over_hT = lay(14280, 2, P)

        def overflowing(eng):
            eng.wait_ge(flag_ready, 1)
            return eng.value_load(flag[0:1, 0:1], min_val=0, max_val=1)

        def sp_overflow(sp):
            with sp.If(overflowing(sp) == 1):
                sp.wait_ge(xg_low, JOBS)
                g = sp.value_load(flag[0:1, 1:2], min_val=0, max_val=NG - 1)
                with sp.Fori(0, EG) as e:
                    sp.wait_ge(ov["zeroed"], e + 1)
                    for j, name in enumerate(("w_exp_gate", "w_exp_up")):
                        v = A[name][0].rearrange("g e (p k) n -> p (g e) k n", k=KC)[:, ds(g * EG + e, 1), :, :]
                        sp.dma_start(over_gu[:, :, DE * j:DE * j + DE].unsqueeze(1), v).then_inc(ov["loaded"], 16)
                    v = A["w_exp_down"][0].rearrange("g e (p k) n -> p (g e) k n", k=2)[:, ds(g * EG + e, 1), :, :]
                    sp.dma_start(over_d.unsqueeze(1), v).then_inc(ov["loaded"], 16)

        def pe_overflow(pe):
            with pe.If(overflowing(pe) == 1):
                pe.wait_ge(xg_low, JOBS)
                pe.wait_ge(x_added, 4 * JOBS)
                with pe.Fori(0, EG) as e:
                    pe.wait_ge(ov["loaded"], 48 * e + 48)
                    for k in range(KC):
                        for part in (t0h, t0l):
                            mm = nc.tensor.matmul(bank[0][:, :], part[:, k, 0:P].bitcast(F32), over_gu[:, k, :],
                                                  start=k == 0 and part is t0h, stop=k == KC - 1 and part is t0l)
                    mm.then_inc(ov["up"], 1)
                    pe.wait_ge(ov["hid"], e + 1)
                    for c in range(2):
                        tr = nc.tensor.transpose(bank[2][:, c * P:(c + 1) * P],
                                                 hid[0].rearrange("p (f c) -> p f c", c=2)[:, :, c], ident)
                    tr.then_inc(ov["turned"], 1)
                    pe.wait_ge(ov["copied"], e + 1)
                    for h in range(2):
                        for c in range(2):
                            mm = nc.tensor.matmul(bank[4 + h][:, :], over_hT[:, c, :], over_d[:, c, 512 * h:512 * h + 512],
                                                  start=c == 0, stop=c == 1)
                    mm.then_inc(ov["down"], 1)
                pe.wait_ge(ov["zeroed"], EG + 1)
                for z in range(4):
                    t, h = z // 2, z % 2
                    nc.tensor.matmul(bank[(3, 6, 7, 1)[z]][:, :], back[:, NG, t, :], ysum[:, 512 * h:512 * h + 512],
                                     start=True, stop=True).then_inc(ov["scattered"], 1)

        def act_overflow(act):
            with act.If(overflowing(act) == 1):
                with act.Fori(0, EG) as e:
                    act.wait_ge(ov["up"], e + 1)
                    nc.scalar.activation(sg[0], bank[0][:, 0:DE], ACT.Silu).then_inc(ov["silu"], 1)

        def dve_overflow(dve):
            with dve.If(overflowing(dve) == 1):
                dve.wait_ge(x_added, 4 * JOBS)
                nc.vector.memset(ysum, 0.0).then_inc(ov["zeroed"], 1)
                with dve.Fori(0, EG) as e:
                    dve.wait_ge(ov["silu"], e + 1)
                    nc.vector.scalar_tensor_tensor(out=hid[0], in0=bank[0][:, DE:2 * DE],
                                                   scalar=comb[:, NG, ds(e, 1)], in1=sg[0],
                                                   op0=ALU.mult, op1=ALU.mult).then_inc(ov["hid"], 1)
                    dve.wait_ge(ov["turned"], e + 1)
                    nc.vector.tensor_copy(over_hT.rearrange("p c s -> p (c s)"), bank[2][:, 0:2 * P]).then_inc(ov["copied"], 1)
                    dve.wait_ge(ov["down"], e + 1)
                    dve.wait_ge(ov["zeroed"], e + 1)
                    nc.vector.tensor_tensor(ysum[:, 0:512], ysum[:, 0:512], bank[4][:, :], ALU.add).then_inc(ov["summed"], 1)
                    nc.vector.tensor_tensor(ysum[:, 512:D], ysum[:, 512:D], bank[5][:, :], ALU.add).then_inc(ov["zeroed"], 1)
                for z in range(4):
                    t, h = z // 2, z % 2
                    dve.wait_ge(ov["scattered"], z + 1)
                    o = xres[:, t, 512 * h:512 * h + 512]
                    nc.vector.tensor_tensor(o, o, bank[(3, 6, 7, 1)[z]][:, :], ALU.add).then_inc(ov["added"], 1)
                dve.wait_ge(ov["added"], 4)
            dve.wait_ge(x_added, 4 * JOBS)
            nc.vector.tensor_copy(flagf, flag[:, :]).then_inc(experts_added, 1)

        experts_added = sem("experts_added")
        norm_p = RmsNorm(xres, xn, stat)
        turn_p = Turn(xn, gain("ple_norm_w"), t0h, t0l)
        norm_f = RmsNorm(xres, xn, stat)
        emb_turned, emb_high, emb_low, ple_copied, gated, gate_used, first_done = (
            sem(s) for s in ("emb_turned", "emb_high", "emb_low", "ple_copied", "gated", "gate_used", "first_done"))

        def sp_ple(sp):
            v = A["w_ple"][0].rearrange("(p k) n -> p k n", k=2)
            for k in range(2):
                load(sp, Q_PLE + k, [(raw[:, (Q_PLE + k) % RING, :], v[:, k, :])])
            load_square(sp, Q_GATE, A["w_ple_gate"][0])

        def pe_ple(pe):
            pe.wait_ge(ple_bank_free, 1)
            for k in range(2):
                for t in range(NT):
                    tr = nc.tensor.transpose(bank[4][:, k * SEQ + t * P:k * SEQ + (t + 1) * P],
                                             emb[:, t, :].rearrange("p (f k) -> p f k", k=2)[:, :, k], ident)
            tr.then_inc(emb_turned, 1)
            pe.wait_ge(emb_low, 1)
            for k in range(2):
                n = Q_PLE + k
                wait_low(pe, n)
                for h in range(2):
                    f = slice(512 * h, 512 * h + 512)
                    for t in range(NT):
                        s = slice(t * P, (t + 1) * P)
                        mm = times(bank[2 * h + t][:, :], t1h[:, k, s], t1l[:, k, s], whi[:, n % RING, f],
                                   wlo[:, n % RING, f], k == 0, k == 1)
                mm.then_inc(quarter_done, 1)
            turn_p.pe(pe, [norm_p.ready()])
            square_product(pe, Q_GATE, t0h, t0l, [turn_p.done(), (ple_copied, 4)])

        ple_bank_free = experts_added

        def act_ple(act):
            for k in range(2):
                split_high(act, Q_PLE + k)
            act.wait_ge(emb_turned, 1)
            nc.scalar.activation(t1h[:, 0:2, :], bank[4][:, :].rearrange("p (k s) -> p k s", k=2), ACT.Copy).then_inc(emb_high, 1)
            for q in range(2):
                split_high(act, Q_GATE + q)
            norm_p.act(act, [(experts_added, 1)])
            act.wait_ge(quarter_done, Q_GATE)
            for h in range(2):
                for t in range(NT):
                    nc.scalar.copy(ple[:, t, 512 * h:512 * h + 512], bank[2 * h + t][:, :]).then_inc(ple_copied, 1)
            turn_p.act(act, Q_PLE)
            for q in range(2, 8):
                split_high(act, Q_GATE + q)
            for h in range(2):
                act.wait_ge(quarter_done, Q_GATE + 4 * h + 4)
                for t in range(NT):
                    nc.scalar.activation(sgate[:, t, 512 * h:512 * h + 512], bank[2 * h + t][:, :],
                                         ACT.Sigmoid).then_inc(gated, 1)
            norm_f.act(act, [(gate_used, 4)])

        def dve_ple(dve, order):
            dve.wait_ge(emb_high, 1)
            nc.vector.tensor_tensor(t1l[:, 0:2, :], bank[4][:, :].rearrange("p (k s) -> p k s", k=2),
                                    t1h[:, 0:2, :].bitcast(F32), ALU.subtract).then_inc(emb_low, 1)
            norm_p.dve(dve, order)
            turn_p.dve(dve)
            for h in range(2):
                for t in range(NT):
                    dve.wait_ge(gated, 2 * h + t + 1)
                    f = slice(512 * h, 512 * h + 512)
                    order.step(nc.vector.tensor_tensor(sgate[:, t, f], sgate[:, t, f], ple[:, t, f], ALU.mult))
                    nc.vector.tensor_tensor(xres[:, t, f], xres[:, t, f], sgate[:, t, f], ALU.add).then_inc(gate_used, 1)
            norm_f.dve(dve, order)
            dve.wait_ge(*norm_f.ready())
            nc.vector.tensor_tensor(xres[:, :, :], xn, fnw.unsqueeze(1).to_broadcast([P, NT, D]),
                                    ALU.mult).then_inc(first_done, 1)


        rkv = lay(0, NT, 3 * D)
        glu = lay(6144, NT, 2 * D)
        gates = lay(10240, NT, 2 * D)
        hT = lay(6144, KC, SEQ)
        dhT = lay(8192, KC, SEQ)
        decay = lay(6144, NT, D)
        gain_a = lay(8192, NT, D)
        taps2 = lay(14336, 2 * P)
        W2, K2 = 31, KC
        H2 = W2 - 1
        shifted = [carve(1024 * b, NT, TW) for b in range(2)]
        xw = carve(0, KC, SEQ)
        uT = carve(2048, K2, H2 + SEQ)
        cvT = carve(4336, K2, SEQ)
        ctok = carve(2048, NT, D)
        w1, a1, g1 = carve(6384, KC, 64), carve(6896, KC, 64), carve(7408, KC, P)
        w2, a2 = carve(8432, D), carve(9456, D)
        dT, aT = carve(10480, SEQ), carve(10736, SEQ)
        rows2 = carve(10992, 2, P)
        rowbuf = [carve(11248 + 512 * b, TW) for b in range(2)]
        gT, g2 = carve(12272, SEQ), carve(12528, D)
        st2 = tiny(0, 16)
        norm_g = RmsNorm(xres, xn, stat)
        turn_g = Turn(xn, gain("norm_mix_g_2"), t0h, t0l)
        row_loaded, shift_loaded = ([sem(f"{n}{b}") for b in range(2)] for n in ("row_loaded", "shift_loaded"))
        row_used = sem("row_used")
        evac2 = Again(evac_in, NT * IN_T)
        lora_loaded = Again(router_loaded, 96)
        glu_ready = Again(y_gated, NT)
        u_turned = Again(xbc_turned, XCH // 2)
        u_copied = Again(xbc_copied, XCH // 2)
        taps2_turned = Again(taps_turned, 1)
        taps2_ready = Again(taps_ready, 1)
        conv2_done = Again(conv_done, XCH)
        c_var = sem("c_var")
        c_back = Again(x_back, 2 * NT)
        c_copied = Again(ple_copied, 4)
        c_mean = Again(y_mean, 1)
        c_squared = Again(y_squared, 2 * NT)
        c_root = Again(y_root, 1)
        c_normed = Again(y_normed, 2 * NT)
        c_active = Again(conv_active, XCH)
        c_high = Again(emb_high, 1)
        c_low = Again(emb_low, 1)
        shift_done = sem("shift_done")
        gates_ready = Again(gate_active, 4)
        xw_ready, lora_mid, lora_ones = (
            sem(s) for s in ("xw_ready", "lora_mid", "lora_ones"))
        lora_act = Again(dt_exp, 2)
        lora_done = Again(cum_done, 1)
        lora_ready = Again(dec_ready, 2)
        state_decay_done = Again(state_done, 1)
        state_decay_ready = Again(state_ready, 1)
        conv_gated = Again(ssd_merged, 4)

        TILES2 = [6, 8, 7, 9] + list(range(6)) + list(range(10, 14))

        def sp_in2(sp):
            v = A["w_in_2"][0].rearrange("(p k) n -> p k n", k=KC)
            for p, c in enumerate(TILES2):
                for q in range(4):
                    n = Q_IN2 + 4 * p + q
                    load(sp, n, [(pair_view(raw, n, TW), v[:, 2 * q:2 * q + 2, c * TW:(c + 1) * TW])])
            load_square(sp, Q_CONV, A["w_conv_proj_2"][0])
            load_square(sp, Q_RWKV, A["w_rwkv_proj_2"][0])
            load_square(sp, Q_OUT2, A["w_out_2"][0])

        def lora_loads(act):
            act.wait_ge(first_done, 1)
            def ld(dst, src):
                act.dma_start(dst, src).then_inc(lora_loaded.sem, 16)
            ld(w1, A["decay_w1_2"][0].rearrange("(p k) n -> p k n", k=KC))
            ld(a1, A["aaa_a1_2"][0].rearrange("(p k) n -> p k n", k=KC))
            ld(g1, A["gate_g1_2"][0].rearrange("(p k) n -> p k n", k=KC))
            for dst, w, b in ((w2, "decay_w2_2", "decay_w0_2"), (a2, "aaa_a2_2", "aaa_a0_2")):
                ld(dst[0:64, :], A[w][0])
                ld(dst[64:65, :], A[b])
            ld(g2, A["gate_g2_2"][0])
            taps = A["conv_w_2"][0].rearrange("w (k p) -> (w k) p", p=P)
            ld(rows2[:, 0, :], taps[0:P, :])
            ld(rows2[0:120, 1, :], taps[P:248, :])
            ld(rows2[120:128, 1, :], A["conv_b_2"][0].rearrange("(k p) -> k p", p=P))

        N_LORA = 16 * 11

        def pe_in2(pe):
            turn_g.pe(pe, [norm_g.ready(), (gate_used, 4)])
            pe.wait_ge(*turn_g.done())

            def tile(p):
                wait_from(pe, *evac2.at(NT * (p - 1)))
                for q in range(4):
                    wide_quarter(pe, Q_IN2 + 4 * p + q, q, bank[2 * (p % 2):2 * (p % 2) + 2], t0h, t0l)

            for p in range(6):
                tile(p)
            pe.wait_ge(*glu_ready.at(4))
            for b in range(K2 // 2):
                for kk in range(2):
                    for t in range(NT):
                        c = (2 * b + kk) * P
                        tr = nc.tensor.transpose(bank[4 + b][:, kk * SEQ + t * P:kk * SEQ + (t + 1) * P],
                                                 glu[:, t, c:c + P], ident)
                tr.then_inc(u_turned.sem, 1)
            pe.wait_ge(*u_copied.at(1))
            pe.wait_ge(*lora_loaded.at(N_LORA))
            for j in range(2):
                tr = nc.tensor.transpose(bank[4][:, j * P:(j + 1) * P], rows2[:, j, :], ident)
            tr.then_inc(taps2_turned.sem, 1)
            for p in range(6, 14):
                tile(p)

        def act_in2(act):
            for q in range(4):
                split_high(act, Q_IN2 + q)
            norm_g.act(act, [(first_done, 1)])
            turn_g.act(act, Q_IN2)
            lora_loads(act)

            def row_load(p):
                b = p % 2
                if 4 <= p < 10:
                    src = A["mu_rkv_2"][0][(p - 4) * TW:(p - 3) * TW]
                else:
                    src = A["b_gate_2"][0][(p - 10) * TW:(p - 9) * TW]
                wait_from(act, row_used, p - 5)
                act.dma_start(rowbuf[b], row(src, TW)).then_inc(row_loaded[b], 16)

            def evac(p):
                act.wait_ge(quarter_done, Q_IN2 + 4 * p + 4)
                b = 2 * (p % 2)
                if p < 4:
                    f = slice((p // 2) * TW + (p % 2) * D, (p // 2) * TW + (p % 2) * D + TW)
                    for t in range(NT):
                        nc.scalar.activation(glu[:, t, f], bank[b + t][:, :], ACT.Sigmoid if p % 2 else ACT.Copy
                                             ).then_inc(evac2.sem, 1)
                elif p < 10:
                    f = slice((p - 4) * TW, (p - 3) * TW)
                    for t in range(NT):
                        nc.scalar.copy(rkv[:, t, f], bank[b + t][:, :]).then_inc(evac2.sem, 1)
                    wait_from(act, shift_done, p - 5)
                    act.wait_ge(*evac2.at(NT * (p + 1)))
                    s = shifted[p % 2]
                    act.dma_start(s[1:P, :, :], rkv[0:P - 1, :, f]).then_inc(shift_loaded[p % 2], 16)
                    act.dma_start(s[0:1, 1, :], rkv[P - 1:P, 0, f]).then_inc(shift_loaded[p % 2], 16)
                else:
                    f = slice((p - 10) * TW, (p - 9) * TW)
                    for t in range(NT):
                        nc.scalar.copy(gates[:, t, f], bank[b + t][:, :]).then_inc(evac2.sem, 1)

            for p in range(1, 14):
                for q in range(4):
                    split_high(act, Q_IN2 + 4 * p + q)
                if p >= 4:
                    row_load(p)
                evac(p - 1)
            for q in range(4):
                split_high(act, Q_CONV + q)
            evac(13)
            for j in range(4):
                act.wait_ge(row_used, 6 + j + 1)
                f = slice(j * TW, (j + 1) * TW)
                nc.scalar.activation(gates[:, :, f], gates[:, :, f], ACT.Sigmoid).then_inc(gates_ready.sem, 1)

        def dve_in2(dve, order):
            norm_g.dve(dve, order)
            turn_g.dve(dve)
            dve.wait_ge(*norm_g.ready())
            dve.wait_ge(*turn_g.written())
            for b in range(2):
                order.mark(nc.vector.memset(shifted[b][0:1, 0, :], 0.0))
            order.mark(nc.vector.memset(uT[:, :, 0:H2], 0.0))
            for j in range(2):
                dve.wait_ge(*evac2.at(NT * (2 * j + 2)))
                f, g = slice(j * TW, (j + 1) * TW), slice(D + j * TW, D + (j + 1) * TW)
                for t in range(NT):
                    nc.vector.tensor_tensor(glu[:, t, f], glu[:, t, f], glu[:, t, g], ALU.mult).then_inc(glu_ready.sem, 1)
            for b in range(K2 // 2):
                dve.wait_ge(*u_turned.at(b + 1))
                nc.vector.tensor_copy(uT[:, 2 * b:2 * b + 2, H2:H2 + SEQ],
                                      bank[4 + b][:, :].rearrange("p (k s) -> p k s", k=2)).then_inc(u_copied.sem, 1)
            dve.wait_ge(*taps2_turned.at(1))
            nc.vector.tensor_copy(taps2, bank[4][:, 0:2 * P]).then_inc(taps2_ready.sem, 1)
            dve.wait_ge(*u_copied.at(4))
            dve.wait_ge(*taps2_ready.at(1))

            def convolve(c0):
                for w in range(W2):
                    for c in (c0, c0 + 1):
                        tap = taps2[:, w * K2 + c:w * K2 + c + 1]
                        if w == 0:
                            order.mark(nc.vector.tensor_scalar(cvT[:, c, :], uT[:, c, 0:SEQ], tap,
                                                               taps2[:, 248 + c:249 + c], ALU.mult, ALU.add))
                        else:
                            ins = nc.vector.scalar_tensor_tensor(out=cvT[:, c, :], in0=uT[:, c, w:w + SEQ], scalar=tap,
                                                                 in1=cvT[:, c, :], op0=ALU.mult, op1=ALU.add)
                            if w < W2 - 1:
                                order.mark(ins)
                            else:
                                ins.then_inc(conv2_done.sem, 1)
                    if w < W2 - 1:
                        order.settle()

            def shift(p):
                f = slice((p - 4) * TW, (p - 3) * TW)
                z, s = rkv[:, :, f], shifted[p % 2]
                order.settle()
                dve.wait_ge(shift_loaded[p % 2], 32 * (p // 2 - 1))
                dve.wait_ge(row_loaded[p % 2], 16 * (p // 2 - 1))
                order.step(nc.vector.tensor_tensor(s, s, z, ALU.subtract))
                nc.vector.tensor_tensor(s, s, rowbuf[p % 2].unsqueeze(1).to_broadcast([P, NT, TW]),
                                        ALU.mult).then_inc(row_used, 1)
                dve.wait_ge(row_used, p - 3)
                nc.vector.tensor_tensor(z, z, s, ALU.add).then_inc(shift_done, 1)
                if p < 8:
                    dve.wait_ge(shift_done, p - 3)
                    order.mark(nc.vector.memset(s[0:1, 0, :], 0.0))

            convolve(0)
            shift(4)
            shift(5)
            convolve(2)
            shift(6)
            shift(7)
            convolve(4)
            shift(8)
            shift(9)
            convolve(6)
            for j in range(4):
                p = 10 + j
                f = slice(j * TW, (j + 1) * TW)
                dve.wait_ge(row_loaded[p % 2], 16 * (p // 2 - 1))
                dve.wait_ge(*evac2.at(NT * (p + 1)))
                nc.vector.tensor_tensor(gates[:, :, f], gates[:, :, f],
                                        rowbuf[p % 2].unsqueeze(1).to_broadcast([P, NT, TW]),
                                        ALU.add).then_inc(row_used, 1)

        def dve_lora(dve, order):
            dve.wait_ge(shift_done, 6)
            order.mark(nc.vector.tensor_tensor(hT, t0h[:, :, :].bitcast(F32), t0l[:, :, :].bitcast(F32), ALU.add))
            order.settle()
            order.mark(nc.vector.tensor_tensor(dhT[:, :, 1:SEQ], hT[:, :, 0:SEQ - 1], hT[:, :, 1:SEQ], ALU.subtract))
            order.step(nc.vector.tensor_scalar(dhT[:, :, 0:1], hT[:, :, 0:1], -1.0, None, ALU.mult))
            for buf in (dT, aT):
                nc.vector.memset(buf[64:65, :], 1.0).then_inc(lora_ones, 1)
            for j in range(3):
                if j:
                    dve.wait_ge(lora_mid, j)
                for k in range(KC):
                    nc.vector.scalar_tensor_tensor(out=xw[:, k, :], in0=dhT[:, k, :], scalar=mul[:, j, k:k + 1],
                                                   in1=hT[:, k, :], op0=ALU.mult, op1=ALU.add).then_inc(xw_ready, 1)

        def pe_lora(pe):
            pe.wait_ge(*evac2.at(NT * 14))
            pe.wait_ge(*lora_loaded.at(N_LORA))
            for j, (w, m) in enumerate(((w1, 64), (a1, 64), (g1, P))):
                for k in range(KC):
                    pe.wait_ge(xw_ready, KC * j + k + 1)
                    mm = nc.tensor.matmul(bank[j][0:m, 0:SEQ], w[:, k, :], xw[:, k, :], start=k == 0, stop=k == KC - 1)
                mm.then_inc(lora_mid, 1)
            pe.wait_ge(lora_ones, 2)
            for j, (mid, w) in enumerate(((dT, w2), (aT, a2))):
                pe.wait_ge(*lora_act.at(j + 1))
                if j == 0:
                    pe.wait_ge(*lora_act.at(3))
                else:
                    pe.wait_ge(*lora_ready.at(4))
                for t in range(NT):
                    for h in range(2):
                        nc.tensor.matmul(bank[2 * t + h][:, :], mid[0:65, t * P:(t + 1) * P], w[0:65, 512 * h:512 * h + 512],
                                         start=True, stop=True).then_inc(lora_done.sem, 1)
            pe.wait_ge(*lora_ready.at(8))
            for c in range(KC):
                nc.tensor.matmul(bank[0][:, c:c + 1], decay[:, 0, c * P:(c + 1) * P], con("high"), start=True, stop=False)
                mm = nc.tensor.matmul(bank[0][:, c:c + 1], decay[:, 1, c * P:(c + 1) * P], con("low"), start=False, stop=True)
            mm.then_inc(state_decay_done.sem, 1)

        S_DECAY = math.exp(-0.5)

        def act_lora(act):
            act.wait_ge(lora_mid, 1)
            nc.scalar.activation(dT[0:64, :], bank[0][0:64, 0:SEQ], ACT.Tanh).then_inc(lora_act.sem, 1)
            act.wait_ge(lora_mid, 2)
            nc.scalar.copy(aT[0:64, :], bank[1][0:64, 0:SEQ]).then_inc(lora_act.sem, 1)
            act.wait_ge(lora_mid, 3)
            nc.scalar.activation(gT, bank[2][:, 0:SEQ], ACT.Sigmoid).then_inc(lora_act.sem, 1)
            for j, dst in enumerate((decay, gain_a)):
                for t in range(NT):
                    for h in range(2):
                        act.wait_ge(*lora_done.at(4 * j + 2 * t + h + 1))
                        nc.scalar.activation(dst[:, t, 512 * h:512 * h + 512], bank[2 * t + h][:, :],
                                             ACT.Sigmoid).then_inc(lora_ready.sem, 1)
            act.wait_ge(*state_decay_done.at(1))
            nc.scalar.activation(sdec, bank[0][:, 0:KC], ACT.Exp, scale=-S_DECAY).then_inc(state_decay_ready.sem, 1)

        sdec = tiny(16, KC)

        def pe_conv(pe):
            pe.wait_ge(*conv2_done.at(K2))
            pe.wait_ge(*taps2_ready.at(1))
            for t in range(NT):
                for h in range(2):
                    for c in range(4):
                        tr = nc.tensor.transpose(bank[4 + 2 * t + h][:, c * P:(c + 1) * P],
                                                 cvT[:, 4 * h + c, t * P:(t + 1) * P], ident)
                    tr.then_inc(c_back.sem, 1)
            turn_c.pe(pe, [c_normed.at(NT), c_copied.at(4)])
            square_product(pe, Q_CONV, t0h, t0l, [c_low.at(1), state_decay_ready.at(1)])

        turn_c = Turn(ctok, None, None, None)

        def act_conv(act):
            act.wait_ge(*conv2_done.at(K2))
            for t in range(NT):
                for h in range(2):
                    act.wait_ge(*c_back.at(2 * t + h + 1))
                    nc.scalar.activation(ctok[:, t, 512 * h:512 * h + 512], bank[4 + 2 * t + h][:, :], ACT.Copy,
                                         accum_out=st2[:, 4 + 2 * t + h:5 + 2 * t + h]).then_inc(c_copied.sem, 1)
            act.wait_ge(*c_mean.at(1))
            for t in range(NT):
                nc.scalar.activation(xw_flat[:, t, :], ctok[:, t, :], ACT.Square, bias=st2[:, 8 + t:9 + t],
                                     accum_out=st2[:, 10 + t:11 + t]).then_inc(c_squared.sem, 1)
            act.wait_ge(c_var, 1)
            nc.scalar.activation(st2[:, 10:12], st2[:, 10:12], ACT.Sqrt).then_inc(c_root.sem, 1)
            for k in range(KC):
                if k % 2 == 0:
                    act.wait_ge(*turn_c.written(k // 2 + 1))
                nc.scalar.activation(cvT[:, k, :], turn_c.part(k), ACT.Silu, scale=gain("conv_ln_g_2")[:, k:k + 1],
                                     bias=gain("conv_ln_b_2")[:, k:k + 1]).then_inc(c_active.sem, 1)
            act.wait_ge(*c_active.at(KC))
            act.wait_ge(quarter_done, Q_CONV)
            act.wait_ge(*lora_ready.at(8))
            nc.scalar.activation(t0h[:, :, :], cvT, ACT.Copy).then_inc(c_high.sem, 1)
            for q in range(4, 8):
                split_high(act, Q_CONV + q)
            for q in range(4):
                split_high(act, Q_RWKV + q)

        xw_flat = carve(0, NT, D)

        def dve_conv(dve, order):
            dve.wait_ge(*c_copied.at(4))
            for t in range(NT):
                order.mark(nc.vector.tensor_tensor(st2[:, 8 + t:9 + t], st2[:, 4 + 2 * t:5 + 2 * t],
                                                   st2[:, 5 + 2 * t:6 + 2 * t], ALU.add))
            order.settle()
            nc.vector.tensor_scalar(st2[:, 8:10], st2[:, 8:10], -1.0 / D, None, ALU.mult).then_inc(c_mean.sem, 1)
            dve.wait_ge(*c_squared.at(NT))
            nc.vector.tensor_scalar(st2[:, 10:12], st2[:, 10:12], 1.0 / D, 1e-5, ALU.mult, ALU.add).then_inc(c_var, 1)
            dve.wait_ge(*c_root.at(1))
            dve.wait_ge(*c_mean.at(1))
            order.step(nc.vector.reciprocal(st2[:, 10:12], st2[:, 10:12]))
            for t in range(NT):
                nc.vector.tensor_scalar(ctok[:, t, :], ctok[:, t, :], st2[:, 8 + t:9 + t], st2[:, 10 + t:11 + t],
                                        ALU.add, ALU.mult).then_inc(c_normed.sem, 1)
            dve.wait_ge(*c_high.at(1))
            nc.vector.tensor_tensor(t0l[:, :, :], cvT, t0h[:, :, :].bitcast(F32), ALU.subtract).then_inc(c_low.sem, 1)
            dve.wait_ge(*gates_ready.at(4))
            for c in range(2):
                dve.wait_ge(quarter_done, Q_CONV + 4 * c + 4)
                for t in range(NT):
                    o = gates[:, t, D + c * TW:D + (c + 1) * TW]
                    nc.vector.tensor_tensor(o, o, bank[2 * c + t][:, :], ALU.mult).then_inc(conv_gated.sem, 1)

        PB = 5632
        rows3 = carve(2 * PB, 3, 2 * P)
        hst = [tiny(24 + 64 * x, 64) for x in range(2)]

        def pbuf(x, at, *shape):
            return carve(PB * x + at, *shape)

        Rt = [pbuf(x, 0, NT, P) for x in range(2)]
        At = [pbuf(x, 256, NT, P) for x in range(2)]
        Bt = [pbuf(x, 512, NT, P) for x in range(2)]
        Kt = [pbuf(x, 768, NT, P) for x in range(2)]
        AR = [pbuf(x, 1024, NT, 2, P) for x in range(2)]
        BK = [pbuf(x, 1536, 2, NT, P) for x in range(2)]
        gram = [pbuf(x, 2048, 4, 512) for x in range(2)]
        Xm = [pbuf(x, 4096, 4, P) for x in range(2)]
        XT = [pbuf(x, 4608, 4, P) for x in range(2)]
        Ym = [pbuf(x, 5120, 4, P) for x in range(2)]
        kkb = [pbuf(x, 5120, NT, P) for x in range(2)]
        tmpb = [pbuf(x, 5376, NT, P) for x in range(2)]
        Pex = [pbuf(x, 4096, NT, P) for x in range(2)]
        Pm = [pbuf(x, 4352, NT, P) for x in range(2)]
        Pi = [pbuf(x, 4608, NT, P) for x in range(2)]
        kpb = [pbuf(x, 4864, NT, P) for x in range(2)]
        Wn = [pbuf(x, 4096, NT, P) for x in range(2)]
        Uo = [pbuf(x, 4352, NT, P) for x in range(2)]
        SB = [pbuf(x, 5120, P) for x in range(2)]
        ob = [pbuf(x, 5248, NT, P) for x in range(2)]
        rows3_loaded, cs_done, pdiff, pexp, kk_squared, kk_root = (
            sem(s) for s in ("rows3_loaded", "cs_done", "pdiff", "pexp", "kk_squared", "kk_root"))
        gram_masked = sem("gram_masked")
        rows3_used = Again(xdt_ready, 1)
        tok_ready = Again(rot_ready, PAIRS)
        hturned = Again(qk_turned, PAIRS)
        ft_copied = Again(qk_copied, PAIRS)
        gram_done = Again(scored, 2 * PAIRS)
        y_made, y_masked, x_made, x_copied, w_made, w_copied, u_made, u_copied2 = (
            sem(s) for s in ("y_made", "y_masked", "x_made", "x_copied", "w_made", "w_copied", "u_made", "u_copied2"))
        s_made, s_ready, pair_var, pair_root = (
            sem(s) for s in ("s_made", "s_ready", "pair_var", "pair_root"))
        o_made = Again(pv_done, PAIRS)
        pair_done = Again(att_ready, PAIRS)

        def unit(h, t):
            return 2 * h + t

        def act_rows3(act, i):
            act.wait_ge(*rows3_used.at(i))
            for j, name in enumerate(("k_k_2", "k_a_2")):
                src = A[name][0].rearrange("(a n) -> a n", a=1)[:, ds(2 * P * i, 2 * P)].to_broadcast([P, 2 * P])
                act.dma_start(rows3[:, j, :], src).then_inc(rows3_loaded, 16)
            src = A["r_k_2"][0].rearrange("h d -> (h d)").rearrange("(a n) -> a n", a=1)[:, ds(2 * P * i, 2 * P)]
            act.dma_start(rows3[:, 2, :], src.to_broadcast([P, 2 * P])).then_inc(rows3_loaded, 16)

        LEV = 7

        def pe_heads(pe):
            pe.wait_ge(*state_decay_ready.at(1))
            pe.wait_ge(*conv_gated.at(4))

            def body(i):
                for x in range(2):
                    C = P * (2 * i + x)
                    for t in range(NT):
                        mm = nc.tensor.matmul(bank[4 * x][:, t * P:(t + 1) * P], con("centred"), decay[:, t, ds(C, P)],
                                              start=True, stop=True)
                    mm.then_inc(cs_done, 1)
                for x in range(2):
                    pe.wait_ge(*tok_ready.at(4 * i + 2 * x + 1))
                    for t in range(NT):
                        for j, src in enumerate((At, Rt)):
                            tr = nc.tensor.transpose(bank[4 * x + 1][:, (2 * t + j) * P:(2 * t + j + 1) * P], src[x][:, t, :],
                                                     ident)
                    tr.then_inc(hturned.sem, 1)
                    pe.wait_ge(*tok_ready.at(4 * i + 2 * x + 2))
                    for j, src in enumerate((Bt, Kt)):
                        for t in range(NT):
                            tr = nc.tensor.transpose(bank[4 * x + 2][:, (2 * j + t) * P:(2 * j + t + 1) * P], src[x][:, t, :],
                                                     ident)
                    tr.then_inc(hturned.sem, 1)
                for x in range(2):
                    pe.wait_ge(*ft_copied.at(4 * i + 2 * x + 2))
                    for h in range(2):
                        r = slice(64 * h, 64 * h + 64)
                        for t in range(NT):
                            u = unit(h, t)
                            ar = AR[x][r, t].rearrange("p a s -> p (a s)")
                            for j in range(2):
                                mm = nc.tensor.matmul(bank[4 * x + u][:, 256 * j:256 * j + 256], BK[x][r, j, t, :], ar,
                                                      start=True, stop=True)
                            mm.then_inc(gram_done.sem, 1)
                for lev in range(LEV):
                    for x in range(2):
                        if lev == 0:
                            pe.wait_ge(gram_masked, 2 * i + x + 1)
                        elif lev == 1:
                            pe.wait_ge(y_masked, 2 * LEV * i + x + 1)
                        else:
                            pe.wait_ge(x_copied, 2 * (LEV - 1) * i + 2 * lev + x - 3)
                        for u in range(4):
                            mm = nc.tensor.matmul(bank[4 * x][:, u * P:(u + 1) * P], gram[x][:, u, 0:P],
                                                  ident if lev == 0 else Xm[x][:, u, :], start=True, stop=True)
                        mm.then_inc(y_made, 1)
                    if lev == 0:
                        continue
                    for x in range(2):
                        pe.wait_ge(y_masked, 2 * LEV * i + 2 * lev + x + 1)
                        if lev < LEV - 1:
                            for u in range(4):
                                nc.tensor.matmul(bank[4 * x + 1][:, u * P:(u + 1) * P], XT[x][:, u, :], Ym[x][:, u, :],
                                                 start=True, stop=True)
                        for u in range(4):
                            mm = nc.tensor.matmul(bank[4 * x + 2][:, u * P:(u + 1) * P], Ym[x][:, u, :], XT[x][:, u, :],
                                                  start=True, stop=True)
                        mm.then_inc(x_made, 1)
                for t in range(NT):
                    for x in range(2):
                        C = 2 * D + P * (2 * i + x)
                        pe.wait_ge(x_copied, 2 * (LEV - 1) * i + 2 * LEV + x - 3)
                        if t:
                            pe.wait_ge(s_ready, 2 * i + x + 1)
                        for h in range(2):
                            f = slice(h * DH, (h + 1) * DH)
                            if t:
                                nc.tensor.matmul(bank[4 * x + 3][:, f], AR[x][:, 1, 0, :], SB[x][:, f], start=True, stop=False)
                            mm = nc.tensor.matmul(bank[4 * x + 3][:, f], gram[x][:, unit(h, t), 256:384],
                                                  rkv[:, t, ds(C + DH * h, DH)], start=t == 0, stop=True)
                        mm.then_inc(w_made, 1)
                    for x in range(2):
                        pe.wait_ge(w_copied, 4 * i + 2 * t + x + 1)
                        for h in range(2):
                            mm = nc.tensor.matmul(bank[4 * x + 3][:, 128 + h * DH:128 + (h + 1) * DH], XT[x][:, unit(h, t), :],
                                                  Wn[x][:, t, h * DH:(h + 1) * DH], start=True, stop=True)
                        mm.then_inc(u_made, 1)
                    if t == 0:
                        for x in range(2):
                            C = 2 * D + P * (2 * i + x)
                            pe.wait_ge(u_copied2, 4 * i + x + 1)
                            nc.tensor.matmul(bank[4 * x + 3][:, 256:384], Bt[x][:, 0, :], Uo[x][:, 0, :], start=True, stop=False)
                            nc.tensor.matmul(bank[4 * x + 3][:, 256:384], Kt[x][:, 0, :], rkv[:, 0, ds(C, P)], start=False,
                                             stop=True).then_inc(s_made, 1)
                for x in range(2):
                    C = 2 * D + P * (2 * i + x)
                    pe.wait_ge(u_copied2, 4 * i + x + 3)
                    for t in range(NT):
                        for h in range(2):
                            f = slice(h * DH, (h + 1) * DH)
                            oh = bank[4 * x][:, t * P + h * DH:t * P + (h + 1) * DH]
                            if t:
                                nc.tensor.matmul(oh, AR[x][:, 1, 1, :], SB[x][:, f], start=True, stop=False)
                            nc.tensor.matmul(oh, gram[x][:, unit(h, t), 128:256], Uo[x][:, t, f], start=t == 0, stop=False)
                            mm = nc.tensor.matmul(oh, gram[x][:, unit(h, t), 384:512], rkv[:, t, ds(C + DH * h, DH)],
                                                  start=False, stop=True)
                    mm.then_inc(o_made.sem, 1)
                for x in range(2):
                    pe.wait_ge(*pair_done.at(2 * i + x + 1))

            with pe.Fori(0, PAIRS // 2) as i:
                body(i)

        def act_heads(act):
            act.wait_ge(*conv_gated.at(4))

            def body(i):
                act_rows3(act, i)
                for x in range(2):
                    act.wait_ge(cs_done, 2 * i + x + 1)
                    cs = bank[4 * x][:, 0:2 * P].rearrange("p (t s) -> p t s", t=NT)
                    nc.scalar.activation(Pm[x], cs, ACT.Exp, scale=-S_DECAY).then_inc(pexp, 1)
                    nc.scalar.activation(Pi[x], cs, ACT.Exp, scale=S_DECAY).then_inc(pexp, 1)
                for x in range(2):
                    act.wait_ge(pdiff, 2 * i + x + 1)
                    nc.scalar.activation(Pex[x], Pex[x], ACT.Exp, scale=-S_DECAY).then_inc(pexp, 1)
                for x in range(2):
                    act.wait_ge(kk_squared, 2 * i + x + 1)
                    nc.scalar.activation(hst[x][:, 0:4], hst[x][:, 0:4], ACT.Sqrt).then_inc(kk_root, 1)
                for x in range(2):
                    act.wait_ge(*hturned.at(4 * i + 2 * x + 1))
                    nc.scalar.copy(AR[x].rearrange("p t a s -> p (t a s)"), bank[4 * x + 1][:, :]).then_inc(ft_copied.sem, 1)
                    act.wait_ge(*hturned.at(4 * i + 2 * x + 2))
                    nc.scalar.copy(BK[x].rearrange("p a t s -> p (a t s)"), bank[4 * x + 2][:, :]).then_inc(ft_copied.sem, 1)
                for lev in range(1, LEV):
                    for x in range(2):
                        act.wait_ge(x_made, 2 * (LEV - 1) * i + 2 * lev + x - 1)
                        if lev < LEV - 1:
                            nc.scalar.copy(Xm[x].rearrange("p u s -> p (u s)"), bank[4 * x + 1][:, :]).then_inc(act_order, 1)
                        nc.scalar.copy(XT[x].rearrange("p u s -> p (u s)"), bank[4 * x + 2][:, :]).then_inc(x_copied, 1)
                for t in range(NT):
                    for x in range(2):
                        act.wait_ge(w_made, 4 * i + 2 * t + x + 1)
                        nc.scalar.mul(Wn[x][:, t, :], bank[4 * x + 3][:, 0:P], -1.0).then_inc(w_copied, 1)
                    for x in range(2):
                        act.wait_ge(u_made, 4 * i + 2 * t + x + 1)
                        nc.scalar.copy(Uo[x][:, t, :], bank[4 * x + 3][:, P:2 * P]).then_inc(u_copied2, 1)
                for x in range(2):
                    act.wait_ge(kk_squared, 2 * i + x + 1)
                    act.wait_ge(pair_var, 2 * i + x + 1)
                    nc.scalar.activation(hst[x][:, 12:16], hst[x][:, 12:16], ACT.Sqrt).then_inc(pair_root, 1)

            with act.Fori(0, PAIRS // 2) as i:
                body(i)

        HEAD_DVE = 51

        def dve_heads(dve, order):
            start = order.count()
            def by_head(v):
                return v.rearrange("p t (h d) -> p t h d", h=2)

            def per_head(v):
                return v.rearrange("p (t h) -> p t h", t=NT).unsqueeze(3).to_broadcast([P, NT, 2, DH])

            def body(i):
                order.body(start, i, HEAD_DVE)

                def cut(base, x):
                    return rkv[:, :, ds(base + P * (2 * i + x), P)]

                dve.wait_ge(rows3_loaded, 48 * i + 48)
                for x in range(2):
                    C = P * (2 * i + x)
                    dve.wait_ge(cs_done, 2 * i + x + 1)
                    dve.wait_ge(pexp, 6 * i + 2 * x + 2)
                    cs = bank[4 * x][:, 0:2 * P].rearrange("p (t s) -> p t s", t=NT)
                    nc.vector.tensor_tensor(Pex[x], cs, decay[:, :, ds(C, P)], ALU.subtract).then_inc(pdiff, 1)
                for x in range(2):
                    C = P * (2 * i + x)
                    rw3 = [rows3[:, j, P * x:P * x + P].unsqueeze(1).to_broadcast([P, NT, P]) for j in range(3)]
                    k, r, a = cut(D, x), cut(0, x), gain_a[:, :, ds(C, P)]
                    order.step(nc.vector.tensor_tensor(kkb[x], k, rw3[0], ALU.mult))
                    order.step(nc.vector.tensor_tensor(tmpb[x], kkb[x], kkb[x], ALU.mult))
                    nc.vector.tensor_reduce(hst[x][:, 0:4].rearrange("p (t h) -> p t h", t=NT), by_head(tmpb[x]), AX.X,
                                            ALU.add).then_inc(kk_squared, 1)
                    dve.wait_ge(kk_squared, 2 * i + x + 1)
                    order.step(nc.vector.scalar_tensor_tensor(out=tmpb[x], in0=a, scalar=-1.0, in1=rw3[1], op0=ALU.add,
                                                              op1=ALU.mult))
                    order.step(nc.vector.scalar_tensor_tensor(out=kpb[x], in0=tmpb[x], scalar=1.0, in1=k, op0=ALU.add,
                                                              op1=ALU.mult))
                    order.step(nc.vector.tensor_tensor(tmpb[x], r, kpb[x], ALU.mult))
                    if x == 0:
                        order.step(nc.vector.tensor_tensor(tmpb[x], tmpb[x], rw3[2], ALU.mult))
                    else:
                        nc.vector.tensor_tensor(tmpb[x], tmpb[x], rw3[2], ALU.mult).then_inc(rows3_used.sem, 1)
                        dve.wait_ge(*rows3_used.at(i + 1))
                    order.mark(nc.vector.tensor_reduce(hst[x][:, 4:8].rearrange("p (t h) -> p t h", t=NT), by_head(tmpb[x]),
                                                       AX.X, ALU.add))
                    dve.wait_ge(kk_root, 2 * i + x + 1)
                    order.step(nc.vector.tensor_scalar(hst[x][:, 0:4], hst[x][:, 0:4], 1e-12, None, ALU.max))
                    order.step(nc.vector.reciprocal(hst[x][:, 0:4], hst[x][:, 0:4]))
                    order.step(nc.vector.tensor_tensor(by_head(kkb[x]), by_head(kkb[x]), per_head(hst[x][:, 0:4]), ALU.mult))
                    dve.wait_ge(pexp, 6 * i + x + 5)
                    order.mark(nc.vector.tensor_tensor(Rt[x], r, Pm[x], ALU.mult))
                    nc.vector.tensor_tensor(At[x], kkb[x], Pex[x], ALU.mult).then_inc(tok_ready.sem, 1)
                    order.mark(nc.vector.tensor_tensor(Kt[x], kpb[x], Pi[x], ALU.mult))
                    order.step(nc.vector.tensor_tensor(kkb[x], kkb[x], a, ALU.mult))
                    nc.vector.tensor_tensor(Bt[x], kkb[x], Pi[x], ALU.mult).then_inc(tok_ready.sem, 1)
                for x in range(2):
                    for u in range(4):
                        dve.wait_ge(*gram_done.at(8 * i + 4 * x + u + 1))
                        order.mark(nc.vector.tensor_tensor(
                            gram[x][:, u, :].rearrange("p (a m) -> p a m", a=2),
                            bank[4 * x + u][:, :].rearrange("p (a m) -> p a m", a=2),
                            const[:, CONST["strict"][0]:CONST["tri"][1]].unsqueeze(1).to_broadcast([P, 2, 2 * P]),
                            ALU.mult))
                    order.settle()
                    lt = gram[x][:, :, 0:P]
                    order.step(nc.vector.scalar_tensor_tensor(out=lt, in0=lt, scalar=-1.0,
                                                              in1=ident.unsqueeze(1).to_broadcast([P, 4, P]),
                                                              op0=ALU.mult, op1=ALU.add))
                    dve.wait_ge(*tok_ready.at(4 * i + 2 * x + 2))
                    nc.vector.tensor_tensor(XT[x], lt, con("level0_t").unsqueeze(1).to_broadcast([P, 4, P]),
                                            ALU.mult).then_inc(gram_masked, 1)
                for lev in range(LEV):
                    for x in range(2):
                        dve.wait_ge(y_made, 2 * LEV * i + 2 * lev + x + 1)
                        dst = Xm[x] if lev == 0 else Ym[x]
                        ins = nc.vector.tensor_tensor(dst, bank[4 * x][:, :].rearrange("p (u s) -> p u s", u=4),
                                                      con(f"level{lev}").unsqueeze(1).to_broadcast([P, 4, P]), ALU.mult)
                        ins.then_inc(y_masked, 1)
                for x in range(2):
                    dve.wait_ge(s_made, 2 * i + x + 1)
                    nc.vector.scalar_tensor_tensor(out=SB[x], in0=bank[4 * x + 3][:, 256:384],
                                                   scalar=sdec[:, ds(2 * i + x, 1)], in1=con("heads"),
                                                   op0=ALU.mult, op1=ALU.mult).then_inc(s_ready, 1)
                for x in range(2):
                    dve.wait_ge(*o_made.at(2 * i + x + 1))
                    order.step(nc.vector.tensor_copy(ob[x], bank[4 * x][:, 0:2 * P].rearrange("p (t s) -> p t s", t=NT)))
                    order.step(nc.vector.tensor_reduce(hst[x][:, 8:12].rearrange("p (t h) -> p t h", t=NT), by_head(ob[x]),
                                                       AX.X, ALU.add))
                    order.step(nc.vector.tensor_scalar(hst[x][:, 8:12], hst[x][:, 8:12], 1.0 / DH, None, ALU.mult))
                    order.step(nc.vector.tensor_tensor(by_head(ob[x]), by_head(ob[x]), per_head(hst[x][:, 8:12]),
                                                       ALU.subtract))
                    order.step(nc.vector.tensor_tensor(Rt[x], ob[x], ob[x], ALU.mult))
                    order.step(nc.vector.tensor_reduce(hst[x][:, 12:16].rearrange("p (t h) -> p t h", t=NT), by_head(Rt[x]),
                                                       AX.X, ALU.add))
                    nc.vector.tensor_scalar(hst[x][:, 12:16], hst[x][:, 12:16], 1.0 / DH, 64e-5, ALU.mult,
                                            ALU.add).then_inc(pair_var, 1)
                    v = by_head(cut(2 * D, x))
                    order.mark(nc.vector.tensor_tensor(v, v, per_head(hst[x][:, 4:8]), ALU.mult))
                for x in range(2):
                    dve.wait_ge(pair_root, 2 * i + x + 1)
                    order.step(nc.vector.reciprocal(hst[x][:, 12:16], hst[x][:, 12:16]))
                    nc.vector.tensor_tensor(by_head(cut(0, x)), by_head(ob[x]), per_head(hst[x][:, 12:16]),
                                            ALU.mult).then_inc(pair_done.sem, 1)

            with dve.Fori(0, PAIRS // 2) as i:
                body(i)
            order.after(start, PAIRS // 2, HEAD_DVE)

        lng, lnb, fing = carve(0, D), carve(D, D), carve(2 * D, D)
        sq = [carve(4096 + 512 * b, TW) for b in range(NT)]
        heads = rkv[:, :, 0:D]
        vbon = rkv[:, :, 2 * D:3 * D]
        merged2 = gates[:, :, 0:D]
        ln_loaded, g_made = sem("ln_loaded"), sem("g_made")
        heads_gated = Again(gate_used, 4)
        merged2_ready = Again(att_merged, 4)
        mixed2 = Again(mixed, 4)
        turn_h = Turn(heads, None, t0h, t0l)
        turn_o = Turn(merged2, None, t0h, t0l)
        norm_2 = RmsNorm(xres, carve(9216, NT, D), stat)
        turn_f = Turn(carve(9216, NT, D), gain("norm_ff_g_2"), t0h, t0l)
        ff_relu = Again(silu_done, N_EXP)
        ff_squared = Again(hid_ready, 2 + N_EXP)
        ff_turned = Again(hid_turned, N_EXP)
        ff_high = Again(hid_high, N_EXP)
        ff_low = Again(hid_low, N_EXP)
        ff_added = Again(x_added, 4 * JOBS)
        norm_l = RmsNorm(xres, carve(9216, NT, D), stat)
        finished = sem("finished")

        def pe_out2(pe):
            for t in range(NT):
                for h in range(2):
                    nc.tensor.matmul(bank[2 * t + h][:, :], gT[:, t * P:(t + 1) * P], g2[:, 512 * h:512 * h + 512],
                                     start=True, stop=True).then_inc(g_made, 1)
            turn_h.pe(pe, [heads_gated.at(4)])
            square_product(pe, Q_RWKV, t0h, t0l, [turn_h.done(), heads_gated.at(4)])
            turn_o.pe(pe, [merged2_ready.at(4)])
            square_product(pe, Q_OUT2, t0h, t0l, [turn_o.done(), merged2_ready.at(4)])
            turn_f.pe(pe, [norm_2.ready()])
            pe.wait_ge(*turn_f.done())
            pe.wait_ge(*mixed2.at(4))

            def first(n, q, i=0, per=0):
                wide_quarter(pe, n, q, bank[0:2], t0h, t0l, TW, i, per)

            def turn(j):
                pe.wait_ge(*ff_squared.at(2 * j + 2))
                for b in range(2):
                    for cc in range(2):
                        for t in range(NT):
                            at = cc * SEQ + t * P
                            tr = nc.tensor.transpose(bank[2 + b][:, at:at + P],
                                                     sq[t].rearrange("p (f c) -> p f c", c=4)[:, :, 2 * b + cc], ident)
                    tr.then_inc(ff_turned.sem, 1)

            def second(n, c, j, i=0, per=0, last=False):
                if c == 0:
                    pe.wait_ge(*ff_low.at(2 * j + 2))
                wait_low(pe, n, i, per)
                s = n % RING
                for h in range(2):
                    f = slice(512 * h, 512 * h + 512)
                    for t in range(NT):
                        r = slice(t * P, (t + 1) * P)
                        o = bank[4 + 2 * h + t][:, :]
                        nc.tensor.matmul(o, t1h[:, c, r], whi[:, s, f], start=False, stop=False, skip_group_check=True)
                        nc.tensor.matmul(o, t1h[:, c, r], wlo[:, s, f], start=False, stop=False, skip_group_check=True)
                        mm = nc.tensor.matmul(o, t1l[:, c, r], whi[:, s, f], start=False, stop=last, skip_group_check=True)
                mm.then_inc(quarter_done, 1)

            for q in range(4):
                first(Q_FF + q, q)
            for b in range(4):
                nc.tensor.matmul(bank[4 + b][:, :].rearrange("p (k s) -> p k s", k=2), zero[:, :], t0h[:, 0:2, :],
                                 start=True, stop=False, skip_group_check=True)
            with pe.Fori(0, FF_J - 1) as j:
                for q in range(4):
                    if q == 0:
                        pe.wait_ge(*ff_relu.at(2 * j + 2))
                    first(Q_FF + 4 + q, q, j, 8)
                    if q == 1:
                        turn(j)
                for c in range(4):
                    second(Q_FF + 8 + c, c, j, j, 8)
            turn(FF_J - 1)
            for c in range(4):
                second(Q_END - 4 + c, c, FF_J - 1, last=c == 3)

        def sp_ff(sp):
            v1 = A["w_ff1_2"][0].rearrange("(p k) n -> p k n", k=KC)
            v2 = A["w_ff2_2"][0].rearrange("(j p c) n -> p j c n", j=FF_J, c=4)

            def first(n, q, j, i=0, per=0):
                load(sp, n, [(pair_view(raw, n, TW), v1[:, 2 * q:2 * q + 2, ds(TW * j, TW)])], i, per)

            def second(n, c, j, i=0, per=0):
                load(sp, n, [(raw[:, n % RING, :].rearrange("p (a c n) -> p a c n", a=1, c=1), v2[:, ds(j, 1), c:c + 1, :])],
                     i, per)

            for q in range(4):
                first(Q_FF + q, q, 0)
            with sp.Fori(0, FF_J - 1) as j:
                for q in range(4):
                    first(Q_FF + 4 + q, q, j + 1, j, 8)
                for c in range(4):
                    second(Q_FF + 8 + c, c, j, j, 8)
            for c in range(4):
                second(Q_END - 4 + c, c, FF_J - 1)

        def act_out2(act):
            act.wait_ge(*pair_done.at(PAIRS))
            for dst, src in ((lng, A["ln_x_g_2"][0]), (lnb, A["ln_x_b_2"][0]), (fing, A["norm_final_g_2"])):
                act.dma_start(dst, row(src, D)).then_inc(ln_loaded, 16)
            turn_h.act(act, Q_RWKV)
            for q in range(4, 8):
                split_high(act, Q_RWKV + q)
            for q in range(4):
                split_high(act, Q_OUT2 + q)
            turn_o.act(act, Q_OUT2)
            for q in range(4, 8):
                split_high(act, Q_OUT2 + q)
            for q in range(4):
                split_high(act, Q_FF + q)
            norm_2.act(act, [mixed2.at(4)])
            turn_f.act(act, Q_FF)

            def relu(j):
                act.wait_ge(quarter_done, Q_FF + 4 + 8 * j if not isinstance(j, int) or j else Q_FF + 4)
                for t in range(NT):
                    nc.scalar.activation(sq[t], bank[t][:, :], ACT.Relu).then_inc(ff_relu.sem, 1)

            def high(j):
                for b in range(2):
                    act.wait_ge(*ff_turned.at(2 * j + b + 1))
                    nc.scalar.activation(t1h[:, 2 * b:2 * b + 2, :], bank[2 + b][:, :].rearrange("p (c s) -> p c s", c=2),
                                         ACT.Copy).then_inc(ff_high.sem, 1)

            with act.Fori(0, FF_J - 1) as j:
                split_high(act, Q_FF + 4, j, 8)
                relu(j)
                for q in range(1, 4):
                    split_high(act, Q_FF + 4 + q, j, 8)
                high(j)
                for c in range(4):
                    split_high(act, Q_FF + 8 + c, j, 8)
            act.wait_ge(quarter_done, Q_END - 8)
            for t in range(NT):
                nc.scalar.activation(sq[t], bank[t][:, :], ACT.Relu).then_inc(ff_relu.sem, 1)
            for c in range(4):
                split_high(act, Q_END - 4 + c)
            high(FF_J - 1)
            norm_l.act(act, [ff_added.at(4)])

        def dve_out2(dve, order):
            dve.wait_ge(ln_loaded, 48)
            wide_row = lambda v: v.unsqueeze(1).to_broadcast([P, NT, D])
            dve.wait_ge(*pair_done.at(PAIRS))
            order.settle()
            order.step(nc.vector.tensor_tensor(heads, heads, wide_row(lng), ALU.mult))
            order.step(nc.vector.tensor_tensor(heads, heads, wide_row(lnb), ALU.add))
            order.step(nc.vector.tensor_tensor(heads, heads, vbon, ALU.add))
            for t in range(NT):
                for h in range(2):
                    dve.wait_ge(g_made, 2 * t + h + 1)
                    o = heads[:, t, 512 * h:512 * h + 512]
                    nc.vector.tensor_tensor(o, o, bank[2 * t + h][:, :], ALU.mult).then_inc(heads_gated.sem, 1)
            turn_h.dve(dve)
            for c in range(2):
                dve.wait_ge(quarter_done, Q_RWKV + 4 * c + 4)
                for t in range(NT):
                    o = merged2[:, t, c * TW:(c + 1) * TW]
                    order.step(nc.vector.tensor_tensor(o, o, bank[2 * c + t][:, :], ALU.mult))
                    nc.vector.tensor_tensor(o, o, gates[:, t, D + c * TW:D + (c + 1) * TW], ALU.add).then_inc(merged2_ready.sem, 1)
            turn_o.dve(dve)
            for c in range(2):
                dve.wait_ge(quarter_done, Q_OUT2 + 4 * c + 4)
                for t in range(NT):
                    o = xres[:, t, c * TW:(c + 1) * TW]
                    nc.vector.tensor_tensor(o, o, bank[2 * c + t][:, :], ALU.add).then_inc(mixed2.sem, 1)
            norm_2.dve(dve, order)
            turn_f.dve(dve)

            def ff(j):
                for t in range(NT):
                    dve.wait_ge(*ff_relu.at(2 * j + t + 1))
                    nc.vector.tensor_tensor(sq[t], sq[t], sq[t], ALU.mult).then_inc(ff_squared.sem, 1)
                for b in range(2):
                    dve.wait_ge(*ff_high.at(2 * j + b + 1))
                    nc.vector.tensor_tensor(t1l[:, 2 * b:2 * b + 2, :], bank[2 + b][:, :].rearrange("p (c s) -> p c s", c=2),
                                            t1h[:, 2 * b:2 * b + 2, :].bitcast(F32), ALU.subtract).then_inc(ff_low.sem, 1)

            with dve.Fori(0, FF_J) as j:
                ff(j)
            dve.wait_ge(quarter_done, Q_END)
            for h in range(2):
                for t in range(NT):
                    o = xres[:, t, 512 * h:512 * h + 512]
                    nc.vector.tensor_tensor(o, o, bank[4 + 2 * h + t][:, :], ALU.add).then_inc(ff_added.sem, 1)
            norm_l.dve(dve, order)
            for t in range(NT):
                dve.wait_ge(*norm_l.ready(t + 1))
                nc.vector.tensor_tensor(xres[:, t, :], norm_l.xn[:, t, :], fing, ALU.mult).then_inc(finished, 1)

        Q_END_RUN = Q_END

        block = ctx.enter_context(nc.Block())
        out_done = sem("out_done")

        @block.sync
        def _(sp):
            sp_block1(sp)
            sp_experts(sp)
            sp_overflow(sp)
            sp_ple(sp)
            sp_in2(sp)
            sp_ff(sp)
            for t in range(NT):
                sp.wait_ge(finished, t + 1)
                sp.dma_start(out[t * P:(t + 1) * P, :], xres[:, t, :]).then_inc(out_done, 16)
            sp.wait_ge(out_done, 16 * NT)

        @block.gpsimd
        def _(pool):
            pool_stream(pool)

        @block.scalar
        def _(act):
            act_loads(act)
            norm_a.act(act, [(x_loaded, 16)])
            act.wait_ge(vec_loaded, N_VEC)
            turn_a.act(act, 0)
            act_in(act)
            act_ssd(act)
            act_angles(act)
            act_attention(act)
            router_loads(act)
            act_router(act)
            act_experts(act)
            act_overflow(act)
            act_ple(act)
            act_in2(act)
            act_lora(act)
            act_conv(act)
            act_heads(act)
            act_out2(act)

        @block.vector
        def _(dve):
            order = Order(dve, dve_order)
            norm_a.dve(dve, order)
            turn_a.dve(dve)
            dve_ssd(dve, order)
            dve_angles(dve, order)
            dve_attention(dve, order)
            dve_router(dve, order)
            dve_experts(dve)
            dve_overflow(dve)
            dve_ple(dve, order)
            dve_in2(dve, order)
            dve_lora(dve, order)
            dve_conv(dve, order)
            dve_heads(dve, order)
            dve_out2(dve, order)

        @block.tensor
        def _(pe):
            pe_in(pe)
            pe_ssd(pe)
            pe_attention(pe)
            pe_router(pe)
            pe_experts(pe)
            pe_overflow(pe)
            pe_ple(pe)
            pe_in2(pe)
            pe_lora(pe)
            pe_conv(pe)
            pe_heads(pe)
            pe_out2(pe)


def kernel(**inputs):
    import concourse.bacc as bacc
    from concourse.bass_utils import run_bass_kernel_spmd

    nc = bacc.Bacc("TRN2", target_bir_lowering=False, num_devices=1)
    arrays, views = {}, {}
    given = {name: np.ascontiguousarray(a) for name, a in inputs.items()}
    given["const"] = constants()
    for name, a in given.items():
        arrays["in_" + name] = a
        views[name] = nc.dram_tensor("in_" + name, a.shape, mybir.dt.from_np(a.dtype), kind="ExternalInput").ap()
    result = nc.dram_tensor("result", (SEQ, D), F32, kind="ExternalOutput").ap()
    build(nc, views, result)
    r = run_bass_kernel_spmd(nc, [arrays], core_ids=[0])
    return r.results[0]["result"].reshape(1, SEQ, D)
```

```python
import math
from contextlib import ExitStack

import numpy as np

import concourse.bass as bass
from concourse import mybir

F32 = mybir.dt.float32
F32R = mybir.dt.float32r
I32 = mybir.dt.int32
ALU = mybir.AluOpType
ACT = mybir.ActivationFunctionType
AX = mybir.AxisListType
ds = bass.ds

P = 128
SEQ = 256
NT = SEQ // P
D = 1024
KC = D // P
EPS = 1e-6
IN_W = 7440
IN_TW = 496
IN_T = IN_W // IN_TW
IN2_W = 7168
TW = 512
QF = 2 * TW
RING = 4
MOE_RING = 6

C_Z, C_XBC, C_DT, C_Q, C_K, C_V, C_GS, C_GA = 0, 1024, 2304, 2320, 3344, 4368, 5392, 6416
NH, DH = 16, 64
XCH = 10
PAD = 3
TWO_PI = 2.0 * math.pi

Q_IN = 0
Q_SSD = Q_IN + 4 * IN_T
Q_ATT = Q_SSD + 8
Q_OUT = Q_ATT + 8
Q_MOE = Q_OUT + 8
N_EXP = 32
DE = 256
Q_PLE = Q_MOE + 6 * N_EXP
Q_GATE = Q_PLE + 2
Q_IN2 = Q_GATE + 8
Q_CONV = Q_IN2 + 4 * (IN2_W // TW)
Q_RWKV = Q_CONV + 8
Q_OUT2 = Q_RWKV + 8
Q_FF = Q_OUT2 + 8
FF_J = 8
Q_END = Q_FF + 8 * FF_J

CONST = {}


def constants():
    i = np.arange(P)
    parts = []

    def put(name, a):
        at = sum(x.shape[1] for x in parts)
        CONST[name] = (at, at + a.shape[1])
        parts.append(np.ascontiguousarray(a, dtype=np.float32))

    put("ident", np.eye(P))
    put("strict", (i[:, None] < i[None, :]) * 1.0)
    put("tri", (i[:, None] <= i[None, :]) * 1.0)
    put("centred", (i[:, None] <= i[None, :]) * 1.0 - (i[:, None] < 64) * np.ones((P, P)))
    put("ones", np.ones((P, P)))
    neg = np.where(i[None, :] <= i[:, None], 0.0, -1e30)
    put("amask", np.concatenate([neg, np.zeros((P, P)), neg], axis=1))
    for lev in range(7):
        m = 1 << lev
        pick = ((i[:, None] // m) % 2 == 1) & (i[None, :] // m == i[:, None] // m - 1)
        put(f"level{lev}", np.eye(P) + pick)
        if lev == 0:
            put("level0_t", np.eye(P) + pick.T)
    put("heads", (i[:, None] // 64 == i[None, :] // 64) * 1.0)
    put("low", (i[:, None] < 64) * 1.0)
    put("high", (i[:, None] >= 64) * 1.0)
    half = DH // 2
    freq = (np.float32(10000.0) ** (-np.arange(half, dtype=np.float32) / np.float32(half))).astype(np.float32)
    put("freq", np.broadcast_to(freq, (P, half)))
    put("slot", np.broadcast_to(np.arange(P), (P, P)))
    put("rev8", np.broadcast_to(8.0 - np.arange(8), (P, 8)))
    put("rev4", np.broadcast_to(4.0 - np.arange(4), (P, 4)))
    return np.concatenate(parts, axis=1)


constants()
N_CONST = max(b for _, b in CONST.values())


class Order:

    def __init__(self, eng, sem):
        self.eng, self.sem, self.base, self.n = eng, sem, 0, 0

    def mark(self, ins):
        ins.then_inc(self.sem, 1)
        self.n += 1

    def settle(self):
        self.eng.wait_ge(self.sem, self.base + self.n)

    def step(self, ins):
        self.mark(ins)
        self.settle()

    def body(self, start, i, per):
        self.base, self.n = start + i * per, 0

    def after(self, start, times, per):
        assert self.n == per, (self.n, per)
        self.base, self.n = start + times * per, 0

    def count(self):
        return self.base + self.n


class Again:

    def __init__(self, sem, before):
        self.sem, self.before = sem, before

    def at(self, n):
        return self.sem, self.before + n


def wait_from(eng, sem, value):
    if not (isinstance(value, int) and value <= 0):
        eng.wait_ge(sem, value)



JOB = 6 * 8


def split_by_vector(n):
    return Q_MOE - MOE_RING <= n < Q_PLE and n % 2 == 1


def slot(n):
    return (n - Q_MOE) % MOE_RING if Q_MOE <= n < Q_PLE else n % RING


RAW_DONE, LOW_DONE = [], []
_shown = [0] * MOE_RING
for _n in range(Q_END):
    _shown[slot(_n)] += 32 if Q_MOE <= _n < Q_PLE else 16
    RAW_DONE.append(_shown[slot(_n)])
    LOW_DONE.append(sum(split_by_vector(m) == split_by_vector(_n) for m in range(_n + 1)))


def at_turn(counts, n, i, per):
    if not per:
        return counts[n]
    span = JOB if per < JOB and JOB % per == 0 and n + JOB < Q_PLE and n >= Q_MOE - MOE_RING else per
    return counts[n] + (counts[n + span] - counts[n]) * per // span * i


NORMS = ["attn_norm_w", "moe_norm_w", "ple_norm_w", "ssd_norm_w", "norm_mix_g_2", "norm_ff_g_2",
         "conv_ln_g_2", "conv_ln_b_2"]


def build(nc, A, out):
    ctx = ExitStack()
    with ctx:
        def sb(name, shape, dt=F32):
            return ctx.enter_context(nc.sbuf_tensor(name, shape, dt))

        def sem(name):
            return ctx.enter_context(nc.semaphore(name))

        raw = sb("raw", [P, RING, QF])
        whi = sb("whi", [P, RING, QF], F32R)
        wlo = sb("wlo", [P, RING, QF], F32R)
        const = sb("const", [P, N_CONST])
        cols = sb("cols", [P, len(NORMS), KC])
        mul = sb("mul", [P, 3, KC])
        xres = sb("xres", [P, NT, D])
        t0h = sb("t0h", [P, KC, SEQ], F32R)
        t0l = sb("t0l", [P, KC, SEQ], F32R)
        t1h = sb("t1h", [P, 4, SEQ], F32R)
        t1l = sb("t1l", [P, 4, SEQ], F32R)
        proj = sb("proj", [P, NT, IN_W])
        WORK = 14320
        work = sb("work", [P, WORK])
        small = sb("small", [P, 360])
        bank = [ctx.enter_context(nc.psum_tensor(f"bank{b}", [P, 512], F32)) for b in range(8)]

        def con(name):
            a, b = CONST[name]
            return const[:, a:b]

        ident = con("ident")

        def carve(at, *shape):
            n = int(np.prod(shape))
            assert at + n <= WORK, (at, n)
            v = work[:, at:at + n]
            if len(shape) == 1:
                return v
            names = "abcd"[:len(shape)]
            return v.rearrange(f"p ({' '.join(names)}) -> p {' '.join(names)}", **dict(zip(names, shape)))

        def tiny(at, *shape):
            n = int(np.prod(shape))
            v = small[:, at:at + n]
            if len(shape) == 1:
                return v
            names = "abcd"[:len(shape)]
            return v.rearrange(f"p ({' '.join(names)}) -> p {' '.join(names)}", **dict(zip(names, shape)))

        raw_full = [sem(f"raw_full{s}") for s in range(MOE_RING)]
        hi_ready = sem("hi_ready")
        lo_by_pool = sem("lo_by_pool")
        lo_by_dve = sem("lo_by_dve")
        quarter_done = sem("quarter_done")
        consts_loaded = sem("consts_loaded")
        x_loaded = sem("x_loaded")
        vec_loaded = sem("vec_loaded")
        dve_order = sem("dve_order")
        act_order = sem("act_order")

        more_raw = proj[:, :, :].rearrange("p t n -> p (t n)")[:, 12232:12232 + (MOE_RING - RING) * QF]

        def raw_of(n):
            s = slot(n)
            return raw[:, s, :] if s < RING else more_raw[:, (s - RING) * QF:(s - RING + 1) * QF]

        def wait_low(eng, n, i=0, per=0):
            eng.wait_ge(lo_by_dve if split_by_vector(n) else lo_by_pool, at_turn(LOW_DONE, n, i, per))

        def load(sp, n, pairs, i=0, per=0):
            before = n - (MOE_RING if Q_MOE + RING <= n < Q_PLE else RING)
            if before >= 0:
                wait_low(sp, before, i, per)
            for dst, src in pairs:
                sp.dma_start(dst, src).then_inc(raw_full[slot(n)], 16)

        def split_high(act, n, i=0, per=0, width=QF):
            s = n % RING
            act.wait_ge(raw_full[slot(n)], at_turn(RAW_DONE, n, i, per))
            wait_from(act, quarter_done, n - RING + 1 + per * i)
            nc.scalar.activation(whi[:, s, 0:width], raw_of(n)[:, 0:width], ACT.Copy).then_inc(hi_ready, 1)

        def split_low(eng, n, i=0, per=0, width=QF):
            s = n % RING
            eng.wait_ge(hi_ready, n + 1 + per * i)
            ins = (nc.vector if split_by_vector(n) else nc.gpsimd).tensor_tensor(
                wlo[:, s, 0:width], raw_of(n)[:, 0:width], whi[:, s, 0:width].bitcast(F32), ALU.subtract)
            ins.then_inc(lo_by_dve if split_by_vector(n) else lo_by_pool, 1)

        def times(dst, hi, lo, wh, wl, first, last):
            nc.tensor.matmul(dst, hi, wh, start=first, stop=False)
            nc.tensor.matmul(dst, hi, wl, start=False, stop=False)
            return nc.tensor.matmul(dst, lo, wh, start=False, stop=last)

        def pair_view(buf, n, width):
            return buf[:, n % RING, 0:2 * width].rearrange("p (k n) -> p k n", k=2)

        def wide_quarter(pe, n, q, dst, hi, lo, width=TW, i=0, per=0, begun=False):
            wait_low(pe, n, i, per)
            wh, wl = pair_view(whi, n, width), pair_view(wlo, n, width)
            for t in range(NT):
                for kk in range(2):
                    k = 2 * q + kk
                    mm = times(dst[t][:, 0:width], hi[:, k, t * P:(t + 1) * P], lo[:, k, t * P:(t + 1) * P],
                               wh[:, kk, :], wl[:, kk, :], k == 0 and not begun, k == KC - 1)
            mm.then_inc(quarter_done, 1)

        def load_square(sp, n, w, quarters=range(8)):
            v = w.rearrange("(p k) n -> p k n", k=KC)
            for j in quarters:
                c, q, m = j // 4, j % 4, n + j
                load(sp, m, [(pair_view(raw, m, TW), v[:, 2 * q:2 * q + 2, c * TW:(c + 1) * TW])])

        def square_product(pe, n, hi, lo, waits, turn=None):
            for s, v in waits:
                pe.wait_ge(s, v)
            for c in range(2):
                for q in range(4):
                    if turn is not None and c == 0:
                        pe.wait_ge(*turn.done(2 * q + 2))
                    wide_quarter(pe, n + 4 * c + q, q, bank[2 * c:2 * c + 2], hi, lo)

        class Turn:
            turned = sem("turned")
            high = sem("turned_high")
            low = sem("turned_low")
            index = splits = 0

            def __init__(self, src, gain, hi, lo):
                self.src = src.rearrange("p t (f k) -> p t f k", k=KC)
                self.gain, self.hi, self.lo = gain, hi, lo
                self.banks, self.chunks = Turn.index * (KC // 2), Turn.splits * KC
                Turn.index += 1
                Turn.splits += hi is not None

            def written(self, banks=KC // 2):
                return self.turned, self.banks + banks

            def done(self, chunks=KC):
                return self.low, self.chunks + chunks

            def part(self, k):
                return bank[4 + k // 2][:, (k % 2) * SEQ:(k % 2) * SEQ + SEQ]

            def pe(self, pe, waits):
                for s, v in waits:
                    pe.wait_ge(s, v)
                for b in range(KC // 2):
                    for kk in range(2):
                        for t in range(NT):
                            at = kk * SEQ + t * P
                            tr = nc.tensor.transpose(bank[4 + b][:, at:at + P], self.src[:, t, :, 2 * b + kk],
                                                     ident)
                    tr.then_inc(self.turned, 1)

            def act(self, act, used):
                wait_from(act, quarter_done, used)
                for k in range(KC):
                    if k % 2 == 0:
                        act.wait_ge(*self.written(k // 2 + 1))
                    scale = 1.0 if self.gain is None else self.gain[:, k:k + 1]
                    nc.scalar.activation(self.hi[:, k, :], self.part(k), ACT.Copy if self.gain is None else ACT.Identity,
                                         scale=scale).then_inc(self.high, 1)

            def dve(self, dve):
                for k in range(KC):
                    dve.wait_ge(self.high, self.chunks + 2 * (k // 2) + 2)
                    hi = self.hi[:, k, :].bitcast(F32)
                    if self.gain is None:
                        ins = nc.vector.tensor_tensor(self.lo[:, k, :], self.part(k), hi, ALU.subtract)
                    else:
                        ins = nc.vector.scalar_tensor_tensor(out=self.lo[:, k, :], in0=self.part(k),
                                                             scalar=self.gain[:, k:k + 1], in1=hi,
                                                             op0=ALU.mult, op1=ALU.subtract)
                    ins.then_inc(self.low, 1)

        class RmsNorm:
            squared, mean, root, normed = sem("rms_squared"), sem("rms_mean"), sem("rms_root"), sem("rms_normed")
            index = 0

            def __init__(self, src, xn, stat):
                self.src, self.xn, self.stat = src, xn, stat
                self.before = RmsNorm.index
                RmsNorm.index += 1

            def ready(self, tiles=NT):
                return self.normed, NT * self.before + tiles

            def act(self, act, waits):
                for s, v in waits:
                    act.wait_ge(s, v)
                for t in range(NT):
                    nc.scalar.activation(self.xn[:, t, :], self.src[:, t, :], ACT.Square,
                                         accum_out=self.stat[:, t:t + 1]).then_inc(self.squared, 1)
                act.wait_ge(self.mean, self.before + 1)
                nc.scalar.activation(self.stat[:, 0:NT], self.stat[:, 0:NT], ACT.Sqrt).then_inc(self.root, 1)

            def dve(self, dve, order):
                dve.wait_ge(self.squared, NT * self.before + NT)
                nc.vector.tensor_scalar(self.stat[:, 0:NT], self.stat[:, 0:NT], 1.0 / D, EPS,
                                        ALU.mult, ALU.add).then_inc(self.mean, 1)
                dve.wait_ge(self.root, self.before + 1)
                order.step(nc.vector.reciprocal(self.stat[:, 0:NT], self.stat[:, 0:NT]))
                for t in range(NT):
                    nc.vector.tensor_scalar(self.xn[:, t, :], self.src[:, t, :], self.stat[:, t:t + 1], None,
                                            ALU.mult).then_inc(self.normed, 1)

        def gain(name):
            return cols[:, NORMS.index(name), :]

        xn = carve(0, NT, D)
        stat = tiny(0, 8)
        norm_a = RmsNorm(xres, xn, stat)
        turn_a = Turn(xn, gain("attn_norm_w"), t0h, t0l)
        evac_in = sem("evac_in")

        y = carve(0, NT, D)
        xbcT = carve(2048, XCH, PAD + SEQ)
        convT = carve(2048 + 2590, XCH, SEQ)
        xdt = carve(7198, NT, D)
        xdtd = carve(9246, D)
        dif = carve(10270, NT, 4, P)
        mt = carve(11294, NT, 4, P)
        prevT = carve(12318, 512)
        cbm = carve(12830, 4, P)
        btok = carve(13342, P)
        xs = proj[:, :, C_XBC:C_XBC + D]
        cwT = tiny(8, 50)
        dtb, alog, dsk = tiny(58, 16), tiny(74, 16), tiny(90, 16)
        s_raw, s_neg, s_exp, s_u = (tiny(106 + 32 * j, NT, 16) for j in range(4))
        dt, dA = tiny(234, NT, 16), tiny(266, NT, 16)
        ecum = tiny(298, NT, 16)
        edec = tiny(330, 16)
        acum = dif[:, 0, 0, 0:64].rearrange("p (t a h) -> p t a h", t=NT, a=2)
        rows = carve(13470, P)
        cum = carve(13598, NT, 2, 16)
        xbc_turned, xbc_copied = sem("xbc_turned"), sem("xbc_copied")
        taps_turned, taps_ready = sem("taps_turned"), sem("taps_ready")
        conv_done, conv_active = sem("conv_done"), sem("conv_active")
        x_back, cb_done = sem("x_back"), sem("cb_done")
        dt_arg, dt_exp, dt_ln_arg, dt_ln = sem("dt_arg"), sem("dt_exp"), sem("dt_ln_arg"), sem("dt_ln")
        dA_ready, cum_done, cum_ready, dec_arg, dec_ready = (
            sem(s) for s in ("dA_ready", "cum_done", "cum_ready", "dec_arg", "dec_ready"))
        xdt_ready, state_done, state_ready, off_done = (
            sem(s) for s in ("xdt_ready", "state_done", "state_ready", "off_done"))
        abc_done, dif_ready, lmat_ready, mt_ready, diag_done, y_ready = (
            sem(s) for s in ("abc_done", "dif_ready", "lmat_ready", "mt_ready", "diag_done", "y_ready"))
        z_active, gate_active, y_gated, y_squared, y_normed = (
            sem(s) for s in ("z_active", "gate_active", "y_gated", "y_squared", "y_normed"))
        y_mean, y_root = sem("y_mean"), sem("y_root")
        turn_y = Turn(y, gain("ssd_norm_w"), t0h, t0l)
        ssd_merged = sem("ssd_merged")

        yatt = carve(0, NT, D)
        rot = [carve(2048 + 512 * x, 2, NT, P) for x in range(2)]
        rtmp = [carve(3072 + 128 * x, NT, 2, 32) for x in range(2)]
        qkT = [carve(3328 + 512 * x, 4, P) for x in range(2)]
        sc = [carve(4352 + 384 * x, 384) for x in range(4)]
        pT = [carve(5888 + 384 * x, 384) for x in range(4)]
        cosb, sinb = carve(7424, NT, 32), carve(7488, NT, 32)
        ang, tr1 = carve(7552, NT, 32), carve(7616, NT, 32)
        posf = tiny(0, NT)
        amax, asum = tiny(2, 4, 2), tiny(10, 2, 2, 2)
        posi = sb("posi", [P, NT], I32)
        pos_loaded = sem("pos_loaded")
        sin_arg, sin_done = sem("sin_arg"), sem("sin_done")
        rot_ready, qk_turned, qk_copied, scored, maxed, exped, p_turned, p_copied, pv_done, att_ready = (
            sem(s) for s in ("rot_ready", "qk_turned", "qk_copied", "scored", "maxed", "exped", "p_turned",
                             "p_copied", "pv_done", "att_ready"))
        turn_att = Turn(yatt, None, t0h, t0l)
        merged = proj[:, :, C_GS:C_GS + D]
        att_merged = sem("att_merged")
        turn_m = Turn(merged, None, t0h, t0l)
        mixed = sem("mixed")

        PAIRS = NH // 2

        def in_views(q, j):
            v = A["w_in"][0].rearrange("(p k) n -> p k n", k=KC)
            return v[:, 2 * q:2 * q + 2, ds(IN_TW * j, IN_TW)]

        def sp_block1(sp):
            sp.dma_start(xres[:, :, :], A["x"][0].rearrange("(t p) n -> p t n", p=P)).then_inc(x_loaded, 16)
            for q in range(4):
                load(sp, q, [(pair_view(raw, q, IN_TW), in_views(q, 0))])
            with sp.Fori(1, IN_T) as j:
                for q in range(4):
                    load(sp, 4 + q, [(pair_view(raw, q, IN_TW), in_views(q, j))], i=j - 1, per=4)
            load_square(sp, Q_SSD, A["w_ssd_out"][0])
            load_square(sp, Q_ATT, A["w_attn_out"][0])
            load_square(sp, Q_OUT, A["w_out"][0])

        def row(ap, n):
            return ap.rearrange("(a n) -> a n", a=1).to_broadcast([P, n])

        def act_loads(act):
            act.dma_start(const[:, :], A["const"]).then_inc(consts_loaded, 16)
            for j, name in enumerate(NORMS):
                v = A[name][0]
                act.dma_start(cols[:, j, :], v.rearrange("(p k) -> p k", k=KC)).then_inc(vec_loaded, 16)
            act.dma_start(rows[0:40, :], A["conv_w"][0].rearrange("w (k p) -> (w k) p", p=P)).then_inc(vec_loaded, 16)
            act.dma_start(rows[40:50, :], A["conv_b"][0].rearrange("(k p) -> k p", p=P)).then_inc(vec_loaded, 16)
            for dst, name in ((dtb, "dt_bias"), (alog, "a_log"), (dsk, "d_skip")):
                act.dma_start(dst, row(A[name][0], NH)).then_inc(vec_loaded, 16)
            act.dma_start(mul[:, :, :], A["mu_lora_2"][0].rearrange("a (p k) -> p a k", k=KC)).then_inc(vec_loaded, 16)
            with nc.allow_non_contiguous_dma(reason="256 positions, one per partition"):
                act.dma_start(posi[:, :], A["positions"][0].rearrange("(t p) -> p t", p=P)).then_inc(pos_loaded, 16)

        N_VEC = 16 * (len(NORMS) + 6)

        def pool_stream(pool):
            with pool.Fori(0, IN_T) as j:
                for q in range(4):
                    split_low(pool, q, j, 4, 2 * IN_TW)
            with pool.Fori(0, (Q_MOE - Q_SSD) // 4 - 2) as j:
                for q in range(4):
                    split_low(pool, Q_SSD + q, j, 4)
            for n in range(Q_MOE - 8, Q_MOE):
                if not split_by_vector(n):
                    split_low(pool, n)
            with pool.Fori(0, (Q_PLE - Q_MOE) // U) as j:
                for q in range(0, U, 2):
                    split_low(pool, Q_MOE + q, j, U)
            ahead = Q_RWKV + RING
            with pool.Fori(0, (ahead - Q_PLE) // 4) as j:
                for q in range(4):
                    split_low(pool, Q_PLE + q, j, 4)
            for n in range(ahead - (ahead - Q_PLE) % 4, ahead):
                split_low(pool, n)
            pool_heads(pool)
            with pool.Fori(0, (Q_END - ahead) // 4) as j:
                for q in range(4):
                    split_low(pool, ahead + q, j, 4)

        def pe_in(pe):
            pe.wait_ge(consts_loaded, 16)
            turn_a.pe(pe, [norm_a.ready()])
            pe.wait_ge(*turn_a.done())

            def tile(j, c):
                b = bank[2 * c:2 * c + 2]
                wait_from(pe, evac_in, NT * (j - 1))
                for q in range(4):
                    i = 0 if isinstance(j, int) else j
                    wide_quarter(pe, (4 * j if isinstance(j, int) else 0) + q, q, b, t0h, t0l, IN_TW, i,
                                 0 if isinstance(j, int) else 4)

            tile(0, 0)
            tile(1, 1)
            with pe.Fori(1, IN_T // 2) as i:
                for c in range(2):
                    tile(2 * i + c, c)
            tile(IN_T - 1, 0)

        def act_in(act):
            for q in range(4):
                split_high(act, q, width=2 * IN_TW)

            def evac(j, c):
                act.wait_ge(quarter_done, 4 * j + 4)
                for t in range(NT):
                    nc.scalar.copy(proj[:, t, ds(IN_TW * j, IN_TW)], bank[2 * c + t][:, 0:IN_TW]).then_inc(evac_in, 1)

            with act.Fori(0, IN_T // 2) as i:
                for c in range(2):
                    j = 2 * i + 1 + c
                    for q in range(4):
                        split_high(act, 4 * (1 + c) + q, i, 8, 2 * IN_TW)
                    evac(j - 1, c)
            for q in range(4):
                split_high(act, Q_SSD + q)
            evac(IN_T - 1, 0)

        def pe_ssd(pe):
            pe.wait_ge(evac_in, NT * IN_T)
            pe.wait_ge(vec_loaded, N_VEC)
            nc.tensor.transpose(bank[1][:, 0:50], rows[0:50, :], ident[0:50, 0:50]).then_inc(taps_turned, 1)
            pe.wait_ge(*turn_a.done())
            for b in range(XCH // 2):
                dst = bank[4 + b] if b < 4 else bank[0]
                for kk in range(2):
                    for t in range(NT):
                        c = C_XBC + (2 * b + kk) * P
                        tr = nc.tensor.transpose(dst[:, kk * SEQ + t * P:kk * SEQ + (t + 1) * P],
                                                 proj[:, t, c:c + P], ident)
                tr.then_inc(xbc_turned, 1)
            pe.wait_ge(dA_ready, 1)
            for t in range(NT):
                nc.tensor.matmul(bank[3][:, 32 * t:32 * t + 16], con("tri"), dA[:, t, :], start=True, stop=True)
                mm = nc.tensor.matmul(bank[3][:, 32 * t + 16:32 * t + 32], con("ones"), dA[:, t, :],
                                      start=True, stop=True)
            mm.then_inc(cum_done, 1)
            pe.wait_ge(conv_active, XCH)
            pe.wait_ge(xbc_copied, XCH // 2)
            pe.wait_ge(taps_ready, 1)
            for t in range(NT):
                for h in range(2):
                    for c in range(4):
                        tr = nc.tensor.transpose(bank[4 + 2 * t + h][:, c * P:(c + 1) * P],
                                                 convT[:, 4 * h + c, t * P:(t + 1) * P], ident)
                    tr.then_inc(x_back, 1)
            nc.tensor.transpose(bank[1][:, 0:P], convT[:, 8, 0:P], ident)
            pe.wait_ge(cum_ready, 1)
            for g in range(2):
                for t in range(NT):
                    mm = nc.tensor.matmul(bank[2 + g][:, (1 + t) * P:(2 + t) * P],
                                          convT[64 * g:64 * g + 64, 8, t * P:(t + 1) * P],
                                          convT[64 * g:64 * g + 64, 9, t * P:(t + 1) * P], start=True, stop=True)
            mm.then_inc(cb_done, 1)
            pe.wait_ge(xdt_ready, 1)
            for g in range(2):
                mm = nc.tensor.matmul(bank[0][64 * g:64 * g + 64, :], btok[:, 64 * g:64 * g + 64],
                                      xdtd[:, 512 * g:512 * g + 512], start=True, stop=True)
            mm.then_inc(state_done, 1)
            pe.wait_ge(state_ready, 1)
            for g in range(2):
                mm = nc.tensor.matmul(bank[6 + g][:, :], convT[64 * g:64 * g + 64, 9, P:2 * P],
                                      prevT[64 * g:64 * g + 64, :], start=True, stop=True)
            mm.then_inc(off_done, 1)

            def sums(q):
                for t in range(NT):
                    wait_from(pe, dif_ready, 2 * (q - 1) + t + 1)
                    for h in range(4):
                        e = 4 * q + h
                        mm = nc.tensor.matmul(bank[t][:, h * P:(h + 1) * P],
                                              dA[:, t, e:e + 1].to_broadcast([P, P]), con("tri"),
                                              start=True, stop=True)
                    mm.then_inc(abc_done, 1)

            def diagonal(q):
                for t in range(NT):
                    pe.wait_ge(mt_ready, 2 * q + t + 1)
                    wait_from(pe, y_ready, 2 * (q - 1) + t + 1)
                    for h in range(4):
                        e = 4 * q + h
                        mm = nc.tensor.matmul(bank[4 + t][:, h * DH:(h + 1) * DH], mt[:, t, h, :],
                                              xdt[:, t, e * DH:(e + 1) * DH], start=True, stop=True)
                    mm.then_inc(diag_done, 1)

            sums(0)
            for q in range(4):
                if q < 3:
                    sums(q + 1)
                diagonal(q)
            turn_y.pe(pe, [(y_normed, 4)])
            square_product(pe, Q_SSD, t0h, t0l, [(dif_ready, 8)], turn_y)

        def dve_ssd(dve, order):
            dve.wait_ge(vec_loaded, N_VEC)
            dve.wait_ge(evac_in, NT * IN_T)
            order.mark(nc.vector.memset(xbcT[:, :, 0:PAD], 0.0))
            order.step(nc.vector.tensor_tensor(s_raw, proj[:, :, C_DT:C_DT + NH],
                                               dtb.unsqueeze(1).to_broadcast([P, NT, NH]), ALU.add))
            nc.vector.scalar_tensor_tensor(out=s_neg, in0=s_raw, scalar=-1.0, in1=s_raw, op0=ALU.mult,
                                           op1=ALU.min).then_inc(dt_arg, 1)
            dve.wait_ge(taps_turned, 1)
            nc.vector.tensor_copy(cwT, bank[1][:, 0:50]).then_inc(taps_ready, 1)
            for b in range(XCH // 2):
                dve.wait_ge(xbc_turned, b + 1)
                src = (bank[4 + b] if b < 4 else bank[0])[:, :].rearrange("p (k s) -> p k s", k=2)
                nc.vector.tensor_copy(xbcT[:, 2 * b:2 * b + 2, PAD:PAD + SEQ], src).then_inc(xbc_copied, 1)
            dve.wait_ge(xbc_copied, XCH // 2)
            dve.wait_ge(taps_ready, 1)
            for w in range(4):
                for c in range(XCH):
                    tap = cwT[:, w * XCH + c:w * XCH + c + 1]
                    if w == 0:
                        order.mark(nc.vector.tensor_scalar(convT[:, c, :], xbcT[:, c, 0:SEQ], tap, None, ALU.mult))
                    else:
                        ins = nc.vector.scalar_tensor_tensor(out=convT[:, c, :], in0=xbcT[:, c, w:w + SEQ], scalar=tap,
                                                             in1=convT[:, c, :], op0=ALU.mult, op1=ALU.add)
                        if w < 3:
                            order.mark(ins)
                        else:
                            ins.then_inc(conv_done, 1)
                order.settle()
            dve.wait_ge(dt_exp, 2)
            order.step(nc.vector.tensor_scalar(s_u, s_exp, 1.0, None, ALU.add))
            order.step(nc.vector.tensor_scalar(dt, s_u, 1.0, None, ALU.subtract))
            order.mark(nc.vector.reciprocal(dA, s_u))
            order.step(nc.vector.tensor_tensor(dt, s_exp, dt, ALU.subtract))
            nc.vector.tensor_tensor(dt, dt, dA, ALU.mult).then_inc(dt_ln_arg, 1)
            dve.wait_ge(dt_ln_arg, 1)
            dve.wait_ge(dt_ln, 1)
            order.step(nc.vector.tensor_tensor(dt, dt, s_neg, ALU.add))
            order.step(nc.vector.scalar_tensor_tensor(out=dt, in0=s_raw, scalar=0.0, in1=dt, op0=ALU.max, op1=ALU.add))
            nc.vector.scalar_tensor_tensor(out=dA, in0=dt, scalar=-1.0,
                                           in1=alog.unsqueeze(1).to_broadcast([P, NT, NH]),
                                           op0=ALU.mult, op1=ALU.mult).then_inc(dA_ready, 1)
            dve.wait_ge(cum_done, 1)
            nc.vector.tensor_copy(cum, bank[3][:, 0:64].rearrange("p (t a h) -> p t a h", t=NT, a=2)).then_inc(cum_ready, 1)
            dve.wait_ge(cum_ready, 1)
            nc.vector.tensor_tensor(edec, cum[:, 0, 1, :], cum[:, 0, 0, :], ALU.subtract).then_inc(dec_arg, 1)
            for t in range(NT):
                for h in range(2):
                    dve.wait_ge(x_back, 2 * t + h + 1)
                    src = bank[4 + 2 * t + h]
                    order.mark(nc.vector.tensor_copy(xs[:, t, 512 * h:512 * h + 512], src[:, :]))
                    order.mark(nc.vector.tensor_tensor(
                        xdt[:, t, 512 * h:512 * h + 512].rearrange("p (e d) -> p e d", d=DH),
                        src[:, :].rearrange("p (e d) -> p e d", d=DH),
                        dt[:, t, 8 * h:8 * h + 8].unsqueeze(2).to_broadcast([P, 8, DH]), ALU.mult))
            dve.wait_ge(cb_done, 1)
            order.mark(nc.vector.tensor_copy(btok, bank[1][:, 0:P]))
            for g in range(2):
                order.mark(nc.vector.tensor_tensor(cbm[:, 2 * g:2 * g + 2, :],
                                                   bank[2 + g][:, P:3 * P].rearrange("p (a l) -> p a l", a=2),
                                                   con("tri").unsqueeze(1).to_broadcast([P, 2, P]), ALU.mult))
            order.settle()
            dve.wait_ge(dec_ready, 2)
            nc.vector.tensor_tensor(xdtd.rearrange("p (e d) -> p e d", d=DH),
                                    xdt[:, 0, :].rearrange("p (e d) -> p e d", d=DH),
                                    edec.unsqueeze(2).to_broadcast([P, NH, DH]), ALU.mult).then_inc(xdt_ready, 1)
            dve.wait_ge(state_done, 1)
            nc.vector.tensor_copy(prevT, bank[0][:, :]).then_inc(state_ready, 1)
            for t in range(NT):
                order.mark(nc.vector.tensor_tensor(y[:, t, :].rearrange("p (e d) -> p e d", d=DH),
                                                   xs[:, t, :].rearrange("p (e d) -> p e d", d=DH),
                                                   dsk.unsqueeze(2).to_broadcast([P, NH, DH]), ALU.mult))
            dve.wait_ge(off_done, 1)
            for g in range(2):
                order.mark(nc.vector.tensor_tensor(xdtd[:, 512 * g:512 * g + 512].rearrange("p (e d) -> p e d", d=DH),
                                                   bank[6 + g][:, :].rearrange("p (e d) -> p e d", d=DH),
                                                   ecum[:, 1, 8 * g:8 * g + 8].unsqueeze(2).to_broadcast([P, 8, DH]),
                                                   ALU.mult))
            order.settle()
            order.step(nc.vector.tensor_tensor(y[:, 1, :], y[:, 1, :], xdtd, ALU.add))

            def differences(q):
                for t in range(NT):
                    dve.wait_ge(abc_done, 2 * q + t + 1)
                    wait_from(dve, mt_ready, 2 * (q - 1) + t + 1)
                    for h in range(4):
                        e = 4 * q + h
                        ins = nc.vector.tensor_scalar(dif[:, t, h, :], bank[t][:, h * P:(h + 1) * P],
                                                      cum[:, t, 0, e:e + 1], 0.0, ALU.subtract, ALU.min)
                        if h < 3:
                            order.mark(ins)
                    ins.then_inc(dif_ready, 1)

            def add_diagonal(q):
                for t in range(NT):
                    dve.wait_ge(diag_done, 2 * q + t + 1)
                    o = y[:, t, 256 * q:256 * q + 256]
                    nc.vector.tensor_tensor(o, o, bank[4 + t][:, 0:256], ALU.add).then_inc(y_ready, 1)

            for q in range(4):
                differences(q)
                if q:
                    add_diagonal(q - 1)
                for t in range(NT):
                    dve.wait_ge(lmat_ready, 2 * q + t + 1)
                    nc.vector.tensor_tensor(mt[:, t], dif[:, t],
                                            cbm[:, 2 * (q // 2) + t, :].unsqueeze(1).to_broadcast([P, 4, P]),
                                            ALU.mult).then_inc(mt_ready, 1)
            add_diagonal(3)
            dve.wait_ge(z_active, NT)
            dve.wait_ge(y_ready, 8)
            for t in range(NT):
                nc.vector.tensor_tensor(y[:, t, :], y[:, t, :], proj[:, t, C_Z:C_Z + D], ALU.mult).then_inc(y_gated, 1)
            dve.wait_ge(y_squared, 4)
            nc.vector.tensor_scalar(stat[:, 0:4], stat[:, 0:4], 1.0 / 512, EPS, ALU.mult, ALU.add).then_inc(y_mean, 1)
            dve.wait_ge(y_root, 1)
            order.step(nc.vector.reciprocal(stat[:, 0:4], stat[:, 0:4]))
            for t in range(NT):
                for g in range(2):
                    o = y[:, t, 512 * g:512 * g + 512]
                    nc.vector.tensor_scalar(o, o, stat[:, 2 * t + g:2 * t + g + 1], None, ALU.mult).then_inc(y_normed, 1)
            turn_y.dve(dve)
            dve.wait_ge(gate_active, 4)
            for c in range(2):
                dve.wait_ge(quarter_done, Q_SSD + 4 * c + 4)
                for t in range(NT):
                    o = merged[:, t, c * TW:(c + 1) * TW]
                    nc.vector.tensor_tensor(o, o, bank[2 * c + t][:, :], ALU.mult).then_inc(ssd_merged, 1)

        def act_ssd(act):
            act.wait_ge(vec_loaded, N_VEC)
            act.wait_ge(dt_arg, 1)
            nc.scalar.activation(s_exp, s_neg, ACT.Exp).then_inc(dt_exp, 1)
            nc.scalar.activation(alog, alog, ACT.Exp).then_inc(dt_exp, 1)
            act.wait_ge(dt_ln_arg, 1)
            nc.scalar.activation(s_neg, s_u, ACT.Ln).then_inc(dt_ln, 1)
            for c in range(XCH):
                act.wait_ge(conv_done, c + 1)
                nc.scalar.activation(convT[:, c, :], convT[:, c, :], ACT.Silu,
                                     bias=cwT[:, 40 + c:41 + c]).then_inc(conv_active, 1)
            act.wait_ge(evac_in, NT * IN_T)
            for t in range(NT):
                z = proj[:, t, C_Z:C_Z + D]
                nc.scalar.activation(z, z, ACT.Silu).then_inc(z_active, 1)
            act.wait_ge(cum_ready, 1)
            nc.scalar.activation(ecum, cum[:, :, 0, :], ACT.Exp).then_inc(dec_ready, 1)
            act.wait_ge(dec_arg, 1)
            nc.scalar.activation(edec, edec, ACT.Exp).then_inc(dec_ready, 1)
            for q in range(4):
                for t in range(NT):
                    act.wait_ge(dif_ready, 2 * q + t + 1)
                    nc.scalar.activation(dif[:, t], dif[:, t], ACT.Exp).then_inc(lmat_ready, 1)
            act.wait_ge(y_gated, NT)
            act.wait_ge(diag_done, 8)
            for t in range(NT):
                for g in range(2):
                    nc.scalar.activation(xdt[:, t, 512 * g:512 * g + 512], y[:, t, 512 * g:512 * g + 512], ACT.Square,
                                         accum_out=stat[:, 2 * t + g:2 * t + g + 1]).then_inc(y_squared, 1)
            act.wait_ge(y_mean, 1)
            nc.scalar.activation(stat[:, 0:4], stat[:, 0:4], ACT.Sqrt).then_inc(y_root, 1)
            for c in (C_GS, C_GA):
                for t in range(NT):
                    g = proj[:, t, c:c + D]
                    nc.scalar.activation(g, g, ACT.Sigmoid).then_inc(gate_active, 1)
            turn_y.act(act, Q_SSD)
            for q in range(4, 8):
                split_high(act, Q_SSD + q)
            for q in range(4):
                split_high(act, Q_ATT + q)

        def dve_angles(dve, order):
            dve.wait_ge(pos_loaded, 16)
            dve.wait_ge(ssd_merged, 4)
            order.step(nc.vector.tensor_copy(posf, posi[:, :]))
            for t in range(NT):
                order.mark(nc.vector.tensor_scalar(ang[:, t, :], con("freq"), posf[:, t:t + 1], None, ALU.mult))
            order.settle()
            order.step(nc.vector.tensor_scalar(tr1, ang, 1.0 / TWO_PI, None, ALU.mult))
            order.step(nc.vector.tensor_scalar(tr1, tr1, 12582912.0, None, ALU.add))
            order.step(nc.vector.tensor_scalar(tr1, tr1, 12582912.0, None, ALU.subtract))
            c1 = 6.28125
            c2 = float(np.float32(np.round((TWO_PI - c1) * 2.0 ** 20) / 2.0 ** 20))
            c3 = TWO_PI - c1 - c2
            for c in (c1, c2, c3):
                order.step(nc.vector.scalar_tensor_tensor(out=ang, in0=tr1, scalar=-c, in1=ang, op0=ALU.mult, op1=ALU.add))
            top = float(np.nextafter(np.float32(math.pi), np.float32(0)))
            order.step(nc.vector.tensor_scalar(sinb, ang, top, -top, ALU.min, ALU.max))
            order.step(nc.vector.tensor_scalar(ang, ang, math.pi / 2, None, ALU.add))
            order.step(nc.vector.tensor_scalar(tr1, ang, math.pi, -TWO_PI, ALU.is_gt, ALU.mult))
            order.step(nc.vector.tensor_tensor(ang, ang, tr1, ALU.add))
            nc.vector.tensor_scalar(cosb, ang, top, -top, ALU.min, ALU.max).then_inc(sin_arg, 1)

        def act_angles(act):
            act.wait_ge(sin_arg, 1)
            nc.scalar.activation(sinb, sinb, ACT.Sin).then_inc(sin_done, 1)
            nc.scalar.activation(cosb, cosb, ACT.Sin).then_inc(sin_done, 1)

        ATT_DVE = 36

        def dve_attention(dve, order):
            dve.wait_ge(sin_done, 2)
            cos = cosb.unsqueeze(2).to_broadcast([P, NT, 2, 32])
            sin = sinb.unsqueeze(2).to_broadcast([P, NT, 2, 32])
            start = order.count()

            def body(i):
                order.body(start, i, ATT_DVE)
                for x in range(2):
                    for a, c in ((0, C_Q), (1, C_K)):
                        src = proj[:, :, ds(c + P * (2 * i + x), P)].rearrange("p t (h a d) -> p t h a d", h=2, a=2)
                        x1, x2 = src[:, :, :, 0, :], src[:, :, :, 1, :]
                        dst = rot[x][:, a].rearrange("p t (h a d) -> p t h a d", h=2, a=2)
                        o1, o2 = dst[:, :, :, 0, :], dst[:, :, :, 1, :]
                        order.mark(nc.vector.tensor_tensor(o1, x1, cos, ALU.mult))
                        order.mark(nc.vector.tensor_tensor(rtmp[0], x2, sin, ALU.mult))
                        order.mark(nc.vector.tensor_tensor(o2, x2, cos, ALU.mult))
                        order.step(nc.vector.tensor_tensor(rtmp[1], x1, sin, ALU.mult))
                        order.mark(nc.vector.tensor_tensor(o1, o1, rtmp[0], ALU.subtract))
                        last = nc.vector.tensor_tensor(o2, o2, rtmp[1], ALU.add)
                        if a == 0:
                            order.step(last)
                    last.then_inc(rot_ready, 1)
                    dve.wait_ge(rot_ready, 2 * i + x + 1)
                for z in range(4):
                    dve.wait_ge(scored, 4 * i + z + 1)
                    order.step(nc.vector.tensor_tensor(sc[z], bank[2 + z][:, 0:384], con("amask"), ALU.add))
                    order.mark(nc.vector.tensor_reduce(amax[:, z, 0:1], sc[z][:, 0:P], AX.X, ALU.max))
                    order.step(nc.vector.tensor_reduce(amax[:, z, 1:2], sc[z][:, P:384], AX.X, ALU.max))
                    nc.vector.tensor_scalar(amax[:, z, :], amax[:, z, :], -(DH ** -0.5), None, ALU.mult).then_inc(maxed, 1)
                for x in range(2):
                    dve.wait_ge(pv_done, 2 * i + x + 1)
                    order.step(nc.vector.reciprocal(asum[:, x], asum[:, x]))
                    nc.vector.tensor_tensor(
                        yatt[:, :, ds(P * (2 * i + x), P)].rearrange("p t (h d) -> p t h d", h=2),
                        bank[6 + x][:, 0:256].rearrange("p (h t d) -> p t h d", h=2, t=NT),
                        asum[:, x].unsqueeze(3).to_broadcast([P, NT, 2, DH]), ALU.mult).then_inc(att_ready, 1)

            body(0)
            with dve.Fori(1, PAIRS // 2) as i:
                body(i)
            order.after(start, PAIRS // 2, ATT_DVE)
            turn_att.dve(dve)
            for c in range(2):
                dve.wait_ge(quarter_done, Q_ATT + 4 * c + 4)
                for t in range(NT):
                    g = proj[:, t, C_GA + c * TW:C_GA + (c + 1) * TW]
                    order.step(nc.vector.tensor_tensor(g, g, bank[2 * c + t][:, :], ALU.mult))
                    o = merged[:, t, c * TW:(c + 1) * TW]
                    nc.vector.tensor_tensor(o, o, g, ALU.add).then_inc(att_merged, 1)
            split_low(dve, Q_OUT + 3)
            turn_m.dve(dve)
            for c in range(2):
                split_low(dve, Q_OUT + 5 + 2 * c)
                dve.wait_ge(quarter_done, Q_OUT + 4 * c + 4)
                for t in range(NT):
                    o = xres[:, t, c * TW:(c + 1) * TW]
                    nc.vector.tensor_tensor(o, o, bank[2 * c + t][:, :], ALU.add).then_inc(mixed, 1)

        def act_attention(act):
            def body(i):
                for x in range(2):
                    act.wait_ge(qk_turned, 2 * i + x + 1)
                    nc.scalar.copy(qkT[x].rearrange("p a s -> p (a s)"), bank[x][:, :]).then_inc(qk_copied, 1)
                for z in range(4):
                    act.wait_ge(maxed, 4 * i + z + 1)
                    wait_from(act, att_ready, 2 * i)
                    x, h = z // 2, z % 2
                    nc.scalar.activation(sc[z][:, 0:P], sc[z][:, 0:P], ACT.Exp, bias=amax[:, z, 0:1], scale=DH ** -0.5,
                                         accum_out=asum[:, x, 0, h:h + 1]).then_inc(exped, 1)
                    nc.scalar.activation(sc[z][:, P:384], sc[z][:, P:384], ACT.Exp, bias=amax[:, z, 1:2],
                                         scale=DH ** -0.5, accum_out=asum[:, x, 1, h:h + 1]).then_inc(exped, 1)
                for z in range(4):
                    act.wait_ge(p_turned, 4 * i + z + 1)
                    nc.scalar.copy(pT[z], bank[2 + z][:, 0:384]).then_inc(p_copied, 1)

            body(0)
            with act.Fori(1, PAIRS // 2) as i:
                body(i)
            turn_att.act(act, Q_ATT)
            for q in range(4, 8):
                split_high(act, Q_ATT + q)
            for q in range(4):
                split_high(act, Q_OUT + q)
            turn_m.act(act, Q_OUT)
            for q in range(4, 8):
                split_high(act, Q_OUT + q)

        def pe_attention(pe):
            pe.wait_ge(ssd_merged, 4)

            def body(i):
                for x in range(2):
                    pe.wait_ge(rot_ready, 2 * i + x + 1)
                    for a in range(2):
                        for t in range(NT):
                            tr = nc.tensor.transpose(bank[x][:, (2 * a + t) * P:(2 * a + t + 1) * P], rot[x][:, a, t, :],
                                                     ident)
                    tr.then_inc(qk_turned, 1)
                for x in range(2):
                    pe.wait_ge(qk_copied, 2 * i + x + 1)
                    for h in range(2):
                        r = slice(64 * h, 64 * h + 64)
                        keys = qkT[x][r, 2:4, :].rearrange("p t s -> p (t s)")
                        b = bank[2 + 2 * x + h]
                        nc.tensor.matmul(b[:, 0:P], qkT[x][r, 0, :], keys[:, 0:P], start=True, stop=True)
                        nc.tensor.matmul(b[:, P:384], qkT[x][r, 1, :], keys, start=True, stop=True).then_inc(scored, 1)
                for z in range(4):
                    pe.wait_ge(exped, 8 * i + 2 * z + 2)
                    for blk in range(3):
                        tr = nc.tensor.transpose(bank[2 + z][:, blk * P:(blk + 1) * P], sc[z][:, blk * P:(blk + 1) * P],
                                                 ident)
                    tr.then_inc(p_turned, 1)
                for x in range(2):
                    wait_from(pe, att_ready, 2 * i)
                    for h in range(2):
                        z = 2 * x + h
                        pe.wait_ge(p_copied, 4 * i + z + 1)
                        c = C_V + P * (2 * i + x) + DH * h
                        o = bank[6 + x][:, h * P:(h + 1) * P]
                        nc.tensor.matmul(o[:, 0:DH], pT[z][:, 0:P], proj[:, 0, ds(c, DH)], start=True, stop=True)
                        nc.tensor.matmul(o[:, DH:P], pT[z][:, P:2 * P], proj[:, 0, ds(c, DH)], start=True, stop=False)
                        mm = nc.tensor.matmul(o[:, DH:P], pT[z][:, 2 * P:384], proj[:, 1, ds(c, DH)], start=False, stop=True)
                    mm.then_inc(pv_done, 1)

            body(0)
            with pe.Fori(1, PAIRS // 2) as i:
                body(i)
            turn_att.pe(pe, [(att_ready, PAIRS)])
            square_product(pe, Q_ATT, t0h, t0l, [], turn_att)
            turn_m.pe(pe, [(att_merged, 4)])
            square_product(pe, Q_OUT, t0h, t0l, [(att_merged, 4)], turn_m)


        pw = proj[:, :, :].rearrange("p t n -> p (t n)")

        def lay(at, *shape):
            n = int(np.prod(shape))
            assert at + n <= NT * IN_W
            v = pw[:, at:at + n]
            if len(shape) == 1:
                return v
            names = "abcd"[:len(shape)]
            return v.rearrange(f"p ({' '.join(names)}) -> p {' '.join(names)}", **dict(zip(names, shape)))

        NG, EG = 4, 8
        JOBS = NG + 1
        xgf = lay(0, KC, P)
        pick = lay(1024, JOBS, NT, P)
        back = lay(2304, JOBS, NT, P)
        ysum = lay(3840, D)
        sg = [lay(4864 + DE * x, DE) for x in range(2)]
        hid = [lay(5376 + DE * x, DE) for x in range(2)]
        comb = lay(5888, JOBS, EG)
        rw = lay(5928, KC, 36)
        rbias = lay(6216, 36)
        logit = lay(6252, NT, 36)
        one_g, key_g = lay(6324, NT, NG), lay(6332, NT, NG)
        key = lay(6340, NT, JOBS)
        eg = lay(6350, NT, NG, EG)
        el, one1, one2, tmp8 = (lay(6414 + 16 * j, NT, EG) for j in range(4))
        ew = lay(6478, NT, EG)
        r1 = [lay(6494 + 2 * j, NT) for j in range(8)]
        cnt, over = lay(6510, NG), lay(6514, NG)
        flagf = lay(6518, 2)
        flag = sb("flag", [P, 2], I32)
        rwh = sb("rwh", [P, KC, 36], F32R)
        rwl = sb("rwl", [P, KC, 36], F32R)
        zero = sb("zero", [P, P], F32R)
        emb = lay(6600, NT, DE)
        ple = lay(7112, NT, D)
        fnw = lay(9160, D)
        sgate = lay(10184, NT, D)
        norm_m = RmsNorm(xres, xn, stat)
        turn_e = Turn(xn, gain("moe_norm_w"), t0h, t0l)
        router_loaded, zeroed = sem("router_loaded"), sem("zeroed")
        rw_high, rw_low, logits_done = (sem(s) for s in ("rw_high", "rw_low", "logits_done"))
        exp_arg, exp_done, group_ready, ranked, picked = (
            sem(s) for s in ("exp_arg", "exp_done", "group_ready", "ranked", "picked"))
        e2_arg, e2_done, weights_ready, combed, comb_ready, back_turned, back_ready = (
            sem(s) for s in ("e2_arg", "e2_done", "weights_ready", "combed", "comb_ready", "back_turned", "back_ready"))
        gathered, xg_raw, xg_high, xg_low = (sem(s) for s in ("gathered", "xg_raw", "xg_high", "xg_low"))
        silu_done, hid_ready, hid_turned, hid_high, hid_low = (
            sem(s) for s in ("silu_done", "hid_ready", "hid_turned", "hid_high", "hid_low"))
        ysum_ready, scattered, x_added = (sem(s) for s in ("ysum_ready", "scattered", "x_added"))
        flag_ready = sem("flag_ready")
        ov = {s: sem("over_" + s) for s in ("loaded", "up", "silu", "hid", "turned", "copied", "down", "summed",
                                            "zeroed", "scattered", "added")}

        def gu_loads(sp, n, e, q, u=0, per=0):
            pairs = []
            for j, name in enumerate(("w_exp_gate", "w_exp_up")):
                v = A[name][0].rearrange("g e (p k) n -> p (g e) k n", k=KC)[:, ds(e, 1), 2 * q:2 * q + 2, :]
                dst = raw_of(n)[:, 512 * j:512 * j + 512].rearrange("p (a k n) -> p a k n", a=1, k=2)
                pairs.append((dst, v))
            load(sp, n, pairs, u, per)

        def down_load(sp, n, e, c, u=0, per=0):
            v = A["w_exp_down"][0].rearrange("g e (p k) n -> p (g e) k n", k=2)[:, ds(e, 1), c:c + 1, :]
            load(sp, n, [(raw_of(n)[:, f:f + 512].rearrange("p (a k n) -> p a k n", a=1, k=1), v[:, :, :, f:f + 512])
                         for f in (0, 512)], u, per)

        U = 12

        def first_of(J):
            return Q_MOE + 4 + JOB * J

        def sp_experts(sp):
            def block(E, m, i=0, per=0):
                if not (isinstance(E, int) and E == N_EXP - 1):
                    for q in range(4):
                        gu_loads(sp, m + q, E + 1, q, i, per)
                    m += 4
                for c in range(2):
                    down_load(sp, m + c, E, c, i, per)

            for q in range(4):
                gu_loads(sp, Q_MOE + q, 0, q)
            sp.wait_ge(quarter_done, Q_OUT + 1)
            for J in range(NG):
                n = first_of(J)
                with sp.Fori(0, 3) as i:
                    for b in range(2):
                        block(EG * J + 2 * i + b, n + 6 * b, i, U)
                for e in (6, 7):
                    block(EG * J + e, n + 6 * e)

        def router_loads(act):
            act.wait_ge(att_merged, 4)
            v = A["w_router_group"][0].rearrange("(p k) n -> p k n", k=KC)
            act.dma_start(rw[:, :, 0:NG], v).then_inc(router_loaded, 16)
            v = A["w_router_expert"][0].rearrange("(p k) n -> p k n", k=KC)
            act.dma_start(rw[:, :, NG:36], v).then_inc(router_loaded, 16)
            act.dma_start(rbias[:, 0:NG], row(A["b_router_group"][0], NG)).then_inc(router_loaded, 16)
            act.dma_start(rbias[:, NG:36], row(A["b_router_expert"][0], 32)).then_inc(router_loaded, 16)
            act.dma_start(emb[:, :, :], A["p"][0, 0].rearrange("(t p) n -> p t n", p=P)).then_inc(router_loaded, 16)
            act.dma_start(fnw, row(A["final_norm_w"], D)).then_inc(router_loaded, 16)

        def act_router(act):
            act.wait_ge(router_loaded, 96)
            nc.scalar.activation(rwh[:, :, :], rw, ACT.Copy).then_inc(rw_high, 1)
            norm_m.act(act, [(mixed, 4)])
            turn_e.act(act, Q_MOE)
            act.wait_ge(exp_arg, 1)
            nc.scalar.activation(key_g, key_g, ACT.Exp).then_inc(exp_done, 1)
            act.wait_ge(e2_arg, 1)
            nc.scalar.activation(r1[4], r1[4], ACT.Exp).then_inc(e2_done, 1)

        def pe_router(pe):
            turn_e.pe(pe, [norm_m.ready(), (mixed, 4)])
            pe.wait_ge(rw_low, 1)
            pe.wait_ge(*turn_e.done())
            for t in range(NT):
                for k in range(KC):
                    mm = times(bank[t][:, 0:36], t0h[:, k, t * P:(t + 1) * P], t0l[:, k, t * P:(t + 1) * P],
                               rwh[:, k, :], rwl[:, k, :], k == 0, k == KC - 1)
            mm.then_inc(logits_done, 1)
            pe.wait_ge(group_ready, 1)
            nc.tensor.matmul(bank[2][:, 0:NG], con("strict"), one_g[:, 0, :], start=True, stop=True)
            nc.tensor.matmul(bank[2][:, NG:2 * NG], con("strict"), one_g[:, 1, :], start=True, stop=False)
            nc.tensor.matmul(bank[2][:, NG:2 * NG], con("ones"), one_g[:, 0, :], start=False, stop=True)
            nc.tensor.matmul(bank[2][:, 2 * NG:3 * NG], con("ones"), one_g[:, 0, :], start=True, stop=False)
            nc.tensor.matmul(bank[2][:, 2 * NG:3 * NG], con("ones"), one_g[:, 1, :], start=False, stop=True
                             ).then_inc(ranked, 1)
            pe.wait_ge(picked, 1)
            for j in range(JOBS):
                for t in range(NT):
                    at = (j % 2) * SEQ + t * P
                    tr = nc.tensor.transpose(bank[(0, 1, 3)[j // 2]][:, at:at + P], pick[:, j, t, :], ident)
            tr.then_inc(back_turned, 1)
            pe.wait_ge(weights_ready, 1)
            for j in range(JOBS):
                for t in range(NT):
                    mm = nc.tensor.matmul(bank[2][:, 16 + EG * j:16 + EG * (j + 1)], pick[:, j, t, :], ew[:, t, :],
                                          start=t == 0, stop=t == NT - 1)
            mm.then_inc(combed, 1)

        def dve_router(dve, order):
            dve.wait_ge(rw_high, 1)
            nc.vector.tensor_tensor(rwl[:, :, :], rw, rwh[:, :, :].bitcast(F32), ALU.subtract).then_inc(rw_low, 1)
            norm_m.dve(dve, order)
            turn_e.dve(dve)
            nc.vector.memset(zero[:, :].bitcast(F32), 0.0).then_inc(zeroed, 1)
            dve.wait_ge(logits_done, 1)
            for t in range(NT):
                order.mark(nc.vector.tensor_tensor(logit[:, t, :], bank[t][:, 0:36], rbias, ALU.add))
            order.settle()
            gl = logit[:, :, 0:NG]
            ex = logit[:, :, NG:36].rearrange("p t (g e) -> p t g e", g=NG)

            def wide(v, n):
                return v.unsqueeze(2).to_broadcast([P, NT, n])

            def first_max(hot, val, top, tmp, rev, n):
                order.step(nc.vector.tensor_reduce(top, val, AX.X, ALU.max))
                order.step(nc.vector.tensor_tensor(tmp, val, wide(top, n), ALU.is_equal))
                order.step(nc.vector.tensor_tensor(tmp, tmp, con(rev).unsqueeze(1).to_broadcast([P, NT, n]), ALU.mult))
                order.step(nc.vector.tensor_reduce(r1[7], tmp, AX.X, ALU.max))
                order.step(nc.vector.tensor_tensor(hot, tmp, wide(r1[7], n), ALU.is_equal))

            first_max(one_g, gl, r1[0], key_g, "rev4", NG)
            nc.vector.tensor_tensor(key_g, gl, wide(r1[0], NG), ALU.subtract).then_inc(exp_arg, 1)
            order.step(nc.vector.tensor_tensor(eg, ex, one_g.unsqueeze(3).to_broadcast([P, NT, NG, EG]), ALU.mult))
            nc.vector.tensor_reduce(el, eg.rearrange("p t g e -> p t e g"), AX.X, ALU.add).then_inc(group_ready, 1)
            dve.wait_ge(group_ready, 1)
            first_max(one1, el, r1[1], tmp8, "rev8", EG)
            order.step(nc.vector.scalar_tensor_tensor(out=el, in0=one1, scalar=-3e38, in1=el, op0=ALU.mult, op1=ALU.add))
            first_max(one2, el, r1[2], tmp8, "rev8", EG)
            nc.vector.tensor_tensor(r1[4], r1[2], r1[1], ALU.subtract).then_inc(e2_arg, 1)
            dve.wait_ge(ranked, 1)
            dve.wait_ge(exp_done, 1)
            order.step(nc.vector.tensor_reduce(r1[3], key_g, AX.X, ALU.add))
            order.mark(nc.vector.reciprocal(r1[3], r1[3]))
            order.mark(nc.vector.tensor_copy(cnt, bank[2][:, 2 * NG:3 * NG]))
            order.step(nc.vector.scalar_tensor_tensor(out=key_g, in0=bank[2][:, 0:2 * NG].rearrange("p (t g) -> p t g", t=NT),
                                                      scalar=1.0, in1=one_g, op0=ALU.add, op1=ALU.mult))
            order.mark(nc.vector.tensor_reduce(key[:, :, NG], key_g, AX.X, ALU.add))
            order.step(nc.vector.tensor_scalar(key[:, :, 0:NG], key_g, 1.0, None, ALU.subtract))
            order.step(nc.vector.tensor_scalar(key[:, :, NG], key[:, :, NG], float(P + 1), None, ALU.subtract))
            for j in range(JOBS):
                for t in range(NT):
                    ins = nc.vector.tensor_scalar(pick[:, j, t, :], con("slot"), key[:, t, j:j + 1], None, ALU.is_equal)
                    if (j, t) != (JOBS - 1, NT - 1):
                        order.mark(ins)
            ins.then_inc(picked, 1)
            dve.wait_ge(e2_done, 1)
            order.step(nc.vector.tensor_scalar(r1[5], r1[4], 1.0, None, ALU.add))
            order.step(nc.vector.reciprocal(r1[5], r1[5]))
            order.step(nc.vector.tensor_tensor(r1[5], r1[5], r1[3], ALU.mult))
            order.mark(nc.vector.tensor_tensor(r1[6], r1[5], r1[4], ALU.mult))
            order.step(nc.vector.tensor_tensor(ew, one1, wide(r1[5], EG), ALU.mult))
            order.step(nc.vector.tensor_tensor(tmp8, one2, wide(r1[6], EG), ALU.mult))
            nc.vector.tensor_tensor(ew, ew, tmp8, ALU.add).then_inc(weights_ready, 1)
            order.step(nc.vector.tensor_scalar(over, cnt, P + 0.5, None, ALU.is_gt))
            order.mark(nc.vector.tensor_reduce(flagf[:, 0:1], over, AX.X, ALU.max))
            order.step(nc.vector.tensor_scalar(cnt, con("rev4"), -1.0, float(NG), ALU.mult, ALU.add))
            order.step(nc.vector.tensor_tensor(cnt, cnt, over, ALU.mult))
            order.step(nc.vector.tensor_reduce(flagf[:, 1:2], cnt, AX.X, ALU.add))
            nc.vector.tensor_copy(flag[:, :], flagf).then_inc(flag_ready, 1)
            dve.wait_ge(back_turned, 1)
            for j in range(0, JOBS, 2):
                n = min(2, JOBS - j)
                order.mark(nc.vector.tensor_copy(back[:, j:j + n].rearrange("p j t s -> p (j t s)"),
                                                 bank[(0, 1, 3)[j // 2]][:, 0:n * SEQ]))
            nc.vector.tensor_copy(logit[:, 0, 0:1], flagf[:, 0:1]).then_inc(back_ready, 1)
            dve.wait_ge(combed, 1)
            nc.vector.tensor_copy(comb.rearrange("p j e -> p (j e)"), bank[2][:, 16:16 + EG * JOBS]).then_inc(comb_ready, 1)
            for b in range(2):
                nc.vector.memset(hid[b], 0.0).then_inc(hid_ready, 1)
            dve.wait_ge(hid_ready, 2)

        def pe_gather(J):
            for b in range(2):
                for kk in range(4):
                    for t in range(NT):
                        mm = nc.tensor.matmul(bank[6 + b][:, kk * P:(kk + 1) * P],
                                              xn.rearrange("p t (f k) -> p t f k", k=KC)[:, t, :, 4 * b + kk],
                                              pick[:, ds(J, 1), t, :].rearrange("p a s -> p (a s)"),
                                              start=t == 0, stop=t == NT - 1)
                mm.then_inc(gathered, 1)

        def dve_gather(dve, J):
            g = gain("moe_norm_w")
            for b in range(2):
                dve.wait_ge(gathered, 2 * J + b + 1)
                nc.vector.tensor_tensor(xgf[:, 4 * b:4 * b + 4, :], bank[6 + b][:, :].rearrange("p (k s) -> p k s", k=4),
                                        g[:, 4 * b:4 * b + 4].unsqueeze(2).to_broadcast([P, 4, P]),
                                        ALU.mult).then_inc(xg_raw, 1)

        def act_gather(act, J, par):
            act.wait_ge(xg_raw, 2 * J + 2)
            nc.scalar.activation(t0h[:, :, par * P:(par + 1) * P], xgf, ACT.Copy).then_inc(xg_high, 1)

        def dve_gather_low(dve, J, par):
            dve.wait_ge(xg_high, J + 1)
            s = slice(par * P, (par + 1) * P)
            nc.vector.tensor_tensor(t0l[:, :, s], xgf, t0h[:, :, s].bitcast(F32), ALU.subtract).then_inc(xg_low, 1)

        def pe_experts(pe):
            pe.wait_ge(zeroed, 1)
            pe.wait_ge(picked, 1)
            pe.wait_ge(*turn_e.done())
            pe_gather(0)

            def gate_up(n, q, E, e_par, par, u, per):
                if q == 0:
                    pe.wait_ge(hid_ready, E + 1)
                wait_low(pe, n, u, per)
                s = n % RING
                wh, wl = (w[:, s, :].rearrange("p (a k n) -> p a k n", a=2, k=2) for w in (whi, wlo))
                dst = bank[e_par][:, :].rearrange("p (a n) -> p a n", a=2)
                r = slice(par * P, (par + 1) * P)
                for kk in range(2):
                    k = 2 * q + kk
                    mm = times(dst, t0h[:, k, r], t0l[:, k, r], wh[:, :, kk, :], wl[:, :, kk, :], k == 0, k == KC - 1)
                mm.then_inc(quarter_done, 1)

            def turn_hidden(E, e_par):
                pe.wait_ge(hid_ready, E + 3)
                for c in range(2):
                    tr = nc.tensor.transpose(bank[2][:, c * P:(c + 1) * P],
                                             hid[e_par].rearrange("p (f c) -> p f c", c=2)[:, :, c], ident)
                tr.then_inc(hid_turned, 1)

            def down(n, c, E, e_par, u, per, first=False, last=False):
                if c == 0:
                    pe.wait_ge(hid_low, E + 1)
                wait_low(pe, n, u, per)
                s = n % RING
                for h in range(2):
                    f = slice(512 * h, 512 * h + 512)
                    hh, hl = t1h[:, 2 * e_par + c, 0:P], t1l[:, 2 * e_par + c, 0:P]
                    nc.tensor.matmul(bank[4 + h][:, :], hh, whi[:, s, f], start=first, stop=False, skip_group_check=True)
                    nc.tensor.matmul(bank[4 + h][:, :], hh, wlo[:, s, f], start=False, stop=False, skip_group_check=True)
                    mm = nc.tensor.matmul(bank[4 + h][:, :], hl, whi[:, s, f], start=False, stop=last,
                                          skip_group_check=True)
                mm.then_inc(quarter_done, 1)

            def block(J, E, b, m, i=0, per=0, first=False, last=False):
                for q in range(4):
                    if not (isinstance(E, int) and E == N_EXP - 1):
                        gate_up(m + q, q, E + 1, 1 - b, (J + last) % 2, i, per)
                    if q == 1:
                        turn_hidden(E, b)
                if not (isinstance(E, int) and E == N_EXP - 1):
                    m += 4
                if first and J:
                    pe.wait_ge(ysum_ready, 2 * J)
                for c in range(2):
                    down(m + c, c, E, b, i, per, first and c == 0, last and c == 1)

            pe.wait_ge(xg_low, 1)
            for q in range(4):
                gate_up(Q_MOE + q, q, 0, 0, 0, 0, 0)
            for J in range(NG):
                n = first_of(J)
                block(J, EG * J, 0, n, first=True)
                if J:
                    pe_scatter(pe, J)
                block(J, EG * J + 1, 1, n + 6)
                with pe.Fori(1, 3) as i:
                    for b in range(2):
                        block(J, EG * J + 2 * i + b, b, n + 6 * b, i, U)
                if J:
                    pe.wait_ge(x_added, 4 * J)
                pe_gather(J + 1)
                block(J, EG * J + 6, 0, n + 36)
                if J < NG - 1:
                    pe.wait_ge(xg_low, J + 2)
                block(J, EG * J + 7, 1, n + 42, last=True)
            pe_scatter(pe, NG)

        def pe_scatter(pe, J):
            pe.wait_ge(ysum_ready, 2 * J)
            pe.wait_ge(xg_raw, 2 * J + 2)
            for z in range(4):
                t, h = z // 2, z % 2
                if z == 3:
                    pe.wait_ge(x_added, 4 * J - 3)
                nc.tensor.matmul(bank[(3, 6, 7, 3)[z]][:, :], back[:, J - 1, t, :], ysum[:, 512 * h:512 * h + 512],
                                 start=True, stop=True).then_inc(scattered, 1)

        def dve_scatter(dve, J):
            for z in range(4):
                t, h = z // 2, z % 2
                dve.wait_ge(scattered, 4 * J + z - 3)
                o = xres[:, t, 512 * h:512 * h + 512]
                nc.vector.tensor_tensor(o, o, bank[(3, 6, 7, 3)[z]][:, :], ALU.add).then_inc(x_added, 1)

        def act_experts(act):
            def silu(e_par, n, u):
                act.wait_ge(quarter_done, n + 1 + U * u)
                nc.scalar.activation(sg[e_par], bank[e_par][:, 0:DE], ACT.Silu).then_inc(silu_done, 1)

            def high(E, e_par):
                act.wait_ge(hid_turned, E + 1)
                nc.scalar.activation(t1h[:, 2 * e_par:2 * e_par + 2, 0:P],
                                     bank[2][:, 0:2 * P].rearrange("p (c s) -> p c s", c=2),
                                     ACT.Copy).then_inc(hid_high, 1)

            act_gather(act, 0, 0)

            def block(E, b, m, gate_quarter, i=0, per=0, gather=None):
                more = not (isinstance(E, int) and E == N_EXP - 1)
                if more:
                    split_high(act, m, i, per)
                silu(b, gate_quarter, i)
                if more:
                    for q in range(1, 4):
                        split_high(act, m + q, i, per)
                    m += 4
                if gather is not None:
                    act_gather(act, gather, gather % 2)
                high(E, b)
                for c in range(2):
                    split_high(act, m + c, i, per)

            for q in range(4):
                split_high(act, Q_MOE + q)
            for J in range(NG):
                n = first_of(J)
                block(EG * J, 0, n, n - 3 if J else n - 1)
                block(EG * J + 1, 1, n + 6, n + 3)
                with act.Fori(1, 3) as i:
                    for b in range(2):
                        block(EG * J + 2 * i + b, b, n + 6 * b, n + 6 * b - 3, i, U)
                block(EG * J + 6, 0, n + 36, n + 33, gather=J + 1)
                block(EG * J + 7, 1, n + 42, n + 39)

        def dve_experts(dve):
            def hidden(J, e, E, e_par):
                dve.wait_ge(silu_done, E + 1)
                w = comb[:, ds(J, 1), ds(e, 1)].rearrange("p a b -> p (a b)")
                nc.vector.scalar_tensor_tensor(out=hid[e_par], in0=bank[e_par][:, DE:2 * DE], scalar=w, in1=sg[e_par],
                                               op0=ALU.mult, op1=ALU.mult).then_inc(hid_ready, 1)

            def low(E, e_par):
                dve.wait_ge(hid_high, E + 1)
                nc.vector.tensor_tensor(t1l[:, 2 * e_par:2 * e_par + 2, 0:P],
                                        bank[2][:, 0:2 * P].rearrange("p (c s) -> p c s", c=2),
                                        t1h[:, 2 * e_par:2 * e_par + 2, 0:P].bitcast(F32),
                                        ALU.subtract).then_inc(hid_low, 1)

            dve_gather(dve, 0)
            dve_gather_low(dve, 0, 0)

            def group_done(J):
                dve.wait_ge(quarter_done, first_of(J) + JOB - (4 if J == NG - 1 else 0))
                if J:
                    dve.wait_ge(x_added, 4 * J)
                for h in range(2):
                    nc.vector.tensor_copy(ysum[:, 512 * h:512 * h + 512], bank[4 + h][:, :]).then_inc(ysum_ready, 1)

            def block(J, e, b, m, i=0, per=0):
                E = EG * J + e
                more = not (isinstance(E, int) and E == N_EXP - 1)
                hidden(J, e, E, b)
                if more:
                    split_low(dve, m + 1, i, per)
                    split_low(dve, m + 3, i, per)
                    m += 4
                if isinstance(e, int) and J:
                    if e == 0:
                        group_done(J - 1)
                    if e == 1:
                        dve_scatter(dve, J)
                if isinstance(e, int) and e == 6:
                    dve_gather(dve, J + 1)
                low(E, b)
                split_low(dve, m + 1, i, per)

            for q in (1, 3):
                split_low(dve, Q_MOE + q)
            for J in range(NG):
                n = first_of(J)
                block(J, 0, 0, n)
                block(J, 1, 1, n + 6)
                with dve.Fori(1, 3) as i:
                    for b in range(2):
                        block(J, 2 * i + b, b, n + 6 * b, i, U)
                block(J, 6, 0, n + 36)
                dve_gather_low(dve, J + 1, (J + 1) % 2)
                block(J, 7, 1, n + 42)
            group_done(NG - 1)
            dve_scatter(dve, NG)

        over_gu = lay(10184, KC, 2 * DE)
        over_d = lay(7112, 2, D)
        over_hT = lay(14280, 2, P)

        def overflowing(eng):
            eng.wait_ge(flag_ready, 1)
            return eng.value_load(flag[0:1, 0:1], min_val=0, max_val=1)

        def sp_overflow(sp):
            with sp.If(overflowing(sp) == 1):
                sp.wait_ge(xg_low, JOBS)
                for n in (Q_PLE - 2, Q_PLE - 1):
                    wait_low(sp, n)
                g = sp.value_load(flag[0:1, 1:2], min_val=0, max_val=NG - 1)
                with sp.Fori(0, EG) as e:
                    sp.wait_ge(ov["zeroed"], e + 1)
                    for j, name in enumerate(("w_exp_gate", "w_exp_up")):
                        v = A[name][0].rearrange("g e (p k) n -> p (g e) k n", k=KC)[:, ds(g * EG + e, 1), :, :]
                        sp.dma_start(over_gu[:, :, DE * j:DE * j + DE].unsqueeze(1), v).then_inc(ov["loaded"], 16)
                    v = A["w_exp_down"][0].rearrange("g e (p k) n -> p (g e) k n", k=2)[:, ds(g * EG + e, 1), :, :]
                    sp.dma_start(over_d.unsqueeze(1), v).then_inc(ov["loaded"], 16)

        def pe_overflow(pe):
            with pe.If(overflowing(pe) == 1):
                pe.wait_ge(xg_low, JOBS)
                pe.wait_ge(x_added, 4 * NG)
                with pe.Fori(0, EG) as e:
                    pe.wait_ge(ov["loaded"], 48 * e + 48)
                    for k in range(KC):
                        for part in (t0h, t0l):
                            mm = nc.tensor.matmul(bank[0][:, :], part[:, k, 0:P].bitcast(F32), over_gu[:, k, :],
                                                  start=k == 0 and part is t0h, stop=k == KC - 1 and part is t0l)
                    mm.then_inc(ov["up"], 1)
                    pe.wait_ge(ov["hid"], e + 1)
                    for c in range(2):
                        tr = nc.tensor.transpose(bank[2][:, c * P:(c + 1) * P],
                                                 hid[0].rearrange("p (f c) -> p f c", c=2)[:, :, c], ident)
                    tr.then_inc(ov["turned"], 1)
                    pe.wait_ge(ov["copied"], e + 1)
                    for h in range(2):
                        for c in range(2):
                            mm = nc.tensor.matmul(bank[4 + h][:, :], over_hT[:, c, :], over_d[:, c, 512 * h:512 * h + 512],
                                                  start=c == 0, stop=c == 1)
                    mm.then_inc(ov["down"], 1)
                pe.wait_ge(ov["zeroed"], EG + 1)
                for z in range(4):
                    t, h = z // 2, z % 2
                    nc.tensor.matmul(bank[(3, 6, 7, 1)[z]][:, :], back[:, NG, t, :], ysum[:, 512 * h:512 * h + 512],
                                     start=True, stop=True).then_inc(ov["scattered"], 1)

        def act_overflow(act):
            with act.If(overflowing(act) == 1):
                with act.Fori(0, EG) as e:
                    act.wait_ge(ov["up"], e + 1)
                    nc.scalar.activation(sg[0], bank[0][:, 0:DE], ACT.Silu).then_inc(ov["silu"], 1)

        def dve_overflow(dve):
            with dve.If(overflowing(dve) == 1):
                dve.wait_ge(x_added, 4 * NG)
                nc.vector.memset(ysum, 0.0).then_inc(ov["zeroed"], 1)
                with dve.Fori(0, EG) as e:
                    dve.wait_ge(ov["silu"], e + 1)
                    nc.vector.scalar_tensor_tensor(out=hid[0], in0=bank[0][:, DE:2 * DE],
                                                   scalar=comb[:, NG, ds(e, 1)], in1=sg[0],
                                                   op0=ALU.mult, op1=ALU.mult).then_inc(ov["hid"], 1)
                    dve.wait_ge(ov["turned"], e + 1)
                    nc.vector.tensor_copy(over_hT.rearrange("p c s -> p (c s)"), bank[2][:, 0:2 * P]).then_inc(ov["copied"], 1)
                    dve.wait_ge(ov["down"], e + 1)
                    dve.wait_ge(ov["zeroed"], e + 1)
                    nc.vector.tensor_tensor(ysum[:, 0:512], ysum[:, 0:512], bank[4][:, :], ALU.add).then_inc(ov["summed"], 1)
                    nc.vector.tensor_tensor(ysum[:, 512:D], ysum[:, 512:D], bank[5][:, :], ALU.add).then_inc(ov["zeroed"], 1)
                for z in range(4):
                    t, h = z // 2, z % 2
                    dve.wait_ge(ov["scattered"], z + 1)
                    o = xres[:, t, 512 * h:512 * h + 512]
                    nc.vector.tensor_tensor(o, o, bank[(3, 6, 7, 1)[z]][:, :], ALU.add).then_inc(ov["added"], 1)
                dve.wait_ge(ov["added"], 4)
            dve.wait_ge(x_added, 4 * NG)
            nc.vector.tensor_copy(flagf, flag[:, :]).then_inc(experts_added, 1)

        experts_added = sem("experts_added")
        norm_p = RmsNorm(xres, xn, stat)
        turn_p = Turn(xn, gain("ple_norm_w"), t0h, t0l)
        norm_f = RmsNorm(xres, xn, stat)
        emb_turned, emb_high, emb_low, ple_copied, gated, gate_used, first_done = (
            sem(s) for s in ("emb_turned", "emb_high", "emb_low", "ple_copied", "gated", "gate_used", "first_done"))

        def sp_ple(sp):
            v = A["w_ple"][0].rearrange("(p k) n -> p k n", k=2)
            for k in range(2):
                load(sp, Q_PLE + k, [(raw[:, (Q_PLE + k) % RING, :], v[:, k, :])])
            load_square(sp, Q_GATE, A["w_ple_gate"][0])

        def pe_ple(pe):
            pe.wait_ge(ple_bank_free, 1)
            for k in range(2):
                for t in range(NT):
                    tr = nc.tensor.transpose(bank[4][:, k * SEQ + t * P:k * SEQ + (t + 1) * P],
                                             emb[:, t, :].rearrange("p (f k) -> p f k", k=2)[:, :, k], ident)
            tr.then_inc(emb_turned, 1)
            pe.wait_ge(emb_low, 1)
            for k in range(2):
                n = Q_PLE + k
                wait_low(pe, n)
                for h in range(2):
                    f = slice(512 * h, 512 * h + 512)
                    for t in range(NT):
                        s = slice(t * P, (t + 1) * P)
                        mm = times(bank[2 * h + t][:, :], t1h[:, k, s], t1l[:, k, s], whi[:, n % RING, f],
                                   wlo[:, n % RING, f], k == 0, k == 1)
                mm.then_inc(quarter_done, 1)
            turn_p.pe(pe, [norm_p.ready()])
            square_product(pe, Q_GATE, t0h, t0l, [(ple_copied, 4)], turn_p)

        ple_bank_free = experts_added

        def act_ple(act):
            for k in range(2):
                split_high(act, Q_PLE + k)
            act.wait_ge(emb_turned, 1)
            nc.scalar.activation(t1h[:, 0:2, :], bank[4][:, :].rearrange("p (k s) -> p k s", k=2), ACT.Copy).then_inc(emb_high, 1)
            for q in range(2):
                split_high(act, Q_GATE + q)
            norm_p.act(act, [(experts_added, 1)])
            act.wait_ge(quarter_done, Q_GATE)
            for h in range(2):
                for t in range(NT):
                    nc.scalar.copy(ple[:, t, 512 * h:512 * h + 512], bank[2 * h + t][:, :]).then_inc(ple_copied, 1)
            turn_p.act(act, Q_PLE)
            for q in range(2, 8):
                split_high(act, Q_GATE + q)
            for h in range(2):
                act.wait_ge(quarter_done, Q_GATE + 4 * h + 4)
                for t in range(NT):
                    nc.scalar.activation(sgate[:, t, 512 * h:512 * h + 512], bank[2 * h + t][:, :],
                                         ACT.Sigmoid).then_inc(gated, 1)
            norm_f.act(act, [(gate_used, 4)])

        def dve_ple(dve, order):
            dve.wait_ge(emb_high, 1)
            nc.vector.tensor_tensor(t1l[:, 0:2, :], bank[4][:, :].rearrange("p (k s) -> p k s", k=2),
                                    t1h[:, 0:2, :].bitcast(F32), ALU.subtract).then_inc(emb_low, 1)
            norm_p.dve(dve, order)
            turn_p.dve(dve)
            for h in range(2):
                for t in range(NT):
                    dve.wait_ge(gated, 2 * h + t + 1)
                    f = slice(512 * h, 512 * h + 512)
                    order.step(nc.vector.tensor_tensor(sgate[:, t, f], sgate[:, t, f], ple[:, t, f], ALU.mult))
                    nc.vector.tensor_tensor(xres[:, t, f], xres[:, t, f], sgate[:, t, f], ALU.add).then_inc(gate_used, 1)
            norm_f.dve(dve, order)
            dve.wait_ge(*norm_f.ready())
            nc.vector.tensor_tensor(xres[:, :, :], xn, fnw.unsqueeze(1).to_broadcast([P, NT, D]),
                                    ALU.mult).then_inc(first_done, 1)


        rkv = lay(0, NT, 3 * D)
        glu = lay(6144, NT, 2 * D)
        gates = lay(10240, NT, 2 * D)
        hT = lay(6144, KC, SEQ)
        dhT = lay(8192, KC, SEQ)
        decay = lay(6144, NT, D)
        gain_a = lay(8192, NT, D)
        taps2 = lay(14336, 2 * P)
        W2, K2 = 31, KC
        H2 = W2 - 1
        shifted = [carve(1024 * b, NT, TW) for b in range(2)]
        xw = [lay(2048 * j, KC, SEQ) for j in range(3)]
        gate_bias = carve(0, 2 * D)
        uT = carve(2048, K2, H2 + SEQ)
        cvT = carve(4336, K2, SEQ)
        ctok = carve(2048, NT, D)
        w1, a1, g1 = carve(6384, KC, 64), carve(6896, KC, 64), carve(7408, KC, P)
        w2, a2 = carve(8432, D), carve(9456, D)
        dT, aT = carve(10480, SEQ), carve(10736, SEQ)
        rows2 = carve(10992, 2, P)
        rowbuf = [carve(11248 + 512 * b, TW) for b in range(2)]
        gT, g2 = lay(14592, SEQ), carve(12272, D)
        st2 = tiny(0, 16)
        norm_g = RmsNorm(xres, xn, stat)
        turn_g = Turn(xn, gain("norm_mix_g_2"), t0h, t0l)
        row_loaded, shift_loaded = ([sem(f"{n}{b}") for b in range(2)] for n in ("row_loaded", "shift_loaded"))
        row_used = sem("row_used")
        evac2 = Again(evac_in, NT * IN_T)
        lora_loaded = Again(router_loaded, 96)
        glu_ready = Again(y_gated, NT)
        u_turned = Again(xbc_turned, XCH // 2)
        u_copied = Again(xbc_copied, XCH // 2)
        taps2_turned = Again(taps_turned, 1)
        taps2_ready = Again(taps_ready, 1)
        conv2_done = Again(conv_done, XCH)
        c_var = sem("c_var")
        c_back = Again(x_back, 2 * NT)
        c_copied = Again(ple_copied, 4)
        c_mean = Again(y_mean, 1)
        c_squared = Again(y_squared, 2 * NT)
        c_root = Again(y_root, 1)
        c_normed = Again(y_normed, 2 * NT)
        c_active = Again(conv_active, XCH)
        c_high = Again(emb_high, 1)
        c_low = Again(emb_low, 1)
        shift_done = sem("shift_done")
        xw_ready, lora_mid, lora_ones = (
            sem(s) for s in ("xw_ready", "lora_mid", "lora_ones"))
        lora_act = Again(dt_exp, 2)
        lora_done = Again(cum_done, 1)
        lora_ready = Again(dec_ready, 2)
        state_decay_done = Again(state_done, 1)
        state_decay_ready = Again(state_ready, 1)
        conv_gated = Again(ssd_merged, 4)

        TILES2 = [6, 8, 7, 9] + list(range(10, 14)) + list(range(6))
        GATES2, RKV2 = 4, 8
        CONV_SETS = ((0, 1, 2, 3), (4, 5, 6))
        CONV_FIRST, CONV_NEXT = 30, 5

        def sp_in2(sp):
            v = A["w_in_2"][0].rearrange("(p k) n -> p k n", k=KC)
            for p, c in enumerate(TILES2):
                for q in range(4):
                    n = Q_IN2 + 4 * p + q
                    load(sp, n, [(pair_view(raw, n, TW), v[:, 2 * q:2 * q + 2, c * TW:(c + 1) * TW])])
            load_square(sp, Q_CONV, A["w_conv_proj_2"][0])
            load_square(sp, Q_RWKV, A["w_rwkv_proj_2"][0], range(4))
            for j, (dst, name) in enumerate(((ka_row, "k_a_2"), (lng, "ln_x_g_2"), (lnb, "ln_x_b_2"))):
                wait_low(sp, Q_RWKV + j)
                sp.dma_start(dst, row(A[name][0], D)).then_inc(rows_loaded, 16)
            sp.wait_ge(*heads_gated.at(1))
            load_square(sp, Q_RWKV, A["w_rwkv_proj_2"][0], range(4, 8))
            load_square(sp, Q_OUT2, A["w_out_2"][0])

        def lora_loads(act):
            act.wait_ge(first_done, 1)
            def ld(dst, src):
                act.dma_start(dst, src).then_inc(lora_loaded.sem, 16)
            ld(w1, A["decay_w1_2"][0].rearrange("(p k) n -> p k n", k=KC))
            ld(a1, A["aaa_a1_2"][0].rearrange("(p k) n -> p k n", k=KC))
            ld(g1, A["gate_g1_2"][0].rearrange("(p k) n -> p k n", k=KC))
            for dst, w, b in ((w2, "decay_w2_2", "decay_w0_2"), (a2, "aaa_a2_2", "aaa_a0_2")):
                ld(dst[0:64, :], A[w][0])
                ld(dst[64:65, :], A[b])
            ld(g2, A["gate_g2_2"][0])
            ld(kk_row, row(A["k_k_2"][0], D))
            ld(gate_bias[0:1, :], A["b_gate_2"])
            taps = A["conv_w_2"][0].rearrange("w (k p) -> (w k) p", p=P)
            ld(rows2[:, 0, :], taps[0:P, :])
            ld(rows2[0:120, 1, :], taps[P:248, :])
            ld(rows2[120:128, 1, :], A["conv_b_2"][0].rearrange("(k p) -> k p", p=P))

        N_LORA = 16 * 13

        def pe_in2(pe):
            turn_g.pe(pe, [norm_g.ready(), (gate_used, 4)])
            pe.wait_ge(*turn_g.done())

            def tile(p):
                wait_from(pe, *evac2.at(NT * (p - 1)))
                dst = bank[2 * (p % 2):2 * (p % 2) + 2]
                gate = GATES2 <= p < RKV2
                for q in range(4):
                    if gate and q == 0:
                        pe.wait_ge(*lora_loaded.at(N_LORA))
                        f = slice((p - GATES2) * TW, (p - GATES2 + 1) * TW)
                        for t in range(NT):
                            nc.tensor.matmul(dst[t][:, :], con("ones")[0:1, :], gate_bias[0:1, f], start=True, stop=False)
                    wide_quarter(pe, Q_IN2 + 4 * p + q, q, dst, t0h, t0l, begun=gate)

            for p in range(5):
                tile(p)
            pe.wait_ge(*glu_ready.at(4))
            for b in range(K2 // 2):
                for kk in range(2):
                    for t in range(NT):
                        c = (2 * b + kk) * P
                        tr = nc.tensor.transpose(bank[4 + b][:, kk * SEQ + t * P:kk * SEQ + (t + 1) * P],
                                                 glu[:, t, c:c + P], ident)
                tr.then_inc(u_turned.sem, 1)
            pe.wait_ge(*u_copied.at(1))
            pe.wait_ge(*lora_loaded.at(N_LORA))
            for j in range(2):
                tr = nc.tensor.transpose(bank[4][:, j * P:(j + 1) * P], rows2[:, j, :], ident)
            tr.then_inc(taps2_turned.sem, 1)
            for p in range(5, 7):
                tile(p)
            pe.wait_ge(*u_copied.at(4))
            for j, (w, m) in enumerate(((w1, 64), (a1, 64), (g1, P))):
                for k in range(KC):
                    pe.wait_ge(xw_ready, KC * j + k + 1)
                    mm = nc.tensor.matmul(bank[5 + j][0:m, 0:SEQ], w[:, k, :], xw[j][:, k, :], start=k == 0,
                                          stop=k == KC - 1)
                mm.then_inc(lora_mid, 1)
            tile(7)
            pe.wait_ge(lora_ones, 2)
            pe.wait_ge(*taps2_ready.at(1))
            for j, (mid, w) in enumerate(((dT, w2), (aT, a2))):
                pe.wait_ge(*(lora_ready.at(4) if j else lora_act.at(3)))
                for t in range(NT):
                    for h in range(2):
                        nc.tensor.matmul(bank[4 + 2 * t + h][:, :], mid[0:65, t * P:(t + 1) * P],
                                         w[0:65, 512 * h:512 * h + 512], start=True, stop=True).then_inc(lora_done.sem, 1)
                tile(8 + j)
            pe.wait_ge(*lora_ready.at(8))
            for c in range(KC):
                nc.tensor.matmul(bank[4][:, c:c + 1], decay[:, 0, c * P:(c + 1) * P], con("high"), start=True, stop=False)
                mm = nc.tensor.matmul(bank[4][:, c:c + 1], decay[:, 1, c * P:(c + 1) * P], con("low"), start=False, stop=True)
            mm.then_inc(state_decay_done.sem, 1)
            for p in range(10, 14):
                tile(p)
            pe.wait_ge(*state_decay_ready.at(1))
            for w in range(W2):
                pe.wait_ge(diag_made, w + 1)
                mm = nc.tensor.matmul(bank[5][:, 0:SEQ], tap_diag[:, w, :], uT[:, K2 - 1, w:w + SEQ], start=w == 0,
                                      stop=w == W2 - 1)
            mm.then_inc(chunk_made, 1)

        def act_in2(act):
            for q in range(4):
                split_high(act, Q_IN2 + q)
            norm_g.act(act, [(first_done, 1)])
            turn_g.act(act, Q_IN2)
            lora_loads(act)

            def mu_load(p):
                wait_from(act, row_used, p - RKV2 - 1)
                act.dma_start(rowbuf[p % 2], row(A["mu_rkv_2"][0][(p - RKV2) * TW:(p - RKV2 + 1) * TW], TW)
                              ).then_inc(row_loaded[p % 2], 16)

            def evac(p):
                act.wait_ge(quarter_done, Q_IN2 + 4 * p + 4)
                b = 2 * (p % 2)
                if p < GATES2:
                    f = slice((p // 2) * TW + (p % 2) * D, (p // 2) * TW + (p % 2) * D + TW)
                    for t in range(NT):
                        nc.scalar.activation(glu[:, t, f], bank[b + t][:, :], ACT.Sigmoid if p % 2 else ACT.Copy
                                             ).then_inc(evac2.sem, 1)
                elif p < RKV2:
                    f = slice((p - GATES2) * TW, (p - GATES2 + 1) * TW)
                    for t in range(NT):
                        nc.scalar.activation(gates[:, t, f], bank[b + t][:, :], ACT.Sigmoid).then_inc(evac2.sem, 1)
                else:
                    f = slice((p - RKV2) * TW, (p - RKV2 + 1) * TW)
                    for t in range(NT):
                        nc.scalar.copy(rkv[:, t, f], bank[b + t][:, :]).then_inc(evac2.sem, 1)
                    wait_from(act, shift_done, p - RKV2 - 1)
                    act.wait_ge(*evac2.at(NT * (p + 1)))
                    s = shifted[p % 2]
                    act.dma_start(s[1:P, :, :], rkv[0:P - 1, :, f]).then_inc(shift_loaded[p % 2], 16)
                    act.dma_start(s[0:1, 1, :], rkv[P - 1:P, 0, f]).then_inc(shift_loaded[p % 2], 16)

            for p in range(1, 14):
                for q in range(4):
                    split_high(act, Q_IN2 + 4 * p + q)
                if p >= RKV2:
                    mu_load(p)
                evac(p - 1)
                if p == 7:
                    act.wait_ge(lora_mid, 1)
                    nc.scalar.activation(dT[0:64, :], bank[5][0:64, 0:SEQ], ACT.Tanh).then_inc(lora_act.sem, 1)
                    act.wait_ge(lora_mid, 2)
                    nc.scalar.copy(aT[0:64, :], bank[6][0:64, 0:SEQ]).then_inc(lora_act.sem, 1)
                    act.wait_ge(lora_mid, 3)
                    nc.scalar.activation(gT, bank[7][:, 0:SEQ], ACT.Sigmoid).then_inc(lora_act.sem, 1)
                if p in (8, 9):
                    j = p - 8
                    for t in range(NT):
                        for h in range(2):
                            act.wait_ge(*lora_done.at(4 * j + 2 * t + h + 1))
                            nc.scalar.activation((decay, gain_a)[j][:, t, 512 * h:512 * h + 512], bank[4 + 2 * t + h][:, :],
                                                 ACT.Sigmoid).then_inc(lora_ready.sem, 1)
                if p >= 10:
                    for w in range(8 * (p - 10), min(8 * (p - 9), W2)):
                        nc.scalar.activation(tap_diag[:, w, :], ident, ACT.Copy,
                                             scale=taps2[:, w * K2 + K2 - 1:w * K2 + K2]).then_inc(diag_made, 1)
                if p == 10:
                    act.wait_ge(*state_decay_done.at(1))
                    nc.scalar.activation(sdec, bank[4][:, 0:KC], ACT.Exp, scale=-S_DECAY).then_inc(state_decay_ready.sem, 1)
            for q in range(4):
                split_high(act, Q_CONV + q)
            evac(13)
            act.wait_ge(chunk_made, 1)
            nc.scalar.activation(cvT[:, K2 - 1, :], bank[5][:, 0:SEQ], ACT.Identity,
                                 bias=taps2[:, 248 + K2 - 1:248 + K2]).then_inc(chunk_done, 1)
            act.wait_ge(row_used, 6)
            act.dma_start(rk_row, row(A["r_k_2"][0].rearrange("h d -> (h d)"), D)).then_inc(rk_loaded, 16)
            act.wait_ge(kk_squared, 1)
            nc.scalar.activation(kinv, kinv, ACT.Sqrt).then_inc(kk_root, 1)

        def dve_in2(dve, order):
            norm_g.dve(dve, order)
            turn_g.dve(dve)
            dve.wait_ge(*norm_g.ready())
            dve.wait_ge(*turn_g.written())
            order.mark(nc.vector.memset(uT[:, :, 0:H2], 0.0))
            for j in range(2):
                dve.wait_ge(*evac2.at(NT * (2 * j + 2)))
                f, g = slice(j * TW, (j + 1) * TW), slice(D + j * TW, D + (j + 1) * TW)
                for t in range(NT):
                    nc.vector.tensor_tensor(glu[:, t, f], glu[:, t, f], glu[:, t, g], ALU.mult).then_inc(glu_ready.sem, 1)
            for b in range(K2 // 2):
                dve.wait_ge(*u_turned.at(b + 1))
                nc.vector.tensor_copy(uT[:, 2 * b:2 * b + 2, H2:H2 + SEQ],
                                      bank[4 + b][:, :].rearrange("p (k s) -> p k s", k=2)).then_inc(u_copied.sem, 1)
            dve.wait_ge(*taps2_turned.at(1))
            nc.vector.tensor_copy(taps2, bank[4][:, 0:2 * P]).then_inc(taps2_ready.sem, 1)
            order.step(nc.vector.tensor_tensor(hT, t0h[:, :, :].bitcast(F32), t0l[:, :, :].bitcast(F32), ALU.add))
            order.mark(nc.vector.tensor_tensor(dhT[:, :, 1:SEQ], hT[:, :, 0:SEQ - 1], hT[:, :, 1:SEQ], ALU.subtract))
            order.step(nc.vector.tensor_scalar(dhT[:, :, 0:1], hT[:, :, 0:1], -1.0, None, ALU.mult))
            for buf in (dT, aT):
                nc.vector.memset(buf[64:65, :], 1.0).then_inc(lora_ones, 1)
            for j in range(3):
                for k in range(KC):
                    nc.vector.scalar_tensor_tensor(out=xw[j][:, k, :], in0=dhT[:, k, :], scalar=mul[:, j, k:k + 1],
                                                   in1=hT[:, k, :], op0=ALU.mult, op1=ALU.add).then_inc(xw_ready, 1)
            dve.wait_ge(*u_copied.at(4))
            dve.wait_ge(*taps2_ready.at(1))

            def convolve(at, steps):
                for z in range(at, min(at + steps, W2 * len(CONV_SETS))):
                    w = z % W2
                    for c in CONV_SETS[z // W2]:
                        tap = taps2[:, w * K2 + c:w * K2 + c + 1]
                        if w == 0:
                            order.mark(nc.vector.tensor_scalar(cvT[:, c, :], uT[:, c, 0:SEQ], tap,
                                                               taps2[:, 248 + c:249 + c], ALU.mult, ALU.add))
                        else:
                            ins = nc.vector.scalar_tensor_tensor(out=cvT[:, c, :], in0=uT[:, c, w:w + SEQ], scalar=tap,
                                                                 in1=cvT[:, c, :], op0=ALU.mult, op1=ALU.add)
                            if w < W2 - 1:
                                order.mark(ins)
                            else:
                                ins.then_inc(conv2_done.sem, 1)
                    if w < W2 - 1:
                        order.settle()
                return at + steps

            def shift(p):
                f = slice((p - RKV2) * TW, (p - RKV2 + 1) * TW)
                z, s = rkv[:, :, f], shifted[p % 2]
                order.settle()
                dve.wait_ge(shift_loaded[p % 2], 32 * ((p - RKV2) // 2 + 1))
                dve.wait_ge(row_loaded[p % 2], 16 * ((p - RKV2) // 2 + 1))
                order.step(nc.vector.tensor_tensor(s, s, z, ALU.subtract))
                nc.vector.tensor_tensor(s, s, rowbuf[p % 2].unsqueeze(1).to_broadcast([P, NT, TW]),
                                        ALU.mult).then_inc(row_used, 1)
                dve.wait_ge(row_used, p - RKV2 + 1)
                nc.vector.tensor_tensor(z, z, s, ALU.add).then_inc(shift_done, 1)
                if p < 12:
                    dve.wait_ge(shift_done, p - RKV2 + 1)
                    order.mark(nc.vector.memset(s[0:1, 0, :], 0.0))

            at = convolve(0, CONV_FIRST)
            dve.wait_ge(quarter_done, Q_IN2 + 4 * RKV2)
            for b in range(2):
                order.mark(nc.vector.memset(shifted[b][0:1, 0, :], 0.0))
            for p in range(RKV2, 14):
                shift(p)
                if p < 13:
                    at = convolve(at, CONV_NEXT)
            dve.wait_ge(shift_done, 6)
            kk = carve(0, NT, D)
            order.step(nc.vector.tensor_tensor(kk, rkv[:, :, D:2 * D], kk_row.unsqueeze(1).to_broadcast([P, NT, D]),
                                               ALU.mult))
            order.step(nc.vector.tensor_tensor(kk, kk, kk, ALU.mult))
            nc.vector.tensor_reduce(kinv, by_head(kk, NH), AX.X, ALU.add).then_inc(kk_squared, 1)
            convolve(at, W2 * len(CONV_SETS))

        S_DECAY = math.exp(-0.5)
        sdec = tiny(16, KC)
        tap_diag = carve(6384, W2, P)
        diag_made, chunk_made, chunk_done = (sem(s) for s in ("diag_made", "chunk_made", "chunk_done"))

        def pe_conv(pe):
            pe.wait_ge(*conv2_done.at(K2 - 1))
            pe.wait_ge(chunk_done, 1)
            pe.wait_ge(*taps2_ready.at(1))
            for t in range(NT):
                for h in range(2):
                    for c in range(4):
                        tr = nc.tensor.transpose(bank[4 + 2 * t + h][:, c * P:(c + 1) * P],
                                                 cvT[:, 4 * h + c, t * P:(t + 1) * P], ident)
                    tr.then_inc(c_back.sem, 1)
            turn_c.pe(pe, [c_normed.at(NT), c_copied.at(4)])
            square_product(pe, Q_CONV, t0h, t0l, [c_low.at(1), state_decay_ready.at(1)])

        turn_c = Turn(ctok, None, None, None)

        def act_conv(act):
            for t in range(NT):
                for h in range(2):
                    act.wait_ge(*c_back.at(2 * t + h + 1))
                    nc.scalar.activation(ctok[:, t, 512 * h:512 * h + 512], bank[4 + 2 * t + h][:, :], ACT.Copy,
                                         accum_out=st2[:, 4 + 2 * t + h:5 + 2 * t + h]).then_inc(c_copied.sem, 1)
            act.wait_ge(*c_mean.at(1))
            for t in range(NT):
                nc.scalar.activation(xw_flat[:, t, :], ctok[:, t, :], ACT.Square, bias=st2[:, 8 + t:9 + t],
                                     accum_out=st2[:, 10 + t:11 + t]).then_inc(c_squared.sem, 1)
            act.wait_ge(c_var, 1)
            nc.scalar.activation(st2[:, 10:12], st2[:, 10:12], ACT.Sqrt).then_inc(c_root.sem, 1)
            for k in range(KC):
                if k % 2 == 0:
                    act.wait_ge(*turn_c.written(k // 2 + 1))
                nc.scalar.activation(cvT[:, k, :], turn_c.part(k), ACT.Silu, scale=gain("conv_ln_g_2")[:, k:k + 1],
                                     bias=gain("conv_ln_b_2")[:, k:k + 1]).then_inc(c_active.sem, 1)
            act.wait_ge(*c_active.at(KC))
            act.wait_ge(quarter_done, Q_CONV)
            act.wait_ge(*lora_ready.at(8))
            nc.scalar.activation(t0h[:, :, :], cvT, ACT.Copy).then_inc(c_high.sem, 1)
            for q in range(4, 8):
                split_high(act, Q_CONV + q)
            for q in range(4):
                split_high(act, Q_RWKV + q)

        xw_flat = carve(0, NT, D)

        def dve_conv(dve, order):
            dve.wait_ge(kk_root, 1)
            order.step(nc.vector.tensor_scalar(kinv, kinv, 1e-12, None, ALU.max))
            order.mark(nc.vector.reciprocal(kinv, kinv))
            dve.wait_ge(*c_copied.at(4))
            for t in range(NT):
                order.mark(nc.vector.tensor_tensor(st2[:, 8 + t:9 + t], st2[:, 4 + 2 * t:5 + 2 * t],
                                                   st2[:, 5 + 2 * t:6 + 2 * t], ALU.add))
            order.settle()
            nc.vector.tensor_scalar(st2[:, 8:10], st2[:, 8:10], -1.0 / D, None, ALU.mult).then_inc(c_mean.sem, 1)
            dve.wait_ge(*c_squared.at(NT))
            nc.vector.tensor_scalar(st2[:, 10:12], st2[:, 10:12], 1.0 / D, 1e-5, ALU.mult, ALU.add).then_inc(c_var, 1)
            dve.wait_ge(*c_root.at(1))
            dve.wait_ge(*c_mean.at(1))
            order.step(nc.vector.reciprocal(st2[:, 10:12], st2[:, 10:12]))
            for t in range(NT):
                nc.vector.tensor_scalar(ctok[:, t, :], ctok[:, t, :], st2[:, 8 + t:9 + t], st2[:, 10 + t:11 + t],
                                        ALU.add, ALU.mult).then_inc(c_normed.sem, 1)
            dve.wait_ge(*c_high.at(1))
            nc.vector.tensor_tensor(t0l[:, :, :], cvT, t0h[:, :, :].bitcast(F32), ALU.subtract).then_inc(c_low.sem, 1)
            dve.wait_ge(*evac2.at(NT * RKV2))
            for c in range(2):
                dve.wait_ge(quarter_done, Q_CONV + 4 * c + 4)
                for t in range(NT):
                    o = gates[:, t, D + c * TW:D + (c + 1) * TW]
                    nc.vector.tensor_tensor(o, o, bank[2 * c + t][:, :], ALU.mult).then_inc(conv_gated.sem, 1)

        LEV = 7
        gram = [carve(2048 * c, 4, 512) for c in range(2)]
        AR = [carve(4096 + 512 * c, NT, 2, P) for c in range(2)]
        Bt = [carve(5120 + 512 * c, NT, P) for c in range(2)]
        Kt = [carve(5376 + 512 * c, NT, P) for c in range(2)]
        XT = [carve(6144 + 512 * c, 4, P) for c in range(2)]
        Rt, At, Pi, kkb, tmpb = (carve(7168 + 256 * j, NT, P) for j in range(5))
        BK = carve(8448, 2, NT, P)
        Xm, Ym = carve(8960, 4, P), carve(9472, 4, P)
        Wn, Uo = carve(9984, NT, P), carve(10240, NT, P)
        SB = carve(10496, P)
        kk_row = carve(13296, D)
        ka_row, lng, lnb = (raw[:, (Q_RWKV + j) % RING, :] for j in range(3))
        rk_row = carve(11248, D)
        kinv, hbonus, hvar = (tiny(24 + 32 * j, NT, NH) for j in range(3))
        hmean = tiny(120, 4)
        rk_loaded, kk_squared, kk_root = (sem(s) for s in ("rk_loaded", "kk_squared", "kk_root"))
        cs_done, pdiff, inverse_begun = (
            sem(s) for s in ("cs_done", "pdiff", "inverse_begun"))
        pexp = Again(exped, 4 * PAIRS)
        gram_masked = Again(mt_ready, 8)
        tok_ready = Again(rot_ready, PAIRS)
        hturned = Again(qk_turned, PAIRS)
        ft_copied = Again(qk_copied, PAIRS)
        gram_done = Again(scored, 2 * PAIRS)
        y_made, x_made, xt_copied = (
            sem(s) for s in ("y_made", "x_made", "xt_copied"))
        y_masked = Again(dif_ready, 8)
        xm_copied = Again(p_copied, 2 * PAIRS)
        uo_copied, s_made, s_ready, bonus_used = (
            sem(s) for s in ("uo_copied", "s_made", "s_ready", "bonus_used"))
        w_made = Again(abc_done, 8)
        w_copied = Again(lmat_ready, 8)
        u_made = Again(diag_done, 8)
        o_made = Again(pv_done, PAIRS)
        pair_done = Again(att_ready, PAIRS)
        head_var, head_root = sem("head_var"), sem("head_root")

        def unit(h, t):
            return 2 * h + t

        def halves(v, lev):
            v = v.rearrange("p u (n a m) -> p u n a m", a=2, m=1 << lev)
            return v[:, :, :, 0, :], v[:, :, :, 1, :]

        def step_loop(eng, first, step, last):
            first()
            with eng.Fori(0, (PAIRS - 2) // 2) as u:
                for c in (1, 0):
                    step(2 * u + (2 - c), c)
            last()

        def pe_heads(pe):
            pe.wait_ge(*state_decay_ready.at(1))
            pe.wait_ge(*conv_gated.at(4))

            def decays(p):
                if not (isinstance(p, int) and p == 0):
                    pe.wait_ge(*gram_masked.at(4 * p))
                for t in range(NT):
                    mm = nc.tensor.matmul(bank[4][:, t * P:(t + 1) * P], con("centred"), decay[:, t, ds(P * p, P)],
                                          start=True, stop=True)
                mm.then_inc(cs_done, 1)

            def turn_ar(p):
                pe.wait_ge(*tok_ready.at(2 * p + 1))
                for t in range(NT):
                    for j, src in enumerate((At, Rt)):
                        tr = nc.tensor.transpose(bank[5][:, (2 * t + j) * P:(2 * t + j + 1) * P], src[:, t, :], ident)
                tr.then_inc(hturned.sem, 1)

            def turn_bk(p, c):
                pe.wait_ge(*tok_ready.at(2 * p + 2))
                for j, src in enumerate((Bt[c], Kt[c])):
                    for t in range(NT):
                        tr = nc.tensor.transpose(bank[4][:, (2 * j + t) * P:(2 * j + t + 1) * P], src[:, t, :], ident)
                tr.then_inc(hturned.sem, 1)

            def grams(p, c, units):
                pe.wait_ge(*ft_copied.at(2 * p + 2))
                for u in units:
                    h, t = u // 2, u % 2
                    if u >= 2:
                        pe.wait_ge(*gram_masked.at(4 * p + u - 1))
                    r = slice(64 * h, 64 * h + 64)
                    ar = AR[c][r, t].rearrange("p a s -> p (a s)")
                    for j in range(2):
                        mm = nc.tensor.matmul(bank[5 - u % 2][:, 256 * j:256 * j + 256], BK[r, j, t, :], ar,
                                              start=True, stop=True)
                    mm.then_inc(gram_done.sem, 1)

            def below(p, b, lev):
                for g in range(2):
                    if lev == 0:
                        pe.wait_ge(inverse_begun, 2 * p + g + 1)
                    elif lev == 1:
                        pe.wait_ge(*y_masked.at(2 * LEV * p + g + 1))
                    else:
                        pe.wait_ge(*xm_copied.at(2 * (LEV - 2) * p + 2 * lev + g - 3))
                    for v in range(2):
                        u = 2 * g + v
                        mm = nc.tensor.matmul(bank[g][:, v * P:(v + 1) * P], gram[b][:, u, 0:P],
                                              ident if lev == 0 else Xm[:, u, :], start=True, stop=True)
                    mm.then_inc(y_made, 1)

            def grow(p, b, lev):
                even, odd = halves(Ym, lev)[0], halves(XT[b], lev)[1]
                for g in range(2):
                    pe.wait_ge(*y_masked.at(2 * LEV * p + 2 * lev + g + 1))
                    if not (isinstance(p, int) and p == 0 and lev == 1):
                        pe.wait_ge(xt_copied, 2 * (LEV - 1) * p + 2 * lev + g - 3)
                    if lev < LEV - 1:
                        for v in range(2):
                            u = 2 * g + v
                            nc.tensor.matmul(bank[2 + g][:, v * 64:(v + 1) * 64], XT[b][:, u, :], even[:, u], start=True,
                                             stop=True)
                    for v in range(2):
                        u = 2 * g + v
                        mm = nc.tensor.matmul(bank[2 + g][:, P + v * 64:P + (v + 1) * 64], Ym[:, u, :], odd[:, u],
                                              start=True, stop=True)
                    mm.then_inc(x_made, 1)

            def rest(p, c, t):
                if t:
                    pe.wait_ge(s_ready, p + 1)
                for h in range(2):
                    f = slice(h * DH, (h + 1) * DH)
                    if t:
                        nc.tensor.matmul(bank[6][:, f], AR[c][:, 1, 0, :], SB[:, f], start=True, stop=False)
                    mm = nc.tensor.matmul(bank[6][:, f], gram[c][:, unit(h, t), 256:384],
                                          rkv[:, t, ds(2 * D + P * p + DH * h, DH)], start=t == 0, stop=True)
                mm.then_inc(w_made.sem, 1)

            def solve(p, c, t):
                pe.wait_ge(xt_copied, 2 * (LEV - 1) * (p + 1))
                pe.wait_ge(*w_copied.at(2 * p + t + 1))
                for h in range(2):
                    mm = nc.tensor.matmul(bank[6][:, P + h * DH:P + (h + 1) * DH], XT[c][:, unit(h, t), :],
                                          Wn[:, t, h * DH:(h + 1) * DH], start=True, stop=True)
                mm.then_inc(u_made.sem, 1)

            def state(p, c):
                pe.wait_ge(uo_copied, 2 * p + 1)
                nc.tensor.matmul(bank[6][:, 256:384], Bt[c][:, 0, :], Uo[:, 0, :], start=True, stop=False)
                nc.tensor.matmul(bank[6][:, 256:384], Kt[c][:, 0, :], rkv[:, 0, ds(2 * D + P * p, P)], start=False,
                                 stop=True).then_inc(s_made, 1)

            def outputs(p, c):
                pe.wait_ge(uo_copied, 2 * p + 2)
                if not (isinstance(p, int) and p == 0):
                    pe.wait_ge(*pair_done.at(p))
                for t in range(NT):
                    for h in range(2):
                        f = slice(h * DH, (h + 1) * DH)
                        oh = bank[7][:, t * P + h * DH:t * P + (h + 1) * DH]
                        if t:
                            nc.tensor.matmul(oh, AR[c][:, 1, 1, :], SB[:, f], start=True, stop=False)
                        nc.tensor.matmul(oh, gram[c][:, unit(h, t), 128:256], Uo[:, t, f], start=t == 0, stop=False)
                        mm = nc.tensor.matmul(oh, gram[c][:, unit(h, t), 384:512],
                                              rkv[:, t, ds(2 * D + P * p + DH * h, DH)], start=False, stop=True)
                mm.then_inc(o_made.sem, 1)

            def step(p, b, tail=True, prep=True):
                c = 1 - b
                below(p, b, 0)
                if prep:
                    decays(p + 1)
                if tail:
                    rest(p - 1, c, 0)
                below(p, b, 1)
                if tail:
                    solve(p - 1, c, 0)
                grow(p, b, 1)
                if tail:
                    state(p - 1, c)
                below(p, b, 2)
                grow(p, b, 2)
                if tail:
                    rest(p - 1, c, 1)
                below(p, b, 3)
                grow(p, b, 3)
                if tail:
                    solve(p - 1, c, 1)
                below(p, b, 4)
                if tail:
                    outputs(p - 1, c)
                grow(p, b, 4)
                if prep:
                    turn_ar(p + 1)
                below(p, b, 5)
                if prep:
                    turn_bk(p + 1, c)
                grow(p, b, 5)
                if prep:
                    grams(p + 1, c, (0, 1))
                below(p, b, 6)
                grow(p, b, 6)
                if prep:
                    grams(p + 1, c, (2, 3))

            def first():
                decays(0)
                turn_ar(0)
                turn_bk(0, 0)
                grams(0, 0, range(4))
                step(0, 0, tail=False)

            def last():
                p = PAIRS - 1
                step(p, 1, prep=False)
                for t in range(NT):
                    rest(p, 1, t)
                    solve(p, 1, t)
                    if t == 0:
                        state(p, 1)
                outputs(p, 1)

            step_loop(pe, first, step, last)

        def act_heads(act):
            act.wait_ge(*conv_gated.at(4))

            def decays(p):
                act.wait_ge(cs_done, p + 1)
                cs = bank[4][:, 0:2 * P].rearrange("p (t s) -> p t s", t=NT)
                nc.scalar.activation(Rt, cs, ACT.Exp, scale=-S_DECAY).then_inc(pexp.sem, 1)
                nc.scalar.activation(Pi, cs, ACT.Exp, scale=S_DECAY).then_inc(pexp.sem, 1)

            def decays_before(p):
                act.wait_ge(pdiff, p + 1)
                nc.scalar.activation(At, At, ACT.Exp, scale=-S_DECAY).then_inc(pexp.sem, 1)

            def copy_ar(p, c):
                act.wait_ge(*hturned.at(2 * p + 1))
                nc.scalar.copy(AR[c].rearrange("p t a s -> p (t a s)"), bank[5][:, :]).then_inc(ft_copied.sem, 1)

            def copy_bk(p):
                act.wait_ge(*hturned.at(2 * p + 2))
                nc.scalar.copy(BK.rearrange("p a t s -> p (a t s)"), bank[4][:, :]).then_inc(ft_copied.sem, 1)

            def grown(p, b, lev):
                for g in range(2):
                    r = slice(2 * g, 2 * g + 2)
                    new = bank[2 + g][:, 0:2 * P].rearrange("p (a u n m) -> p a u n m", a=2, u=2, m=1 << lev)
                    act.wait_ge(x_made, 2 * (LEV - 1) * p + 2 * lev + g - 1)
                    if lev < LEV - 1:
                        nc.scalar.copy(halves(Xm[:, r, :], lev)[0], new[:, 0]).then_inc(xm_copied.sem, 1)
                    nc.scalar.copy(halves(XT[b][:, r, :], lev)[1], new[:, 1]).then_inc(xt_copied, 1)

            def copy_rest(p, t):
                act.wait_ge(*w_made.at(2 * p + t + 1))
                nc.scalar.mul(Wn[:, t, :], bank[6][:, 0:P], -1.0).then_inc(w_copied.sem, 1)

            def copy_u(p, t):
                act.wait_ge(*u_made.at(2 * p + t + 1))
                nc.scalar.copy(Uo[:, t, :], bank[6][:, P:2 * P]).then_inc(uo_copied, 1)

            def step(p, b, tail=True, prep=True):
                c = 1 - b
                if prep:
                    decays(p + 1)
                if tail:
                    copy_rest(p - 1, 0)
                    copy_u(p - 1, 0)
                grown(p, b, 1)
                if prep:
                    decays_before(p + 1)
                grown(p, b, 2)
                if tail:
                    copy_rest(p - 1, 1)
                grown(p, b, 3)
                if tail:
                    copy_u(p - 1, 1)
                grown(p, b, 4)
                if prep:
                    copy_ar(p + 1, c)
                    copy_bk(p + 1)
                grown(p, b, 5)
                grown(p, b, 6)

            def first():
                decays(0)
                decays_before(0)
                copy_ar(0, 0)
                copy_bk(0)
                step(0, 0, tail=False)

            def last():
                p = PAIRS - 1
                step(p, 1, prep=False)
                for t in range(NT):
                    copy_rest(p, t)
                    copy_u(p, t)

            step_loop(act, first, step, last)
            act.wait_ge(head_var, 1)
            nc.scalar.activation(hvar, hvar, ACT.Sqrt).then_inc(head_root, 1)

        def pool_heads(pool):
            with pool.Fori(0, PAIRS) as p:
                pool.wait_ge(*o_made.at(p + 1))
                v = by_head(rkv[:, :, ds(2 * D + P * p, P)])
                nc.gpsimd.tensor_tensor(v, v, per_head(hbonus[:, :, ds(2 * p, 2)]), ALU.mult).then_inc(bonus_used, 1)

        def by_head(v, heads=2):
            return v.rearrange("p t (h d) -> p t h d", h=heads)

        def per_head(v, heads=2):
            return v.unsqueeze(3).to_broadcast([P, NT, heads, DH])

        HEAD_DVE = 16

        def dve_heads(dve, order):
            def of(v, p):
                return v[:, :, ds(2 * p, 2)]

            def cut(base, p):
                return rkv[:, :, ds(base + P * p, P)]

            def row_of(v, p):
                return v[:, ds(P * p, P)].unsqueeze(1).to_broadcast([P, NT, P])

            def differences(p):
                dve.wait_ge(*pexp.at(3 * p + 2))
                cs = bank[4][:, 0:2 * P].rearrange("p (t s) -> p t s", t=NT)
                nc.vector.tensor_tensor(At, cs, decay[:, :, ds(P * p, P)], ALU.subtract).then_inc(pdiff, 1)

            def key_direction(p):
                order.mark(nc.vector.scalar_tensor_tensor(out=tmpb, in0=gain_a[:, :, ds(P * p, P)], scalar=-1.0,
                                                          in1=row_of(ka_row, p), op0=ALU.add, op1=ALU.mult))
                order.step(nc.vector.tensor_tensor(kkb, cut(D, p), row_of(kk_row, p), ALU.mult))
                order.step(nc.vector.tensor_tensor(by_head(kkb), by_head(kkb), per_head(of(kinv, p)), ALU.mult))

            dve.wait_ge(rk_loaded, 16)
            dve.wait_ge(rows_loaded, 48)

            def key_and_bonus(p, c):
                if not (isinstance(p, int) and p < 2):
                    dve.wait_ge(s_made, p - 1)
                r = cut(0, p)
                order.step(nc.vector.scalar_tensor_tensor(out=Kt[c], in0=tmpb, scalar=1.0, in1=cut(D, p), op0=ALU.add,
                                                          op1=ALU.mult))
                order.step(nc.vector.tensor_tensor(tmpb, r, Kt[c], ALU.mult))
                order.step(nc.vector.tensor_tensor(tmpb, tmpb, row_of(rk_row, p), ALU.mult))

            def make_ar(p):
                order.mark(nc.vector.tensor_reduce(of(hbonus, p), by_head(tmpb), AX.X, ALU.add))
                dve.wait_ge(*pexp.at(3 * p + 3))
                order.mark(nc.vector.tensor_tensor(Rt, cut(0, p), Rt, ALU.mult))
                nc.vector.tensor_tensor(At, kkb, At, ALU.mult).then_inc(tok_ready.sem, 1)

            def make_bk(p, c):
                order.mark(nc.vector.tensor_tensor(Kt[c], Kt[c], Pi, ALU.mult))
                dve.wait_ge(*tok_ready.at(2 * p + 1))
                order.step(nc.vector.tensor_tensor(kkb, kkb, gain_a[:, :, ds(P * p, P)], ALU.mult))
                nc.vector.tensor_tensor(Bt[c], kkb, Pi, ALU.mult).then_inc(tok_ready.sem, 1)

            def mask_grams(p, c):
                for u in range(4):
                    dve.wait_ge(*gram_done.at(4 * p + u + 1))
                    nc.vector.tensor_tensor(gram[c][:, u, :].rearrange("p (a m) -> p a m", a=2),
                                            bank[5 - u % 2][:, :].rearrange("p (a m) -> p a m", a=2),
                                            const[:, CONST["strict"][0]:CONST["tri"][1]].unsqueeze(1).to_broadcast(
                                                [P, 2, 2 * P]), ALU.mult).then_inc(gram_masked.sem, 1)
                    if u % 2:
                        g = slice(u - 1, u + 1)
                        dve.wait_ge(*gram_masked.at(4 * p + u + 1))
                        lt = gram[c][:, g, 0:P]
                        order.step(nc.vector.scalar_tensor_tensor(out=lt, in0=lt, scalar=-1.0,
                                                                  in1=ident.unsqueeze(1).to_broadcast([P, 2, P]),
                                                                  op0=ALU.mult, op1=ALU.add))
                        nc.vector.tensor_tensor(XT[c][:, g, :], lt, con("level0_t").unsqueeze(1).to_broadcast([P, 2, P]),
                                                ALU.mult).then_inc(inverse_begun, 1)

            def mask(p, lev):
                for g in range(2):
                    dve.wait_ge(y_made, 2 * LEV * p + 2 * lev + g + 1)
                    nc.vector.tensor_tensor((Xm if lev == 0 else Ym)[:, 2 * g:2 * g + 2, :],
                                            bank[g][:, 0:2 * P].rearrange("p (u s) -> p u s", u=2),
                                            con(f"level{lev}").unsqueeze(1).to_broadcast([P, 2, P]),
                                            ALU.mult).then_inc(y_masked.sem, 1)

            def state(p):
                dve.wait_ge(s_made, p + 1)
                nc.vector.scalar_tensor_tensor(out=SB, in0=bank[6][:, 256:384], scalar=sdec[:, ds(p, 1)],
                                               in1=con("heads"), op0=ALU.mult, op1=ALU.mult).then_inc(s_ready, 1)

            def centre(p):
                dve.wait_ge(*o_made.at(p + 1))
                o = bank[7][:, 0:2 * P].rearrange("p (t s) -> p t s", t=NT)
                mean = hmean.rearrange("p (t h) -> p t h", t=NT)
                order.step(nc.vector.tensor_reduce(mean, by_head(o), AX.X, ALU.add))
                order.step(nc.vector.tensor_scalar(hmean, hmean, 1.0 / DH, None, ALU.mult))
                nc.vector.tensor_tensor(by_head(cut(0, p)), by_head(o), per_head(mean), ALU.subtract
                                        ).then_inc(pair_done.sem, 1)
                dve.wait_ge(*pair_done.at(p + 1))
                order.step(nc.vector.tensor_tensor(centred_sq, cut(0, p), cut(0, p), ALU.mult))
                order.mark(nc.vector.tensor_reduce(of(hvar, p), by_head(centred_sq), AX.X, ALU.add))

            centred_sq = carve(10624, NT, P)

            def step(p, b, tail=True, prep=True):
                c = 1 - b
                mask(p, 0)
                if prep:
                    differences(p + 1)
                mask(p, 1)
                if prep:
                    key_direction(p + 1)
                if tail:
                    state(p - 1)
                mask(p, 2)
                if prep:
                    key_and_bonus(p + 1, c)
                mask(p, 3)
                if prep:
                    make_ar(p + 1)
                mask(p, 4)
                if prep:
                    make_bk(p + 1, c)
                mask(p, 5)
                if tail:
                    centre(p - 1)
                mask(p, 6)
                if prep:
                    mask_grams(p + 1, c)

            def first():
                differences(0)
                key_direction(0)
                key_and_bonus(0, 0)
                make_ar(0)
                make_bk(0, 0)
                mask_grams(0, 0)
                step(0, 0, tail=False)

            first()
            start = order.count()
            with dve.Fori(0, (PAIRS - 2) // 2) as u:
                order.body(start, u, 2 * HEAD_DVE)
                for c in (1, 0):
                    step(2 * u + (2 - c), c)
            order.after(start, (PAIRS - 2) // 2, 2 * HEAD_DVE)
            step(PAIRS - 1, 1, prep=False)
            state(PAIRS - 1)
            centre(PAIRS - 1)
            order.settle()
            nc.vector.tensor_scalar(hvar, hvar, 1.0 / DH, 64e-5, ALU.mult, ALU.add).then_inc(head_var, 1)

        fing = carve(2 * D, D)
        sq = [carve(4096 + 512 * b, TW) for b in range(NT)]
        heads = rkv[:, :, 0:D]
        vbon = rkv[:, :, 2 * D:3 * D]
        merged2 = gates[:, :, 0:D]
        rows_loaded, fing_loaded = sem("rows_loaded"), sem("fing_loaded")
        g_made = Again(scattered, 4 * NG)
        heads_gated = Again(gate_used, 4)
        merged2_ready = Again(att_merged, 4)
        mixed2 = Again(mixed, 4)
        turn_h = Turn(heads, None, t0h, t0l)
        turn_o = Turn(merged2, None, t0h, t0l)
        norm_2 = RmsNorm(xres, carve(9216, NT, D), stat)
        turn_f = Turn(carve(9216, NT, D), gain("norm_ff_g_2"), t0h, t0l)
        ff_relu = Again(silu_done, N_EXP)
        ff_squared = Again(hid_ready, 2 + N_EXP)
        ff_turned = Again(hid_turned, N_EXP)
        ff_high = Again(hid_high, N_EXP)
        ff_low = Again(hid_low, N_EXP)
        ff_added = Again(x_added, 4 * NG)
        norm_l = RmsNorm(xres, carve(9216, NT, D), stat)
        finished = sem("finished")

        def pe_out2(pe):
            for t in range(NT):
                for h in range(2):
                    nc.tensor.matmul(bank[2 * t + h][:, :], gT[:, t * P:(t + 1) * P], g2[:, 512 * h:512 * h + 512],
                                     start=True, stop=True).then_inc(g_made.sem, 1)
            turn_h.pe(pe, [heads_gated.at(4)])
            square_product(pe, Q_RWKV, t0h, t0l, [heads_gated.at(4)], turn_h)
            turn_o.pe(pe, [merged2_ready.at(4)])
            square_product(pe, Q_OUT2, t0h, t0l, [merged2_ready.at(4)], turn_o)
            turn_f.pe(pe, [norm_2.ready()])
            pe.wait_ge(*turn_f.done())
            pe.wait_ge(*mixed2.at(4))

            def first(n, q, i=0, per=0):
                wide_quarter(pe, n, q, bank[0:2], t0h, t0l, TW, i, per)

            def turn(j):
                pe.wait_ge(*ff_squared.at(2 * j + 2))
                for b in range(2):
                    for cc in range(2):
                        for t in range(NT):
                            at = cc * SEQ + t * P
                            tr = nc.tensor.transpose(bank[2 + b][:, at:at + P],
                                                     sq[t].rearrange("p (f c) -> p f c", c=4)[:, :, 2 * b + cc], ident)
                    tr.then_inc(ff_turned.sem, 1)

            def second(n, c, j, i=0, per=0, last=False):
                if c == 0:
                    pe.wait_ge(*ff_low.at(2 * j + 2))
                wait_low(pe, n, i, per)
                s = n % RING
                for h in range(2):
                    f = slice(512 * h, 512 * h + 512)
                    for t in range(NT):
                        r = slice(t * P, (t + 1) * P)
                        o = bank[4 + 2 * h + t][:, :]
                        nc.tensor.matmul(o, t1h[:, c, r], whi[:, s, f], start=False, stop=False, skip_group_check=True)
                        nc.tensor.matmul(o, t1h[:, c, r], wlo[:, s, f], start=False, stop=False, skip_group_check=True)
                        mm = nc.tensor.matmul(o, t1l[:, c, r], whi[:, s, f], start=False, stop=last, skip_group_check=True)
                mm.then_inc(quarter_done, 1)

            for q in range(4):
                first(Q_FF + q, q)
            for b in range(4):
                nc.tensor.matmul(bank[4 + b][:, :].rearrange("p (k s) -> p k s", k=2), zero[:, :], t0h[:, 0:2, :],
                                 start=True, stop=False, skip_group_check=True)
            with pe.Fori(0, FF_J - 1) as j:
                for q in range(4):
                    if q == 0:
                        pe.wait_ge(*ff_relu.at(2 * j + 2))
                    first(Q_FF + 4 + q, q, j, 8)
                    if q == 1:
                        turn(j)
                for c in range(4):
                    second(Q_FF + 8 + c, c, j, j, 8)
            turn(FF_J - 1)
            for c in range(4):
                second(Q_END - 4 + c, c, FF_J - 1, last=c == 3)

        def sp_ff(sp):
            v1 = A["w_ff1_2"][0].rearrange("(p k) n -> p k n", k=KC)
            v2 = A["w_ff2_2"][0].rearrange("(j p c) n -> p j c n", j=FF_J, c=4)

            def first(n, q, j, i=0, per=0):
                load(sp, n, [(pair_view(raw, n, TW), v1[:, 2 * q:2 * q + 2, ds(TW * j, TW)])], i, per)

            def second(n, c, j, i=0, per=0):
                load(sp, n, [(raw[:, n % RING, :].rearrange("p (a c n) -> p a c n", a=1, c=1), v2[:, ds(j, 1), c:c + 1, :])],
                     i, per)

            for q in range(4):
                first(Q_FF + q, q, 0)
            with sp.Fori(0, FF_J - 1) as j:
                for q in range(4):
                    first(Q_FF + 4 + q, q, j + 1, j, 8)
                for c in range(4):
                    second(Q_FF + 8 + c, c, j, j, 8)
            for c in range(4):
                second(Q_END - 4 + c, c, FF_J - 1)

        def act_out2(act):
            act.wait_ge(*pair_done.at(PAIRS))
            act.dma_start(fing, row(A["norm_final_g_2"], D)).then_inc(fing_loaded, 16)
            turn_h.act(act, Q_RWKV)
            for q in range(4, 8):
                split_high(act, Q_RWKV + q)
            for q in range(4):
                split_high(act, Q_OUT2 + q)
            turn_o.act(act, Q_OUT2)
            for q in range(4, 8):
                split_high(act, Q_OUT2 + q)
            for q in range(4):
                split_high(act, Q_FF + q)
            norm_2.act(act, [mixed2.at(4)])
            turn_f.act(act, Q_FF)

            def relu(j):
                act.wait_ge(quarter_done, Q_FF + 4 + 8 * j if not isinstance(j, int) or j else Q_FF + 4)
                for t in range(NT):
                    nc.scalar.activation(sq[t], bank[t][:, :], ACT.Relu).then_inc(ff_relu.sem, 1)

            def high(j):
                for b in range(2):
                    act.wait_ge(*ff_turned.at(2 * j + b + 1))
                    nc.scalar.activation(t1h[:, 2 * b:2 * b + 2, :], bank[2 + b][:, :].rearrange("p (c s) -> p c s", c=2),
                                         ACT.Copy).then_inc(ff_high.sem, 1)

            with act.Fori(0, FF_J - 1) as j:
                split_high(act, Q_FF + 4, j, 8)
                relu(j)
                for q in range(1, 4):
                    split_high(act, Q_FF + 4 + q, j, 8)
                high(j)
                for c in range(4):
                    split_high(act, Q_FF + 8 + c, j, 8)
            act.wait_ge(quarter_done, Q_END - 8)
            for t in range(NT):
                nc.scalar.activation(sq[t], bank[t][:, :], ACT.Relu).then_inc(ff_relu.sem, 1)
            for c in range(4):
                split_high(act, Q_END - 4 + c)
            high(FF_J - 1)
            norm_l.act(act, [ff_added.at(4)])

        def dve_out2(dve, order):
            dve.wait_ge(head_root, 1)
            wide_row = lambda v: v.unsqueeze(1).to_broadcast([P, NT, D])
            order.step(nc.vector.reciprocal(hvar, hvar))
            order.step(nc.vector.tensor_tensor(by_head(heads, NH), by_head(heads, NH), per_head(hvar, NH), ALU.mult))
            order.step(nc.vector.tensor_tensor(heads, heads, wide_row(lng), ALU.mult))
            order.step(nc.vector.tensor_tensor(heads, heads, wide_row(lnb), ALU.add))
            dve.wait_ge(bonus_used, PAIRS)
            order.step(nc.vector.tensor_tensor(heads, heads, vbon, ALU.add))
            for t in range(NT):
                for h in range(2):
                    dve.wait_ge(*g_made.at(2 * t + h + 1))
                    o = heads[:, t, 512 * h:512 * h + 512]
                    nc.vector.tensor_tensor(o, o, bank[2 * t + h][:, :], ALU.mult).then_inc(heads_gated.sem, 1)
            turn_h.dve(dve)
            for c in range(2):
                dve.wait_ge(quarter_done, Q_RWKV + 4 * c + 4)
                for t in range(NT):
                    o = merged2[:, t, c * TW:(c + 1) * TW]
                    order.step(nc.vector.tensor_tensor(o, o, bank[2 * c + t][:, :], ALU.mult))
                    nc.vector.tensor_tensor(o, o, gates[:, t, D + c * TW:D + (c + 1) * TW], ALU.add).then_inc(merged2_ready.sem, 1)
            turn_o.dve(dve)
            for c in range(2):
                dve.wait_ge(quarter_done, Q_OUT2 + 4 * c + 4)
                for t in range(NT):
                    o = xres[:, t, c * TW:(c + 1) * TW]
                    nc.vector.tensor_tensor(o, o, bank[2 * c + t][:, :], ALU.add).then_inc(mixed2.sem, 1)
            norm_2.dve(dve, order)
            turn_f.dve(dve)

            def ff(j):
                for t in range(NT):
                    dve.wait_ge(*ff_relu.at(2 * j + t + 1))
                    nc.vector.tensor_tensor(sq[t], sq[t], sq[t], ALU.mult).then_inc(ff_squared.sem, 1)
                for b in range(2):
                    dve.wait_ge(*ff_high.at(2 * j + b + 1))
                    nc.vector.tensor_tensor(t1l[:, 2 * b:2 * b + 2, :], bank[2 + b][:, :].rearrange("p (c s) -> p c s", c=2),
                                            t1h[:, 2 * b:2 * b + 2, :].bitcast(F32), ALU.subtract).then_inc(ff_low.sem, 1)

            with dve.Fori(0, FF_J) as j:
                ff(j)
            dve.wait_ge(quarter_done, Q_END)
            for h in range(2):
                for t in range(NT):
                    o = xres[:, t, 512 * h:512 * h + 512]
                    nc.vector.tensor_tensor(o, o, bank[4 + 2 * h + t][:, :], ALU.add).then_inc(ff_added.sem, 1)
            norm_l.dve(dve, order)
            dve.wait_ge(fing_loaded, 16)
            for t in range(NT):
                dve.wait_ge(*norm_l.ready(t + 1))
                nc.vector.tensor_tensor(xres[:, t, :], norm_l.xn[:, t, :], fing, ALU.mult).then_inc(finished, 1)

        block = ctx.enter_context(nc.Block())
        out_done = sem("out_done")

        @block.sync
        def _(sp):
            sp_block1(sp)
            sp_experts(sp)
            sp_overflow(sp)
            sp_ple(sp)
            sp_in2(sp)
            sp_ff(sp)
            for t in range(NT):
                sp.wait_ge(finished, t + 1)
                sp.dma_start(out[t * P:(t + 1) * P, :], xres[:, t, :]).then_inc(out_done, 16)
            sp.wait_ge(out_done, 16 * NT)

        @block.gpsimd
        def _(pool):
            pool_stream(pool)

        @block.scalar
        def _(act):
            act_loads(act)
            norm_a.act(act, [(x_loaded, 16)])
            act.wait_ge(vec_loaded, N_VEC)
            turn_a.act(act, 0)
            act_in(act)
            act_ssd(act)
            act_angles(act)
            act_attention(act)
            router_loads(act)
            act_router(act)
            act_experts(act)
            act_overflow(act)
            act_ple(act)
            act_in2(act)
            act_conv(act)
            act_heads(act)
            act_out2(act)

        @block.vector
        def _(dve):
            order = Order(dve, dve_order)
            norm_a.dve(dve, order)
            turn_a.dve(dve)
            dve_ssd(dve, order)
            dve_angles(dve, order)
            dve_attention(dve, order)
            dve_router(dve, order)
            dve_experts(dve)
            dve_overflow(dve)
            dve_ple(dve, order)
            dve_in2(dve, order)
            dve_conv(dve, order)
            dve_heads(dve, order)
            dve_out2(dve, order)

        @block.tensor
        def _(pe):
            pe_in(pe)
            pe_ssd(pe)
            pe_attention(pe)
            pe_router(pe)
            pe_experts(pe)
            pe_overflow(pe)
            pe_ple(pe)
            pe_in2(pe)
            pe_conv(pe)
            pe_heads(pe)
            pe_out2(pe)


def kernel(**inputs):
    import concourse.bacc as bacc
    from concourse.bass_utils import run_bass_kernel_spmd

    nc = bacc.Bacc("TRN2", target_bir_lowering=False, num_devices=1)
    arrays, views = {}, {}
    given = {name: np.ascontiguousarray(a) for name, a in inputs.items()}
    given["const"] = constants()
    for name, a in given.items():
        arrays["in_" + name] = a
        views[name] = nc.dram_tensor("in_" + name, a.shape, mybir.dt.from_np(a.dtype), kind="ExternalInput").ap()
    result = nc.dram_tensor("result", (SEQ, D), F32, kind="ExternalOutput").ap()
    build(nc, views, result)
    r = run_bass_kernel_spmd(nc, [arrays], core_ids=[0])
    return r.results[0]["result"].reshape(1, SEQ, D)
```

```python
import math
from contextlib import ExitStack

import numpy as np

import concourse.bass as bass
from concourse import mybir

F32 = mybir.dt.float32
F32R = mybir.dt.float32r
I32 = mybir.dt.int32
ALU = mybir.AluOpType
ACT = mybir.ActivationFunctionType
AX = mybir.AxisListType
ds = bass.ds

P = 128
SEQ = 256
NT = SEQ // P
D = 1024
KC = D // P
EPS = 1e-6
IN_W = 7440
IN_TW = 496
IN_T = IN_W // IN_TW
IN2_W = 7168
TW = 512
QF = 2 * TW
RING = 4
MOE_RING = 6

C_Z, C_XBC, C_DT, C_Q, C_K, C_V, C_GS, C_GA = 0, 1024, 2304, 2320, 3344, 4368, 5392, 6416
NH, DH = 16, 64
XCH = 10
PAD = 3
TWO_PI = 2.0 * math.pi

Q_IN = 0
Q_SSD = Q_IN + 4 * IN_T
Q_ATT = Q_SSD + 8
Q_OUT = Q_ATT + 8
Q_MOE = Q_OUT + 8
N_EXP = 32
DE = 256
Q_PLE = Q_MOE + 6 * N_EXP
Q_GATE = Q_PLE + 2
Q_IN2 = Q_GATE + 8
Q_CONV = Q_IN2 + 4 * (IN2_W // TW)
Q_RWKV = Q_CONV + 8
Q_OUT2 = Q_RWKV + 8
Q_FF = Q_OUT2 + 8
FF_J = 8
Q_END = Q_FF + 8 * FF_J

CONST = {}


def constants():
    i = np.arange(P)
    parts = []

    def put(name, a):
        at = sum(x.shape[1] for x in parts)
        CONST[name] = (at, at + a.shape[1])
        parts.append(np.ascontiguousarray(a, dtype=np.float32))

    put("ident", np.eye(P))
    put("strict", (i[:, None] < i[None, :]) * 1.0)
    put("tri", (i[:, None] <= i[None, :]) * 1.0)
    put("centred", (i[:, None] <= i[None, :]) * 1.0 - (i[:, None] < 64) * np.ones((P, P)))
    put("ones", np.ones((P, P)))
    neg = np.where(i[None, :] <= i[:, None], 0.0, -1e30)
    put("amask", np.concatenate([neg, np.zeros((P, P)), neg], axis=1))
    for lev in range(7):
        m = 1 << lev
        pick = ((i[:, None] // m) % 2 == 1) & (i[None, :] // m == i[:, None] // m - 1)
        put(f"level{lev}", np.eye(P) + pick)
        if lev == 0:
            put("level0_t", np.eye(P) + pick.T)
    put("heads", (i[:, None] // 64 == i[None, :] // 64) * 1.0)
    put("low", (i[:, None] < 64) * 1.0)
    put("high", (i[:, None] >= 64) * 1.0)
    half = DH // 2
    freq = (np.float32(10000.0) ** (-np.arange(half, dtype=np.float32) / np.float32(half))).astype(np.float32)
    put("freq", np.broadcast_to(freq, (P, half)))
    put("slot", np.broadcast_to(np.arange(P), (P, P)))
    put("rev8", np.broadcast_to(8.0 - np.arange(8), (P, 8)))
    put("rev4", np.broadcast_to(4.0 - np.arange(4), (P, 4)))
    return np.concatenate(parts, axis=1)


constants()
N_CONST = max(b for _, b in CONST.values())


class Order:

    def __init__(self, eng, sem):
        self.eng, self.sem, self.base, self.n = eng, sem, 0, 0

    def mark(self, ins):
        ins.then_inc(self.sem, 1)
        self.n += 1

    def settle(self):
        self.eng.wait_ge(self.sem, self.base + self.n)

    def step(self, ins):
        self.mark(ins)
        self.settle()

    def body(self, start, i, per):
        self.base, self.n = start + i * per, 0

    def after(self, start, times, per):
        assert self.n == per, (self.n, per)
        self.base, self.n = start + times * per, 0

    def count(self):
        return self.base + self.n


class Again:

    def __init__(self, sem, before):
        self.sem, self.before = sem, before

    def at(self, n):
        return self.sem, self.before + n


def wait_from(eng, sem, value):
    if not (isinstance(value, int) and value <= 0):
        eng.wait_ge(sem, value)



JOB = 6 * 8


def split_by_vector(n):
    return Q_MOE - MOE_RING <= n < Q_PLE and n % 2 == 1


def slot(n):
    return (n - Q_MOE) % MOE_RING if Q_MOE <= n < Q_PLE else n % RING


RAW_DONE, LOW_DONE = [], []
_shown = [0] * MOE_RING
for _n in range(Q_END):
    _shown[slot(_n)] += 32 if Q_MOE <= _n < Q_PLE else 16
    RAW_DONE.append(_shown[slot(_n)])
    LOW_DONE.append(sum(split_by_vector(m) == split_by_vector(_n) for m in range(_n + 1)))


def at_turn(counts, n, i, per):
    if not per:
        return counts[n]
    span = JOB if per < JOB and JOB % per == 0 and n + JOB < Q_PLE and n >= Q_MOE - MOE_RING else per
    return counts[n] + (counts[n + span] - counts[n]) * per // span * i


NORMS = ["attn_norm_w", "moe_norm_w", "ple_norm_w", "ssd_norm_w", "norm_mix_g_2", "norm_ff_g_2",
         "conv_ln_g_2", "conv_ln_b_2"]


def build(nc, A, out):
    ctx = ExitStack()
    with ctx:
        def sb(name, shape, dt=F32):
            return ctx.enter_context(nc.sbuf_tensor(name, shape, dt))

        def sem(name):
            return ctx.enter_context(nc.semaphore(name))

        raw = sb("raw", [P, RING, QF])
        whi = sb("whi", [P, RING, QF], F32R)
        wlo = sb("wlo", [P, RING, QF], F32R)
        const = sb("const", [P, N_CONST])
        cols = sb("cols", [P, len(NORMS), KC])
        mul = sb("mul", [P, 3, KC])
        xres = sb("xres", [P, NT, D])
        t0h = sb("t0h", [P, KC, SEQ], F32R)
        t0l = sb("t0l", [P, KC, SEQ], F32R)
        t1h = sb("t1h", [P, 4, SEQ], F32R)
        t1l = sb("t1l", [P, 4, SEQ], F32R)
        proj = sb("proj", [P, NT, IN_W])
        WORK = 14320
        work = sb("work", [P, WORK])
        small = sb("small", [P, 360])
        bank = [ctx.enter_context(nc.psum_tensor(f"bank{b}", [P, 512], F32)) for b in range(8)]

        def con(name):
            a, b = CONST[name]
            return const[:, a:b]

        ident = con("ident")

        def carve(at, *shape):
            n = int(np.prod(shape))
            assert at + n <= WORK, (at, n)
            v = work[:, at:at + n]
            if len(shape) == 1:
                return v
            names = "abcd"[:len(shape)]
            return v.rearrange(f"p ({' '.join(names)}) -> p {' '.join(names)}", **dict(zip(names, shape)))

        def tiny(at, *shape):
            n = int(np.prod(shape))
            v = small[:, at:at + n]
            if len(shape) == 1:
                return v
            names = "abcd"[:len(shape)]
            return v.rearrange(f"p ({' '.join(names)}) -> p {' '.join(names)}", **dict(zip(names, shape)))

        raw_full = [sem(f"raw_full{s}") for s in range(MOE_RING)]
        hi_ready = sem("hi_ready")
        lo_by_pool = sem("lo_by_pool")
        lo_by_dve = sem("lo_by_dve")
        quarter_done = sem("quarter_done")
        consts_loaded = sem("consts_loaded")
        x_loaded, early_ready = sem("x_loaded"), sem("early_ready")
        vec_loaded = sem("vec_loaded")
        dve_order = sem("dve_order")
        pool_order = sem("pool_order")

        more_raw = proj[:, :, :].rearrange("p t n -> p (t n)")[:, 12232:12232 + (MOE_RING - RING) * QF]

        def raw_of(n):
            s = slot(n)
            return raw[:, s, :] if s < RING else more_raw[:, (s - RING) * QF:(s - RING + 1) * QF]

        def wait_low(eng, n, i=0, per=0):
            eng.wait_ge(lo_by_dve if split_by_vector(n) else lo_by_pool, at_turn(LOW_DONE, n, i, per))

        def load(sp, n, pairs, i=0, per=0):
            before = n - (MOE_RING if Q_MOE + RING <= n < Q_PLE else RING)
            if before >= 0:
                wait_low(sp, before, i, per)
            for dst, src in pairs:
                sp.dma_start(dst, src).then_inc(raw_full[slot(n)], 16)

        def split_high(act, n, i=0, per=0, width=QF):
            s = n % RING
            act.wait_ge(raw_full[slot(n)], at_turn(RAW_DONE, n, i, per))
            wait_from(act, quarter_done, n - RING + 1 + per * i)
            nc.scalar.activation(whi[:, s, 0:width], raw_of(n)[:, 0:width], ACT.Copy).then_inc(hi_ready, 1)

        def split_low(eng, n, i=0, per=0, width=QF):
            s = n % RING
            eng.wait_ge(hi_ready, n + 1 + per * i)
            ins = (nc.vector if split_by_vector(n) else nc.gpsimd).tensor_tensor(
                wlo[:, s, 0:width], raw_of(n)[:, 0:width], whi[:, s, 0:width].bitcast(F32), ALU.subtract)
            ins.then_inc(lo_by_dve if split_by_vector(n) else lo_by_pool, 1)

        def times(dst, hi, lo, wh, wl, first, last):
            nc.tensor.matmul(dst, hi, wh, start=first, stop=False)
            nc.tensor.matmul(dst, hi, wl, start=False, stop=False)
            return nc.tensor.matmul(dst, lo, wh, start=False, stop=last)

        def pair_view(buf, n, width):
            return buf[:, n % RING, 0:2 * width].rearrange("p (k n) -> p k n", k=2)

        def wide_quarter(pe, n, q, dst, hi, lo, width=TW, i=0, per=0, begun=False):
            wait_low(pe, n, i, per)
            wh, wl = pair_view(whi, n, width), pair_view(wlo, n, width)
            for t in range(NT):
                for kk in range(2):
                    k = 2 * q + kk
                    mm = times(dst[t][:, 0:width], hi[:, k, t * P:(t + 1) * P], lo[:, k, t * P:(t + 1) * P],
                               wh[:, kk, :], wl[:, kk, :], k == 0 and not begun, k == KC - 1)
            mm.then_inc(quarter_done, 1)

        def load_square(sp, n, w, quarters=range(8), order="(p k) n -> p k n"):
            v = w.rearrange(order, k=KC)
            for j in quarters:
                c, q, m = j // 4, j % 4, n + j
                load(sp, m, [(pair_view(raw, m, TW), v[:, 2 * q:2 * q + 2, c * TW:(c + 1) * TW])])

        def square_product(pe, n, hi, lo, waits, turn=None):
            for s, v in waits:
                pe.wait_ge(s, v)
            for c in range(2):
                for q in range(4):
                    if turn is not None and c == 0:
                        pe.wait_ge(*turn.done(2 * q + 2))
                    wide_quarter(pe, n + 4 * c + q, q, bank[2 * c:2 * c + 2], hi, lo)

        class Turn:
            turned = sem("turned")
            high = sem("turned_high")
            low = sem("turned_low")
            index = splits = 0

            def __init__(self, src, gain, hi, lo, order="p t (f k) -> p t f k"):
                self.src = src.rearrange(order, k=KC)
                self.gain, self.hi, self.lo = gain, hi, lo
                self.banks, self.chunks = Turn.index * (KC // 2), Turn.splits * KC
                Turn.index += 1
                Turn.splits += hi is not None

            def written(self, banks=KC // 2):
                return self.turned, self.banks + banks

            def done(self, chunks=KC):
                return self.low, self.chunks + chunks

            def part(self, k):
                return bank[4 + k // 2][:, (k % 2) * SEQ:(k % 2) * SEQ + SEQ]

            def pe(self, pe, waits, banks=range(KC // 2)):
                for s, v in waits:
                    pe.wait_ge(s, v)
                for b in banks:
                    for kk in range(2):
                        for t in range(NT):
                            at = kk * SEQ + t * P
                            tr = nc.tensor.transpose(bank[4 + b][:, at:at + P], self.src[:, t, :, 2 * b + kk],
                                                     ident)
                    tr.then_inc(self.turned, 1)

            def act(self, act, used, chunks=range(KC)):
                wait_from(act, quarter_done, used)
                for k in chunks:
                    if k % 2 == 0:
                        act.wait_ge(*self.written(k // 2 + 1))
                    scale = 1.0 if self.gain is None else self.gain[:, k:k + 1]
                    nc.scalar.activation(self.hi[:, k, :], self.part(k), ACT.Copy if self.gain is None else ACT.Identity,
                                         scale=scale).then_inc(self.high, 1)

            def dve(self, dve, chunks=range(KC)):
                for k in chunks:
                    dve.wait_ge(self.high, self.chunks + 2 * (k // 2) + 2)
                    hi = self.hi[:, k, :].bitcast(F32)
                    if self.gain is None:
                        ins = nc.vector.tensor_tensor(self.lo[:, k, :], self.part(k), hi, ALU.subtract)
                    else:
                        ins = nc.vector.scalar_tensor_tensor(out=self.lo[:, k, :], in0=self.part(k),
                                                             scalar=self.gain[:, k:k + 1], in1=hi,
                                                             op0=ALU.mult, op1=ALU.subtract)
                    ins.then_inc(self.low, 1)

        class RmsNorm:
            squared, mean, root, normed = sem("rms_squared"), sem("rms_mean"), sem("rms_root"), sem("rms_normed")
            index = squares = 0

            def __init__(self, src, xn, stat, parts=1):
                self.src, self.xn, self.stat, self.parts = src, xn, stat, parts
                self.before = RmsNorm.index
                RmsNorm.index += 1
                RmsNorm.squares += NT * parts
                self.all_squared = RmsNorm.squares

            def ready(self, tiles=NT):
                return self.normed, NT * self.before + tiles

            def act_table(self, act):
                nc.scalar.activation(early[:, self.before:self.before + 1],
                                     ident[:, 0:1] if self.before else early[:, 0:1], ACT.Sqrt)

            def act_squares(self, act, part, ready):
                f = slice(part * D // self.parts, (part + 1) * D // self.parts)
                for t in range(NT):
                    act.wait_ge(*ready(t))
                    at = NT * part + t
                    nc.scalar.activation(self.xn[:, t, f], self.src[:, t, f], ACT.Square,
                                         accum_out=self.stat[:, at:at + 1]).then_inc(self.squared, 1)

            def act_root(self, act):
                act.wait_ge(self.mean, self.before + 1)
                nc.scalar.activation(self.stat[:, 0:NT], self.stat[:, 0:NT], ACT.Sqrt).then_inc(self.root, 1)

            def act(self, act, ready):
                self.act_table(act)
                for part in range(self.parts):
                    self.act_squares(act, part, lambda t: ready(part, t))
                self.act_root(act)

            def dve(self, dve, order, gain=None):
                dve.wait_ge(self.squared, self.all_squared)
                if self.parts == 2:
                    order.step(nc.vector.tensor_tensor(self.stat[:, 0:NT], self.stat[:, 0:NT], self.stat[:, NT:2 * NT],
                                                       ALU.add))
                nc.vector.tensor_scalar(self.stat[:, 0:NT], self.stat[:, 0:NT], 1.0 / D, EPS,
                                        ALU.mult, ALU.add).then_inc(self.mean, 1)
                dve.wait_ge(self.root, self.before + 1)
                order.step(nc.vector.reciprocal(self.stat[:, 0:NT], self.stat[:, 0:NT]))
                for t in range(NT):
                    if gain is None:
                        ins = nc.vector.tensor_scalar(self.xn[:, t, :], self.src[:, t, :], self.stat[:, t:t + 1], None,
                                                      ALU.mult)
                    else:
                        ins = nc.vector.scalar_tensor_tensor(out=self.src[:, t, :], in0=self.src[:, t, :],
                                                             scalar=self.stat[:, t:t + 1], in1=gain, op0=ALU.mult,
                                                             op1=ALU.mult)
                    ins.then_inc(self.normed, 1)

        def gain(name):
            return cols[:, NORMS.index(name), :]

        xn = carve(0, NT, D)
        stat = tiny(0, 8)
        early = tiny(346, 10)
        norm_a = RmsNorm(xres, xn, stat)
        turn_a = Turn(xn, gain("attn_norm_w"), t0h, t0l)
        evac_in = sem("evac_in")

        y = carve(0, NT, D)
        xbcT = carve(2048, XCH, PAD + SEQ)
        convT = carve(2048 + 2590, XCH, SEQ)
        xdt = carve(7198, NT, D)
        xdtd = carve(9246, D)
        dif = carve(10270, NT, 4, P)
        mt = carve(11294, NT, 4, P)
        prevT = carve(12318, 512)
        cbm = carve(12830, 4, P)
        btok = carve(13342, P)
        xs = proj[:, :, C_XBC:C_XBC + D]
        cwT = tiny(8, 50)
        dtb, alog, dsk = tiny(58, 16), tiny(74, 16), tiny(90, 16)
        s_raw, s_neg, s_exp, s_u = (tiny(106 + 32 * j, NT, 16) for j in range(4))
        dt, dA = tiny(234, NT, 16), tiny(266, NT, 16)
        ecum = tiny(298, NT, 16)
        edec = tiny(330, 16)
        acum = dif[:, 0, 0, 0:64].rearrange("p (t a h) -> p t a h", t=NT, a=2)
        rows = carve(13470, P)
        cum = carve(13598, NT, 2, 16)
        xbc_turned, xbc_copied = sem("xbc_turned"), sem("xbc_copied")
        taps_turned, taps_ready = sem("taps_turned"), sem("taps_ready")
        conv_done, conv_active = sem("conv_done"), sem("conv_active")
        x_back, x_split, cb_done = sem("x_back"), sem("x_split"), sem("cb_done")
        dt_arg, dt_exp, dt_ln_arg, dt_ln = sem("dt_arg"), sem("dt_exp"), sem("dt_ln_arg"), sem("dt_ln")
        dA_ready, cum_done, cum_ready, dec_arg, dec_ready = (
            sem(s) for s in ("dA_ready", "cum_done", "cum_ready", "dec_arg", "dec_ready"))
        xdt_ready, state_done, state_ready, off_done = (
            sem(s) for s in ("xdt_ready", "state_done", "state_ready", "off_done"))
        abc_done, dif_ready, lmat_ready, mt_ready, diag_done, y_ready = (
            sem(s) for s in ("abc_done", "dif_ready", "lmat_ready", "mt_ready", "diag_done", "y_ready"))
        z_active, gate_active, y_gated, y_squared, y_normed = (
            sem(s) for s in ("z_active", "gate_active", "y_gated", "y_squared", "y_normed"))
        y_mean, y_root = sem("y_mean"), sem("y_root")
        turn_y = Turn(y, gain("ssd_norm_w"), t0h, t0l)
        ssd_merged = sem("ssd_merged")

        yatt = carve(0, NT, D)
        cosb, sinb, ang, tr1 = (carve(2048 + 64 * j, NT, 32) for j in range(4))
        rot = [carve(2304 + 512 * x, 2, NT, P) for x in range(2)]
        rtmp = [carve(3328 + 128 * x, NT, 2, 32) for x in range(2)]
        qkT = [carve(3584 + 512 * x, 4, P) for x in range(2)]
        sc = [carve(4608 + 384 * x, 384) for x in range(4)]
        pT = [carve(6144 + 384 * x, 384) for x in range(4)]
        posf = tiny(0, NT)
        amax, asum = tiny(2, 4, 2), tiny(10, 2, 2, 2)
        posi = sb("posi", [P, NT], I32)
        pos_loaded = sem("pos_loaded")
        sin_arg, sin_done = sem("sin_arg"), sem("sin_done")
        rot_ready, qk_turned, qk_copied, scored, maxed, exped, p_turned, p_copied, pv_done, att_ready = (
            sem(s) for s in ("rot_ready", "qk_turned", "qk_copied", "scored", "maxed", "exped", "p_turned",
                             "p_copied", "pv_done", "att_ready"))
        turn_att = Turn(yatt, None, t0h, t0l)
        merged = proj[:, :, C_GS:C_GS + D]
        att_merged = sem("att_merged")
        turn_m = Turn(merged, None, t0h, t0l)
        mixed = sem("mixed")

        PAIRS = NH // 2

        TILES1 = [2, 3, 4, 0, 1] + list(range(5, IN_T))
        XBC_TILES, Z_TILES = 3, 5

        def in_views(q, j):
            v = A["w_in"][0].rearrange("(p k) n -> p k n", k=KC)
            return v[:, 2 * q:2 * q + 2, IN_TW * j:IN_TW * (j + 1)]

        def sp_block1(sp):
            sp.dma_start(xres[:, :, :], A["x"][0].rearrange("(t p) n -> p t n", p=P)).then_inc(x_loaded, 16)
            for p, j in enumerate(TILES1):
                for q in range(4):
                    n = Q_IN + 4 * p + q
                    load(sp, n, [(pair_view(raw, n, IN_TW), in_views(q, j))])
            load_square(sp, Q_SSD, A["w_ssd_out"][0])
            load_square(sp, Q_ATT, A["w_attn_out"][0])
            load_square(sp, Q_OUT, A["w_out"][0])

        def row(ap, n):
            return ap.rearrange("(a n) -> a n", a=1).to_broadcast([P, n])

        def act_loads(act):
            act.dma_start(const[:, :], A["const"]).then_inc(consts_loaded, 16)
            act.dma_start(cols[:, 0, :], A[NORMS[0]][0].rearrange("(p k) -> p k", k=KC)).then_inc(consts_loaded, 16)

        def act_vectors(act):
            for j, name in enumerate(NORMS[1:]):
                act.dma_start(cols[:, 1 + j, :], A[name][0].rearrange("(p k) -> p k", k=KC)).then_inc(vec_loaded, 16)
            act.dma_start(rows[0:40, :], A["conv_w"][0].rearrange("w (k p) -> (w k) p", p=P)).then_inc(vec_loaded, 16)
            act.dma_start(rows[40:50, :], A["conv_b"][0].rearrange("(k p) -> k p", p=P)).then_inc(vec_loaded, 16)
            for dst, name in ((dtb, "dt_bias"), (alog, "a_log"), (dsk, "d_skip")):
                act.dma_start(dst, row(A[name][0], NH)).then_inc(vec_loaded, 16)
            act.dma_start(mul[:, :, :], A["mu_lora_2"][0].rearrange("a (p k) -> p a k", k=KC)).then_inc(vec_loaded, 16)
            with nc.allow_non_contiguous_dma(reason="256 positions, one per partition"):
                act.dma_start(posi[:, :], A["positions"][0].rearrange("(t p) -> p t", p=P)).then_inc(pos_loaded, 16)

        N_VEC = 16 * (len(NORMS) + 5)

        def pool_stream(pool):
            with pool.Fori(0, IN_T) as j:
                for q in range(4):
                    split_low(pool, q, j, 4, 2 * IN_TW)
            with pool.Fori(0, (Q_ATT + 4 - Q_SSD) // 4) as j:
                for q in range(4):
                    split_low(pool, Q_SSD + q, j, 4)
            pool_rotations(pool)
            for n in range(Q_ATT + 4, Q_MOE):
                if not split_by_vector(n):
                    split_low(pool, n)
            with pool.Fori(0, (Q_PLE - Q_MOE) // U) as j:
                for q in range(0, U, 2):
                    split_low(pool, Q_MOE + q, j, U)
            ahead = Q_RWKV + RING
            with pool.Fori(0, (ahead - Q_PLE) // 4) as j:
                for q in range(4):
                    split_low(pool, Q_PLE + q, j, 4)
            for n in range(ahead - (ahead - Q_PLE) % 4, ahead):
                split_low(pool, n)
            pool_heads(pool)
            with pool.Fori(0, (Q_END - ahead) // 4) as j:
                for q in range(4):
                    split_low(pool, ahead + q, j, 4)

        def pe_in(pe):
            pe.wait_ge(consts_loaded, 32)
            turn_a.pe(pe, [norm_a.ready()])
            pe.wait_ge(*turn_a.done())

            def tile(p):
                wait_from(pe, evac_in, NT * (p - 1))
                for q in range(4):
                    wide_quarter(pe, Q_IN + 4 * p + q, q, bank[2 * (p % 2):2 * (p % 2) + 2], t0h, t0l, IN_TW)

            between = {3: [pe_xbc], 6: [pe_sums_of_decay, pe_x_back], 7: [pe_cb], 8: [pe_state], 9: [pe_off]}
            for p in range(IN_T):
                tile(p)
                for part in between.get(p, ()):
                    part(pe)
                if 9 <= p < 13:
                    pe_sums(pe, p - 9)
                if 10 <= p < 14:
                    pe_diagonal(pe, p - 10)
            turn_y.pe(pe, [(y_normed, 4)])
            square_product(pe, Q_SSD, t0h, t0l, [(evac_in, NT * IN_T)], turn_y)

        def act_in(act):
            for q in range(2, 4):
                split_high(act, Q_IN + q, width=2 * IN_TW)
            act_vectors(act)

            def evac(p):
                act.wait_ge(quarter_done, Q_IN + 4 * p + 4)
                c = IN_TW * TILES1[p]
                for t in range(NT):
                    nc.scalar.copy(proj[:, t, c:c + IN_TW], bank[2 * (p % 2) + t][:, 0:IN_TW]).then_inc(evac_in, 1)

            between = {3: [act_dt_exp], 5: [act_dt_ln, act_conv_silu], 6: [act_z], 7: [act_decays], 8: [act_angles], 13: [act_squares]}
            for p in range(1, IN_T):
                for q in range(4):
                    split_high(act, Q_IN + 4 * p + q, width=2 * IN_TW)
                evac(p - 1)
                for part in between.get(p - 1, ()):
                    part(act)
                if 9 <= p - 1 < 13:
                    act_lmat(act, p - 10)
            for q in range(4):
                split_high(act, Q_SSD + q)
            evac(IN_T - 1)
            act_after_in(act)

        def pe_xbc(pe):
            pe.wait_ge(evac_in, NT * XBC_TILES)
            pe.wait_ge(vec_loaded, N_VEC)
            pe.wait_ge(*turn_a.done())
            for b in range(XCH // 2):
                if b == 4:
                    pe.wait_ge(xbc_copied, 1)
                for kk in range(2):
                    for t in range(NT):
                        c = C_XBC + (2 * b + kk) * P
                        tr = nc.tensor.transpose(bank[4 + b % 4][:, kk * SEQ + t * P:kk * SEQ + (t + 1) * P],
                                                 proj[:, t, c:c + P], ident)
                tr.then_inc(xbc_turned, 1)
            pe.wait_ge(xbc_copied, 2)
            nc.tensor.transpose(bank[5][:, 0:50], rows[0:50, :], ident[0:50, 0:50]).then_inc(taps_turned, 1)

        def pe_sums_of_decay(pe):
            pe.wait_ge(dA_ready, 1)
            pe.wait_ge(xbc_copied, XCH // 2)
            for t in range(NT):
                nc.tensor.matmul(bank[6][:, 32 * t:32 * t + 16], con("tri"), dA[:, t, :], start=True, stop=True)
                mm = nc.tensor.matmul(bank[6][:, 32 * t + 16:32 * t + 32], con("ones"), dA[:, t, :],
                                      start=True, stop=True)
            mm.then_inc(cum_done, 1)

        def pe_x_back(pe):
            pe.wait_ge(conv_active, XCH)
            pe.wait_ge(taps_ready, 1)
            pe.wait_ge(cum_ready, 1)
            for t in range(NT):
                for h in range(2):
                    for c in range(4):
                        tr = nc.tensor.transpose(bank[4 + 2 * t + h][:, c * P:(c + 1) * P],
                                                 convT[:, 4 * h + c, t * P:(t + 1) * P], ident)
                    tr.then_inc(x_back, 1)

        def pe_cb(pe):
            pe.wait_ge(x_split, 2 * NT)
            nc.tensor.transpose(bank[4][:, 0:P], convT[:, 8, 0:P], ident)
            for g in range(2):
                for t in range(NT):
                    mm = nc.tensor.matmul(bank[5 + g][:, (1 + t) * P:(2 + t) * P],
                                          convT[64 * g:64 * g + 64, 8, t * P:(t + 1) * P],
                                          convT[64 * g:64 * g + 64, 9, t * P:(t + 1) * P], start=True, stop=True)
            mm.then_inc(cb_done, 1)

        def pe_state(pe):
            pe.wait_ge(xdt_ready, 1)
            for g in range(2):
                mm = nc.tensor.matmul(bank[7][64 * g:64 * g + 64, :], btok[:, 64 * g:64 * g + 64],
                                      xdtd[:, 512 * g:512 * g + 512], start=True, stop=True)
            mm.then_inc(state_done, 1)

        def pe_off(pe):
            pe.wait_ge(state_ready, 1)
            for g in range(2):
                mm = nc.tensor.matmul(bank[4 + g][:, :], convT[64 * g:64 * g + 64, 9, P:2 * P],
                                      prevT[64 * g:64 * g + 64, :], start=True, stop=True)
            mm.then_inc(off_done, 1)

        def pe_sums(pe, q):
            for t in range(NT):
                wait_from(pe, dif_ready, 2 * (q - 1) + t + 1)
                for h in range(4):
                    e = 4 * q + h
                    mm = nc.tensor.matmul(bank[6 + t][:, h * P:(h + 1) * P],
                                          dA[:, t, e:e + 1].to_broadcast([P, P]), con("tri"),
                                          start=True, stop=True)
                mm.then_inc(abc_done, 1)

        def pe_diagonal(pe, q):
            for t in range(NT):
                pe.wait_ge(mt_ready, 2 * q + t + 1)
                wait_from(pe, y_ready, 2 * (q - 1) + t + 1)
                for h in range(4):
                    e = 4 * q + h
                    mm = nc.tensor.matmul(bank[4 + t][:, h * DH:(h + 1) * DH], mt[:, t, h, :],
                                          xdt[:, t, e * DH:(e + 1) * DH], start=True, stop=True)
                mm.then_inc(diag_done, 1)

        def dve_ssd(dve, order):
            dve.wait_ge(vec_loaded, N_VEC)
            dve.wait_ge(evac_in, NT * XBC_TILES)
            order.mark(nc.vector.memset(xbcT[:, :, 0:PAD], 0.0))
            order.step(nc.vector.tensor_tensor(s_raw, proj[:, :, C_DT:C_DT + NH],
                                               dtb.unsqueeze(1).to_broadcast([P, NT, NH]), ALU.add))
            nc.vector.scalar_tensor_tensor(out=s_neg, in0=s_raw, scalar=-1.0, in1=s_raw, op0=ALU.mult,
                                           op1=ALU.min).then_inc(dt_arg, 1)
            for b in range(XCH // 2):
                dve.wait_ge(xbc_turned, b + 1)
                src = bank[4 + b % 4][:, :].rearrange("p (k s) -> p k s", k=2)
                nc.vector.tensor_copy(xbcT[:, 2 * b:2 * b + 2, PAD:PAD + SEQ], src).then_inc(xbc_copied, 1)
            dve.wait_ge(taps_turned, 1)
            nc.vector.tensor_copy(cwT, bank[5][:, 0:50]).then_inc(taps_ready, 1)
            dve.wait_ge(xbc_copied, XCH // 2)
            dve.wait_ge(taps_ready, 1)
            for w in range(4):
                for c in range(XCH):
                    tap = cwT[:, w * XCH + c:w * XCH + c + 1]
                    if w == 0:
                        order.mark(nc.vector.tensor_scalar(convT[:, c, :], xbcT[:, c, 0:SEQ], tap, None, ALU.mult))
                    else:
                        ins = nc.vector.scalar_tensor_tensor(out=convT[:, c, :], in0=xbcT[:, c, w:w + SEQ], scalar=tap,
                                                             in1=convT[:, c, :], op0=ALU.mult, op1=ALU.add)
                        if w < 3:
                            order.mark(ins)
                        else:
                            ins.then_inc(conv_done, 1)
                order.settle()
            dve.wait_ge(dt_exp, 2)
            order.step(nc.vector.tensor_scalar(s_u, s_exp, 1.0, None, ALU.add))
            order.step(nc.vector.tensor_scalar(dt, s_u, 1.0, None, ALU.subtract))
            order.mark(nc.vector.reciprocal(dA, s_u))
            order.step(nc.vector.tensor_tensor(dt, s_exp, dt, ALU.subtract))
            nc.vector.tensor_tensor(dt, dt, dA, ALU.mult).then_inc(dt_ln_arg, 1)
            dve.wait_ge(dt_ln_arg, 1)
            dve.wait_ge(dt_ln, 1)
            order.step(nc.vector.tensor_tensor(dt, dt, s_neg, ALU.add))
            order.step(nc.vector.scalar_tensor_tensor(out=dt, in0=s_raw, scalar=0.0, in1=dt, op0=ALU.max, op1=ALU.add))
            nc.vector.scalar_tensor_tensor(out=dA, in0=dt, scalar=-1.0,
                                           in1=alog.unsqueeze(1).to_broadcast([P, NT, NH]),
                                           op0=ALU.mult, op1=ALU.mult).then_inc(dA_ready, 1)
            dve_angles(dve, order)
            dve.wait_ge(cum_done, 1)
            nc.vector.tensor_copy(cum, bank[6][:, 0:64].rearrange("p (t a h) -> p t a h", t=NT, a=2)).then_inc(cum_ready, 1)
            dve.wait_ge(cum_ready, 1)
            nc.vector.tensor_tensor(edec, cum[:, 0, 1, :], cum[:, 0, 0, :], ALU.subtract).then_inc(dec_arg, 1)
            for t in range(NT):
                for h in range(2):
                    dve.wait_ge(x_back, 2 * t + h + 1)
                    src = bank[4 + 2 * t + h]
                    order.mark(nc.vector.tensor_copy(xs[:, t, 512 * h:512 * h + 512], src[:, :]))
                    nc.vector.tensor_tensor(
                        xdt[:, t, 512 * h:512 * h + 512].rearrange("p (e d) -> p e d", d=DH),
                        src[:, :].rearrange("p (e d) -> p e d", d=DH),
                        dt[:, t, 8 * h:8 * h + 8].unsqueeze(2).to_broadcast([P, 8, DH]), ALU.mult).then_inc(x_split, 1)
            dve.wait_ge(cb_done, 1)
            order.mark(nc.vector.tensor_copy(btok, bank[4][:, 0:P]))
            for g in range(2):
                order.mark(nc.vector.tensor_tensor(cbm[:, 2 * g:2 * g + 2, :],
                                                   bank[5 + g][:, P:3 * P].rearrange("p (a l) -> p a l", a=2),
                                                   con("tri").unsqueeze(1).to_broadcast([P, 2, P]), ALU.mult))
            order.settle()
            dve.wait_ge(dec_ready, 2)
            nc.vector.tensor_tensor(xdtd.rearrange("p (e d) -> p e d", d=DH),
                                    xdt[:, 0, :].rearrange("p (e d) -> p e d", d=DH),
                                    edec.unsqueeze(2).to_broadcast([P, NH, DH]), ALU.mult).then_inc(xdt_ready, 1)
            dve.wait_ge(state_done, 1)
            nc.vector.tensor_copy(prevT, bank[7][:, :]).then_inc(state_ready, 1)
            for t in range(NT):
                order.mark(nc.vector.tensor_tensor(y[:, t, :].rearrange("p (e d) -> p e d", d=DH),
                                                   xs[:, t, :].rearrange("p (e d) -> p e d", d=DH),
                                                   dsk.unsqueeze(2).to_broadcast([P, NH, DH]), ALU.mult))
            dve.wait_ge(off_done, 1)
            for g in range(2):
                order.mark(nc.vector.tensor_tensor(xdtd[:, 512 * g:512 * g + 512].rearrange("p (e d) -> p e d", d=DH),
                                                   bank[4 + g][:, :].rearrange("p (e d) -> p e d", d=DH),
                                                   ecum[:, 1, 8 * g:8 * g + 8].unsqueeze(2).to_broadcast([P, 8, DH]),
                                                   ALU.mult))
            order.settle()
            order.step(nc.vector.tensor_tensor(y[:, 1, :], y[:, 1, :], xdtd, ALU.add))

            def differences(q):
                for t in range(NT):
                    dve.wait_ge(abc_done, 2 * q + t + 1)
                    wait_from(dve, mt_ready, 2 * (q - 1) + t + 1)
                    for h in range(4):
                        e = 4 * q + h
                        ins = nc.vector.tensor_scalar(dif[:, t, h, :], bank[6 + t][:, h * P:(h + 1) * P],
                                                      cum[:, t, 0, e:e + 1], 0.0, ALU.subtract, ALU.min)
                        if h < 3:
                            order.mark(ins)
                    ins.then_inc(dif_ready, 1)

            def add_diagonal(q):
                for t in range(NT):
                    dve.wait_ge(diag_done, 2 * q + t + 1)
                    o = y[:, t, 256 * q:256 * q + 256]
                    nc.vector.tensor_tensor(o, o, bank[4 + t][:, 0:256], ALU.add).then_inc(y_ready, 1)

            for q in range(4):
                differences(q)
                if q:
                    add_diagonal(q - 1)
                for t in range(NT):
                    dve.wait_ge(lmat_ready, 2 * q + t + 1)
                    nc.vector.tensor_tensor(mt[:, t], dif[:, t],
                                            cbm[:, 2 * (q // 2) + t, :].unsqueeze(1).to_broadcast([P, 4, P]),
                                            ALU.mult).then_inc(mt_ready, 1)
            add_diagonal(3)
            dve.wait_ge(z_active, NT)
            dve.wait_ge(y_ready, 8)
            for t in range(NT):
                nc.vector.tensor_tensor(y[:, t, :], y[:, t, :], proj[:, t, C_Z:C_Z + D], ALU.mult).then_inc(y_gated, 1)
            dve.wait_ge(y_squared, 4)
            nc.vector.tensor_scalar(stat[:, 0:4], stat[:, 0:4], 1.0 / 512, EPS, ALU.mult, ALU.add).then_inc(y_mean, 1)
            dve.wait_ge(y_root, 1)
            order.step(nc.vector.reciprocal(stat[:, 0:4], stat[:, 0:4]))
            for t in range(NT):
                for g in range(2):
                    o = y[:, t, 512 * g:512 * g + 512]
                    nc.vector.tensor_scalar(o, o, stat[:, 2 * t + g:2 * t + g + 1], None, ALU.mult).then_inc(y_normed, 1)
            turn_y.dve(dve)
            rotate(dve, nc.vector, order, 0)
            dve.wait_ge(gate_active, 4)
            for c in range(2):
                dve.wait_ge(quarter_done, Q_SSD + 4 * c + 4)
                for t in range(NT):
                    o = merged[:, t, c * TW:(c + 1) * TW]
                    nc.vector.tensor_tensor(o, o, bank[2 * c + t][:, :], ALU.mult).then_inc(ssd_merged, 1)

        def act_dt_exp(act):
            act.wait_ge(vec_loaded, N_VEC)
            act.wait_ge(dt_arg, 1)
            nc.scalar.activation(s_exp, s_neg, ACT.Exp).then_inc(dt_exp, 1)
            nc.scalar.activation(alog, alog, ACT.Exp).then_inc(dt_exp, 1)

        def act_dt_ln(act):
            act.wait_ge(dt_ln_arg, 1)
            nc.scalar.activation(s_neg, s_u, ACT.Ln).then_inc(dt_ln, 1)

        def act_conv_silu(act):
            for c in range(XCH):
                act.wait_ge(conv_done, c + 1)
                nc.scalar.activation(convT[:, c, :], convT[:, c, :], ACT.Silu,
                                     bias=cwT[:, 40 + c:41 + c]).then_inc(conv_active, 1)

        def act_z(act):
            act.wait_ge(evac_in, NT * Z_TILES)
            for t in range(NT):
                z = proj[:, t, C_Z:C_Z + D]
                nc.scalar.activation(z, z, ACT.Silu).then_inc(z_active, 1)

        def act_decays(act):
            act.wait_ge(cum_ready, 1)
            nc.scalar.activation(ecum, cum[:, :, 0, :], ACT.Exp).then_inc(dec_ready, 1)
            act.wait_ge(dec_arg, 1)
            nc.scalar.activation(edec, edec, ACT.Exp).then_inc(dec_ready, 1)

        def act_lmat(act, q):
            for t in range(NT):
                act.wait_ge(dif_ready, 2 * q + t + 1)
                nc.scalar.activation(dif[:, t], dif[:, t], ACT.Exp).then_inc(lmat_ready, 1)

        def act_squares(act):
            act.wait_ge(y_gated, NT)
            act.wait_ge(diag_done, 8)
            for t in range(NT):
                for g in range(2):
                    nc.scalar.activation(xdt[:, t, 512 * g:512 * g + 512], y[:, t, 512 * g:512 * g + 512], ACT.Square,
                                         accum_out=stat[:, 2 * t + g:2 * t + g + 1]).then_inc(y_squared, 1)
            act.wait_ge(y_mean, 1)
            nc.scalar.activation(stat[:, 0:4], stat[:, 0:4], ACT.Sqrt).then_inc(y_root, 1)

        def act_after_in(act):
            turn_y.act(act, Q_SSD)
            act.wait_ge(evac_in, NT * IN_T)
            for c in (C_GS, C_GA):
                for t in range(NT):
                    g = proj[:, t, c:c + D]
                    nc.scalar.activation(g, g, ACT.Sigmoid).then_inc(gate_active, 1)
            for q in range(4, 8):
                split_high(act, Q_SSD + q)
            for q in range(4):
                split_high(act, Q_ATT + q)

        def dve_angles(dve, order):
            dve.wait_ge(pos_loaded, 16)
            order.step(nc.vector.tensor_copy(posf, posi[:, :]))
            for t in range(NT):
                order.mark(nc.vector.tensor_scalar(ang[:, t, :], con("freq"), posf[:, t:t + 1], None, ALU.mult))
            order.settle()
            order.step(nc.vector.tensor_scalar(tr1, ang, 1.0 / TWO_PI, None, ALU.mult))
            order.step(nc.vector.tensor_scalar(tr1, tr1, 12582912.0, None, ALU.add))
            order.step(nc.vector.tensor_scalar(tr1, tr1, 12582912.0, None, ALU.subtract))
            c1 = 6.28125
            c2 = float(np.float32(np.round((TWO_PI - c1) * 2.0 ** 20) / 2.0 ** 20))
            c3 = TWO_PI - c1 - c2
            for c in (c1, c2, c3):
                order.step(nc.vector.scalar_tensor_tensor(out=ang, in0=tr1, scalar=-c, in1=ang, op0=ALU.mult, op1=ALU.add))
            top = float(np.nextafter(np.float32(math.pi), np.float32(0)))
            order.step(nc.vector.tensor_scalar(sinb, ang, top, -top, ALU.min, ALU.max))
            order.step(nc.vector.tensor_scalar(ang, ang, math.pi / 2, None, ALU.add))
            order.step(nc.vector.tensor_scalar(tr1, ang, math.pi, -TWO_PI, ALU.is_gt, ALU.mult))
            order.step(nc.vector.tensor_tensor(ang, ang, tr1, ALU.add))
            nc.vector.tensor_scalar(cosb, ang, top, -top, ALU.min, ALU.max).then_inc(sin_arg, 1)

        def act_angles(act):
            act.wait_ge(sin_arg, 1)
            nc.scalar.activation(sinb, sinb, ACT.Sin).then_inc(sin_done, 1)
            nc.scalar.activation(cosb, cosb, ACT.Sin).then_inc(sin_done, 1)

        ATT_DVE, ATT_POOL = 14, 22

        def rotate(eng, ops, order, i):
            if isinstance(i, int) and i == 0:
                eng.wait_ge(sin_done, 2)
                eng.wait_ge(evac_in, NT * IN_T)
            cos = cosb.unsqueeze(2).to_broadcast([P, NT, 2, 32])
            sin = sinb.unsqueeze(2).to_broadcast([P, NT, 2, 32])
            if not (isinstance(i, int) and i == 0):
                eng.wait_ge(qk_turned, 2 * i)
            for x in range(2):
                for a, c in ((0, C_Q), (1, C_K)):
                    src = proj[:, :, ds(c + P * (2 * i + x), P)].rearrange("p t (h a d) -> p t h a d", h=2, a=2)
                    x1, x2 = src[:, :, :, 0, :], src[:, :, :, 1, :]
                    dst = rot[x][:, a].rearrange("p t (h a d) -> p t h a d", h=2, a=2)
                    o1, o2 = dst[:, :, :, 0, :], dst[:, :, :, 1, :]
                    order.mark(ops.tensor_tensor(o1, x1, cos, ALU.mult))
                    order.mark(ops.tensor_tensor(rtmp[0], x2, sin, ALU.mult))
                    order.mark(ops.tensor_tensor(o2, x2, cos, ALU.mult))
                    order.step(ops.tensor_tensor(rtmp[1], x1, sin, ALU.mult))
                    order.mark(ops.tensor_tensor(o1, o1, rtmp[0], ALU.subtract))
                    last = ops.tensor_tensor(o2, o2, rtmp[1], ALU.add)
                    if a == 0:
                        order.step(last)
                last.then_inc(rot_ready, 1)
                eng.wait_ge(rot_ready, 2 * i + x + 1)

        def pool_rotations(pool):
            order = Order(pool, pool_order)
            with pool.Fori(0, PAIRS // 2 - 1) as i:
                order.body(0, i, ATT_POOL)
                rotate(pool, nc.gpsimd, order, i + 1)
            order.after(0, PAIRS // 2 - 1, ATT_POOL)

        def dve_attention(dve, order):
            def step(i):
                for z in range(4):
                    dve.wait_ge(scored, 4 * i + z + 1)
                    order.step(nc.vector.tensor_tensor(sc[z], bank[2 + z][:, 0:384], con("amask"), ALU.add))
                    order.mark(nc.vector.tensor_reduce(amax[:, z, 0:1], sc[z][:, 0:P], AX.X, ALU.max))
                    order.step(nc.vector.tensor_reduce(amax[:, z, 1:2], sc[z][:, P:384], AX.X, ALU.max))
                    nc.vector.tensor_scalar(amax[:, z, :], amax[:, z, :], -(DH ** -0.5), None, ALU.mult).then_inc(maxed, 1)
                for x in range(2):
                    dve.wait_ge(pv_done, 2 * i + x + 1)
                    order.step(nc.vector.reciprocal(asum[:, x], asum[:, x]))
                    nc.vector.tensor_tensor(
                        yatt[:, :, ds(P * (2 * i + x), P)].rearrange("p t (h d) -> p t h d", h=2),
                        bank[x][:, 0:256].rearrange("p (h t d) -> p t h d", h=2, t=NT),
                        asum[:, x].unsqueeze(3).to_broadcast([P, NT, 2, DH]), ALU.mult).then_inc(att_ready, 1)

            step(0)
            start = order.count() - ATT_DVE
            with dve.Fori(1, PAIRS // 2) as i:
                order.body(start, i, ATT_DVE)
                step(i)
            order.after(start, PAIRS // 2, ATT_DVE)

            turn_att.dve(dve)
            for c in range(2):
                dve.wait_ge(quarter_done, Q_ATT + 4 * c + 4)
                for t in range(NT):
                    g = proj[:, t, C_GA + c * TW:C_GA + (c + 1) * TW]
                    order.step(nc.vector.tensor_tensor(g, g, bank[2 * c + t][:, :], ALU.mult))
                    o = merged[:, t, c * TW:(c + 1) * TW]
                    nc.vector.tensor_tensor(o, o, g, ALU.add).then_inc(att_merged, 1)
            split_low(dve, Q_OUT + 3)
            turn_m.dve(dve)
            for c in range(2):
                split_low(dve, Q_OUT + 5 + 2 * c)
                dve.wait_ge(quarter_done, Q_OUT + 4 * c + 4)
                for t in range(NT):
                    o = xres[:, t, c * TW:(c + 1) * TW]
                    nc.vector.tensor_tensor(o, o, bank[2 * c + t][:, :], ALU.add).then_inc(mixed, 1)

        def act_attention(act):
            def copy_qk(i):
                for x in range(2):
                    act.wait_ge(qk_turned, 2 * i + x + 1)
                    nc.scalar.copy(qkT[x].rearrange("p a s -> p (a s)"), bank[6 + x][:, :]).then_inc(qk_copied, 1)

            def step(i, more=True):
                for z in range(4):
                    act.wait_ge(maxed, 4 * i + z + 1)
                    wait_from(act, att_ready, 2 * i)
                    x, h = z // 2, z % 2
                    nc.scalar.activation(sc[z][:, 0:P], sc[z][:, 0:P], ACT.Exp, bias=amax[:, z, 0:1], scale=DH ** -0.5,
                                         accum_out=asum[:, x, 0, h:h + 1]).then_inc(exped, 1)
                    nc.scalar.activation(sc[z][:, P:384], sc[z][:, P:384], ACT.Exp, bias=amax[:, z, 1:2],
                                         scale=DH ** -0.5, accum_out=asum[:, x, 1, h:h + 1]).then_inc(exped, 1)
                for z in range(4):
                    act.wait_ge(p_turned, 4 * i + z + 1)
                    nc.scalar.copy(pT[z], bank[2 + z][:, 0:384]).then_inc(p_copied, 1)
                if more:
                    copy_qk(i + 1)

            copy_qk(0)
            step(0)
            with act.Fori(1, PAIRS // 2 - 1) as i:
                step(i)
            step(PAIRS // 2 - 1, more=False)
            turn_att.act(act, Q_ATT)
            for q in range(4, 8):
                split_high(act, Q_ATT + q)
            for q in range(4):
                split_high(act, Q_OUT + q)
            turn_m.act(act, Q_OUT)
            for q in range(4, 8):
                split_high(act, Q_OUT + q)

        def pe_attention(pe):
            def turn_qk(i):
                for x in range(2):
                    pe.wait_ge(rot_ready, 2 * i + x + 1)
                    for a in range(2):
                        for t in range(NT):
                            tr = nc.tensor.transpose(bank[6 + x][:, (2 * a + t) * P:(2 * a + t + 1) * P],
                                                     rot[x][:, a, t, :], ident)
                    tr.then_inc(qk_turned, 1)

            def step(i, more=True):
                for x in range(2):
                    pe.wait_ge(qk_copied, 2 * i + x + 1)
                    for h in range(2):
                        r = slice(64 * h, 64 * h + 64)
                        keys = qkT[x][r, 2:4, :].rearrange("p t s -> p (t s)")
                        b = bank[2 + 2 * x + h]
                        nc.tensor.matmul(b[:, 0:P], qkT[x][r, 0, :], keys[:, 0:P], start=True, stop=True)
                        nc.tensor.matmul(b[:, P:384], qkT[x][r, 1, :], keys, start=True, stop=True).then_inc(scored, 1)
                for z in range(4):
                    pe.wait_ge(exped, 8 * i + 2 * z + 2)
                    for blk in range(3):
                        tr = nc.tensor.transpose(bank[2 + z][:, blk * P:(blk + 1) * P], sc[z][:, blk * P:(blk + 1) * P],
                                                 ident)
                    tr.then_inc(p_turned, 1)
                for x in range(2):
                    wait_from(pe, att_ready, 2 * i)
                    for h in range(2):
                        z = 2 * x + h
                        pe.wait_ge(p_copied, 4 * i + z + 1)
                        c = C_V + P * (2 * i + x) + DH * h
                        o = bank[x][:, h * P:(h + 1) * P]
                        nc.tensor.matmul(o[:, 0:DH], pT[z][:, 0:P], proj[:, 0, ds(c, DH)], start=True, stop=True)
                        nc.tensor.matmul(o[:, DH:P], pT[z][:, P:2 * P], proj[:, 0, ds(c, DH)], start=True, stop=False)
                        mm = nc.tensor.matmul(o[:, DH:P], pT[z][:, 2 * P:384], proj[:, 1, ds(c, DH)], start=False, stop=True)
                    mm.then_inc(pv_done, 1)
                if more:
                    turn_qk(i + 1)

            turn_qk(0)
            pe.wait_ge(ssd_merged, 4)
            step(0)
            with pe.Fori(1, PAIRS // 2 - 1) as i:
                step(i)
            step(PAIRS // 2 - 1, more=False)
            turn_att.pe(pe, [(att_ready, PAIRS)])
            square_product(pe, Q_ATT, t0h, t0l, [], turn_att)
            turn_m.pe(pe, [(att_merged, 4)])
            square_product(pe, Q_OUT, t0h, t0l, [(att_merged, 4)], turn_m)


        pw = proj[:, :, :].rearrange("p t n -> p (t n)")

        def lay(at, *shape):
            n = int(np.prod(shape))
            assert at + n <= NT * IN_W
            v = pw[:, at:at + n]
            if len(shape) == 1:
                return v
            names = "abcd"[:len(shape)]
            return v.rearrange(f"p ({' '.join(names)}) -> p {' '.join(names)}", **dict(zip(names, shape)))

        NG, EG = 4, 8
        JOBS = NG + 1
        xgf = lay(0, KC, P)
        pick = lay(1024, JOBS, NT, P)
        back = lay(2304, JOBS, NT, P)
        ysum = lay(3840, D)
        sg = [lay(4864 + DE * x, DE) for x in range(2)]
        hid = [lay(5376 + DE * x, DE) for x in range(2)]
        comb = lay(5888, JOBS, EG)
        rw = lay(5928, KC, 36)
        rbias = lay(6216, 36)
        logit = lay(6252, NT, 36)
        one_g, key_g = lay(6324, NT, NG), lay(6332, NT, NG)
        key = lay(6340, NT, JOBS)
        eg = lay(6350, NT, NG, EG)
        el, one1, one2, tmp8 = (lay(6414 + 16 * j, NT, EG) for j in range(4))
        ew = lay(6478, NT, EG)
        r1 = [lay(6494 + 2 * j, NT) for j in range(8)]
        cnt, over = lay(6510, NG), lay(6514, NG)
        flagf = lay(6518, 2)
        flag = sb("flag", [P, 2], I32)
        rwh = sb("rwh", [P, KC, 36], F32R)
        rwl = sb("rwl", [P, KC, 36], F32R)
        zero = sb("zero", [P, P], F32R)
        emb = lay(6600, NT, DE)
        ple = lay(7112, NT, D)
        logit_t = lay(7112, SEQ)[0:36]
        fnw = lay(9160, D)
        sgate = lay(10184, NT, D)
        norm_m = RmsNorm(xres, xn, stat, 2)
        turn_e = Turn(xn, gain("moe_norm_w"), t0h, t0l)
        router_loaded, zeroed = sem("router_loaded"), sem("zeroed")
        rw_high, rw_low, logits_done, logits_copied = (
            sem(s) for s in ("rw_high", "rw_low", "logits_done", "logits_copied"))
        exp_arg, exp_done, group_ready, ranked, picked = (
            sem(s) for s in ("exp_arg", "exp_done", "group_ready", "ranked", "picked"))
        e2_arg, e2_done, weights_ready, combed, comb_ready, back_turned, back_ready = (
            sem(s) for s in ("e2_arg", "e2_done", "weights_ready", "combed", "comb_ready", "back_turned", "back_ready"))
        gathered, xg_raw, xg_high, xg_low = (sem(s) for s in ("gathered", "xg_raw", "xg_high", "xg_low"))
        silu_done, hid_ready, hid_turned, hid_high, hid_low = (
            sem(s) for s in ("silu_done", "hid_ready", "hid_turned", "hid_high", "hid_low"))
        ysum_ready, scattered, x_added = (sem(s) for s in ("ysum_ready", "scattered", "x_added"))
        flag_ready = sem("flag_ready")
        ov = {s: sem("over_" + s) for s in ("loaded", "up", "silu", "hid", "turned", "copied", "down", "summed",
                                            "zeroed", "scattered", "added")}

        def gu_loads(sp, n, e, q, u=0, per=0):
            pairs = []
            for j, name in enumerate(("w_exp_gate", "w_exp_up")):
                v = A[name][0].rearrange("g e (p k) n -> p (g e) k n", k=KC)[:, ds(e, 1), 2 * q:2 * q + 2, :]
                dst = raw_of(n)[:, 512 * j:512 * j + 512].rearrange("p (a k n) -> p a k n", a=1, k=2)
                pairs.append((dst, v))
            load(sp, n, pairs, u, per)

        def down_load(sp, n, e, c, u=0, per=0):
            v = A["w_exp_down"][0].rearrange("g e (p k) n -> p (g e) k n", k=2)[:, ds(e, 1), c:c + 1, :]
            load(sp, n, [(raw_of(n)[:, f:f + 512].rearrange("p (a k n) -> p a k n", a=1, k=1), v[:, :, :, f:f + 512])
                         for f in (0, 512)], u, per)

        U = 12

        def first_of(J):
            return Q_MOE + 4 + JOB * J

        def sp_experts(sp):
            def block(E, m, i=0, per=0):
                if not (isinstance(E, int) and E == N_EXP - 1):
                    for q in range(4):
                        gu_loads(sp, m + q, E + 1, q, i, per)
                    m += 4
                for c in range(2):
                    down_load(sp, m + c, E, c, i, per)

            for q in range(4):
                gu_loads(sp, Q_MOE + q, 0, q)
            sp.wait_ge(quarter_done, Q_OUT + 1)
            for J in range(NG):
                n = first_of(J)
                with sp.Fori(0, 3) as i:
                    for b in range(2):
                        block(EG * J + 2 * i + b, n + 6 * b, i, U)
                for e in (6, 7):
                    block(EG * J + e, n + 6 * e)

        def router_loads(act):
            act.wait_ge(att_merged, 4)
            v = A["w_router_group"][0].rearrange("(p k) n -> p k n", k=KC)
            act.dma_start(rw[:, :, 0:NG], v).then_inc(router_loaded, 16)
            v = A["w_router_expert"][0].rearrange("(p k) n -> p k n", k=KC)
            act.dma_start(rw[:, :, NG:36], v).then_inc(router_loaded, 16)
            act.dma_start(rbias[:, 0:NG], row(A["b_router_group"][0], NG)).then_inc(router_loaded, 16)
            act.dma_start(rbias[:, NG:36], row(A["b_router_expert"][0], 32)).then_inc(router_loaded, 16)
            act.dma_start(emb[:, :, :], A["p"][0, 0].rearrange("(t p) n -> p t n", p=P)).then_inc(router_loaded, 16)
            act.dma_start(fnw, row(A["final_norm_w"], D)).then_inc(router_loaded, 16)

        def act_router(act):
            act.wait_ge(router_loaded, 96)
            nc.scalar.activation(rwh[:, :, :], rw, ACT.Copy).then_inc(rw_high, 1)
            norm_m.act(act, lambda part, t: (mixed, NT * part + t + 1))
            turn_e.act(act, Q_MOE)
            for q in range(2):
                split_high(act, Q_MOE + q)
            act.wait_ge(logits_done, 1)
            nc.scalar.copy(logit_t, bank[2][0:36, 0:SEQ]).then_inc(logits_copied, 1)
            for q in range(2, 4):
                split_high(act, Q_MOE + q)
            act.wait_ge(exp_arg, 1)
            nc.scalar.activation(key_g, key_g, ACT.Exp).then_inc(exp_done, 1)
            act.wait_ge(e2_arg, 1)
            nc.scalar.activation(r1[4], r1[4], ACT.Exp).then_inc(e2_done, 1)

        def pe_router(pe):
            turn_e.pe(pe, [norm_m.ready(), (mixed, 4)])
            pe.wait_ge(rw_low, 1)
            for k in range(KC):
                pe.wait_ge(*turn_e.done(k + 1))
                mm = times(bank[2][0:36, 0:SEQ], rwh[:, k, :], rwl[:, k, :], t0h[:, k, :], t0l[:, k, :], k == 0,
                           k == KC - 1)
            mm.then_inc(logits_done, 1)
            pe.wait_ge(logits_copied, 1)
            for t in range(NT):
                tr = nc.tensor.transpose(bank[t][:, 0:36], logit_t[:, t * P:(t + 1) * P], ident[0:36, 0:36])
            tr.then_inc(logits_done, 1)
            pe.wait_ge(group_ready, 1)
            nc.tensor.matmul(bank[2][:, 0:NG], con("strict"), one_g[:, 0, :], start=True, stop=True)
            nc.tensor.matmul(bank[2][:, NG:2 * NG], con("strict"), one_g[:, 1, :], start=True, stop=False)
            nc.tensor.matmul(bank[2][:, NG:2 * NG], con("ones"), one_g[:, 0, :], start=False, stop=True)
            nc.tensor.matmul(bank[2][:, 2 * NG:3 * NG], con("ones"), one_g[:, 0, :], start=True, stop=False)
            nc.tensor.matmul(bank[2][:, 2 * NG:3 * NG], con("ones"), one_g[:, 1, :], start=False, stop=True
                             ).then_inc(ranked, 1)
            pe.wait_ge(picked, 1)
            pe_gather(0)
            for j in range(JOBS):
                for t in range(NT):
                    at = (j % 2) * SEQ + t * P
                    tr = nc.tensor.transpose(bank[(0, 1, 3)[j // 2]][:, at:at + P], pick[:, j, t, :], ident)
            tr.then_inc(back_turned, 1)
            pe.wait_ge(weights_ready, 1)
            for j in range(JOBS):
                for t in range(NT):
                    mm = nc.tensor.matmul(bank[2][:, 16 + EG * j:16 + EG * (j + 1)], pick[:, j, t, :], ew[:, t, :],
                                          start=t == 0, stop=t == NT - 1)
            mm.then_inc(combed, 1)

        def dve_router(dve, order):
            dve.wait_ge(rw_high, 1)
            nc.vector.tensor_tensor(rwl[:, :, :], rw, rwh[:, :, :].bitcast(F32), ALU.subtract).then_inc(rw_low, 1)
            norm_m.dve(dve, order)
            turn_e.dve(dve)
            nc.vector.memset(zero[:, :].bitcast(F32), 0.0).then_inc(zeroed, 1)
            for q in (1, 3):
                split_low(dve, Q_MOE + q)
            dve.wait_ge(logits_done, 2)
            for t in range(NT):
                order.mark(nc.vector.tensor_tensor(logit[:, t, :], bank[t][:, 0:36], rbias, ALU.add))
            order.settle()
            gl = logit[:, :, 0:NG]
            ex = logit[:, :, NG:36].rearrange("p t (g e) -> p t g e", g=NG)

            def wide(v, n):
                return v.unsqueeze(2).to_broadcast([P, NT, n])

            def first_max(hot, val, top, tmp, rev, n):
                order.step(nc.vector.tensor_reduce(top, val, AX.X, ALU.max))
                order.step(nc.vector.tensor_tensor(tmp, val, wide(top, n), ALU.is_equal))
                order.step(nc.vector.tensor_tensor(tmp, tmp, con(rev).unsqueeze(1).to_broadcast([P, NT, n]), ALU.mult))
                order.step(nc.vector.tensor_reduce(r1[7], tmp, AX.X, ALU.max))
                order.step(nc.vector.tensor_tensor(hot, tmp, wide(r1[7], n), ALU.is_equal))

            first_max(one_g, gl, r1[0], key_g, "rev4", NG)
            nc.vector.tensor_tensor(key_g, gl, wide(r1[0], NG), ALU.subtract).then_inc(exp_arg, 1)
            order.step(nc.vector.tensor_tensor(eg, ex, one_g.unsqueeze(3).to_broadcast([P, NT, NG, EG]), ALU.mult))
            nc.vector.tensor_reduce(el, eg.rearrange("p t g e -> p t e g"), AX.X, ALU.add).then_inc(group_ready, 1)
            dve.wait_ge(group_ready, 1)
            first_max(one1, el, r1[1], tmp8, "rev8", EG)
            order.step(nc.vector.scalar_tensor_tensor(out=el, in0=one1, scalar=-3e38, in1=el, op0=ALU.mult, op1=ALU.add))
            first_max(one2, el, r1[2], tmp8, "rev8", EG)
            nc.vector.tensor_tensor(r1[4], r1[2], r1[1], ALU.subtract).then_inc(e2_arg, 1)
            dve.wait_ge(ranked, 1)
            dve.wait_ge(exp_done, 1)
            order.step(nc.vector.tensor_reduce(r1[3], key_g, AX.X, ALU.add))
            order.mark(nc.vector.reciprocal(r1[3], r1[3]))
            order.mark(nc.vector.tensor_copy(cnt, bank[2][:, 2 * NG:3 * NG]))
            order.step(nc.vector.scalar_tensor_tensor(out=key_g, in0=bank[2][:, 0:2 * NG].rearrange("p (t g) -> p t g", t=NT),
                                                      scalar=1.0, in1=one_g, op0=ALU.add, op1=ALU.mult))
            order.mark(nc.vector.tensor_reduce(key[:, :, NG], key_g, AX.X, ALU.add))
            order.step(nc.vector.tensor_scalar(key[:, :, 0:NG], key_g, 1.0, None, ALU.subtract))
            order.step(nc.vector.tensor_scalar(key[:, :, NG], key[:, :, NG], float(P + 1), None, ALU.subtract))
            for j in range(JOBS):
                for t in range(NT):
                    ins = nc.vector.tensor_scalar(pick[:, j, t, :], con("slot"), key[:, t, j:j + 1], None, ALU.is_equal)
                    if (j, t) != (JOBS - 1, NT - 1):
                        order.mark(ins)
            ins.then_inc(picked, 1)
            dve.wait_ge(e2_done, 1)
            order.step(nc.vector.tensor_scalar(r1[5], r1[4], 1.0, None, ALU.add))
            order.step(nc.vector.reciprocal(r1[5], r1[5]))
            order.step(nc.vector.tensor_tensor(r1[5], r1[5], r1[3], ALU.mult))
            order.mark(nc.vector.tensor_tensor(r1[6], r1[5], r1[4], ALU.mult))
            order.step(nc.vector.tensor_tensor(ew, one1, wide(r1[5], EG), ALU.mult))
            order.step(nc.vector.tensor_tensor(tmp8, one2, wide(r1[6], EG), ALU.mult))
            nc.vector.tensor_tensor(ew, ew, tmp8, ALU.add).then_inc(weights_ready, 1)
            order.step(nc.vector.tensor_scalar(over, cnt, P + 0.5, None, ALU.is_gt))
            order.mark(nc.vector.tensor_reduce(flagf[:, 0:1], over, AX.X, ALU.max))
            order.step(nc.vector.tensor_scalar(cnt, con("rev4"), -1.0, float(NG), ALU.mult, ALU.add))
            order.step(nc.vector.tensor_tensor(cnt, cnt, over, ALU.mult))
            order.step(nc.vector.tensor_reduce(flagf[:, 1:2], cnt, AX.X, ALU.add))
            nc.vector.tensor_copy(flag[:, :], flagf).then_inc(flag_ready, 1)
            dve_gather(dve, 0)
            dve.wait_ge(back_turned, 1)
            for j in range(0, JOBS, 2):
                n = min(2, JOBS - j)
                order.mark(nc.vector.tensor_copy(back[:, j:j + n].rearrange("p j t s -> p (j t s)"),
                                                 bank[(0, 1, 3)[j // 2]][:, 0:n * SEQ]))
            nc.vector.tensor_copy(logit[:, 0, 0:1], flagf[:, 0:1]).then_inc(back_ready, 1)
            dve.wait_ge(combed, 1)
            nc.vector.tensor_copy(comb.rearrange("p j e -> p (j e)"), bank[2][:, 16:16 + EG * JOBS]).then_inc(comb_ready, 1)
            for b in range(2):
                nc.vector.memset(hid[b], 0.0).then_inc(hid_ready, 1)
            dve.wait_ge(hid_ready, 2)

        def pe_gather(J):
            for b in range(2):
                for kk in range(4):
                    for t in range(NT):
                        mm = nc.tensor.matmul(bank[6 + b][:, kk * P:(kk + 1) * P],
                                              xn.rearrange("p t (f k) -> p t f k", k=KC)[:, t, :, 4 * b + kk],
                                              pick[:, ds(J, 1), t, :].rearrange("p a s -> p (a s)"),
                                              start=t == 0, stop=t == NT - 1)
                mm.then_inc(gathered, 1)

        def dve_gather(dve, J):
            g = gain("moe_norm_w")
            for b in range(2):
                dve.wait_ge(gathered, 2 * J + b + 1)
                nc.vector.tensor_tensor(xgf[:, 4 * b:4 * b + 4, :], bank[6 + b][:, :].rearrange("p (k s) -> p k s", k=4),
                                        g[:, 4 * b:4 * b + 4].unsqueeze(2).to_broadcast([P, 4, P]),
                                        ALU.mult).then_inc(xg_raw, 1)

        def act_gather(act, J, par):
            act.wait_ge(xg_raw, 2 * J + 2)
            nc.scalar.activation(t0h[:, :, par * P:(par + 1) * P], xgf, ACT.Copy).then_inc(xg_high, 1)

        def dve_gather_low(dve, J, par):
            dve.wait_ge(xg_high, J + 1)
            s = slice(par * P, (par + 1) * P)
            nc.vector.tensor_tensor(t0l[:, :, s], xgf, t0h[:, :, s].bitcast(F32), ALU.subtract).then_inc(xg_low, 1)

        def pe_experts(pe):
            pe.wait_ge(zeroed, 1)

            def gate_up(n, q, E, e_par, par, u, per):
                if q == 0:
                    pe.wait_ge(hid_ready, E + 1)
                wait_low(pe, n, u, per)
                s = n % RING
                wh, wl = (w[:, s, :].rearrange("p (a k n) -> p a k n", a=2, k=2) for w in (whi, wlo))
                dst = bank[e_par][:, :].rearrange("p (a n) -> p a n", a=2)
                r = slice(par * P, (par + 1) * P)
                for kk in range(2):
                    k = 2 * q + kk
                    mm = times(dst, t0h[:, k, r], t0l[:, k, r], wh[:, :, kk, :], wl[:, :, kk, :], k == 0, k == KC - 1)
                mm.then_inc(quarter_done, 1)

            def turn_hidden(E, e_par):
                pe.wait_ge(hid_ready, E + 3)
                for c in range(2):
                    tr = nc.tensor.transpose(bank[2][:, c * P:(c + 1) * P],
                                             hid[e_par].rearrange("p (f c) -> p f c", c=2)[:, :, c], ident)
                tr.then_inc(hid_turned, 1)

            def down(n, c, E, e_par, u, per, first=False, last=False):
                if c == 0:
                    pe.wait_ge(hid_low, E + 1)
                wait_low(pe, n, u, per)
                s = n % RING
                for h in range(2):
                    f = slice(512 * h, 512 * h + 512)
                    hh, hl = t1h[:, 2 * e_par + c, 0:P], t1l[:, 2 * e_par + c, 0:P]
                    nc.tensor.matmul(bank[4 + h][:, :], hh, whi[:, s, f], start=first, stop=False, skip_group_check=True)
                    nc.tensor.matmul(bank[4 + h][:, :], hh, wlo[:, s, f], start=False, stop=False, skip_group_check=True)
                    mm = nc.tensor.matmul(bank[4 + h][:, :], hl, whi[:, s, f], start=False, stop=last,
                                          skip_group_check=True)
                mm.then_inc(quarter_done, 1)

            def block(J, E, b, m, i=0, per=0, first=False, last=False):
                for q in range(4):
                    if not (isinstance(E, int) and E == N_EXP - 1):
                        gate_up(m + q, q, E + 1, 1 - b, (J + last) % 2, i, per)
                    if q == 1:
                        turn_hidden(E, b)
                if not (isinstance(E, int) and E == N_EXP - 1):
                    m += 4
                if first and J:
                    pe.wait_ge(ysum_ready, 2 * J)
                for c in range(2):
                    down(m + c, c, E, b, i, per, first and c == 0, last and c == 1)

            pe.wait_ge(xg_low, 1)
            for q in range(4):
                gate_up(Q_MOE + q, q, 0, 0, 0, 0, 0)
            for J in range(NG):
                n = first_of(J)
                block(J, EG * J, 0, n, first=True)
                if J:
                    pe_scatter(pe, J)
                block(J, EG * J + 1, 1, n + 6)
                with pe.Fori(1, 3) as i:
                    for b in range(2):
                        block(J, EG * J + 2 * i + b, b, n + 6 * b, i, U)
                if J:
                    pe.wait_ge(x_added, 4 * J)
                pe_gather(J + 1)
                block(J, EG * J + 6, 0, n + 36)
                if J < NG - 1:
                    pe.wait_ge(xg_low, J + 2)
                block(J, EG * J + 7, 1, n + 42, last=True)
            pe_scatter(pe, NG)

        def pe_scatter(pe, J):
            pe.wait_ge(ysum_ready, 2 * J)
            pe.wait_ge(xg_raw, 2 * J + 2)
            for z in range(4):
                t, h = z // 2, z % 2
                if z == 3:
                    pe.wait_ge(x_added, 4 * J - 3)
                nc.tensor.matmul(bank[(3, 6, 7, 3)[z]][:, :], back[:, J - 1, t, :], ysum[:, 512 * h:512 * h + 512],
                                 start=True, stop=True).then_inc(scattered, 1)

        def dve_scatter(dve, J):
            for z in range(4):
                t, h = z // 2, z % 2
                dve.wait_ge(scattered, 4 * J + z - 3)
                o = xres[:, t, 512 * h:512 * h + 512]
                nc.vector.tensor_tensor(o, o, bank[(3, 6, 7, 3)[z]][:, :], ALU.add).then_inc(x_added, 1)

        def act_experts(act):
            def silu(e_par, n, u):
                act.wait_ge(quarter_done, n + 1 + U * u)
                nc.scalar.activation(sg[e_par], bank[e_par][:, 0:DE], ACT.Silu).then_inc(silu_done, 1)

            def high(E, e_par):
                act.wait_ge(hid_turned, E + 1)
                nc.scalar.activation(t1h[:, 2 * e_par:2 * e_par + 2, 0:P],
                                     bank[2][:, 0:2 * P].rearrange("p (c s) -> p c s", c=2),
                                     ACT.Copy).then_inc(hid_high, 1)

            def block(E, b, m, gate_quarter, i=0, per=0, gather=None):
                more = not (isinstance(E, int) and E == N_EXP - 1)
                if more:
                    split_high(act, m, i, per)
                silu(b, gate_quarter, i)
                if more:
                    for q in range(1, 4):
                        split_high(act, m + q, i, per)
                    m += 4
                if gather is not None:
                    act_gather(act, gather, gather % 2)
                high(E, b)
                for c in range(2):
                    split_high(act, m + c, i, per)

            act_gather(act, 0, 0)
            for J in range(NG):
                n = first_of(J)
                block(EG * J, 0, n, n - 3 if J else n - 1)
                block(EG * J + 1, 1, n + 6, n + 3)
                with act.Fori(1, 3) as i:
                    for b in range(2):
                        block(EG * J + 2 * i + b, b, n + 6 * b, n + 6 * b - 3, i, U)
                block(EG * J + 6, 0, n + 36, n + 33, gather=J + 1)
                block(EG * J + 7, 1, n + 42, n + 39)

        def dve_experts(dve):
            def hidden(J, e, E, e_par):
                dve.wait_ge(silu_done, E + 1)
                w = comb[:, ds(J, 1), ds(e, 1)].rearrange("p a b -> p (a b)")
                nc.vector.scalar_tensor_tensor(out=hid[e_par], in0=bank[e_par][:, DE:2 * DE], scalar=w, in1=sg[e_par],
                                               op0=ALU.mult, op1=ALU.mult).then_inc(hid_ready, 1)

            def low(E, e_par):
                dve.wait_ge(hid_high, E + 1)
                nc.vector.tensor_tensor(t1l[:, 2 * e_par:2 * e_par + 2, 0:P],
                                        bank[2][:, 0:2 * P].rearrange("p (c s) -> p c s", c=2),
                                        t1h[:, 2 * e_par:2 * e_par + 2, 0:P].bitcast(F32),
                                        ALU.subtract).then_inc(hid_low, 1)

            dve_gather_low(dve, 0, 0)

            def group_done(J):
                dve.wait_ge(quarter_done, first_of(J) + JOB - (4 if J == NG - 1 else 0))
                if J:
                    dve.wait_ge(x_added, 4 * J)
                for h in range(2):
                    nc.vector.tensor_copy(ysum[:, 512 * h:512 * h + 512], bank[4 + h][:, :]).then_inc(ysum_ready, 1)

            def block(J, e, b, m, i=0, per=0):
                E = EG * J + e
                more = not (isinstance(E, int) and E == N_EXP - 1)
                hidden(J, e, E, b)
                if more:
                    split_low(dve, m + 1, i, per)
                    split_low(dve, m + 3, i, per)
                    m += 4
                if isinstance(e, int) and J:
                    if e == 0:
                        group_done(J - 1)
                    if e == 1:
                        dve_scatter(dve, J)
                if isinstance(e, int) and e == 6:
                    dve_gather(dve, J + 1)
                low(E, b)
                split_low(dve, m + 1, i, per)

            for J in range(NG):
                n = first_of(J)
                block(J, 0, 0, n)
                block(J, 1, 1, n + 6)
                with dve.Fori(1, 3) as i:
                    for b in range(2):
                        block(J, 2 * i + b, b, n + 6 * b, i, U)
                block(J, 6, 0, n + 36)
                dve_gather_low(dve, J + 1, (J + 1) % 2)
                block(J, 7, 1, n + 42)
            group_done(NG - 1)
            dve_scatter(dve, NG)

        over_gu = lay(10184, KC, 2 * DE)
        over_d = lay(7112, 2, D)
        over_hT = lay(14280, 2, P)

        def overflowing(eng):
            eng.wait_ge(flag_ready, 1)
            return eng.value_load(flag[0:1, 0:1], min_val=0, max_val=1)

        def sp_overflow(sp):
            with sp.If(overflowing(sp) == 1):
                sp.wait_ge(xg_low, JOBS)
                for n in (Q_PLE - 2, Q_PLE - 1):
                    wait_low(sp, n)
                g = sp.value_load(flag[0:1, 1:2], min_val=0, max_val=NG - 1)
                with sp.Fori(0, EG) as e:
                    sp.wait_ge(ov["zeroed"], e + 1)
                    for j, name in enumerate(("w_exp_gate", "w_exp_up")):
                        v = A[name][0].rearrange("g e (p k) n -> p (g e) k n", k=KC)[:, ds(g * EG + e, 1), :, :]
                        sp.dma_start(over_gu[:, :, DE * j:DE * j + DE].unsqueeze(1), v).then_inc(ov["loaded"], 16)
                    v = A["w_exp_down"][0].rearrange("g e (p k) n -> p (g e) k n", k=2)[:, ds(g * EG + e, 1), :, :]
                    sp.dma_start(over_d.unsqueeze(1), v).then_inc(ov["loaded"], 16)

        def pe_overflow(pe):
            with pe.If(overflowing(pe) == 1):
                pe.wait_ge(xg_low, JOBS)
                pe.wait_ge(x_added, 4 * NG)
                with pe.Fori(0, EG) as e:
                    pe.wait_ge(ov["loaded"], 48 * e + 48)
                    for k in range(KC):
                        for part in (t0h, t0l):
                            mm = nc.tensor.matmul(bank[0][:, :], part[:, k, 0:P].bitcast(F32), over_gu[:, k, :],
                                                  start=k == 0 and part is t0h, stop=k == KC - 1 and part is t0l)
                    mm.then_inc(ov["up"], 1)
                    pe.wait_ge(ov["hid"], e + 1)
                    for c in range(2):
                        tr = nc.tensor.transpose(bank[2][:, c * P:(c + 1) * P],
                                                 hid[0].rearrange("p (f c) -> p f c", c=2)[:, :, c], ident)
                    tr.then_inc(ov["turned"], 1)
                    pe.wait_ge(ov["copied"], e + 1)
                    for h in range(2):
                        for c in range(2):
                            mm = nc.tensor.matmul(bank[4 + h][:, :], over_hT[:, c, :], over_d[:, c, 512 * h:512 * h + 512],
                                                  start=c == 0, stop=c == 1)
                    mm.then_inc(ov["down"], 1)
                pe.wait_ge(ov["zeroed"], EG + 1)
                for z in range(4):
                    t, h = z // 2, z % 2
                    nc.tensor.matmul(bank[(3, 6, 7, 1)[z]][:, :], back[:, NG, t, :], ysum[:, 512 * h:512 * h + 512],
                                     start=True, stop=True).then_inc(ov["scattered"], 1)

        def act_overflow(act):
            with act.If(overflowing(act) == 1):
                with act.Fori(0, EG) as e:
                    act.wait_ge(ov["up"], e + 1)
                    nc.scalar.activation(sg[0], bank[0][:, 0:DE], ACT.Silu).then_inc(ov["silu"], 1)

        def dve_overflow(dve):
            with dve.If(overflowing(dve) == 1):
                dve.wait_ge(x_added, 4 * NG)
                nc.vector.memset(ysum, 0.0).then_inc(ov["zeroed"], 1)
                with dve.Fori(0, EG) as e:
                    dve.wait_ge(ov["silu"], e + 1)
                    nc.vector.scalar_tensor_tensor(out=hid[0], in0=bank[0][:, DE:2 * DE],
                                                   scalar=comb[:, NG, ds(e, 1)], in1=sg[0],
                                                   op0=ALU.mult, op1=ALU.mult).then_inc(ov["hid"], 1)
                    dve.wait_ge(ov["turned"], e + 1)
                    nc.vector.tensor_copy(over_hT.rearrange("p c s -> p (c s)"), bank[2][:, 0:2 * P]).then_inc(ov["copied"], 1)
                    dve.wait_ge(ov["down"], e + 1)
                    dve.wait_ge(ov["zeroed"], e + 1)
                    nc.vector.tensor_tensor(ysum[:, 0:512], ysum[:, 0:512], bank[4][:, :], ALU.add).then_inc(ov["summed"], 1)
                    nc.vector.tensor_tensor(ysum[:, 512:D], ysum[:, 512:D], bank[5][:, :], ALU.add).then_inc(ov["zeroed"], 1)
                for z in range(4):
                    t, h = z // 2, z % 2
                    dve.wait_ge(ov["scattered"], z + 1)
                    o = xres[:, t, 512 * h:512 * h + 512]
                    nc.vector.tensor_tensor(o, o, bank[(3, 6, 7, 1)[z]][:, :], ALU.add).then_inc(ov["added"], 1)
                dve.wait_ge(ov["added"], 4)
            dve.wait_ge(x_added, 4 * NG)
            nc.vector.tensor_copy(flagf, flag[:, :]).then_inc(experts_added, 1)

        experts_added = sem("experts_added")
        norm_p = RmsNorm(xres, xn, stat)
        turn_p = Turn(xn, gain("ple_norm_w"), t0h, t0l)
        norm_f = RmsNorm(xres, xn, stat, 2)
        emb_turned, emb_high, emb_low, ple_copied, gated, gate_used = (
            sem(s) for s in ("emb_turned", "emb_high", "emb_low", "ple_copied", "gated", "gate_used"))

        def sp_ple(sp):
            v = A["w_ple"][0].rearrange("(p k) n -> p k n", k=2)
            for k in range(2):
                load(sp, Q_PLE + k, [(raw[:, (Q_PLE + k) % RING, :], v[:, k, :])])
            load_square(sp, Q_GATE, A["w_ple_gate"][0])

        def pe_ple(pe):
            pe.wait_ge(ple_bank_free, 1)
            for k in range(2):
                for t in range(NT):
                    tr = nc.tensor.transpose(bank[4][:, k * SEQ + t * P:k * SEQ + (t + 1) * P],
                                             emb[:, t, :].rearrange("p (f k) -> p f k", k=2)[:, :, k], ident)
            tr.then_inc(emb_turned, 1)
            pe.wait_ge(emb_low, 1)
            for k in range(2):
                n = Q_PLE + k
                wait_low(pe, n)
                for h in range(2):
                    f = slice(512 * h, 512 * h + 512)
                    for t in range(NT):
                        s = slice(t * P, (t + 1) * P)
                        mm = times(bank[2 * h + t][:, :], t1h[:, k, s], t1l[:, k, s], whi[:, n % RING, f],
                                   wlo[:, n % RING, f], k == 0, k == 1)
                mm.then_inc(quarter_done, 1)
            turn_p.pe(pe, [norm_p.ready()])
            square_product(pe, Q_GATE, t0h, t0l, [(ple_copied, 4)], turn_p)

        ple_bank_free = experts_added

        def act_ple(act):
            for k in range(2):
                split_high(act, Q_PLE + k)
            act.wait_ge(emb_turned, 1)
            nc.scalar.activation(t1h[:, 0:2, :], bank[4][:, :].rearrange("p (k s) -> p k s", k=2), ACT.Copy).then_inc(emb_high, 1)
            for q in range(2):
                split_high(act, Q_GATE + q)
            norm_p.act(act, lambda part, t: (experts_added, 1))
            act.wait_ge(quarter_done, Q_GATE)
            for h in range(2):
                for t in range(NT):
                    nc.scalar.copy(ple[:, t, 512 * h:512 * h + 512], bank[2 * h + t][:, :]).then_inc(ple_copied, 1)
            turn_p.act(act, Q_PLE)
            for q in range(2, 8):
                split_high(act, Q_GATE + q)
            for h in range(2):
                act.wait_ge(quarter_done, Q_GATE + 4 * h + 4)
                for t in range(NT):
                    nc.scalar.activation(sgate[:, t, 512 * h:512 * h + 512], bank[2 * h + t][:, :],
                                         ACT.Sigmoid).then_inc(gated, 1)
                if h:
                    norm_f.act_table(act)
                norm_f.act_squares(act, h, lambda t: (gate_used, NT * h + t + 1))
            norm_f.act_root(act)

        def dve_ple(dve, order):
            dve.wait_ge(emb_high, 1)
            nc.vector.tensor_tensor(t1l[:, 0:2, :], bank[4][:, :].rearrange("p (k s) -> p k s", k=2),
                                    t1h[:, 0:2, :].bitcast(F32), ALU.subtract).then_inc(emb_low, 1)
            norm_p.dve(dve, order)
            turn_p.dve(dve)
            for h in range(2):
                for t in range(NT):
                    dve.wait_ge(gated, 2 * h + t + 1)
                    f = slice(512 * h, 512 * h + 512)
                    order.step(nc.vector.tensor_tensor(sgate[:, t, f], sgate[:, t, f], ple[:, t, f], ALU.mult))
                    nc.vector.tensor_tensor(xres[:, t, f], xres[:, t, f], sgate[:, t, f], ALU.add).then_inc(gate_used, 1)
            norm_f.dve(dve, order, fnw)


        rkv = lay(0, NT, 3 * D)
        glu = lay(6144, NT, 2 * D)
        gates = lay(10240, NT, 2 * D)
        hT = lay(6144, KC, SEQ)
        dhT = lay(8192, KC, SEQ)
        decay = lay(6144, NT, D)
        gain_a = lay(8192, NT, D)
        taps2 = lay(14336, 2 * P)
        W2, K2 = 31, KC
        H2 = W2 - 1
        shifted = [carve(1024 * b, NT, TW) for b in range(2)]
        xw = [lay(2048 * j, KC, SEQ) for j in range(3)]
        gate_bias = carve(0, 2 * D)
        uT = carve(2048, K2, H2 + SEQ)
        cvT = carve(4336, K2, SEQ)
        ctok = carve(2048, NT, D)
        w1, a1, g1 = carve(6384, KC, 64), carve(6896, KC, 64), carve(7408, KC, P)
        w2, a2 = carve(8432, D), carve(9456, D)
        dT, aT = carve(10480, SEQ), carve(10736, SEQ)
        rows2 = carve(10992, 2, P)
        rowbuf = [carve(11248 + 512 * b, TW) for b in range(2)]
        gT, g2 = lay(14592, SEQ), carve(12272, D)
        st2 = tiny(0, 16)
        norm_g = RmsNorm(xres, xn, stat)
        turn_g = Turn(xn, gain("norm_mix_g_2"), t0h, t0l)
        row_loaded, shift_loaded = ([sem(f"{n}{b}") for b in range(2)] for n in ("row_loaded", "shift_loaded"))
        row_used = sem("row_used")
        evac2 = Again(evac_in, NT * IN_T)
        lora_loaded = Again(router_loaded, 96)
        glu_ready = Again(y_gated, NT)
        u_turned = Again(xbc_turned, XCH // 2)
        u_copied = Again(xbc_copied, XCH // 2)
        taps2_turned = Again(taps_turned, 1)
        taps2_ready = Again(taps_ready, 1)
        conv2_done = Again(conv_done, XCH)
        c_var = sem("c_var")
        c_back = Again(x_back, 2 * NT)
        c_copied = Again(ple_copied, 4)
        c_mean = Again(y_mean, 1)
        c_squared = Again(y_squared, 2 * NT)
        c_root = Again(y_root, 1)
        c_normed = Again(y_normed, 2 * NT)
        c_active = Again(conv_active, XCH)
        c_high = Again(emb_high, 1)
        c_low = Again(emb_low, 1)
        shift_done = sem("shift_done")
        xw_ready, lora_mid, lora_ones = (
            sem(s) for s in ("xw_ready", "lora_mid", "lora_ones"))
        lora_act = Again(dt_exp, 2)
        lora_done = Again(cum_done, 1)
        lora_ready = Again(dec_ready, 2)
        state_decay_done = Again(state_done, 1)
        state_decay_ready = Again(state_ready, 1)
        conv_gated = Again(ssd_merged, 4)

        TILES2 = [6, 8, 7, 9] + list(range(10, 14)) + list(range(6))
        GATES2, RKV2 = 4, 8
        CONV_SETS = ((0, 1, 2, 3), (4, 5, 6))
        CONV_FIRST, CONV_NEXT = 30, 5

        def sp_in2(sp):
            v = A["w_in_2"][0].rearrange("(p k) n -> p k n", k=KC)
            for p, c in enumerate(TILES2):
                for q in range(4):
                    n = Q_IN2 + 4 * p + q
                    load(sp, n, [(pair_view(raw, n, TW), v[:, 2 * q:2 * q + 2, c * TW:(c + 1) * TW])])
            load_square(sp, Q_CONV, A["w_conv_proj_2"][0])
            load_square(sp, Q_RWKV, A["w_rwkv_proj_2"][0], range(4), "(k p) n -> p k n")
            for j, (dst, name) in enumerate(((ka_row, "k_a_2"), (lng, "ln_x_g_2"), (lnb, "ln_x_b_2"))):
                wait_low(sp, Q_RWKV + j)
                sp.dma_start(dst, row(A[name][0], D)).then_inc(rows_loaded, 16)
            sp.wait_ge(*heads_gated.at(3))
            load_square(sp, Q_RWKV, A["w_rwkv_proj_2"][0], range(4, 8), "(k p) n -> p k n")
            load_square(sp, Q_OUT2, A["w_out_2"][0])

        def lora_loads(act):
            act.wait_ge(*norm_f.ready())
            def ld(dst, src):
                act.dma_start(dst, src).then_inc(lora_loaded.sem, 16)
            ld(w1, A["decay_w1_2"][0].rearrange("(p k) n -> p k n", k=KC))
            ld(a1, A["aaa_a1_2"][0].rearrange("(p k) n -> p k n", k=KC))
            ld(g1, A["gate_g1_2"][0].rearrange("(p k) n -> p k n", k=KC))
            for dst, w, b in ((w2, "decay_w2_2", "decay_w0_2"), (a2, "aaa_a2_2", "aaa_a0_2")):
                ld(dst[0:64, :], A[w][0])
                ld(dst[64:65, :], A[b])
            ld(g2, A["gate_g2_2"][0])
            ld(kk_row, row(A["k_k_2"][0], D))
            ld(gate_bias[0:1, :], A["b_gate_2"])
            taps = A["conv_w_2"][0].rearrange("w (k p) -> (w k) p", p=P)
            ld(rows2[:, 0, :], taps[0:P, :])
            ld(rows2[0:120, 1, :], taps[P:248, :])
            ld(rows2[120:128, 1, :], A["conv_b_2"][0].rearrange("(k p) -> k p", p=P))

        N_LORA = 16 * 13

        def pe_in2(pe):
            turn_g.pe(pe, [norm_g.ready(), (gate_used, 4)])
            pe.wait_ge(*turn_g.done())

            def tile(p):
                wait_from(pe, *evac2.at(NT * (p - 1)))
                dst = bank[2 * (p % 2):2 * (p % 2) + 2]
                gate = GATES2 <= p < RKV2
                for q in range(4):
                    if gate and q == 0:
                        pe.wait_ge(*lora_loaded.at(N_LORA))
                        f = slice((p - GATES2) * TW, (p - GATES2 + 1) * TW)
                        for t in range(NT):
                            nc.tensor.matmul(dst[t][:, :], con("ones")[0:1, :], gate_bias[0:1, f], start=True, stop=False)
                    wide_quarter(pe, Q_IN2 + 4 * p + q, q, dst, t0h, t0l, begun=gate)

            for p in range(5):
                tile(p)
            pe.wait_ge(*glu_ready.at(4))
            for b in range(K2 // 2):
                for kk in range(2):
                    for t in range(NT):
                        c = (2 * b + kk) * P
                        tr = nc.tensor.transpose(bank[4 + b][:, kk * SEQ + t * P:kk * SEQ + (t + 1) * P],
                                                 glu[:, t, c:c + P], ident)
                tr.then_inc(u_turned.sem, 1)
            pe.wait_ge(*u_copied.at(1))
            pe.wait_ge(*lora_loaded.at(N_LORA))
            for j in range(2):
                tr = nc.tensor.transpose(bank[4][:, j * P:(j + 1) * P], rows2[:, j, :], ident)
            tr.then_inc(taps2_turned.sem, 1)
            for p in range(5, 7):
                tile(p)
            pe.wait_ge(*u_copied.at(4))
            for j, (w, m) in enumerate(((w1, 64), (a1, 64), (g1, P))):
                for k in range(KC):
                    pe.wait_ge(xw_ready, KC * j + k + 1)
                    mm = nc.tensor.matmul(bank[5 + j][0:m, 0:SEQ], w[:, k, :], xw[j][:, k, :], start=k == 0,
                                          stop=k == KC - 1)
                mm.then_inc(lora_mid, 1)
            tile(7)
            pe.wait_ge(lora_ones, 2)
            pe.wait_ge(*taps2_ready.at(1))
            for j, (mid, w) in enumerate(((dT, w2), (aT, a2))):
                pe.wait_ge(*(lora_ready.at(4) if j else lora_act.at(3)))
                for t in range(NT):
                    for h in range(2):
                        nc.tensor.matmul(bank[4 + 2 * t + h][:, :], mid[0:65, t * P:(t + 1) * P],
                                         w[0:65, 512 * h:512 * h + 512], start=True, stop=True).then_inc(lora_done.sem, 1)
                tile(8 + j)
            pe.wait_ge(*lora_ready.at(8))
            for c in range(KC):
                nc.tensor.matmul(bank[4][:, c:c + 1], decay[:, 0, c * P:(c + 1) * P], con("high"), start=True, stop=False)
                mm = nc.tensor.matmul(bank[4][:, c:c + 1], decay[:, 1, c * P:(c + 1) * P], con("low"), start=False, stop=True)
            mm.then_inc(state_decay_done.sem, 1)
            for p in range(10, 14):
                tile(p)
            pe.wait_ge(*state_decay_ready.at(1))
            for w in range(W2):
                pe.wait_ge(diag_made, w + 1)
                mm = nc.tensor.matmul(bank[5][:, 0:SEQ], tap_diag[:, w, :], uT[:, K2 - 1, w:w + SEQ], start=w == 0,
                                      stop=w == W2 - 1)
            mm.then_inc(chunk_made, 1)

        def act_in2(act):
            for q in range(4):
                split_high(act, Q_IN2 + q)
            norm_g.act(act, lambda part, t: norm_f.ready(t + 1))
            turn_g.act(act, Q_IN2)
            lora_loads(act)

            def mu_load(p):
                wait_from(act, row_used, p - RKV2 - 1)
                act.dma_start(rowbuf[p % 2], row(A["mu_rkv_2"][0][(p - RKV2) * TW:(p - RKV2 + 1) * TW], TW)
                              ).then_inc(row_loaded[p % 2], 16)

            def evac(p):
                act.wait_ge(quarter_done, Q_IN2 + 4 * p + 4)
                b = 2 * (p % 2)
                if p < GATES2:
                    f = slice((p // 2) * TW + (p % 2) * D, (p // 2) * TW + (p % 2) * D + TW)
                    for t in range(NT):
                        nc.scalar.activation(glu[:, t, f], bank[b + t][:, :], ACT.Sigmoid if p % 2 else ACT.Copy
                                             ).then_inc(evac2.sem, 1)
                elif p < RKV2:
                    f = slice((p - GATES2) * TW, (p - GATES2 + 1) * TW)
                    for t in range(NT):
                        nc.scalar.activation(gates[:, t, f], bank[b + t][:, :], ACT.Sigmoid).then_inc(evac2.sem, 1)
                else:
                    f = slice((p - RKV2) * TW, (p - RKV2 + 1) * TW)
                    for t in range(NT):
                        nc.scalar.copy(rkv[:, t, f], bank[b + t][:, :]).then_inc(evac2.sem, 1)
                    wait_from(act, shift_done, p - RKV2 - 1)
                    act.wait_ge(*evac2.at(NT * (p + 1)))
                    s = shifted[p % 2]
                    act.dma_start(s[1:P, :, :], rkv[0:P - 1, :, f]).then_inc(shift_loaded[p % 2], 16)
                    act.dma_start(s[0:1, 1, :], rkv[P - 1:P, 0, f]).then_inc(shift_loaded[p % 2], 16)

            for p in range(1, 14):
                for q in range(4):
                    split_high(act, Q_IN2 + 4 * p + q)
                if p >= RKV2:
                    mu_load(p)
                evac(p - 1)
                if p == 7:
                    act.wait_ge(lora_mid, 1)
                    nc.scalar.activation(dT[0:64, :], bank[5][0:64, 0:SEQ], ACT.Tanh).then_inc(lora_act.sem, 1)
                    act.wait_ge(lora_mid, 2)
                    nc.scalar.copy(aT[0:64, :], bank[6][0:64, 0:SEQ]).then_inc(lora_act.sem, 1)
                    act.wait_ge(lora_mid, 3)
                    nc.scalar.activation(gT, bank[7][:, 0:SEQ], ACT.Sigmoid).then_inc(lora_act.sem, 1)
                if p in (8, 9):
                    j = p - 8
                    for t in range(NT):
                        for h in range(2):
                            act.wait_ge(*lora_done.at(4 * j + 2 * t + h + 1))
                            nc.scalar.activation((decay, gain_a)[j][:, t, 512 * h:512 * h + 512], bank[4 + 2 * t + h][:, :],
                                                 ACT.Sigmoid).then_inc(lora_ready.sem, 1)
                if p >= 10:
                    for w in range(8 * (p - 10), min(8 * (p - 9), W2)):
                        nc.scalar.activation(tap_diag[:, w, :], ident, ACT.Copy,
                                             scale=taps2[:, w * K2 + K2 - 1:w * K2 + K2]).then_inc(diag_made, 1)
                if p == 10:
                    act.wait_ge(*state_decay_done.at(1))
                    nc.scalar.activation(sdec, bank[4][:, 0:KC], ACT.Exp, scale=-S_DECAY).then_inc(state_decay_ready.sem, 1)
            for q in range(4):
                split_high(act, Q_CONV + q)
            evac(13)
            act.wait_ge(chunk_made, 1)
            nc.scalar.activation(cvT[:, K2 - 1, :], bank[5][:, 0:SEQ], ACT.Identity,
                                 bias=taps2[:, 248 + K2 - 1:248 + K2]).then_inc(chunk_done, 1)
            act.dma_start(ka_first, row(A["k_a_2"][0, 0:P], P)).then_inc(rk_loaded, 16)

        def shift(dve, order, p):
            f = slice((p - RKV2) * TW, (p - RKV2 + 1) * TW)
            z, s = rkv[:, :, f], shifted[p % 2]
            order.settle()
            dve.wait_ge(shift_loaded[p % 2], 32 * ((p - RKV2) // 2 + 1))
            dve.wait_ge(row_loaded[p % 2], 16 * ((p - RKV2) // 2 + 1))
            order.step(nc.vector.tensor_tensor(s, s, z, ALU.subtract))
            nc.vector.tensor_tensor(s, s, rowbuf[p % 2].unsqueeze(1).to_broadcast([P, NT, TW]),
                                    ALU.mult).then_inc(row_used, 1)
            dve.wait_ge(row_used, p - RKV2 + 1)
            nc.vector.tensor_tensor(z, z, s, ALU.add).then_inc(shift_done, 1)
            if p < 12:
                dve.wait_ge(shift_done, p - RKV2 + 1)
                order.mark(nc.vector.memset(s[0:1, 0, :], 0.0))

        def dve_in2(dve, order):
            norm_g.dve(dve, order)
            turn_g.dve(dve)
            dve.wait_ge(*norm_g.ready())
            dve.wait_ge(*turn_g.written())
            order.mark(nc.vector.memset(uT[:, :, 0:H2], 0.0))
            for j in range(2):
                dve.wait_ge(*evac2.at(NT * (2 * j + 2)))
                f, g = slice(j * TW, (j + 1) * TW), slice(D + j * TW, D + (j + 1) * TW)
                for t in range(NT):
                    nc.vector.tensor_tensor(glu[:, t, f], glu[:, t, f], glu[:, t, g], ALU.mult).then_inc(glu_ready.sem, 1)
            for b in range(K2 // 2):
                dve.wait_ge(*u_turned.at(b + 1))
                nc.vector.tensor_copy(uT[:, 2 * b:2 * b + 2, H2:H2 + SEQ],
                                      bank[4 + b][:, :].rearrange("p (k s) -> p k s", k=2)).then_inc(u_copied.sem, 1)
            dve.wait_ge(*taps2_turned.at(1))
            nc.vector.tensor_copy(taps2, bank[4][:, 0:2 * P]).then_inc(taps2_ready.sem, 1)
            order.step(nc.vector.tensor_tensor(hT, t0h[:, :, :].bitcast(F32), t0l[:, :, :].bitcast(F32), ALU.add))
            order.mark(nc.vector.tensor_tensor(dhT[:, :, 1:SEQ], hT[:, :, 0:SEQ - 1], hT[:, :, 1:SEQ], ALU.subtract))
            order.step(nc.vector.tensor_scalar(dhT[:, :, 0:1], hT[:, :, 0:1], -1.0, None, ALU.mult))
            for buf in (dT, aT):
                nc.vector.memset(buf[64:65, :], 1.0).then_inc(lora_ones, 1)
            for j in range(3):
                for k in range(KC):
                    nc.vector.scalar_tensor_tensor(out=xw[j][:, k, :], in0=dhT[:, k, :], scalar=mul[:, j, k:k + 1],
                                                   in1=hT[:, k, :], op0=ALU.mult, op1=ALU.add).then_inc(xw_ready, 1)
            dve.wait_ge(*u_copied.at(4))
            dve.wait_ge(*taps2_ready.at(1))

            def convolve(at, steps):
                for z in range(at, min(at + steps, W2 * len(CONV_SETS))):
                    w = z % W2
                    for c in CONV_SETS[z // W2]:
                        tap = taps2[:, w * K2 + c:w * K2 + c + 1]
                        if w == 0:
                            order.mark(nc.vector.tensor_scalar(cvT[:, c, :], uT[:, c, 0:SEQ], tap,
                                                               taps2[:, 248 + c:249 + c], ALU.mult, ALU.add))
                        else:
                            ins = nc.vector.scalar_tensor_tensor(out=cvT[:, c, :], in0=uT[:, c, w:w + SEQ], scalar=tap,
                                                                 in1=cvT[:, c, :], op0=ALU.mult, op1=ALU.add)
                            if w < W2 - 1:
                                order.mark(ins)
                            else:
                                ins.then_inc(conv2_done.sem, 1)
                    if w < W2 - 1:
                        order.settle()
                return at + steps

            at = convolve(0, CONV_FIRST)
            dve.wait_ge(quarter_done, Q_IN2 + 4 * RKV2)
            for b in range(2):
                order.mark(nc.vector.memset(shifted[b][0:1, 0, :], 0.0))
            for p in range(RKV2, 13):
                shift(dve, order, p)
                at = convolve(at, CONV_NEXT)
            convolve(at, W2 * len(CONV_SETS))

        S_DECAY = math.exp(-0.5)
        sdec = tiny(16, KC)
        tap_diag = carve(6384, W2, P)
        diag_made, chunk_made, chunk_done = (sem(s) for s in ("diag_made", "chunk_made", "chunk_done"))

        def pe_conv(pe):
            pe.wait_ge(*conv2_done.at(K2 - 1))
            pe.wait_ge(chunk_done, 1)
            pe.wait_ge(*taps2_ready.at(1))
            for t in range(NT):
                for h in range(2):
                    for c in range(4):
                        tr = nc.tensor.transpose(bank[4 + 2 * t + h][:, c * P:(c + 1) * P],
                                                 cvT[:, 4 * h + c, t * P:(t + 1) * P], ident)
                    tr.then_inc(c_back.sem, 1)
            turn_c.pe(pe, [c_normed.at(NT), c_copied.at(4)])

        turn_c = Turn(ctok, None, None, None)

        def act_conv(act):
            nc.scalar.activation(early[:, 8:9], ident[:, 0:1], ACT.Sqrt)
            for t in range(NT):
                for h in range(2):
                    act.wait_ge(*c_back.at(2 * t + h + 1))
                    nc.scalar.activation(ctok[:, t, 512 * h:512 * h + 512], bank[4 + 2 * t + h][:, :], ACT.Copy,
                                         accum_out=st2[:, 4 + 2 * t + h:5 + 2 * t + h]).then_inc(c_copied.sem, 1)
            act.wait_ge(*c_mean.at(1))
            for t in range(NT):
                nc.scalar.activation(c_dev_sq[:, t, :], ctok[:, t, :], ACT.Square, bias=st2[:, 8 + t:9 + t],
                                     accum_out=st2[:, 10 + t:11 + t]).then_inc(c_squared.sem, 1)
            act.wait_ge(c_var, 1)
            nc.scalar.activation(st2[:, 10:12], st2[:, 10:12], ACT.Sqrt).then_inc(c_root.sem, 1)
            act.wait_ge(kk_squared, 1)
            nc.scalar.activation(kinv, kinv, ACT.Sqrt).then_inc(kk_root, 1)
            for k in range(KC):
                if k % 2 == 0:
                    act.wait_ge(*turn_c.written(k // 2 + 1))
                nc.scalar.activation(cvT[:, k, :], turn_c.part(k), ACT.Silu, scale=gain("conv_ln_g_2")[:, k:k + 1],
                                     bias=gain("conv_ln_b_2")[:, k:k + 1]).then_inc(c_active.sem, 1)
                if k % 2:
                    if k == 1:
                        act.wait_ge(quarter_done, Q_CONV)
                        act.wait_ge(*lora_ready.at(8))
                    act.wait_ge(*c_active.at(k + 1))
                    r = slice(k - 1, k + 1)
                    nc.scalar.activation(t0h[:, r, :], cvT[:, r, :], ACT.Copy).then_inc(c_high.sem, 1)
            act.wait_ge(row_used, 6)
            act.dma_start(rk_row, row(A["r_k_2"][0].rearrange("h d -> (h d)"), D)).then_inc(rk_loaded, 16)

        c_dev_sq = carve(6384, NT, D)

        def dve_conv(dve, order):
            kk = carve(8432, NT, D)
            dve.wait_ge(shift_done, 5)
            dve.wait_ge(chunk_made, 1)
            order.step(nc.vector.tensor_tensor(kk, rkv[:, :, D:2 * D], kk_row.unsqueeze(1).to_broadcast([P, NT, D]),
                                               ALU.mult))
            order.mark(nc.vector.tensor_tensor(kk, kk, kk, ALU.mult))
            dve.wait_ge(*c_copied.at(4))
            for t in range(NT):
                order.mark(nc.vector.tensor_tensor(st2[:, 8 + t:9 + t], st2[:, 4 + 2 * t:5 + 2 * t],
                                                   st2[:, 5 + 2 * t:6 + 2 * t], ALU.add))
            order.settle()
            nc.vector.tensor_scalar(st2[:, 8:10], st2[:, 8:10], -1.0 / D, None, ALU.mult).then_inc(c_mean.sem, 1)
            nc.vector.tensor_reduce(kinv, by_head(kk, NH), AX.X, ALU.add).then_inc(kk_squared, 1)
            dve.wait_ge(*c_squared.at(NT))
            nc.vector.tensor_scalar(st2[:, 10:12], st2[:, 10:12], 1.0 / D, 1e-5, ALU.mult, ALU.add).then_inc(c_var, 1)
            dve.wait_ge(*c_root.at(1))
            dve.wait_ge(*c_mean.at(1))
            order.step(nc.vector.reciprocal(st2[:, 10:12], st2[:, 10:12]))
            for t in range(NT):
                nc.vector.tensor_scalar(ctok[:, t, :], ctok[:, t, :], st2[:, 8 + t:9 + t], st2[:, 10 + t:11 + t],
                                        ALU.add, ALU.mult).then_inc(c_normed.sem, 1)
            shift(dve, order, 13)
            dve.wait_ge(kk_root, 1)
            order.step(nc.vector.tensor_scalar(kinv, kinv, 1e-12, None, ALU.max))
            order.mark(nc.vector.reciprocal(kinv, kinv))
            for b in range(KC // 2):
                r = slice(2 * b, 2 * b + 2)
                dve.wait_ge(*c_high.at(b + 1))
                nc.vector.tensor_tensor(t0l[:, r, :], cvT[:, r, :], t0h[:, r, :].bitcast(F32), ALU.subtract
                                        ).then_inc(c_low.sem, 1)

        LEV = 7
        gram = [carve(2048 * c, 4, 512) for c in range(2)]
        AR = [carve(4096 + 512 * c, NT, 2, P) for c in range(2)]
        Bt = [carve(5120 + 512 * c, NT, P) for c in range(2)]
        Kt = [carve(5376 + 512 * c, NT, P) for c in range(2)]
        XT = [carve(6144 + 512 * c, 4, P) for c in range(2)]
        Rt, At, Pi, kkb, tmpb = (carve(7168 + 256 * j, NT, P) for j in range(5))
        BK = carve(8448, 2, NT, P)
        Xm, Ym = carve(8960, 4, P), carve(9472, 4, P)
        Wn, Uo = carve(9984, NT, P), carve(10240, NT, P)
        SB = carve(10496, P)
        kk_row = carve(13296, D)
        ka_row, lng, lnb = (raw[:, (Q_RWKV + j) % RING, :] for j in range(3))
        rk_row = carve(11248, D)
        ka_first = carve(10880, P)
        kinv, hbonus, hvar = (tiny(24 + 32 * j, NT, NH) for j in range(3))
        hmean = tiny(120, 4)
        rk_loaded, kk_squared, kk_root = (sem(s) for s in ("rk_loaded", "kk_squared", "kk_root"))
        cs_done, pdiff, inverse_begun = (
            sem(s) for s in ("cs_done", "pdiff", "inverse_begun"))
        pexp = Again(exped, 4 * PAIRS)
        gram_masked = Again(mt_ready, 8)
        tok_ready = Again(rot_ready, PAIRS)
        hturned = Again(qk_turned, PAIRS)
        ft_copied = Again(qk_copied, PAIRS)
        gram_done = Again(scored, 2 * PAIRS)
        y_made, x_made, xt_copied = (
            sem(s) for s in ("y_made", "x_made", "xt_copied"))
        y_masked = Again(dif_ready, 8)
        xm_copied = Again(p_copied, 2 * PAIRS)
        uo_copied, s_made, s_ready, bonus_made = (
            sem(s) for s in ("uo_copied", "s_made", "s_ready", "bonus_made"))
        w_made = Again(abc_done, 8)
        w_copied = Again(lmat_ready, 8)
        u_made = Again(diag_done, 8)
        o_made = Again(pv_done, PAIRS)
        pair_done = Again(att_ready, PAIRS)
        head_var, head_root = sem("head_var"), sem("head_root")

        def unit(h, t):
            return 2 * h + t

        def halves(v, lev):
            v = v.rearrange("p u (n a m) -> p u n a m", a=2, m=1 << lev)
            return v[:, :, :, 0, :], v[:, :, :, 1, :]

        def step_loop(eng, first, step, last):
            first()
            with eng.Fori(0, (PAIRS - 2) // 2) as u:
                for c in (1, 0):
                    step(2 * u + (2 - c), c)
            last()

        def pe_heads(pe):
            def decays(p):
                if not (isinstance(p, int) and p == 0):
                    pe.wait_ge(*gram_masked.at(4 * p))
                for t in range(NT):
                    mm = nc.tensor.matmul(bank[4][:, t * P:(t + 1) * P], con("centred"), decay[:, t, ds(P * p, P)],
                                          start=True, stop=True)
                mm.then_inc(cs_done, 1)

            def turn_ar(p):
                pe.wait_ge(*tok_ready.at(2 * p + 1))
                for t in range(NT):
                    for j, src in enumerate((At, Rt)):
                        tr = nc.tensor.transpose(bank[5][:, (2 * t + j) * P:(2 * t + j + 1) * P], src[:, t, :], ident)
                tr.then_inc(hturned.sem, 1)

            def turn_bk(p, c):
                pe.wait_ge(*tok_ready.at(2 * p + 2))
                for j, src in enumerate((Bt[c], Kt[c])):
                    for t in range(NT):
                        tr = nc.tensor.transpose(bank[4][:, (2 * j + t) * P:(2 * j + t + 1) * P], src[:, t, :], ident)
                tr.then_inc(hturned.sem, 1)

            def grams(p, c, units):
                pe.wait_ge(*ft_copied.at(2 * p + 2))
                for u in units:
                    h, t = u // 2, u % 2
                    if u >= 2:
                        pe.wait_ge(*gram_masked.at(4 * p + u - 1))
                    r = slice(64 * h, 64 * h + 64)
                    ar = AR[c][r, t].rearrange("p a s -> p (a s)")
                    for j in range(2):
                        mm = nc.tensor.matmul(bank[5 - u % 2][:, 256 * j:256 * j + 256], BK[r, j, t, :], ar,
                                              start=True, stop=True)
                    mm.then_inc(gram_done.sem, 1)

            def below(p, b, lev):
                for g in range(2):
                    if lev == 0:
                        pe.wait_ge(inverse_begun, 2 * p + g + 1)
                    elif lev == 1:
                        pe.wait_ge(*y_masked.at(2 * LEV * p + g + 1))
                    else:
                        pe.wait_ge(*xm_copied.at(2 * (LEV - 2) * p + 2 * lev + g - 3))
                    for v in range(2):
                        u = 2 * g + v
                        mm = nc.tensor.matmul(bank[g][:, v * P:(v + 1) * P], gram[b][:, u, 0:P],
                                              ident if lev == 0 else Xm[:, u, :], start=True, stop=True)
                    mm.then_inc(y_made, 1)

            def grow(p, b, lev):
                even, odd = halves(Ym, lev)[0], halves(XT[b], lev)[1]
                for g in range(2):
                    pe.wait_ge(*y_masked.at(2 * LEV * p + 2 * lev + g + 1))
                    if not (isinstance(p, int) and p == 0 and lev == 1):
                        pe.wait_ge(xt_copied, 2 * (LEV - 1) * p + 2 * lev + g - 3)
                    if lev < LEV - 1:
                        for v in range(2):
                            u = 2 * g + v
                            nc.tensor.matmul(bank[2 + g][:, v * 64:(v + 1) * 64], XT[b][:, u, :], even[:, u], start=True,
                                             stop=True)
                    for v in range(2):
                        u = 2 * g + v
                        mm = nc.tensor.matmul(bank[2 + g][:, P + v * 64:P + (v + 1) * 64], Ym[:, u, :], odd[:, u],
                                              start=True, stop=True)
                    mm.then_inc(x_made, 1)

            def rest(p, c, t):
                if t:
                    pe.wait_ge(s_ready, p + 1)
                for h in range(2):
                    f = slice(h * DH, (h + 1) * DH)
                    if t:
                        nc.tensor.matmul(bank[6][:, f], AR[c][:, 1, 0, :], SB[:, f], start=True, stop=False)
                    mm = nc.tensor.matmul(bank[6][:, f], gram[c][:, unit(h, t), 256:384],
                                          rkv[:, t, ds(2 * D + P * p + DH * h, DH)], start=t == 0, stop=True)
                mm.then_inc(w_made.sem, 1)

            def solve(p, c, t):
                pe.wait_ge(xt_copied, 2 * (LEV - 1) * (p + 1))
                pe.wait_ge(*w_copied.at(2 * p + t + 1))
                for h in range(2):
                    mm = nc.tensor.matmul(bank[6][:, P + h * DH:P + (h + 1) * DH], XT[c][:, unit(h, t), :],
                                          Wn[:, t, h * DH:(h + 1) * DH], start=True, stop=True)
                mm.then_inc(u_made.sem, 1)

            def state(p, c):
                pe.wait_ge(uo_copied, 2 * p + 1)
                nc.tensor.matmul(bank[6][:, 256:384], Bt[c][:, 0, :], Uo[:, 0, :], start=True, stop=False)
                nc.tensor.matmul(bank[6][:, 256:384], Kt[c][:, 0, :], rkv[:, 0, ds(2 * D + P * p, P)], start=False,
                                 stop=True).then_inc(s_made, 1)

            def outputs(p, c, t, h):
                if h == 0:
                    pe.wait_ge(uo_copied, 2 * p + t + 1)
                    if t == 0 and not (isinstance(p, int) and p == 0):
                        pe.wait_ge(*pair_done.at(p))
                f = slice(h * DH, (h + 1) * DH)
                oh = bank[7][:, t * P + h * DH:t * P + (h + 1) * DH]
                if t:
                    nc.tensor.matmul(oh, AR[c][:, 1, 1, :], SB[:, f], start=True, stop=False)
                nc.tensor.matmul(oh, gram[c][:, unit(h, t), 128:256], Uo[:, t, f], start=t == 0, stop=False)
                mm = nc.tensor.matmul(oh, gram[c][:, unit(h, t), 384:512],
                                      rkv[:, t, ds(2 * D + P * p + DH * h, DH)], start=False, stop=True)
                if t == 1 and h == 1:
                    mm.then_inc(o_made.sem, 1)

            def step(p, b, tail=True, prep=True):
                c = 1 - b
                if tail:
                    rest(p - 1, c, 0)
                if prep:
                    decays(p + 1)
                below(p, b, 0)
                if tail:
                    solve(p - 1, c, 0)
                below(p, b, 1)
                if tail:
                    state(p - 1, c)
                    outputs(p - 1, c, 0, 0)
                grow(p, b, 1)
                below(p, b, 2)
                if tail:
                    outputs(p - 1, c, 0, 1)
                grow(p, b, 2)
                if tail:
                    rest(p - 1, c, 1)
                below(p, b, 3)
                if tail:
                    solve(p - 1, c, 1)
                grow(p, b, 3)
                below(p, b, 4)
                if tail:
                    for h in range(2):
                        outputs(p - 1, c, 1, h)
                grow(p, b, 4)
                if prep:
                    turn_ar(p + 1)
                below(p, b, 5)
                if prep:
                    turn_bk(p + 1, c)
                else:
                    output_gate(0)
                grow(p, b, 5)
                if prep:
                    grams(p + 1, c, (0, 1))
                below(p, b, 6)
                if prep:
                    grams(p + 1, c, (2, 3))
                grow(p, b, 6)

            def first():
                pe.wait_ge(*state_decay_ready.at(1))
                prepare = {0: lambda: decays(0), 2: lambda: turn_ar(0), 3: lambda: turn_bk(0, 0),
                           5: lambda: grams(0, 0, (0, 1)), 6: lambda: grams(0, 0, (2, 3))}
                for n in range(8):
                    if n < 4:
                        pe.wait_ge(*c_low.at(n + 1))
                    wide_quarter(pe, Q_CONV + n, n % 4, bank[2 * (n // 4):2 * (n // 4) + 2], t0h, t0l)
                    if n in prepare:
                        prepare[n]()
                pe.wait_ge(*conv_gated.at(4))
                step(0, 0, tail=False)

            def output_gate(h):
                if h:
                    pe.wait_ge(*turn_h.done(4))
                else:
                    pe.wait_ge(*gram_masked.at(4 * PAIRS))
                for t in range(NT):
                    nc.tensor.matmul(bank[4 + t][:, :], gT[:, t * P:(t + 1) * P], g2[:, 512 * h:512 * h + 512],
                                     start=True, stop=True).then_inc(g_made.sem, 1)

            def last():
                p = PAIRS - 1
                step(p, 1, prep=False)
                rest(p, 1, 0)
                solve(p, 1, 0)
                turn_h.pe(pe, [heads_gated.at(2)], (0, 1))
                state(p, 1)
                for h in range(2):
                    outputs(p, 1, 0, h)
                rest(p, 1, 1)
                solve(p, 1, 1)
                for h in range(2):
                    outputs(p, 1, 1, h)
                output_gate(1)
                pe.wait_ge(*y_masked.at(2 * LEV * PAIRS))
                pe.wait_ge(xt_copied, 2 * (LEV - 1) * PAIRS)
                for n in range(8):
                    if n < 4:
                        if n == 2:
                            turn_h.pe(pe, [heads_gated.at(4), pair_done.at(PAIRS), (uo_copied, 2 * PAIRS)], (2, 3))
                        pe.wait_ge(*turn_h.done(2 * n + 2))
                    wide_quarter(pe, Q_RWKV + n, n % 4, bank[2 * (n // 4):2 * (n // 4) + 2], t0h, t0l)

            step_loop(pe, first, step, last)

        def act_heads(act):
            def decays(p):
                act.wait_ge(cs_done, p + 1)
                cs = bank[4][:, 0:2 * P].rearrange("p (t s) -> p t s", t=NT)
                nc.scalar.activation(Rt, cs, ACT.Exp, scale=-S_DECAY).then_inc(pexp.sem, 1)
                nc.scalar.activation(Pi, cs, ACT.Exp, scale=S_DECAY).then_inc(pexp.sem, 1)

            def decays_before(p):
                act.wait_ge(pdiff, p + 1)
                nc.scalar.activation(At, At, ACT.Exp, scale=-S_DECAY).then_inc(pexp.sem, 1)

            def copy_ar(p, c):
                act.wait_ge(*hturned.at(2 * p + 1))
                nc.scalar.copy(AR[c].rearrange("p t a s -> p (t a s)"), bank[5][:, :]).then_inc(ft_copied.sem, 1)

            def copy_bk(p):
                act.wait_ge(*hturned.at(2 * p + 2))
                nc.scalar.copy(BK.rearrange("p a t s -> p (a t s)"), bank[4][:, :]).then_inc(ft_copied.sem, 1)

            def grown(p, b, lev):
                for g in range(2):
                    r = slice(2 * g, 2 * g + 2)
                    new = bank[2 + g][:, 0:2 * P].rearrange("p (a u n m) -> p a u n m", a=2, u=2, m=1 << lev)
                    act.wait_ge(x_made, 2 * (LEV - 1) * p + 2 * lev + g - 1)
                    if lev < LEV - 1:
                        nc.scalar.copy(halves(Xm[:, r, :], lev)[0], new[:, 0]).then_inc(xm_copied.sem, 1)
                    nc.scalar.copy(halves(XT[b][:, r, :], lev)[1], new[:, 1]).then_inc(xt_copied, 1)

            def copy_rest(p, t):
                act.wait_ge(*w_made.at(2 * p + t + 1))
                nc.scalar.mul(Wn[:, t, :], bank[6][:, 0:P], -1.0).then_inc(w_copied.sem, 1)

            def copy_u(p, t):
                act.wait_ge(*u_made.at(2 * p + t + 1))
                nc.scalar.copy(Uo[:, t, :], bank[6][:, P:2 * P]).then_inc(uo_copied, 1)

            def step(p, b, tail=True, prep=True):
                c = 1 - b
                if prep:
                    decays(p + 1)
                else:
                    nc.scalar.activation(early[:, 9:10], ident[:, 0:1], ACT.Sqrt)
                if tail:
                    copy_rest(p - 1, 0)
                    copy_u(p - 1, 0)
                grown(p, b, 1)
                if prep:
                    decays_before(p + 1)
                grown(p, b, 2)
                if tail:
                    copy_rest(p - 1, 1)
                    copy_u(p - 1, 1)
                grown(p, b, 3)
                if not prep:
                    head_roots(0)
                grown(p, b, 4)
                if prep:
                    copy_ar(p + 1, c)
                    copy_bk(p + 1)
                grown(p, b, 5)
                grown(p, b, 6)

            def first():
                act.wait_ge(*c_high.at(4))
                decays(0)
                split_high(act, Q_CONV + 4)
                decays_before(0)
                split_high(act, Q_CONV + 5)
                copy_ar(0, 0)
                split_high(act, Q_CONV + 6)
                copy_bk(0)
                split_high(act, Q_CONV + 7)
                for q in range(4):
                    split_high(act, Q_RWKV + q)
                step(0, 0, tail=False)

            def head_roots(h):
                act.wait_ge(head_var, h + 1)
                r = hvar[:, :, 8 * h:8 * h + 8]
                nc.scalar.activation(r, r, ACT.Sqrt).then_inc(head_root, 1)

            def last():
                p = PAIRS - 1
                step(p, 1, prep=False)
                copy_rest(p, 0)
                copy_u(p, 0)
                turn_h.act(act, Q_RWKV, range(4))
                copy_rest(p, 1)
                copy_u(p, 1)
                head_roots(1)

            step_loop(act, first, step, last)

        def pool_heads(pool):
            pool.wait_ge(rows_loaded, 48)
            with pool.Fori(0, PAIRS) as p:
                pool.wait_ge(*o_made.at(p + 1))
                v = rkv[:, :, ds(2 * D + P * p, P)]
                nc.gpsimd.tensor_tensor(by_head(v), by_head(v), per_head(hbonus[:, :, ds(2 * p, 2)]), ALU.mult
                                        ).then_inc(bonus_made, 1)
                pool.wait_ge(bonus_made, 2 * p + 1)
                nc.gpsimd.tensor_tensor(v, v, lnb[:, ds(P * p, P)].unsqueeze(1).to_broadcast([P, NT, P]), ALU.add
                                        ).then_inc(bonus_made, 1)

        def by_head(v, heads=2):
            return v.rearrange("p t (h d) -> p t h d", h=heads)

        def per_head(v, heads=2):
            return v.unsqueeze(3).to_broadcast([P, NT, heads, DH])

        HEAD_DVE = 16

        def dve_heads(dve, order):
            def of(v, p):
                return v[:, :, ds(2 * p, 2)]

            def cut(base, p):
                return rkv[:, :, ds(base + P * p, P)]

            def row_of(v, p):
                return v[:, ds(P * p, P)].unsqueeze(1).to_broadcast([P, NT, P])

            def differences(p):
                dve.wait_ge(*pexp.at(3 * p + 2))
                cs = bank[4][:, 0:2 * P].rearrange("p (t s) -> p t s", t=NT)
                nc.vector.tensor_tensor(At, cs, decay[:, :, ds(P * p, P)], ALU.subtract).then_inc(pdiff, 1)

            def key_direction(p):
                ka = row_of(ka_first if isinstance(p, int) and p == 0 else ka_row, p)
                order.mark(nc.vector.scalar_tensor_tensor(out=tmpb, in0=gain_a[:, :, ds(P * p, P)], scalar=-1.0,
                                                          in1=ka, op0=ALU.add, op1=ALU.mult))
                order.step(nc.vector.tensor_tensor(kkb, cut(D, p), row_of(kk_row, p), ALU.mult))
                order.step(nc.vector.tensor_tensor(by_head(kkb), by_head(kkb), per_head(of(kinv, p)), ALU.mult))

            def key_and_bonus(p, c):
                if not (isinstance(p, int) and p < 2):
                    dve.wait_ge(s_made, p - 1)
                r = cut(0, p)
                order.step(nc.vector.scalar_tensor_tensor(out=Kt[c], in0=tmpb, scalar=1.0, in1=cut(D, p), op0=ALU.add,
                                                          op1=ALU.mult))
                order.step(nc.vector.tensor_tensor(tmpb, r, Kt[c], ALU.mult))
                order.step(nc.vector.tensor_tensor(tmpb, tmpb, row_of(rk_row, p), ALU.mult))

            def make_ar(p):
                order.mark(nc.vector.tensor_reduce(of(hbonus, p), by_head(tmpb), AX.X, ALU.add))
                dve.wait_ge(*pexp.at(3 * p + 3))
                order.mark(nc.vector.tensor_tensor(Rt, cut(0, p), Rt, ALU.mult))
                nc.vector.tensor_tensor(At, kkb, At, ALU.mult).then_inc(tok_ready.sem, 1)

            def make_bk(p, c):
                order.mark(nc.vector.tensor_tensor(Kt[c], Kt[c], Pi, ALU.mult))
                dve.wait_ge(*tok_ready.at(2 * p + 1))
                order.step(nc.vector.tensor_tensor(kkb, kkb, gain_a[:, :, ds(P * p, P)], ALU.mult))
                nc.vector.tensor_tensor(Bt[c], kkb, Pi, ALU.mult).then_inc(tok_ready.sem, 1)

            def mask_grams(p, c, units):
                for u in units:
                    dve.wait_ge(*gram_done.at(4 * p + u + 1))
                    nc.vector.tensor_tensor(gram[c][:, u, :].rearrange("p (a m) -> p a m", a=2),
                                            bank[5 - u % 2][:, :].rearrange("p (a m) -> p a m", a=2),
                                            const[:, CONST["strict"][0]:CONST["tri"][1]].unsqueeze(1).to_broadcast(
                                                [P, 2, 2 * P]), ALU.mult).then_inc(gram_masked.sem, 1)
                    if u % 2:
                        g = slice(u - 1, u + 1)
                        dve.wait_ge(*gram_masked.at(4 * p + u + 1))
                        lt = gram[c][:, g, 0:P]
                        order.step(nc.vector.scalar_tensor_tensor(out=lt, in0=lt, scalar=-1.0,
                                                                  in1=ident.unsqueeze(1).to_broadcast([P, 2, P]),
                                                                  op0=ALU.mult, op1=ALU.add))
                        nc.vector.tensor_tensor(XT[c][:, g, :], lt, con("level0_t").unsqueeze(1).to_broadcast([P, 2, P]),
                                                ALU.mult).then_inc(inverse_begun, 1)

            def mask(p, lev):
                for g in range(2):
                    dve.wait_ge(y_made, 2 * LEV * p + 2 * lev + g + 1)
                    nc.vector.tensor_tensor((Xm if lev == 0 else Ym)[:, 2 * g:2 * g + 2, :],
                                            bank[g][:, 0:2 * P].rearrange("p (u s) -> p u s", u=2),
                                            con(f"level{lev}").unsqueeze(1).to_broadcast([P, 2, P]),
                                            ALU.mult).then_inc(y_masked.sem, 1)

            def state(p):
                dve.wait_ge(s_made, p + 1)
                nc.vector.scalar_tensor_tensor(out=SB, in0=bank[6][:, 256:384], scalar=sdec[:, ds(p, 1)],
                                               in1=con("heads"), op0=ALU.mult, op1=ALU.mult).then_inc(s_ready, 1)

            def centre(p):
                dve.wait_ge(*o_made.at(p + 1))
                o = bank[7][:, 0:2 * P].rearrange("p (t s) -> p t s", t=NT)
                mean = hmean.rearrange("p (t h) -> p t h", t=NT)
                order.step(nc.vector.tensor_reduce(mean, by_head(o), AX.X, ALU.add))
                order.step(nc.vector.tensor_scalar(hmean, hmean, 1.0 / DH, None, ALU.mult))
                nc.vector.tensor_tensor(by_head(cut(0, p)), by_head(o), per_head(mean), ALU.subtract
                                        ).then_inc(pair_done.sem, 1)
                dve.wait_ge(*pair_done.at(p + 1))
                order.step(nc.vector.tensor_tensor(centred_sq, cut(0, p), cut(0, p), ALU.mult))
                order.mark(nc.vector.tensor_reduce(of(hvar, p), by_head(centred_sq), AX.X, ALU.add))

            centred_sq = carve(10624, NT, P)

            def step(p, b, tail=True, prep=True):
                c = 1 - b
                mask(p, 0)
                if prep:
                    differences(p + 1)
                else:
                    variance(0)
                mask(p, 1)
                if prep:
                    key_direction(p + 1)
                if tail:
                    state(p - 1)
                mask(p, 2)
                if prep:
                    key_and_bonus(p + 1, c)
                mask(p, 3)
                if prep:
                    make_ar(p + 1)
                mask(p, 4)
                if prep:
                    make_bk(p + 1, c)
                else:
                    scale_heads(0)
                mask(p, 5)
                if tail:
                    centre(p - 1)
                if not prep:
                    gate_heads(0)
                if prep:
                    mask_grams(p + 1, c, (0, 1))
                mask(p, 6)
                if prep:
                    mask_grams(p + 1, c, (2, 3))

            def variance(h):
                order.settle()
                r = hvar[:, :, 8 * h:8 * h + 8]
                nc.vector.tensor_scalar(r, r, 1.0 / DH, 64e-5, ALU.mult, ALU.add).then_inc(head_var, 1)

            def scale_heads(h):
                f = slice(512 * h, 512 * h + 512)
                o, r = heads[:, :, f], hvar[:, :, 8 * h:8 * h + 8]
                dve.wait_ge(head_root, h + 1)
                order.step(nc.vector.reciprocal(r, r))
                order.step(nc.vector.tensor_tensor(by_head(o, NH // 2), by_head(o, NH // 2), per_head(r, NH // 2), ALU.mult))
                order.step(nc.vector.tensor_tensor(o, o, lng[:, f].unsqueeze(1).to_broadcast([P, NT, 512]), ALU.mult))

            def gate_heads(h):
                f = slice(512 * h, 512 * h + 512)
                dve.wait_ge(bonus_made, PAIRS * (h + 1))
                order.step(nc.vector.tensor_tensor(heads[:, :, f], heads[:, :, f], vbon[:, :, f], ALU.add))
                for t in range(NT):
                    dve.wait_ge(*g_made.at(2 * h + t + 1))
                    o = heads[:, t, f]
                    nc.vector.tensor_tensor(o, o, bank[4 + t][:, :], ALU.mult).then_inc(heads_gated.sem, 1)

            def gate_convolution(c):
                dve.wait_ge(quarter_done, Q_CONV + 4 * c + 4)
                for t in range(NT):
                    o = gates[:, t, D + c * TW:D + (c + 1) * TW]
                    nc.vector.tensor_tensor(o, o, bank[2 * c + t][:, :], ALU.mult).then_inc(conv_gated.sem, 1)

            def first():
                dve.wait_ge(*c_low.at(4))
                dve.wait_ge(rk_loaded, 32)
                differences(0)
                key_direction(0)
                key_and_bonus(0, 0)
                make_ar(0)
                make_bk(0, 0)
                dve.wait_ge(*evac2.at(NT * RKV2))
                gate_convolution(0)
                mask_grams(0, 0, (0, 1))
                mask_grams(0, 0, (2, 3))
                gate_convolution(1)
                dve.wait_ge(rows_loaded, 48)
                step(0, 0, tail=False)

            first()
            start = order.count()
            with dve.Fori(0, (PAIRS - 2) // 2) as u:
                order.body(start, u, 2 * HEAD_DVE)
                for c in (1, 0):
                    step(2 * u + (2 - c), c)
            order.after(start, (PAIRS - 2) // 2, 2 * HEAD_DVE)
            step(PAIRS - 1, 1, prep=False)
            state(PAIRS - 1)
            turn_h.dve(dve, range(4))
            centre(PAIRS - 1)
            variance(1)
            scale_heads(1)
            gate_heads(1)
            turn_h.dve(dve, range(4, 8))

        fing = carve(2 * D, D)
        sq = [carve(4096 + 512 * b, TW) for b in range(NT)]
        heads = rkv[:, :, 0:D]
        vbon = rkv[:, :, 2 * D:3 * D]
        merged2 = gates[:, :, 0:D]
        rows_loaded, fing_loaded = sem("rows_loaded"), sem("fing_loaded")
        g_made = Again(scattered, 4 * NG)
        heads_gated = Again(gate_used, 4)
        merged2_ready = Again(att_merged, 4)
        mixed2 = Again(mixed, 4)
        turn_h = Turn(heads, None, t0h, t0l, "p t (k f) -> p t f k")
        turn_o = Turn(merged2, None, t0h, t0l)
        norm_2 = RmsNorm(xres, carve(9216, NT, D), stat, 2)
        turn_f = Turn(carve(9216, NT, D), gain("norm_ff_g_2"), t0h, t0l)
        ff_relu = Again(silu_done, N_EXP)
        ff_squared = Again(hid_ready, 2 + N_EXP)
        ff_turned = Again(hid_turned, N_EXP)
        ff_high = Again(hid_high, N_EXP)
        ff_low = Again(hid_low, N_EXP)
        ff_added = Again(x_added, 4 * NG)
        norm_l = RmsNorm(xres, carve(9216, NT, D), stat, 2)

        def pe_out2(pe):
            turn_o.pe(pe, [merged2_ready.at(4)])
            square_product(pe, Q_OUT2, t0h, t0l, [merged2_ready.at(4)], turn_o)
            turn_f.pe(pe, [norm_2.ready()])
            pe.wait_ge(*turn_f.done())
            pe.wait_ge(*mixed2.at(4))

            def first(n, q, i=0, per=0):
                wide_quarter(pe, n, q, bank[0:2], t0h, t0l, TW, i, per)

            def turn(j):
                pe.wait_ge(*ff_squared.at(2 * j + 2))
                for b in range(2):
                    for cc in range(2):
                        for t in range(NT):
                            at = cc * SEQ + t * P
                            tr = nc.tensor.transpose(bank[2 + b][:, at:at + P],
                                                     sq[t].rearrange("p (f c) -> p f c", c=4)[:, :, 2 * b + cc], ident)
                    tr.then_inc(ff_turned.sem, 1)

            def second(n, c, j, i=0, per=0, last=False):
                if c == 0:
                    pe.wait_ge(*ff_low.at(2 * j + 2))
                wait_low(pe, n, i, per)
                s = n % RING
                for h in range(2):
                    f = slice(512 * h, 512 * h + 512)
                    for t in range(NT):
                        r = slice(t * P, (t + 1) * P)
                        o = bank[4 + 2 * h + t][:, :]
                        nc.tensor.matmul(o, t1h[:, c, r], whi[:, s, f], start=False, stop=False, skip_group_check=True)
                        nc.tensor.matmul(o, t1h[:, c, r], wlo[:, s, f], start=False, stop=False, skip_group_check=True)
                        mm = nc.tensor.matmul(o, t1l[:, c, r], whi[:, s, f], start=False, stop=last, skip_group_check=True)
                mm.then_inc(quarter_done, 1)

            for q in range(4):
                first(Q_FF + q, q)
            for b in range(4):
                nc.tensor.matmul(bank[4 + b][:, :].rearrange("p (k s) -> p k s", k=2), zero[:, :], t0h[:, 0:2, :],
                                 start=True, stop=False, skip_group_check=True)
            with pe.Fori(0, FF_J - 1) as j:
                for q in range(4):
                    if q == 0:
                        pe.wait_ge(*ff_relu.at(2 * j + 2))
                    first(Q_FF + 4 + q, q, j, 8)
                    if q == 1:
                        turn(j)
                for c in range(4):
                    second(Q_FF + 8 + c, c, j, j, 8)
            turn(FF_J - 1)
            for c in range(4):
                second(Q_END - 4 + c, c, FF_J - 1, last=c == 3)

        def sp_ff(sp):
            v1 = A["w_ff1_2"][0].rearrange("(p k) n -> p k n", k=KC)
            v2 = A["w_ff2_2"][0].rearrange("(j p c) n -> p j c n", j=FF_J, c=4)

            def first(n, q, j, i=0, per=0):
                load(sp, n, [(pair_view(raw, n, TW), v1[:, 2 * q:2 * q + 2, ds(TW * j, TW)])], i, per)

            def second(n, c, j, i=0, per=0):
                load(sp, n, [(raw[:, n % RING, :].rearrange("p (a c n) -> p a c n", a=1, c=1), v2[:, ds(j, 1), c:c + 1, :])],
                     i, per)

            for q in range(4):
                first(Q_FF + q, q, 0)
            with sp.Fori(0, FF_J - 1) as j:
                for q in range(4):
                    first(Q_FF + 4 + q, q, j + 1, j, 8)
                for c in range(4):
                    second(Q_FF + 8 + c, c, j, j, 8)
            for c in range(4):
                second(Q_END - 4 + c, c, FF_J - 1)

        def act_out2(act):
            act.wait_ge(*pair_done.at(PAIRS))
            act.dma_start(fing, row(A["norm_final_g_2"], D)).then_inc(fing_loaded, 16)
            turn_h.act(act, Q_RWKV, range(4, 8))
            for q in range(4, 8):
                split_high(act, Q_RWKV + q)
            for q in range(4):
                split_high(act, Q_OUT2 + q)
            turn_o.act(act, Q_OUT2)
            for q in range(4, 8):
                split_high(act, Q_OUT2 + q)
            norm_2.act_table(act)
            split_high(act, Q_FF)
            norm_2.act_squares(act, 0, lambda t: mixed2.at(t + 1))
            for q in range(1, 3):
                split_high(act, Q_FF + q)
            norm_2.act_squares(act, 1, lambda t: mixed2.at(NT + t + 1))
            split_high(act, Q_FF + 3)
            norm_2.act_root(act)
            turn_f.act(act, Q_FF)

            def relu():
                for t in range(NT):
                    nc.scalar.activation(sq[t], bank[t][:, :], ACT.Relu).then_inc(ff_relu.sem, 1)

            def high(j):
                for b in range(2):
                    act.wait_ge(*ff_turned.at(2 * j + b + 1))
                    nc.scalar.activation(t1h[:, 2 * b:2 * b + 2, :], bank[2 + b][:, :].rearrange("p (c s) -> p c s", c=2),
                                         ACT.Copy).then_inc(ff_high.sem, 1)

            for q in range(3):
                split_high(act, Q_FF + 4 + q)
            act.wait_ge(quarter_done, Q_FF + 4)
            relu()
            with act.Fori(0, FF_J - 1) as j:
                split_high(act, Q_FF + 7, j, 8)
                high(j)
                for c in range(4):
                    split_high(act, Q_FF + 8 + c, j, 8)
                    if c == 1:
                        act.wait_ge(quarter_done, Q_FF + 8 + 8 * j)
                        relu()
                for q in range(3):
                    split_high(act, Q_FF + 12 + q, j, 8)
            split_high(act, Q_END - 1)
            high(FF_J - 1)
            norm_l.act(act, lambda part, t: ff_added.at(NT * part + t + 1))

        def dve_out2(dve, order):
            for c in range(2):
                dve.wait_ge(quarter_done, Q_RWKV + 4 * c + 4)
                for t in range(NT):
                    o = merged2[:, t, c * TW:(c + 1) * TW]
                    order.step(nc.vector.tensor_tensor(o, o, bank[2 * c + t][:, :], ALU.mult))
                    nc.vector.tensor_tensor(o, o, gates[:, t, D + c * TW:D + (c + 1) * TW], ALU.add).then_inc(merged2_ready.sem, 1)
            turn_o.dve(dve)
            for c in range(2):
                dve.wait_ge(quarter_done, Q_OUT2 + 4 * c + 4)
                for t in range(NT):
                    o = xres[:, t, c * TW:(c + 1) * TW]
                    nc.vector.tensor_tensor(o, o, bank[2 * c + t][:, :], ALU.add).then_inc(mixed2.sem, 1)
            norm_2.dve(dve, order)
            turn_f.dve(dve)

            def ff(j):
                for t in range(NT):
                    dve.wait_ge(*ff_relu.at(2 * j + t + 1))
                    nc.vector.tensor_tensor(sq[t], sq[t], sq[t], ALU.mult).then_inc(ff_squared.sem, 1)
                for b in range(2):
                    dve.wait_ge(*ff_high.at(2 * j + b + 1))
                    nc.vector.tensor_tensor(t1l[:, 2 * b:2 * b + 2, :], bank[2 + b][:, :].rearrange("p (c s) -> p c s", c=2),
                                            t1h[:, 2 * b:2 * b + 2, :].bitcast(F32), ALU.subtract).then_inc(ff_low.sem, 1)

            with dve.Fori(0, FF_J) as j:
                ff(j)
            dve.wait_ge(quarter_done, Q_END)
            for h in range(2):
                for t in range(NT):
                    o = xres[:, t, 512 * h:512 * h + 512]
                    nc.vector.tensor_tensor(o, o, bank[4 + 2 * h + t][:, :], ALU.add).then_inc(ff_added.sem, 1)
            dve.wait_ge(fing_loaded, 16)
            norm_l.dve(dve, order, fing)

        block = ctx.enter_context(nc.Block())
        out_done = sem("out_done")

        @block.sync
        def _(sp):
            sp_block1(sp)
            sp_experts(sp)
            sp_overflow(sp)
            sp_ple(sp)
            sp_in2(sp)
            sp_ff(sp)
            for t in range(NT):
                sp.wait_ge(*norm_l.ready(t + 1))
                sp.dma_start(out[t * P:(t + 1) * P, :], xres[:, t, :]).then_inc(out_done, 16)
            sp.wait_ge(out_done, 16 * NT)

        @block.gpsimd
        def _(pool):
            pool_stream(pool)

        @block.scalar
        def _(act):
            act_loads(act)
            act.wait_ge(early_ready, 1)
            norm_a.act(act, lambda part, t: (x_loaded, 16))
            for q in range(2):
                split_high(act, Q_IN + q, width=2 * IN_TW)
            act.wait_ge(consts_loaded, 32)
            turn_a.act(act, 0)
            act_in(act)
            act_attention(act)
            router_loads(act)
            act_router(act)
            act_experts(act)
            act_overflow(act)
            act_ple(act)
            act_in2(act)
            act_conv(act)
            act_heads(act)
            act_out2(act)

        @block.vector
        def _(dve):
            order = Order(dve, dve_order)
            nc.vector.memset(early, 1.0).then_inc(early_ready, 1)
            norm_a.dve(dve, order)
            dve.wait_ge(consts_loaded, 32)
            turn_a.dve(dve)
            dve_ssd(dve, order)
            dve_attention(dve, order)
            dve_router(dve, order)
            dve_experts(dve)
            dve_overflow(dve)
            dve_ple(dve, order)
            dve_in2(dve, order)
            dve_conv(dve, order)
            dve_heads(dve, order)
            dve_out2(dve, order)

        @block.tensor
        def _(pe):
            pe_in(pe)
            pe_attention(pe)
            pe_router(pe)
            pe_experts(pe)
            pe_overflow(pe)
            pe_ple(pe)
            pe_in2(pe)
            pe_conv(pe)
            pe_heads(pe)
            pe_out2(pe)


def kernel(**inputs):
    import concourse.bacc as bacc
    from concourse.bass_utils import run_bass_kernel_spmd

    nc = bacc.Bacc("TRN2", target_bir_lowering=False, num_devices=1)
    arrays, views = {}, {}
    given = {name: np.ascontiguousarray(a) for name, a in inputs.items()}
    given["const"] = constants()
    for name, a in given.items():
        arrays["in_" + name] = a
        views[name] = nc.dram_tensor("in_" + name, a.shape, mybir.dt.from_np(a.dtype), kind="ExternalInput").ap()
    result = nc.dram_tensor("result", (SEQ, D), F32, kind="ExternalOutput").ap()
    build(nc, views, result)
    r = run_bass_kernel_spmd(nc, [arrays], core_ids=[0])
    return r.results[0]["result"].reshape(1, SEQ, D)
```
